# Optimizing a Trainium2 kernel written in Bass

```python
import math
import jax
import jax.numpy as jnp
from jax import lax
import numpy as np
import jax, jax.numpy as jnp

D_MODEL = 1024
BATCH = 1
SEQ = 256
DEPTH = 2

GRID_W = 64
CTX_LEN = 256
N_MIXERS = 3
N_MOD = 9
NORM_EPS = 1e-6
D_FF = 2816
FFT_GROUPS = 8
FFT_GROUP_W = D_MODEL // FFT_GROUPS
RET_HEADS = D_MODEL // 256
RET_DK = D_MODEL // RET_HEADS
RET_DV = 2 * RET_DK
RET_HK = RET_HEADS * RET_DK
RET_HV = RET_HEADS * RET_DV
RET_CHUNK = 128
ROPE_BASE = 10000.0
ROPE_FREQS = RET_DK // 4
S5_GROUP = 16
S5_GROUPS = D_MODEL // S5_GROUP
S5_STATE = 64
S5_DT_MIN = 0.001
S5_DT_MAX = 0.1
S5_C_STD = 0.5
N_FNET = (DEPTH + 2) // N_MIXERS
N_RET = (DEPTH + 1) // N_MIXERS
N_S5 = DEPTH // N_MIXERS


def _rmsnorm(h, g):
    h32 = h.astype(jnp.float32)
    y = h32 * lax.rsqrt(jnp.mean(h32 * h32, axis=-1, keepdims=True) + NORM_EPS)
    return (y * g.astype(jnp.float32)).astype(h.dtype)

def _modnorm(h, g, shift, scale):
    return _rmsnorm(h, g) * (1.0 + scale) + shift

def _ffn_half(h, g, shift, scale, gate, w_in, w_out):
    a, b = jnp.split(_modnorm(h, g, shift, scale) @ w_in, 2, axis=-1)
    return h + 0.5 * gate * ((jax.nn.silu(a) * b) @ w_out)

def _fourier_mixer(u, w_out):
    b, n, d = u.shape
    ug = u.astype(jnp.float32).reshape(b, n, FFT_GROUPS, FFT_GROUP_W)
    f = jnp.real(jnp.fft.fft2(ug, axes=(1, 3), norm='ortho'))
    return f.reshape(b, n, d).astype(u.dtype) @ w_out

def _heads(t, dh):
    b, n, _ = t.shape
    return jnp.swapaxes(t.reshape(b, n, -1, dh).astype(jnp.float32), 1, 2)

def _rotate(t, cos, sin):
    t1, t2 = jnp.split(t, 2, axis=-1)
    return jnp.concatenate([t1 * cos - t2 * sin, t2 * cos + t1 * sin], axis=-1)

def _rope_2d(t, rope):
    cos_r, sin_r, cos_c, sin_c = rope
    t_row, t_col = jnp.split(t, 2, axis=-1)
    return jnp.concatenate([_rotate(t_row, cos_r, sin_r), _rotate(t_col, cos_c, sin_c)], axis=-1)

def _ret_project(u, w_in, rope):
    q, k, v, g = jnp.split(u @ w_in, [RET_HK, 2 * RET_HK, 2 * RET_HK + RET_HV], axis=-1)
    q, k = _heads(q, RET_DK), _heads(k, RET_DK)
    if rope is not None:
        q, k = _rope_2d(q, rope), _rope_2d(k, rope)
    return q, k * RET_DK ** -0.5, _heads(v, RET_DV), g

def _ret_project_kv(u, w_in):
    k, v = jnp.split(u @ w_in[:, RET_HK:2 * RET_HK + RET_HV], [RET_HK], axis=-1)
    return _heads(k, RET_DK) * RET_DK ** -0.5, _heads(v, RET_DV)

def _ret_scan(q, k, v, log_gamma, s0, strict, reverse):
    if reverse:
        q, k, v = jnp.flip(q, 2), jnp.flip(k, 2), jnp.flip(v, 2)
    b, h, n, _ = q.shape
    dv = v.shape[-1]
    nc = n // RET_CHUNK

    def chunks(t):
        return jnp.moveaxis(t.reshape(b, h, nc, RET_CHUNK, t.shape[-1]), 2, 0)

    idx = jnp.arange(RET_CHUNK, dtype=jnp.float32)
    diff = idx[:, None] - idx[None, :]
    keep = diff > 0 if strict else diff >= 0
    intra = jnp.where(keep, jnp.exp(jnp.maximum(diff, 0.0)[None] * log_gamma[:, None, None]), 0.0)
    q_dec = jnp.exp((idx + 1.0)[None, :] * log_gamma[:, None])[None, :, :, None]
    k_dec = jnp.exp((RET_CHUNK - 1.0 - idx)[None, :] * log_gamma[:, None])[None, :, :, None]
    c_dec = jnp.exp(RET_CHUNK * log_gamma)[None, :, None, None]

    def step(s, qkv):
        qc, kc, vc = qkv
        scores = jnp.einsum('bhld,bhmd->bhlm', qc, kc) * intra
        o = jnp.einsum('bhlm,bhme->bhle', scores, vc) + jnp.einsum('bhld,bhde->bhle', qc * q_dec, s)
        s = c_dec * s + jnp.einsum('bhld,bhle->bhde', kc * k_dec, vc)
        return s, o

    s_fin, o = lax.scan(step, s0, (chunks(q), chunks(k), chunks(v)))
    o = jnp.moveaxis(o, 0, 2).reshape(b, h, n, dv)
    if reverse:
        o = jnp.flip(o, 2)
    return o, s_fin

def _ret_final_state(k, v, log_gamma, reverse):
    n = k.shape[2]
    pos = jnp.arange(n, dtype=jnp.float32)
    expo = pos if reverse else (n - 1.0) - pos
    w = jnp.exp(expo[None, :] * log_gamma[:, None])
    return jnp.einsum('bhnd,bhne,hn->bhde', k, v, w)

def _ret_out(o, g, w_out):
    mu = jnp.mean(o, axis=-1, keepdims=True)
    var = jnp.mean(jnp.square(o - mu), axis=-1, keepdims=True)
    o = (o - mu) * lax.rsqrt(var + NORM_EPS)
    b, h, n, dv = o.shape
    o = jnp.swapaxes(o, 1, 2).reshape(b, n, h * dv).astype(g.dtype)
    return (jax.nn.silu(g) * o) @ w_out

def _retention_mixer(u, uc, w_in, w_out, decay_logit, rope, need_ctx_out):
    log_gamma = jax.nn.log_sigmoid(decay_logit.astype(jnp.float32))
    q, k, v, g = _ret_project(u, w_in, rope)
    yc = None
    if need_ctx_out:
        qc, kc, vc, gc = _ret_project(uc, w_in, None)
        zero = jnp.zeros(kc.shape[:2] + (RET_DK, RET_DV), jnp.float32)
        oc_f, s_f = _ret_scan(qc, kc, vc, log_gamma[0], zero, False, False)
        oc_b, s_b = _ret_scan(qc, kc, vc, log_gamma[1], zero, True, True)
        yc = _ret_out(oc_f + oc_b, gc, w_out)
    else:
        kc, vc = _ret_project_kv(uc, w_in)
        s_f = _ret_final_state(kc, vc, log_gamma[0], False)
        s_b = _ret_final_state(kc, vc, log_gamma[1], True)
    o_f, _ = _ret_scan(q, k, v, log_gamma[0], s_f, False, False)
    o_b, _ = _ret_scan(q, k, v, log_gamma[1], s_b, True, True)
    return _ret_out(o_f + o_b, g, w_out), yc

def _lin_combine(left, right):
    a_l, b_l = left
    a_r, b_r = right
    return a_r * a_l, a_r * b_l + b_r

def _s5_discretise(lam_re, lam_im, log_dt, b_re, b_im):
    lam = lax.complex(lam_re.astype(jnp.float32), lam_im.astype(jnp.float32))
    dt = jnp.exp(log_dt.astype(jnp.float32))[:, None]
    a_bar = jnp.exp(lam * dt)
    b_bar = ((a_bar - 1.0) / lam)[..., None] * lax.complex(b_re.astype(jnp.float32),
                                                          b_im.astype(jnp.float32))
    return a_bar, b_bar

def _s5_drive(u, b_bar):
    b, n, _ = u.shape
    ug = u.astype(jnp.float32).reshape(b, n, S5_GROUPS, S5_GROUP)
    return lax.complex(jnp.einsum('bngc,gpc->nbgp', ug, jnp.real(b_bar)),
                       jnp.einsum('bngc,gpc->nbgp', ug, jnp.imag(b_bar)))

def _s5_scan(a_bar, bu, reverse):
    a = jnp.broadcast_to(a_bar, (bu.shape[0], 1) + a_bar.shape)
    _, h = lax.associative_scan(_lin_combine, (a, bu), reverse=reverse, axis=0)
    return h

def _s5_read(h, c_re, c_im):
    n, b = h.shape[:2]
    y = (jnp.einsum('gcp,nbgp->bngc', c_re, jnp.real(h))
         - jnp.einsum('gcp,nbgp->bngc', c_im, jnp.imag(h)))
    return y.reshape(b, n, D_MODEL)

def _s5_glu(y, w_glu, dtype):
    a, b = jnp.split(jax.nn.gelu(y).astype(dtype) @ w_glu, 2, axis=-1)
    return a * jax.nn.sigmoid(b)

def _s5_mixer(u, uc, lam_re, lam_im, log_dt, b_re, b_im, c_re, c_im, d_skip, w_glu, need_ctx_out):
    d32 = d_skip.astype(jnp.float32)
    y = u.astype(jnp.float32) * d32
    yc = uc.astype(jnp.float32) * d32 if need_ctx_out else None
    for dirn in range(2):
        reverse = dirn == 1
        a_bar, b_bar = _s5_discretise(lam_re[dirn], lam_im[dirn], log_dt[dirn], b_re[dirn], b_im[dirn])
        hc = _s5_scan(a_bar, _s5_drive(uc, b_bar), reverse)
        s_init = hc[0] if reverse else hc[-1]
        bu = _s5_drive(u, b_bar)
        bu = bu.at[-1 if reverse else 0].add(a_bar * s_init)
        hl = _s5_scan(a_bar, bu, reverse)
        cr, ci = c_re[dirn].astype(jnp.float32), c_im[dirn].astype(jnp.float32)
        y = y + _s5_read(hl, cr, ci)
        if need_ctx_out:
            yc = yc + _s5_read(hc, cr, ci)
    out = _s5_glu(y, w_glu, u.dtype)
    out_c = _s5_glu(yc, w_glu, uc.dtype) if need_ctx_out else None
    return out, out_c

def first_inputs(seed: int = 0) -> dict:
    key = jax.random.key(seed)
    ks = jax.random.split(key, 23)
    f32 = jnp.float32
    d = D_MODEL

    def nrm(k, shape, scale):
        return scale * jax.random.normal(k, shape, f32)

    g, p, cg = S5_GROUPS, S5_STATE, S5_GROUP
    base_logit = jnp.log(2.0 ** (5.0 + jnp.arange(RET_HEADS, dtype=f32)) - 1.0)
    return {
        'x': nrm(ks[0], (BATCH, SEQ, d), 1.0),
        'c': nrm(ks[1], (BATCH, d), 1.0),
        'ctx': nrm(ks[2], (BATCH, CTX_LEN, d), 1.0),
        'c_ctx': nrm(ks[3], (d,), 1.0),
        'w_mod': nrm(ks[4], (DEPTH, d, N_MOD * d), 0.5 * d ** -0.5),
        'b_mod': nrm(ks[5], (DEPTH, N_MOD * d), 0.02),
        'norm_g': 1.0 + nrm(ks[6], (DEPTH, 3, d), 0.02),
        'ffn_w_in': nrm(ks[7], (DEPTH, 2, d, 2 * D_FF), d ** -0.5),
        'ffn_w_out': nrm(ks[8], (DEPTH, 2, D_FF, d), D_FF ** -0.5),
        'fnet_w_out': nrm(ks[9], (N_FNET, d, d), d ** -0.5),
        'ret_w_in': nrm(ks[10], (N_RET, d, 2 * RET_HK + 2 * RET_HV), d ** -0.5),
        'ret_w_out': nrm(ks[11], (N_RET, RET_HV, d), RET_HV ** -0.5),
        'ret_decay_logit': base_logit + nrm(ks[12], (N_RET, 2, RET_HEADS), 0.1),
        's5_lam_re': -0.5 + nrm(ks[13], (N_S5, 2, g, p), 0.01),
        's5_lam_im': jnp.pi * jnp.arange(p, dtype=f32) + nrm(ks[14], (N_S5, 2, g, p), 0.01),
        's5_log_dt': jax.random.uniform(ks[15], (N_S5, 2, g), f32,
                                        math.log(S5_DT_MIN), math.log(S5_DT_MAX)),
        's5_b_re': nrm(ks[16], (N_S5, 2, g, p, cg), (2 * cg) ** -0.5),
        's5_b_im': nrm(ks[17], (N_S5, 2, g, p, cg), (2 * cg) ** -0.5),
        's5_c_re': nrm(ks[18], (N_S5, 2, g, cg, p), S5_C_STD),
        's5_c_im': nrm(ks[19], (N_S5, 2, g, cg, p), S5_C_STD),
        's5_d': nrm(ks[20], (N_S5, d), 1.0),
        's5_w_glu': nrm(ks[21], (N_S5, d, 2 * d), d ** -0.5),
        'final_norm_g': 1.0 + nrm(ks[22], (d,), 0.02),
    }

def first_block(x, c, ctx, c_ctx, w_mod, b_mod, norm_g, ffn_w_in, ffn_w_out, fnet_w_out,
              ret_w_in, ret_w_out, ret_decay_logit, s5_lam_re, s5_lam_im, s5_log_dt,
              s5_b_re, s5_b_im, s5_c_re, s5_c_im, s5_d, s5_w_glu, final_norm_g):
    bsz, n_lat, _ = x.shape
    rows = n_lat // GRID_W
    r_idx, c_idx = jnp.meshgrid(jnp.arange(rows, dtype=jnp.float32),
                                jnp.arange(GRID_W, dtype=jnp.float32), indexing='ij')
    inv_freq = jnp.exp(-math.log(ROPE_BASE) * jnp.arange(ROPE_FREQS, dtype=jnp.float32) / ROPE_FREQS)
    ang_r = r_idx.reshape(-1)[:, None] * inv_freq
    ang_c = c_idx.reshape(-1)[:, None] * inv_freq
    rope = (jnp.cos(ang_r), jnp.sin(ang_r), jnp.cos(ang_c), jnp.sin(ang_c))

    silu_c = jax.nn.silu(c)
    silu_cc = jax.nn.silu(c_ctx)
    h, hc = x, ctx
    for i in range(DEPTH):
        kind = i % N_MIXERS
        j = i // N_MIXERS
        last = i == DEPTH - 1
        ctx_used = (not last) or kind != 0
        m = (silu_c @ w_mod[i] + b_mod[i]).reshape(bsz, N_MOD, 1, D_MODEL)
        mc = (silu_cc @ w_mod[i] + b_mod[i]).reshape(N_MOD, D_MODEL)

        h = _ffn_half(h, norm_g[i, 0], m[:, 0], m[:, 1], m[:, 2], ffn_w_in[i, 0], ffn_w_out[i, 0])
        u = _modnorm(h, norm_g[i, 1], m[:, 3], m[:, 4])
        if ctx_used:
            hc = _ffn_half(hc, norm_g[i, 0], mc[0], mc[1], mc[2], ffn_w_in[i, 0], ffn_w_out[i, 0])
            uc = _modnorm(hc, norm_g[i, 1], mc[3], mc[4])

        if kind == 0:
            y = _fourier_mixer(u, fnet_w_out[j])
            yc = _fourier_mixer(uc, fnet_w_out[j]) if not last else None
        elif kind == 1:
            y, yc = _retention_mixer(u, uc, ret_w_in[j], ret_w_out[j], ret_decay_logit[j], rope, not last)
        else:
            y, yc = _s5_mixer(u, uc, s5_lam_re[j], s5_lam_im[j], s5_log_dt[j], s5_b_re[j], s5_b_im[j],
                              s5_c_re[j], s5_c_im[j], s5_d[j], s5_w_glu[j], not last)

        h = h + m[:, 5] * y
        h = _ffn_half(h, norm_g[i, 2], m[:, 6], m[:, 7], m[:, 8], ffn_w_in[i, 1], ffn_w_out[i, 1])
        if not last:
            hc = hc + mc[5] * yc
            hc = _ffn_half(hc, norm_g[i, 2], mc[6], mc[7], mc[8], ffn_w_in[i, 1], ffn_w_out[i, 1])
    return _rmsnorm(h, final_norm_g)


HEAD_DIM = 64
Q_BLOCK = 128

RWKV_HEADS = 8
RWKV_WIDTH = RWKV_HEADS * HEAD_DIM
RWKV_DECAY_RANK = 64
RWKV_ICLR_RANK = 64
RWKV_GATE_RANK = 128
RWKV_GN_EPS = 64e-5

NSA_Q_HEADS = 8
NSA_KV_GROUPS = 2
NSA_CMP_LEN = 32
NSA_CMP_STRIDE = 16
NSA_CMP_HIDDEN = 256
NSA_SEL_BLOCK = 64
NSA_SEL_TOPN = 16
NSA_WINDOW = 512
NSA_FORCE_SCORE = 1e9

SWA_Q_HEADS = 8
SWA_KV_HEADS = 2
SWA_WINDOW = 128

REL_BUCKETS = 32
REL_MAX_DIST = 128

PEER_HEADS = 8
PEER_NKEYS = 128
PEER_EXPERTS = PEER_NKEYS * PEER_NKEYS
PEER_QDIM = 256
PEER_TOPK = 16
PEER_TOK_BLOCK = 128

RWKV_SPLITS = (RWKV_WIDTH, RWKV_WIDTH, RWKV_WIDTH, RWKV_DECAY_RANK, RWKV_ICLR_RANK, RWKV_GATE_RANK)
NSA_SPLITS = (NSA_Q_HEADS * HEAD_DIM,) + (NSA_KV_GROUPS * HEAD_DIM,) * 6 + (NSA_Q_HEADS * 3,)
SWA_SPLITS = (SWA_Q_HEADS * HEAD_DIM, SWA_KV_HEADS * HEAD_DIM, SWA_KV_HEADS * HEAD_DIM)
GATE_SPLITS = (D_MODEL, D_MODEL, D_MODEL)
RWKV_COLS = sum(RWKV_SPLITS)
IN_SPLITS = RWKV_SPLITS + NSA_SPLITS + SWA_SPLITS + GATE_SPLITS
IN_COLS = sum(IN_SPLITS)


def split_cols(z, sizes):
    cuts = [int(c) for c in np.cumsum(sizes)[:-1]]
    return jnp.split(z, cuts, axis=-1)

def rmsnorm(x, w):
    xf = x.astype(jnp.float32)
    y = xf * lax.rsqrt(jnp.mean(xf * xf, axis=-1, keepdims=True) + NORM_EPS)
    return (y * w.astype(jnp.float32)).astype(x.dtype)

def token_shift(z, mu):
    z_prev = jnp.pad(z, ((0, 0), (1, 0), (0, 0)))[:, :-1]
    return z + mu * (z_prev - z)

def t5_bucket(dist):
    n = jnp.maximum(dist, 0)
    max_exact = REL_BUCKETS // 2
    nf = jnp.maximum(n, max_exact).astype(jnp.float32)
    large = max_exact + (jnp.log(nf / max_exact) / math.log(REL_MAX_DIST / max_exact)
                         * (REL_BUCKETS - max_exact)).astype(jnp.int32)
    large = jnp.minimum(large, REL_BUCKETS - 1)
    return jnp.where(n < max_exact, n, large)

def masked_softmax(s, mask):
    s = jnp.where(mask, s.astype(jnp.float32), -jnp.inf)
    m = jnp.max(s, axis=-1, keepdims=True)
    m = jnp.where(jnp.isfinite(m), m, 0.0)
    e = jnp.exp(s - m)
    return e / jnp.maximum(jnp.sum(e, axis=-1, keepdims=True), 1e-30)

def sink_softmax(s, mask, sink):
    s = jnp.where(mask, s.astype(jnp.float32), -jnp.inf)
    sink = sink.astype(jnp.float32)[None, :, :, None, None]
    m = jnp.maximum(jnp.max(s, axis=-1, keepdims=True), sink)
    e = jnp.exp(s - m)
    return e / (jnp.sum(e, axis=-1, keepdims=True) + jnp.exp(sink - m))

def rwkv7_mixer(zr, zk, zv, zw, za, zg, w0, w2, a0, a2, g2, k_k, k_a, r_k, ln_w, ln_b):
    B, S, C = zr.shape
    H, N = RWKV_HEADS, HEAD_DIM
    f32 = jnp.float32
    log_w = -jax.nn.softplus(-(w0 + jnp.tanh(zw) @ w2)) - 0.5
    decay = jnp.exp(-jnp.exp(log_w.astype(f32)))
    a = jax.nn.sigmoid(a0 + za @ a2)
    g = jax.nn.sigmoid(zg) @ g2
    kk = (zk * k_k).reshape(B, S, H, N).astype(f32)
    kk = kk * lax.rsqrt(jnp.maximum(jnp.sum(kk * kk, axis=-1, keepdims=True), 1e-12))
    k = zk * (1.0 + (a - 1.0) * k_a)
    hd = lambda z: z.reshape(B, S, H, N).astype(f32)
    r_h, k_h, v_h, a_h, w_h = hd(zr), hd(k), hd(zv), hd(a), hd(decay)
    tm = lambda z: jnp.swapaxes(z, 0, 1)

    def step(state, inp):
        r_t, w_t, k_t, v_t, kk_t, a_t = inp
        sa = jnp.einsum('bhij,bhj->bhi', state, -kk_t)
        state = (state * w_t[:, :, None, :] + sa[..., None] * (kk_t * a_t)[:, :, None, :]
                 + v_t[..., None] * k_t[:, :, None, :])
        return state, jnp.einsum('bhij,bhj->bhi', state, r_t)

    s0 = jnp.zeros((B, H, N, N), f32)
    _, y = lax.scan(step, s0, (tm(r_h), tm(w_h), tm(k_h), tm(v_h), tm(kk), tm(a_h)))
    y = tm(y)
    mu = jnp.mean(y, axis=-1, keepdims=True)
    var = jnp.mean(jnp.square(y - mu), axis=-1, keepdims=True)
    y = ((y - mu) * lax.rsqrt(var + RWKV_GN_EPS)).reshape(B, S, C) * ln_w + ln_b
    bonus = jnp.sum(r_h * k_h * r_k, axis=-1, keepdims=True) * v_h
    out = (y + bonus.reshape(B, S, C)) * g
    return out.astype(zr.dtype)

def nsa_compress(z, pe, w1, w2):
    B, S, G, dh = z.shape
    n_sub = NSA_CMP_LEN // NSA_CMP_STRIDE
    chunks = z.reshape(B, S // NSA_CMP_STRIDE, NSA_CMP_STRIDE, G, dh)
    n_cmp = S // NSA_CMP_STRIDE - n_sub + 1
    blocks = jnp.concatenate([chunks[:, j:j + n_cmp] for j in range(n_sub)], axis=2)
    blocks = blocks + pe[None, None, :, None, :]
    flat = blocks.transpose(0, 3, 1, 2, 4).reshape(B, G, n_cmp, NSA_CMP_LEN * dh)
    return jax.nn.gelu(flat @ w1, approximate=False) @ w2

def nsa_mixer(q, kc, vc, ks, vs, kw, vw, gates, pe_k, pe_v, ck_w1, ck_w2, cv_w1, cv_w2, bias_tbl):
    B, S, _ = q.shape
    G, Hg, dh = NSA_KV_GROUPS, NSA_Q_HEADS // NSA_KV_GROUPS, HEAD_DIM
    scale = dh ** -0.5
    heads = lambda z: z.reshape(B, S, G, dh)
    kv_t = lambda z: heads(z).transpose(0, 2, 1, 3)
    qh = q.reshape(B, S, G, Hg, dh).transpose(0, 2, 3, 1, 4)
    gh = jax.nn.sigmoid(gates.reshape(B, S, G, Hg, 3)).transpose(0, 2, 3, 1, 4)

    k_cmp = nsa_compress(heads(kc), pe_k, ck_w1, ck_w2)
    v_cmp = nsa_compress(heads(vc), pe_v, cv_w1, cv_w2)
    n_cmp = k_cmp.shape[2]
    cmp_start = jnp.arange(n_cmp) * NSA_CMP_STRIDE
    cmp_end = cmp_start + NSA_CMP_LEN - 1
    n_sel = S // NSA_SEL_BLOCK
    sel_start = jnp.arange(n_sel) * NSA_SEL_BLOCK
    overlap = ((cmp_end[:, None] >= sel_start[None, :])
               & (cmp_start[:, None] <= sel_start[None, :] + NSA_SEL_BLOCK - 1)).astype(jnp.float32)
    ks_blk = kv_t(ks).reshape(B, G, n_sel, NSA_SEL_BLOCK, dh)
    vs_blk = kv_t(vs).reshape(B, G, n_sel, NSA_SEL_BLOCK, dh)
    pad = ((0, 0), (0, 0), (NSA_WINDOW, 0), (0, 0))
    kw_pad = jnp.pad(kv_t(kw), pad)
    vw_pad = jnp.pad(kv_t(vw), pad)

    tbl = bias_tbl.T.reshape(G, Hg, REL_BUCKETS)
    win_len = NSA_WINDOW + Q_BLOCK
    rel = jnp.arange(Q_BLOCK)[:, None] + NSA_WINDOW - jnp.arange(win_len)[None, :]
    win_bias = tbl[:, :, t5_bucket(rel)]
    win_rel_mask = (rel >= 0) & (rel < NSA_WINDOW)
    top_n = min(NSA_SEL_TOPN, n_sel)
    b_ix = jnp.arange(B)[:, None, None, None]
    g_ix = jnp.arange(G)[None, :, None, None]
    g_ix5 = jnp.arange(G)[None, :, None, None, None]
    h_ix5 = jnp.arange(Hg)[None, None, :, None, None]
    blk = jnp.arange(n_sel)

    def block(i):
        s0 = i * Q_BLOCK
        t = s0 + jnp.arange(Q_BLOCK)
        qb = lax.dynamic_slice_in_dim(qh, s0, Q_BLOCK, axis=3)
        gb = lax.dynamic_slice_in_dim(gh, s0, Q_BLOCK, axis=3)
        sc = jnp.einsum('bghqd,bgcd->bghqc', qb, k_cmp) * scale
        pc = masked_softmax(sc, cmp_end[None, :] <= t[:, None])
        o_cmp = jnp.einsum('bghqc,bgcd->bghqd', pc.astype(v_cmp.dtype), v_cmp)
        imp = jnp.einsum('bghqc,cn->bgqn', pc, overlap)
        cur = t // NSA_SEL_BLOCK
        forced = (blk[None, :] == 0) | (blk[None, :] == cur[:, None]) | (blk[None, :] == cur[:, None] - 1)
        valid = blk[None, :] <= cur[:, None]
        imp = jnp.where(forced, NSA_FORCE_SCORE, jnp.where(valid, imp, -1.0))
        _, sel = lax.top_k(imp, top_n)
        k_sel = ks_blk[b_ix, g_ix, sel].reshape(B, G, Q_BLOCK, top_n * NSA_SEL_BLOCK, dh)
        v_sel = vs_blk[b_ix, g_ix, sel].reshape(B, G, Q_BLOCK, top_n * NSA_SEL_BLOCK, dh)
        pos = (sel[..., None] * NSA_SEL_BLOCK + jnp.arange(NSA_SEL_BLOCK)).reshape(B, G, Q_BLOCK, top_n * NSA_SEL_BLOCK)
        dist = t[:, None] - pos
        bias = tbl[g_ix5, h_ix5, t5_bucket(dist)[:, :, None]]
        ss = jnp.einsum('bghqd,bgqkd->bghqk', qb, k_sel) * scale + bias
        ps = masked_softmax(ss, (dist >= 0)[:, :, None])
        o_sel = jnp.einsum('bghqk,bgqkd->bghqd', ps.astype(v_sel.dtype), v_sel)
        k_win = lax.dynamic_slice_in_dim(kw_pad, s0, win_len, axis=2)
        v_win = lax.dynamic_slice_in_dim(vw_pad, s0, win_len, axis=2)
        kpos = s0 - NSA_WINDOW + jnp.arange(win_len)
        sw = jnp.einsum('bghqd,bgkd->bghqk', qb, k_win) * scale + win_bias
        pw = masked_softmax(sw, win_rel_mask & (kpos >= 0)[None, :])
        o_win = jnp.einsum('bghqk,bgkd->bghqd', pw.astype(v_win.dtype), v_win)
        return gb[..., 0:1] * o_cmp + gb[..., 1:2] * o_sel + gb[..., 2:3] * o_win

    out = lax.map(block, jnp.arange(S // Q_BLOCK))
    return out.transpose(1, 0, 4, 2, 3, 5).reshape(B, S, G * Hg * dh)

def swa_sink_mixer(q, k, v, sinks, bias_tbl):
    B, S, _ = q.shape
    G, Hg, dh = SWA_KV_HEADS, SWA_Q_HEADS // SWA_KV_HEADS, HEAD_DIM
    scale = dh ** -0.5
    qh = q.reshape(B, S, G, Hg, dh).transpose(0, 2, 3, 1, 4)
    pad = ((0, 0), (0, 0), (SWA_WINDOW, 0), (0, 0))
    k_pad = jnp.pad(k.reshape(B, S, G, dh).transpose(0, 2, 1, 3), pad)
    v_pad = jnp.pad(v.reshape(B, S, G, dh).transpose(0, 2, 1, 3), pad)
    win_len = SWA_WINDOW + Q_BLOCK
    rel = jnp.arange(Q_BLOCK)[:, None] + SWA_WINDOW - jnp.arange(win_len)[None, :]
    bias = bias_tbl.T.reshape(G, Hg, REL_BUCKETS)[:, :, t5_bucket(rel)]
    rel_mask = (rel >= 0) & (rel < SWA_WINDOW)
    sink = sinks.reshape(G, Hg)

    def block(i):
        s0 = i * Q_BLOCK
        qb = lax.dynamic_slice_in_dim(qh, s0, Q_BLOCK, axis=3)
        kb = lax.dynamic_slice_in_dim(k_pad, s0, win_len, axis=2)
        vb = lax.dynamic_slice_in_dim(v_pad, s0, win_len, axis=2)
        kpos = s0 - SWA_WINDOW + jnp.arange(win_len)
        s = jnp.einsum('bghqd,bgkd->bghqk', qb, kb) * scale + bias
        p = sink_softmax(s, rel_mask & (kpos >= 0)[None, :], sink)
        return jnp.einsum('bghqk,bgkd->bghqd', p.astype(vb.dtype), vb)

    out = lax.map(block, jnp.arange(S // Q_BLOCK))
    return out.transpose(1, 0, 4, 2, 3, 5).reshape(B, S, G * Hg * dh)

def peer_ffn(z, wq, subkeys, u_tab, v_tab):
    B, S, D = z.shape
    Hp, K, half = PEER_HEADS, PEER_TOPK, PEER_QDIM // 2
    zt = z.reshape(B * S // PEER_TOK_BLOCK, PEER_TOK_BLOCK, D)

    def block(zb):
        q = (zb @ wq).reshape(PEER_TOK_BLOCK, Hp, 2, half)
        s = jnp.einsum('thpd,hpnd->thpn', q, subkeys).astype(jnp.float32)
        s_top, i_top = lax.top_k(s, K)
        cand = (s_top[:, :, 0, :, None] + s_top[:, :, 1, None, :]).reshape(PEER_TOK_BLOCK, Hp, K * K)
        score, flat = lax.top_k(cand, K)
        i1 = jnp.take_along_axis(i_top[:, :, 0], flat // K, axis=-1)
        i2 = jnp.take_along_axis(i_top[:, :, 1], flat % K, axis=-1)
        expert = i1 * PEER_NKEYS + i2
        gate = jax.nn.softmax(score, axis=-1)
        h = jnp.einsum('thkd,td->thk', u_tab[expert], zb).astype(jnp.float32)
        act = (gate * jax.nn.gelu(h, approximate=False)).astype(zb.dtype)
        return jnp.einsum('thk,thkd->td', act, v_tab[expert])

    return lax.map(block, zt).reshape(B, S, D)

def second_inputs(seed: int = 0) -> dict:
    key = jax.random.key(seed)
    keys = iter(jax.random.split(key, 40))
    L, D = DEPTH, D_MODEL

    def nrm(shape, scale):
        return jax.random.normal(next(keys), shape, jnp.float32) * scale

    def unif(shape, lo, hi):
        return jax.random.uniform(next(keys), shape, jnp.float32, lo, hi)

    cmp_in = NSA_CMP_LEN * HEAD_DIM
    return {
        'x': nrm((BATCH, SEQ, D), 1.0),
        'ln1_w': 1.0 + nrm((L, D), 0.02),
        'ln2_w': 1.0 + nrm((L, D), 0.02),
        'lnf_w': 1.0 + nrm((D,), 0.02),
        'rel_bias': nrm((REL_BUCKETS, NSA_Q_HEADS + SWA_Q_HEADS), 0.3),
        'w_in': nrm((L, D, IN_COLS), D ** -0.5),
        'rwkv_mu': unif((L, RWKV_COLS), 0.0, 1.0),
        'rwkv_w0': -0.5 + nrm((L, RWKV_WIDTH), 0.5),
        'rwkv_w2': nrm((L, RWKV_DECAY_RANK, RWKV_WIDTH), 0.1),
        'rwkv_a0': nrm((L, RWKV_WIDTH), 0.3),
        'rwkv_a2': nrm((L, RWKV_ICLR_RANK, RWKV_WIDTH), 0.1),
        'rwkv_g2': nrm((L, RWKV_GATE_RANK, RWKV_WIDTH), RWKV_GATE_RANK ** -0.5),
        'rwkv_k_k': 0.85 + nrm((L, RWKV_WIDTH), 0.05),
        'rwkv_k_a': 1.0 + nrm((L, RWKV_WIDTH), 0.05),
        'rwkv_r_k': nrm((L, RWKV_HEADS, HEAD_DIM), 0.1),
        'rwkv_ln_w': 1.0 + nrm((L, RWKV_WIDTH), 0.02),
        'rwkv_ln_b': nrm((L, RWKV_WIDTH), 0.02),
        'nsa_pe_k': nrm((L, NSA_CMP_LEN, HEAD_DIM), 0.1),
        'nsa_pe_v': nrm((L, NSA_CMP_LEN, HEAD_DIM), 0.1),
        'nsa_ck_w1': nrm((L, cmp_in, NSA_CMP_HIDDEN), cmp_in ** -0.5),
        'nsa_ck_w2': nrm((L, NSA_CMP_HIDDEN, HEAD_DIM), NSA_CMP_HIDDEN ** -0.5),
        'nsa_cv_w1': nrm((L, cmp_in, NSA_CMP_HIDDEN), cmp_in ** -0.5),
        'nsa_cv_w2': nrm((L, NSA_CMP_HIDDEN, HEAD_DIM), NSA_CMP_HIDDEN ** -0.5),
        'swa_sinks': nrm((L, SWA_Q_HEADS), 0.5),
        'w_br_a': nrm((L, RWKV_WIDTH, D), RWKV_WIDTH ** -0.5),
        'w_br_b': nrm((L, NSA_Q_HEADS * HEAD_DIM, D), (NSA_Q_HEADS * HEAD_DIM) ** -0.5),
        'w_br_c': nrm((L, SWA_Q_HEADS * HEAD_DIM, D), (SWA_Q_HEADS * HEAD_DIM) ** -0.5),
        'w_out': nrm((L, D, D), D ** -0.5),
        'peer_wq': nrm((L, D, PEER_HEADS * PEER_QDIM), D ** -0.5),
        'peer_subkeys': nrm((L, PEER_HEADS, 2, PEER_NKEYS, PEER_QDIM // 2), (PEER_QDIM // 2) ** -0.5),
        'peer_u': nrm((L, PEER_EXPERTS, D), D ** -0.5),
        'peer_v': nrm((L, PEER_EXPERTS, D), 0.5 * PEER_HEADS ** -0.5),
    }

def second_block(x, ln1_w, ln2_w, lnf_w, rel_bias, w_in, rwkv_mu, rwkv_w0, rwkv_w2, rwkv_a0, rwkv_a2,
              rwkv_g2, rwkv_k_k, rwkv_k_a, rwkv_r_k, rwkv_ln_w, rwkv_ln_b, nsa_pe_k, nsa_pe_v,
              nsa_ck_w1, nsa_ck_w2, nsa_cv_w1, nsa_cv_w2, swa_sinks, w_br_a, w_br_b, w_br_c, w_out,
              peer_wq, peer_subkeys, peer_u, peer_v):
    nsa_tbl = rel_bias[:, :NSA_Q_HEADS]
    swa_tbl = rel_bias[:, NSA_Q_HEADS:]
    for l in range(DEPTH):
        u = rmsnorm(x, ln1_w[l])
        proj = u @ w_in[l]
        rw = token_shift(proj[..., :RWKV_COLS], rwkv_mu[l])
        zr, zk, zv, zw, za, zg = split_cols(rw, RWKV_SPLITS)
        cols = split_cols(proj[..., RWKV_COLS:], NSA_SPLITS + SWA_SPLITS + GATE_SPLITS)
        nq, nkc, nvc, nks, nvs, nkw, nvw, ngate = cols[:8]
        sq, sk, sv = cols[8:11]
        g_a, g_b, g_c = [jax.nn.sigmoid(c) for c in cols[11:14]]
        o_a = rwkv7_mixer(zr, zk, zv, zw, za, zg, rwkv_w0[l], rwkv_w2[l], rwkv_a0[l], rwkv_a2[l],
                          rwkv_g2[l], rwkv_k_k[l], rwkv_k_a[l], rwkv_r_k[l], rwkv_ln_w[l], rwkv_ln_b[l])
        o_b = nsa_mixer(nq, nkc, nvc, nks, nvs, nkw, nvw, ngate, nsa_pe_k[l], nsa_pe_v[l],
                        nsa_ck_w1[l], nsa_ck_w2[l], nsa_cv_w1[l], nsa_cv_w2[l], nsa_tbl)
        o_c = swa_sink_mixer(sq, sk, sv, swa_sinks[l], swa_tbl)
        merged = g_a * (o_a @ w_br_a[l]) + g_b * (o_b @ w_br_b[l]) + g_c * (o_c @ w_br_c[l])
        x = x + merged @ w_out[l]
        x = x + peer_ffn(rmsnorm(x, ln2_w[l]), peer_wq[l], peer_subkeys[l], peer_u[l], peer_v[l])
    return rmsnorm(x, lnf_w)


def setup_inputs(seed=0):
    out = dict(first_inputs(seed))
    for name, value in second_inputs(seed + 1).items():
        if name != "x":
            out[name + "_2"] = value
    return out


def reference(
    x, c, ctx, c_ctx, w_mod, b_mod, norm_g, ffn_w_in, ffn_w_out, fnet_w_out, ret_w_in,
    ret_w_out, ret_decay_logit, s5_lam_re, s5_lam_im, s5_log_dt, s5_b_re, s5_b_im, s5_c_re,
    s5_c_im, s5_d, s5_w_glu, final_norm_g, ln1_w_2, ln2_w_2, lnf_w_2, rel_bias_2, w_in_2,
    rwkv_mu_2, rwkv_w0_2, rwkv_w2_2, rwkv_a0_2, rwkv_a2_2, rwkv_g2_2, rwkv_k_k_2, rwkv_k_a_2,
    rwkv_r_k_2, rwkv_ln_w_2, rwkv_ln_b_2, nsa_pe_k_2, nsa_pe_v_2, nsa_ck_w1_2, nsa_ck_w2_2,
    nsa_cv_w1_2, nsa_cv_w2_2, swa_sinks_2, w_br_a_2, w_br_b_2, w_br_c_2, w_out_2, peer_wq_2,
    peer_subkeys_2, peer_u_2, peer_v_2,
):
    x = first_block(
        x, c, ctx, c_ctx, w_mod, b_mod, norm_g, ffn_w_in, ffn_w_out, fnet_w_out, ret_w_in,
        ret_w_out, ret_decay_logit, s5_lam_re, s5_lam_im, s5_log_dt, s5_b_re, s5_b_im, s5_c_re,
        s5_c_im, s5_d, s5_w_glu, final_norm_g,
    )
    return second_block(
        x, ln1_w_2, ln2_w_2, lnf_w_2, rel_bias_2, w_in_2, rwkv_mu_2, rwkv_w0_2, rwkv_w2_2,
        rwkv_a0_2, rwkv_a2_2, rwkv_g2_2, rwkv_k_k_2, rwkv_k_a_2, rwkv_r_k_2, rwkv_ln_w_2,
        rwkv_ln_b_2, nsa_pe_k_2, nsa_pe_v_2, nsa_ck_w1_2, nsa_ck_w2_2, nsa_cv_w1_2, nsa_cv_w2_2,
        swa_sinks_2, w_br_a_2, w_br_b_2, w_br_c_2, w_out_2, peer_wq_2, peer_subkeys_2, peer_u_2,
        peer_v_2,
    )


_drawn_inputs = setup_inputs


def setup_inputs(seed=0):
    import zlib

    import numpy as np

    out = dict(_drawn_inputs(seed))
    spreads = {}
    factors = {'norm_g': 2.728,
     'ln2_w_2': 3.001,
     'lnf_w_2': 2.851,
     'rwkv_k_k_2': 5.284,
     'rwkv_ln_w_2': 4.086,
     'rwkv_ln_b_2': 3.875,
     'nsa_pe_k_2': 6.996,
     'swa_sinks_2': 5.882}
    for name, (base, spread) in spreads.items():
        noise = np.random.default_rng([zlib.crc32(name.encode()), seed]).standard_normal(out[name].shape)
        drawn = base * np.exp(spread * noise) if base else spread * noise
        out[name] = jnp.asarray(drawn.astype(out[name].dtype))
    for name, factor in factors.items():
        out[name] = (out[name] * factor).astype(out[name].dtype)
    return out
```

```python
import math
from contextlib import ExitStack

import numpy as np
import concourse.bass as bass
from concourse import mybir

F32 = mybir.dt.float32
U32 = mybir.dt.uint32
ACT = mybir.ActivationFunctionType
ALU = mybir.AluOpType
AX = mybir.AxisListType

P = 128
D = 1024
N = 256
KD = D // P
NT = N // P
DEPTH = 2
N_MOD = 9
EPS = 1e-6
FF = 2816
KF = FF // P
TPB = 16
RING = 4
ARENA = 38900

RH, RDK, RDV = 4, 256, 512
DH = 64
GN_EPS = 64e-5
HEADS = 8
CH = 32
NCH = N // CH
CMP_LEN, CMP_STRIDE = 32, 16
NCMP = N // CMP_STRIDE - CMP_LEN // CMP_STRIDE + 1
NEG = -1e30
BUCKETS, MAX_DIST = 32, 128
SWA_WINDOW = 128
NKEYS = 128
TOPK = 16
BIASW = 384

VEC = {}
_n = 0
for _name, _w in [("cond", 2 * KD), ("b_mod", DEPTH * 72), ("norm_g", DEPTH * 3 * KD), ("final_g", KD),
                  ("ln1", DEPTH * KD), ("ln2", DEPTH * KD), ("lnf", KD), ("mu", DEPTH * 14),
                  ("w0", DEPTH * 4), ("a0", DEPTH * 4), ("k_k", DEPTH * 4), ("k_a", DEPTH * 4),
                  ("r_k", DEPTH * 4), ("ln_w", DEPTH * 4), ("ln_b", DEPTH * 4), ("pe", DEPTH * 32),
                  ("decay", 8), ("sinks", DEPTH * 8)]:
    VEC[_name] = (_n, _n + _w)
    _n += _w
NVEC = _n

BLOCKS = {"mod": 36, "ffn_in": KF, "ffn_out": KF // 2, "fnet": KD // 2, "ret_in": 24, "ret_out": 8,
          "in2": 28, "cmp1": 4, "cmp2": 1, "rwkv": 1, "branch": 6, "out2": 4, "wq": 8, "keys": 1,
          "experts": NKEYS}


def columns(table, name, layer=0, width=None):
    a, b = VEC[name]
    if width is None:
        return table[:, a:b]
    return table[:, a + layer * width:a + (layer + 1) * width]


class Signals:

    def __init__(self, nc, ctx):
        self.nc, self.ctx, self.sems, self.total = nc, ctx, {}, {}

    def __call__(self, name, n):
        if name not in self.sems:
            self.sems[name] = self.ctx.enter_context(self.nc.semaphore(name))
            self.total[name] = 0
        base = self.total[name]
        self.total[name] += n
        return Share(self.sems[name], base)


class Share:
    def __init__(self, sem, base):
        self.sem, self.base = sem, base

    def at(self, k):
        return self.base + k


class Link:

    def __init__(self, eng, sem):
        self.eng, self.sem, self.n = eng, sem, 0

    def __call__(self, ins):
        self.n += 1
        ins.then_inc(self.sem, 1)
        self.eng.wait_ge(self.sem, self.n)


class Chip:

    def __init__(self, nc, ctx, io):
        self.nc, self.io = nc, io
        sb = lambda name, shape, dt=F32: ctx.enter_context(nc.sbuf_tensor(name, shape, dt))
        self.signals = Signals(nc, ctx)
        self.ring = sb("ring", [P, RING, TPB, P])
        self.x = sb("x", [P, KD, 2 * N])
        self.arena = sb("arena", [P, ARENA])
        self.vec = sb("vec", [P, NVEC])
        self.cst = sb("cst", [P, 4, P])
        self.ident, self.ones = self.cst[:, 0, :], self.cst[:, 1, :]
        self.headones, self.iota = self.cst[:, 2, :], self.cst[:, 3, :]
        self.mods = sb("mods", [P, N_MOD, KD, 2])
        self.ps = ctx.enter_context(nc.psum_tensor("ps", [P, 8, 512], F32))
        self.loaded = [ctx.enter_context(nc.semaphore(f"block_loaded{i}")) for i in range(RING)]
        self.block_done = ctx.enter_context(nc.semaphore("block_done"))
        self.stage_done = ctx.enter_context(nc.semaphore("stage_done"))
        self.inputs_loaded = ctx.enter_context(nc.semaphore("inputs_loaded"))
        self.links = {e: ctx.enter_context(nc.semaphore(f"{e}_link")) for e in ("act", "dve", "pool")}
        self.n_blocks = 0
        self.n_stages = 0

    def at(self, start, *shape):
        size = int(np.prod(shape))
        assert start + size <= ARENA, (start, shape)
        v = self.arena[:, start:start + size]
        names = "abcd"[:len(shape)]
        if len(shape) > 1:
            v = v.rearrange(f"p ({' '.join(names)}) -> p {' '.join(names)}", **dict(zip(names, shape)))
        return v


class Stage:

    blocks = 0

    def __init__(self, chip):
        self.chip, self.nc = chip, chip.nc
        self.index = chip.n_stages
        chip.n_stages += 1
        self.b0 = chip.n_blocks
        chip.n_blocks += self.blocks

    def arrival(self, j):
        b = self.b0 + j
        return b % RING, 16 * (b // RING + 1)

    def block_count(self, j):
        return self.b0 + j + 1

    def pe(self, pe):
        pass

    def act(self, act, link):
        pass

    def dve(self, dve, link):
        pass

    def pool(self, pool, link):
        pass


A_CST1 = 0
CST1 = {"dft": (0, 256), "cosn": (256, 512), "sinn": (768, 512), "perm": (1280, 128),
        "rope_cos": (1408, 512), "rope_sin": (1920, 512), "expo": (2432, 2048)}
NCST1 = 4480
A_U = NCST1
A_SQ = A_U + KD * 2 * N
A_SMALL = A_SQ + KD * 2 * N
A_WORK = A_SMALL + 3 * 2 * N


class Start(Stage):

    def __init__(self, chip):
        super().__init__(chip)
        self.row = chip.signals("bias_rows", 16)
        self.copied = chip.signals("bias_copied", 16)
        self.stored = chip.signals("bias_stored", 16)
        self.rows = chip.at(A_WORK, 16, BIASW)
        self.lhs = chip.at(A_WORK + 16 * BIASW, 16, P)
        self.hot = chip.at(A_WORK + 16 * BIASW + 16 * P, BIASW)

    def pe(self, pe):
        pe.wait_ge(self.chip.inputs_loaded, 16 * N_INPUT_DMAS)
        for h in range(16):
            if h >= 8:
                pe.wait_ge(self.copied.sem, self.copied.at(h - 7))
            self.nc.tensor.matmul(self.chip.ps[:, h % 8, 0:BIASW], self.lhs[0:34, h, :], self.hot[0:34, :],
                                  start=True, stop=True).then_inc(self.row.sem, 1)

    def act(self, act, link):
        act.wait_ge(self.chip.inputs_loaded, 16 * N_INPUT_DMAS)
        for h in range(16):
            act.wait_ge(self.row.sem, self.row.at(h + 1))
            self.nc.scalar.activation(self.rows[:, h, :], self.chip.ps[:, h % 8, 0:BIASW], ACT.Copy)\
                .then_inc(self.copied.sem, 1)
        act.wait_ge(self.copied.sem, self.copied.at(16))
        act.dma_start(self.chip.io["bias_scratch"], self.rows).then_inc(self.stored.sem, 16)
        act.wait_ge(self.stored.sem, self.stored.at(16))
        act.sem_inc(self.chip.stage_done, 1)

    def dve(self, dve, link):
        dve.wait_ge(self.chip.inputs_loaded, 16 * N_INPUT_DMAS)


class Modulation(Stage):

    blocks = BLOCKS["mod"]

    def __init__(self, chip, layer):
        super().__init__(chip)
        self.layer = layer
        self.silu = chip.signals("cond_ready", 1)
        self.cond = chip.at(A_WORK, KD, 2)

    def act(self, act, link):
        act.wait_ge(self.chip.stage_done, self.index)
        v = columns(self.chip.vec, "cond").rearrange("p (k s) -> p k s", s=2)
        self.nc.scalar.activation(self.cond, v, ACT.Silu).then_inc(self.silu.sem, 1)

    def pe(self, pe):
        pe.wait_ge(self.chip.stage_done, self.index)
        pe.wait_ge(self.silu.sem, self.silu.at(1))
        out = self.chip.ps[:, 0, 0:144].rearrange("p (m s) -> p m s", s=2)
        for j in range(self.blocks):
            slot, count = self.arrival(j)
            pe.wait_ge(self.chip.loaded[slot], count)
            w = self.chip.ring[:, slot]
            for e in range(2):
                for k in range(KD):
                    last = self.nc.tensor.matmul(out[:, 2 * j + e, :], w[:, e * KD + k, :], self.cond[:, k, :],
                                                 start=k == 0, stop=k == KD - 1)
            last.then_inc(self.chip.block_done, 1)

    def dve(self, dve, link):
        c, nc = self.chip, self.nc
        dve.wait_ge(self.chip.stage_done, self.index)
        dve.wait_ge(self.chip.block_done, self.block_count(self.blocks - 1))
        m = c.mods[:].rearrange("p j d s -> p (j d) s")
        b = columns(c.vec, "b_mod", self.layer, 72).unsqueeze(2).broadcast_to([P, 72, 2])
        link(nc.vector.tensor_tensor(m, c.ps[:, 0, 0:144].rearrange("p (m s) -> p m s", s=2), b, ALU.add))
        for n in range(3):
            g = columns(c.vec, "norm_g", 3 * self.layer + n, KD).unsqueeze(2).broadcast_to([P, KD, 2])
            scale, gate = c.mods[:, 3 * n + 1, :, :], c.mods[:, 3 * n + 2, :, :]
            link(nc.vector.tensor_scalar(scale, scale, 1.0, None, ALU.add))
            link(nc.vector.tensor_tensor(scale, scale, g, ALU.mult))
            if n != 1:
                link(nc.vector.tensor_scalar(gate, gate, 0.5, None, ALU.mult))
        dve.sem_inc(c.stage_done, 1)


class Norm(Stage):

    def __init__(self, chip, out, sq, small, tokens, mod=None, gain=None):
        super().__init__(chip)
        self.t, self.mod, self.gain = tokens, mod, gain
        self.u, self.sq = out, sq
        self.ms, self.rt, self.rstd = small
        self.squared = chip.signals("squared", 4)
        self.summed = chip.signals("squares_summed", 1)
        self.mean = chip.signals("mean_square_ready", 1)
        self.root = chip.signals("root_ready", 1)
        self.parts = [(d, s) for d in range(KD) for s in range(tokens // N)]
        self.scaled = chip.signals("scaled", len(self.parts))

    def act(self, act, link):
        c, nc = self.chip, self.nc
        act.wait_ge(self.chip.stage_done, self.index)
        for d in range(0, KD, 2):
            nc.scalar.activation(self.sq[:, d:d + 2, :], c.x[:, d:d + 2, 0:self.t], ACT.Square)\
                .then_inc(self.squared.sem, 1)
        act.wait_ge(self.mean.sem, self.mean.at(1))
        nc.scalar.activation(self.rt, self.ms, ACT.Sqrt).then_inc(self.root.sem, 1)
        if self.mod is not None:
            for i, (d, s) in enumerate(self.parts):
                act.wait_ge(self.scaled.sem, self.scaled.at(i + 1))
                at = self.u[:, d, s * N:(s + 1) * N]
                last = nc.scalar.activation(at, at, ACT.Identity, bias=c.mods[:, 3 * self.mod, d, s:s + 1])
            last.then_inc(self.chip.stage_done, 1)

    def pe(self, pe):
        pe.wait_ge(self.chip.stage_done, self.index)
        for d in range(KD):
            if d % 2 == 0:
                pe.wait_ge(self.squared.sem, self.squared.at(d // 2 + 1))
            last = self.nc.tensor.matmul(self.chip.ps[:, 0, 0:self.t], self.chip.ones, self.sq[:, d, :],
                                         start=d == 0, stop=d == KD - 1)
        last.then_inc(self.summed.sem, 1)

    def dve(self, dve, link):
        c, nc = self.chip, self.nc
        dve.wait_ge(self.chip.stage_done, self.index)
        dve.wait_ge(self.summed.sem, self.summed.at(1))
        nc.vector.tensor_scalar(self.ms, c.ps[:, 0, 0:self.t], 1.0 / D, EPS, ALU.mult, ALU.add)\
            .then_inc(self.mean.sem, 1)
        dve.wait_ge(self.root.sem, self.root.at(1))
        link(nc.vector.reciprocal(self.rstd, self.rt))
        for d, s in self.parts:
            cols = slice(s * N, (s + 1) * N)
            gain = self.gain[:, d:d + 1] if self.mod is None else c.mods[:, 3 * self.mod + 1, d, s:s + 1]
            last = nc.vector.scalar_tensor_tensor(self.u[:, d, cols], c.x[:, d, cols], gain, self.rstd[:, cols],
                                                  ALU.mult, ALU.mult)
            if self.mod is not None:
                last.then_inc(self.scaled.sem, 1)
        if self.mod is None:
            last.then_inc(self.chip.stage_done, 1)


def first_norm(chip, tokens, mod):
    small = [chip.at(A_SMALL + i * 2 * N, 2 * N)[:, 0:tokens] for i in range(3)]
    return Norm(chip, chip.at(A_U, KD, 2 * N)[:, :, 0:tokens], chip.at(A_SQ, KD, 2 * N)[:, :, 0:tokens], small,
                tokens, mod=mod)


class FeedForwardIn(Stage):

    blocks = BLOCKS["ffn_in"]

    def __init__(self, chip, tokens):
        super().__init__(chip)
        self.t = tokens
        self.u = chip.at(A_U, KD, 2 * N)[:, :, 0:tokens]
        self.silu = chip.at(A_SQ, 2, 2 * N)[:, :, 0:tokens]
        self.h = chip.at(A_WORK, KF, 2 * N)[:, :, 0:tokens]
        self.silu_ready = chip.signals("silu_ready", KF)
        self.h_ready = chip.signals("hidden_ready", KF)

    def pe(self, pe):
        pe.wait_ge(self.chip.stage_done, self.index)
        for j in range(KF):
            slot, count = self.arrival(j)
            pe.wait_ge(self.chip.loaded[slot], count)
            w = self.chip.ring[:, slot]
            if j >= 2:
                pe.wait_ge(self.h_ready.sem, self.h_ready.at(j - 1))
            for half in range(2):
                for k in range(KD):
                    last = self.nc.tensor.matmul(self.chip.ps[:, 2 * (j % 2) + half, 0:self.t], w[:, half * KD + k, :],
                                                 self.u[:, k, :], start=k == 0, stop=k == KD - 1)
            last.then_inc(self.chip.block_done, 1)

    def act(self, act, link):
        act.wait_ge(self.chip.stage_done, self.index)
        for j in range(KF):
            act.wait_ge(self.chip.block_done, self.block_count(j))
            if j >= 2:
                act.wait_ge(self.h_ready.sem, self.h_ready.at(j - 1))
            self.nc.scalar.activation(self.silu[:, j % 2, :], self.chip.ps[:, 2 * (j % 2), 0:self.t], ACT.Silu)\
                .then_inc(self.silu_ready.sem, 1)

    def dve(self, dve, link):
        dve.wait_ge(self.chip.stage_done, self.index)
        for j in range(KF):
            dve.wait_ge(self.silu_ready.sem, self.silu_ready.at(j + 1))
            last = self.nc.vector.tensor_tensor(self.h[:, j, :], self.chip.ps[:, 2 * (j % 2) + 1, 0:self.t],
                                                self.silu[:, j % 2, :], ALU.mult)
            last.then_inc(self.h_ready.sem, 1)
        dve.wait_ge(self.h_ready.sem, self.h_ready.at(KF))
        dve.sem_inc(self.chip.stage_done, 1)


class Project(Stage):

    def __init__(self, chip, inp, tiles, tokens, gate=None):
        self.blocks = tiles // 2
        super().__init__(chip)
        self.inp, self.t, self.gate = inp, tokens, gate

    def pe(self, pe):
        pe.wait_ge(self.chip.stage_done, self.index)
        for j in range(self.blocks):
            slot, count = self.arrival(j)
            pe.wait_ge(self.chip.loaded[slot], count)
            w = self.chip.ring[:, slot]
            for k in range(2):
                for m in range(KD):
                    last = self.nc.tensor.matmul(self.chip.ps[:, m, 0:self.t], w[:, k * KD + m, :], self.inp[:, 2 * j + k, :],
                                                 start=j == 0 and k == 0, stop=j == self.blocks - 1 and k == 1)
            last.then_inc(self.chip.block_done, 1)

    def dve(self, dve, link):
        c = self.chip
        dve.wait_ge(self.chip.stage_done, self.index)
        dve.wait_ge(self.chip.block_done, self.block_count(self.blocks - 1))
        for m in range(KD):
            for s in range(self.t // N):
                cols = slice(s * N, (s + 1) * N)
                gate = 1.0 if self.gate is None else c.mods[:, self.gate, m, s:s + 1]
                last = self.nc.vector.scalar_tensor_tensor(c.x[:, m, cols], c.ps[:, m, cols], gate, c.x[:, m, cols],
                                                           ALU.mult, ALU.add)
        last.then_inc(self.chip.stage_done, 1)


def feed_forward(chip, tokens, mod):
    return [first_norm(chip, tokens, mod), FeedForwardIn(chip, tokens),
            Project(chip, chip.at(A_WORK, KF, 2 * N)[:, :, 0:tokens], KF, tokens, gate=3 * mod + 2)]


class Fourier(Stage):

    def __init__(self, chip):
        super().__init__(chip)
        cst = chip.at(A_CST1, NCST1)
        self.dft = cst[:, 0:256]
        self.cosn = cst[:, 256:768].rearrange("p (t n) -> p t n", t=NT)
        self.sinn = cst[:, 768:1280].rearrange("p (t n) -> p t n", t=NT)
        self.u = chip.at(A_U, KD, 2 * N)
        self.half = chip.at(A_WORK, 4, NT, 2 * P)
        self.f = chip.at(A_WORK + 4 * NT * 2 * P, KD, 2 * N)
        n = 2 * KD
        self.by_feature = chip.signals("dft_by_feature", n)
        self.half_ready = chip.signals("dft_half_ready", n)
        self.by_token = chip.signals("dft_by_token", n)
        self.kept = chip.signals("dft_kept", n)

    def pe(self, pe):
        pe.wait_ge(self.chip.stage_done, self.index)
        ps, n = self.chip.ps, 2 * KD

        def along_features(i):
            s, g = divmod(i, KD)
            if i >= 4:
                pe.wait_ge(self.half_ready.sem, self.half_ready.at(i - 3))
            for t in range(NT):
                last = self.nc.tensor.matmul(ps[:, i % 4, t * 256:(t + 1) * 256],
                                             self.u[:, g, s * N + t * P:s * N + (t + 1) * P], self.dft,
                                             start=True, stop=True)
            last.then_inc(self.by_feature.sem, 1)

        def along_tokens(i):
            pe.wait_ge(self.half_ready.sem, self.half_ready.at(i + 1))
            if i >= 4:
                pe.wait_ge(self.kept.sem, self.kept.at(i - 3))
            for t in range(NT):
                self.nc.tensor.matmul(ps[:, 4 + i % 4, 0:N], self.half[:, i % 4, t, 0:P], self.cosn[:, t, :],
                                      start=t == 0, stop=False)
                last = self.nc.tensor.matmul(ps[:, 4 + i % 4, 0:N], self.half[:, i % 4, t, P:2 * P], self.sinn[:, t, :],
                                             start=False, stop=t == NT - 1)
            last.then_inc(self.by_token.sem, 1)

        along_features(0)
        for i in range(n):
            if i + 1 < n:
                along_features(i + 1)
            along_tokens(i)

    def act(self, act, link):
        act.wait_ge(self.chip.stage_done, self.index)
        for i in range(2 * KD):
            act.wait_ge(self.by_feature.sem, self.by_feature.at(i + 1))
            if i >= 4:
                act.wait_ge(self.by_token.sem, self.by_token.at(i - 3))
            self.nc.scalar.activation(self.half[:, i % 4].rearrange("p t c -> p (t c)"), self.chip.ps[:, i % 4, :], ACT.Copy)\
                .then_inc(self.half_ready.sem, 1)

    def dve(self, dve, link):
        dve.wait_ge(self.chip.stage_done, self.index)
        for i in range(2 * KD):
            s, g = divmod(i, KD)
            dve.wait_ge(self.by_token.sem, self.by_token.at(i + 1))
            last = self.nc.vector.tensor_copy(self.f[:, g, s * N:(s + 1) * N], self.chip.ps[:, 4 + i % 4, 0:N])
            last.then_inc(self.kept.sem, 1)
        dve.wait_ge(self.kept.sem, self.kept.at(2 * KD))
        dve.sem_inc(self.chip.stage_done, 1)


R_Q = A_SQ
R_K = R_Q + KD * N
R_V = R_K + KD * 2 * N
R_G = R_V + 4 * RH * RDV
R_O = R_G + 16 * N
R_D = R_O + 16 * N
R_TMP = R_D + RH * 4 * N
R_LG = R_TMP + 2 * 512


class Retention(Stage):

    blocks = BLOCKS["ret_in"]

    def __init__(self, chip):
        super().__init__(chip)
        at, sig = chip.at, chip.signals
        cst = at(A_CST1, NCST1)
        self.perm = cst[:, 1280:1408]
        self.cos = cst[:, 1408:1920].rearrange("p (a n) -> p a n", a=2)
        self.sin = cst[:, 1920:2432].rearrange("p (a n) -> p a n", a=2)
        self.expo = cst[:, 2432:4480].rearrange("p (e n) -> p e n", e=4)
        self.u = at(A_U, KD, 2 * N)
        self.q, self.k = at(R_Q, KD, N), at(R_K, KD, 2 * N)
        self.v = at(R_V, 4, RH * RDV)
        self.g, self.o = at(R_G, 16, N), at(R_O, 16, N)
        self.d = at(R_D, RH, 4 * N)
        self.tmp = at(R_TMP, 2, 512)
        self.lg = at(R_LG, 4, 8)
        self.p = at(A_U, 2, 4 * N)
        self.sq = at(A_U, 16, N)
        self.st = at(R_Q, 3, RH * N)
        self.q_kept = sig("ret_q_kept", 4)
        self.k_kept = sig("ret_k_kept", 4)
        self.turned = sig("ret_turned", 16)
        self.rope_done = sig("ret_rope_done", 16)
        self.v_kept = sig("ret_v_kept", 16)
        self.g_kept = sig("ret_g_kept", 8)
        self.lg_exp = sig("ret_lg_exp", 1)
        self.lg_in = sig("ret_lg_in", 1)
        self.lg_out = sig("ret_lg_out", 1)
        self.d_in = sig("ret_d_in", RH)
        self.d_exp = sig("ret_d_exp", RH)
        self.scores = sig("ret_scores", RH)
        self.weighted = sig("ret_weighted", RH)
        self.o_sum = sig("ret_o_sum", RH)
        self.o_kept = sig("ret_o_kept", RH)
        self.mean = sig("ret_mean", 1)
        self.centred = sig("ret_centred", 1)
        self.squares = sig("ret_squares", 1)
        self.var = sig("ret_var", 1)
        self.var_in = sig("ret_var_in", 1)
        self.root = sig("ret_root", 1)

    def pe(self, pe):
        nc, ps = self.nc, self.chip.ps
        pe.wait_ge(self.chip.stage_done, self.index)
        for j in range(4):
            slot, count = self.arrival(j)
            pe.wait_ge(self.chip.loaded[slot], count)
            w = self.chip.ring[:, slot]
            for e in range(2):
                for k in range(KD):
                    last = nc.tensor.matmul(ps[:, j, e * N:(e + 1) * N], w[:, e * KD + k, :], self.u[:, k, 0:N],
                                            start=k == 0, stop=k == KD - 1)
            last.then_inc(self.chip.block_done, 1)
        for j in range(4):
            slot, count = self.arrival(4 + j)
            pe.wait_ge(self.chip.loaded[slot], count)
            w = self.chip.ring[:, slot]
            if j >= 2:
                pe.wait_ge(self.k_kept.sem, self.k_kept.at(j - 1))
            for e in range(2):
                for k in range(KD):
                    last = nc.tensor.matmul(ps[:, 4 + 2 * (j % 2) + e, :], w[:, e * KD + k, :], self.u[:, k, :],
                                            start=k == 0, stop=k == KD - 1)
            last.then_inc(self.chip.block_done, 1)
        pe.wait_ge(self.q_kept.sem, self.q_kept.at(4))
        pe.wait_ge(self.k_kept.sem, self.k_kept.at(4))
        for i in range(16):
            if i >= 4:
                pe.wait_ge(self.rope_done.sem, self.rope_done.at(i - 3))
            t = self.q[:, i, :] if i < KD else self.k[:, i - KD, 0:N]
            nc.tensor.matmul(ps[:, i % 4, 0:N], self.perm, t, start=True, stop=True).then_inc(self.turned.sem, 1)
        pe.wait_ge(self.rope_done.sem, self.rope_done.at(16))
        for h in range(RH):
            if h >= 2:
                pe.wait_ge(self.v_kept.sem, self.v_kept.at(4 * (h - 1)))
            for j in range(2):
                slot, count = self.arrival(8 + 2 * h + j)
                pe.wait_ge(self.chip.loaded[slot], count)
                w = self.chip.ring[:, slot]
                for t in range(4):
                    for k in range(4):
                        last = nc.tensor.matmul(ps[:, 4 * (h % 2) + t, :], self.u[:, 4 * j + k, t * P:(t + 1) * P],
                                                w[:, 4 * k:4 * k + 4, :], start=j == 0 and k == 0, stop=j == 1 and k == 3)
                last.then_inc(self.chip.block_done, 1)
        pe.wait_ge(self.v_kept.sem, self.v_kept.at(16))
        for j in range(8):
            slot, count = self.arrival(16 + j)
            pe.wait_ge(self.chip.loaded[slot], count)
            w = self.chip.ring[:, slot]
            if j >= 4:
                pe.wait_ge(self.g_kept.sem, self.g_kept.at(j - 3))
            for e in range(2):
                for k in range(KD):
                    last = nc.tensor.matmul(ps[:, j % 4, e * N:(e + 1) * N], w[:, e * KD + k, :], self.u[:, k, 0:N],
                                            start=k == 0, stop=k == KD - 1)
            last.then_inc(self.chip.block_done, 1)
        pe.wait_ge(self.g_kept.sem, self.g_kept.at(8))
        for h in range(RH):
            if h >= 1:
                pe.wait_ge(self.weighted.sem, self.weighted.at(h))
            for m in range(4):
                for e in range(2):
                    last = nc.tensor.matmul(ps[:, m // 2, (m % 2) * N:(m % 2 + 1) * N],
                                            self.k[:, 2 * h + e, m * P:(m + 1) * P], self.q[:, 2 * h + e, :],
                                            start=e == 0, stop=e == 1)
            last.then_inc(self.scores.sem, 1)
            pe.wait_ge(self.weighted.sem, self.weighted.at(h + 1))
            if h >= 1:
                pe.wait_ge(self.o_kept.sem, self.o_kept.at(h))
            for e in range(4):
                for m in range(4):
                    last = nc.tensor.matmul(ps[:, 2 + e // 2, (e % 2) * N:(e % 2 + 1) * N],
                                            self.v[:, m, h * RDV + e * P:h * RDV + (e + 1) * P],
                                            self.p[:, h % 2, m * N:(m + 1) * N], start=m == 0, stop=m == 3)
            last.then_inc(self.o_sum.sem, 1)
        pe.wait_ge(self.o_kept.sem, self.o_kept.at(RH))
        for h in range(RH):
            for e in range(4):
                last = nc.tensor.matmul(ps[:, 4 + h // 2, (h % 2) * N:(h % 2 + 1) * N], self.chip.ones, self.o[:, 4 * h + e, :],
                                        start=e == 0, stop=e == 3)
        last.then_inc(self.mean.sem, 1)
        pe.wait_ge(self.squares.sem, self.squares.at(1))
        for h in range(RH):
            for e in range(4):
                last = nc.tensor.matmul(ps[:, 6 + h // 2, (h % 2) * N:(h % 2 + 1) * N], self.chip.ones, self.sq[:, 4 * h + e, :],
                                        start=e == 0, stop=e == 3)
        last.then_inc(self.var.sem, 1)

    def act(self, act, link):
        nc, ps = self.nc, self.chip.ps
        act.wait_ge(self.chip.stage_done, self.index)
        for j in range(4):
            act.wait_ge(self.chip.block_done, self.block_count(j))
            nc.scalar.activation(self.q[:, 2 * j:2 * j + 2, :].rearrange("p a n -> p (a n)"), ps[:, j, :], ACT.Copy)\
                .then_inc(self.q_kept.sem, 1)
        for j in range(4):
            act.wait_ge(self.chip.block_done, self.block_count(4 + j))
            b = 4 + 2 * (j % 2)
            nc.scalar.activation(self.k[:, 2 * j:2 * j + 2, :], ps[:, b:b + 2, :], ACT.Copy, scale=RDK ** -0.5)\
                .then_inc(self.k_kept.sem, 1)
        act.wait_ge(self.lg_in.sem, self.lg_in.at(1))
        nc.scalar.activation(self.lg[:, 1, :], self.lg[:, 0, :], ACT.Exp, scale=-1.0).then_inc(self.lg_exp.sem, 1)
        act.wait_ge(self.lg_out.sem, self.lg_out.at(1))
        for h in range(RH):
            act.wait_ge(self.d_in.sem, self.d_in.at(h + 1))
            nc.scalar.activation(self.d[:, h, 0:512], self.d[:, h, 0:512], ACT.Exp)
            nc.scalar.activation(self.d[:, h, 512:1024], self.expo[:, 2, :], ACT.Exp, scale=self.lg[:, 3, h:h + 1])
            nc.scalar.activation(self.tmp[:, h % 2, :], self.expo[:, 3, :], ACT.Exp, scale=self.lg[:, 3, 4 + h:5 + h])\
                .then_inc(self.d_exp.sem, 1)
        for h in range(RH):
            act.wait_ge(self.chip.block_done, self.block_count(8 + 2 * h + 1))
            for t in range(4):
                nc.scalar.activation(self.v[:, t, h * RDV:(h + 1) * RDV], ps[:, 4 * (h % 2) + t, :], ACT.Copy)\
                    .then_inc(self.v_kept.sem, 1)
        for j in range(8):
            act.wait_ge(self.chip.block_done, self.block_count(16 + j))
            nc.scalar.activation(self.g[:, 2 * j:2 * j + 2, :].rearrange("p a n -> p (a n)"), ps[:, j % 4, :], ACT.Silu)\
                .then_inc(self.g_kept.sem, 1)
        for h in range(RH):
            act.wait_ge(self.o_sum.sem, self.o_sum.at(h + 1))
            nc.scalar.activation(self.o[:, 4 * h:4 * h + 4, :].rearrange("p (b e) n -> p b (e n)", b=2), ps[:, 2:4, :], ACT.Copy)\
                .then_inc(self.o_kept.sem, 1)
        act.wait_ge(self.centred.sem, self.centred.at(1))
        nc.scalar.activation(self.sq, self.o, ACT.Square).then_inc(self.squares.sem, 1)
        act.wait_ge(self.var_in.sem, self.var_in.at(1))
        nc.scalar.activation(self.st[:, 1, :], self.st[:, 0, :], ACT.Sqrt).then_inc(self.root.sem, 1)

    def dve(self, dve, link):
        nc, ps = self.nc, self.chip.ps
        dve.wait_ge(self.chip.stage_done, self.index)
        lg, v = self.lg, nc.vector
        dec = columns(self.chip.vec, "decay")
        link(v.tensor_scalar(lg[:, 0, :], dec, -1.0, None, ALU.mult))
        v.tensor_tensor(lg[:, 0, :], lg[:, 0, :], dec, ALU.max).then_inc(self.lg_in.sem, 1)
        dve.wait_ge(self.lg_exp.sem, self.lg_exp.at(1))
        link(v.tensor_scalar(lg[:, 0, :], lg[:, 1, :], 2.0, None, ALU.add))
        link(v.reciprocal(lg[:, 0, :], lg[:, 0, :]))
        link(v.tensor_tensor(lg[:, 0, :], lg[:, 0, :], lg[:, 1, :], ALU.mult))
        link(v.tensor_tensor(lg[:, 1, :], lg[:, 0, :], lg[:, 0, :], ALU.mult))
        link(v.tensor_scalar(lg[:, 2, :], lg[:, 1, :], 1.0 / 17, None, ALU.mult))
        for n in range(15, 1, -2):
            link(v.scalar_tensor_tensor(lg[:, 2, :], lg[:, 2, :], 1.0 / n, lg[:, 1, :], ALU.add, ALU.mult))
        link(v.scalar_tensor_tensor(lg[:, 2, :], lg[:, 2, :], 1.0, lg[:, 0, :], ALU.add, ALU.mult))
        link(v.tensor_scalar(lg[:, 3, :], dec, 0.0, None, ALU.min))
        v.scalar_tensor_tensor(lg[:, 3, :], lg[:, 2, :], -2.0, lg[:, 3, :], ALU.mult, ALU.add).then_inc(self.lg_out.sem, 1)
        dve.wait_ge(self.lg_out.sem, self.lg_out.at(1))
        for h in range(RH):
            link(v.tensor_scalar(self.d[:, h, 0:512], self.expo[:, 0, :], lg[:, 3, h:h + 1], None, ALU.mult))
            if h >= 2:
                link(v.tensor_tensor(self.d[:, h - 2, 512:1024], self.d[:, h - 2, 512:1024], self.tmp[:, h % 2, :], ALU.add))
            v.scalar_tensor_tensor(self.d[:, h, 0:512], self.expo[:, 1, :], lg[:, 3, 4 + h:5 + h], self.d[:, h, 0:512],
                                   ALU.mult, ALU.add).then_inc(self.d_in.sem, 1)
            if h >= 1:
                dve.wait_ge(self.d_exp.sem, self.d_exp.at(h))
        dve.wait_ge(self.d_exp.sem, self.d_exp.at(RH))
        for h in range(2, RH):
            link(v.tensor_tensor(self.d[:, h, 512:1024], self.d[:, h, 512:1024], self.tmp[:, h % 2, :], ALU.add))
        dve.wait_ge(self.q_kept.sem, self.q_kept.at(4))
        dve.wait_ge(self.k_kept.sem, self.k_kept.at(4))
        turned_part = self.chip.at(R_O, 2, N)
        for i in range(16):
            t = self.q[:, i, :] if i < KD else self.k[:, i - KD, 0:N]
            dve.wait_ge(self.turned.sem, self.turned.at(i + 1))
            link(v.tensor_tensor(turned_part[:, i % 2, :], ps[:, i % 4, 0:N], self.sin[:, i % 2, :], ALU.mult))
            link(v.tensor_tensor(t, t, self.cos[:, i % 2, :], ALU.mult))
            v.tensor_tensor(t, t, turned_part[:, i % 2, :], ALU.add).then_inc(self.rope_done.sem, 1)
        dve.wait_ge(self.g_kept.sem, self.g_kept.at(8))
        for h in range(RH):
            dve.wait_ge(self.scores.sem, self.scores.at(h + 1))
            if h >= 2:
                dve.wait_ge(self.o_sum.sem, self.o_sum.at(h - 1))
            v.tensor_tensor(self.p[:, h % 2, :], ps[:, 0:2, :].rearrange("p b n -> p (b n)"), self.d[:, h, :], ALU.mult)\
                .then_inc(self.weighted.sem, 1)
        dve.wait_ge(self.mean.sem, self.mean.at(1))
        mean, ms, rstd = self.st[:, 2, :], self.st[:, 0, :], self.st[:, 2, :]
        link(v.tensor_scalar(mean, ps[:, 4:6, :].rearrange("p b n -> p (b n)"), 1.0 / RDV, None, ALU.mult))
        for h in range(RH):
            o = self.o[:, 4 * h:4 * h + 4, :]
            last = v.tensor_tensor(o, o, mean[:, h * N:(h + 1) * N].unsqueeze(1).broadcast_to([P, 4, N]), ALU.subtract)
        last.then_inc(self.centred.sem, 1)
        dve.wait_ge(self.var.sem, self.var.at(1))
        v.tensor_scalar(ms, ps[:, 6:8, :].rearrange("p b n -> p (b n)"), 1.0 / RDV, EPS, ALU.mult, ALU.add)\
            .then_inc(self.var_in.sem, 1)
        dve.wait_ge(self.root.sem, self.root.at(1))
        link(v.reciprocal(rstd, self.st[:, 1, :]))
        for h in range(RH):
            o = self.o[:, 4 * h:4 * h + 4, :]
            link(v.tensor_tensor(o, o, rstd[:, h * N:(h + 1) * N].unsqueeze(1).broadcast_to([P, 4, N]), ALU.mult))
        v.tensor_tensor(self.o, self.o, self.g, ALU.mult).then_inc(self.chip.stage_done, 1)


B_P = 0
B_U = 56 * N
B_SQ = B_U + KD * N
B_SMALL = B_SQ + KD * N
B_OB = 19200
B_OC = B_OB + 4 * N
B_OA = B_OC + 4 * N
B_CST2 = B_OA + 4 * N
NCST2 = 2 * P + 5 * P + 2 * 16
B_BIAS = 23328
assert B_CST2 + NCST2 <= B_BIAS
B_WORK = B_BIAS + 16 * N

T_R, T_K, T_V, T_WA, T_G = 0, 4, 8, 12, 13
T_NQ, T_KV, T_KS, T_KW = 14, 18, 20, 21
T_SQ, T_SK = 22, 26
T_VS, T_VW, T_GATE, T_SV = 28, 29, 30, 31
T_GATES = 32
TOKEN_BLOCKS = (14, 15)


class LoadTables(Stage):

    def __init__(self, chip):
        super().__init__(chip)
        self.n = chip.signals("tables_loaded", 32)

    def act(self, act, link):
        c = self.chip
        act.wait_ge(self.chip.stage_done, self.index)
        act.dma_start(c.at(B_CST2, NCST2), c.io["cst2"]).then_inc(self.n.sem, 16)
        s = c.io["bias_scratch"]
        skewed = bass.AP(s.tensor, s.offset + P - 1, [[16 * BIASW - 1, P], [BIASW, 16], [1, N]])
        act.dma_start(c.at(B_BIAS, 16, N), skewed).then_inc(self.n.sem, 16)
        act.wait_ge(self.n.sem, self.n.at(32))
        act.sem_inc(self.chip.stage_done, 1)


class ProjectIn(Stage):

    blocks = BLOCKS["in2"]

    def __init__(self, chip):
        super().__init__(chip)
        self.u = chip.at(B_U, KD, N)
        self.p = chip.at(B_P, 56, N)
        self.kept = chip.signals("projection_kept", self.blocks)

    def pe(self, pe):
        nc, ps = self.nc, self.chip.ps
        pe.wait_ge(self.chip.stage_done, self.index)
        for j in range(self.blocks):
            slot, count = self.arrival(j)
            pe.wait_ge(self.chip.loaded[slot], count)
            w = self.chip.ring[:, slot]
            if j >= 8:
                pe.wait_ge(self.kept.sem, self.kept.at(j - 7))
            for e in range(2):
                if j in TOKEN_BLOCKS:
                    for t in range(NT):
                        for k in range(KD):
                            last = nc.tensor.matmul(ps[:, j % 8, e * N + t * P:e * N + (t + 1) * P],
                                                    self.u[:, k, t * P:(t + 1) * P], w[:, e * KD + k, :],
                                                    start=k == 0, stop=k == KD - 1)
                else:
                    for k in range(KD):
                        last = nc.tensor.matmul(ps[:, j % 8, e * N:(e + 1) * N], w[:, e * KD + k, :], self.u[:, k, :],
                                                start=k == 0, stop=k == KD - 1)
            last.then_inc(self.chip.block_done, 1)

    def act(self, act, link):
        nc, ps = self.nc, self.chip.ps
        act.wait_ge(self.chip.stage_done, self.index)
        for j in range(self.blocks):
            act.wait_ge(self.chip.block_done, self.block_count(j))
            to = self.p[:, 2 * j:2 * j + 2, :].rearrange("p a n -> p (a n)")
            if 2 * j == T_GATE:
                nc.scalar.activation(to[:, N:], ps[:, j % 8, N:], ACT.Copy)
                last = nc.scalar.activation(to[:, :N], ps[:, j % 8, :N], ACT.Sigmoid)
            else:
                last = nc.scalar.activation(to, ps[:, j % 8, :], ACT.Sigmoid if 2 * j >= T_GATES else ACT.Copy)
            last.then_inc(self.kept.sem, 1)
        act.wait_ge(self.kept.sem, self.kept.at(self.blocks))
        act.sem_inc(self.chip.stage_done, 1)


class Attention(Stage):

    blocks = BLOCKS["cmp1"] + BLOCKS["cmp2"]
    CMP, SEL, WIN, SWA = range(4)
    units = [(t, g, b) for t in range(NT) for g in range(2) for b in range(4)]

    def __init__(self, chip, layer):
        super().__init__(chip)
        at, sig = chip.at, chip.signals
        self.layer = layer
        self.p = at(B_P, 56, N)
        self.o = {self.WIN: at(B_OB, 4, N), self.SWA: at(B_OC, 4, N)}
        self.bias = at(B_BIAS, 16, N)
        self.cmask = at(B_CST2 + 7 * P, 2, 16)
        n = B_U
        self.r = at(n, CMP_LEN, 2, NCMP)
        n += CMP_LEN * 2 * NCMP
        self.hid = at(n, 4, 2 * NCMP)
        n += 4 * 2 * NCMP
        self.kcm, self.vcm = at(n, 16), at(n + 16, P)
        n += 16 + P
        self.stat = at(n, 2, 8, 4)
        self.sc = at(B_WORK, 2, 4, N)
        self.pt = at(B_WORK + 8 * N, 5, 4, P)
        self.pts = at(B_WORK + 8 * N + 20 * P, 2, 4, P)
        u = len(self.units)
        self.blocks_ready = sig("cmp_blocks_ready", 1)
        self.hidden = sig("cmp_hidden", 1)
        self.compressed = sig("cmp_done", 1)
        self.cmp_kept = sig("cmp_kept", 1)
        self.scored = sig("attn_scored", u)
        self.shifted = sig("attn_shifted", u)
        self.exped = sig("attn_exped", u)
        self.weighted = sig("attn_weighted", u)
        self.turned = sig("attn_turned", u)
        self.turned_kept = sig("attn_turned_kept", u)
        self.summed = sig("attn_summed", u // 2)
        self.sum_kept = sig("attn_sum_kept", u // 2)

    def width(self, t, b):
        return NCMP if b == self.CMP else (t + 1) * P

    def key_tiles(self, t, b):
        return 1 if b == self.CMP else t + 1

    def pe(self, pe):
        nc, ps, p = self.nc, self.chip.ps, self.p
        pe.wait_ge(self.chip.stage_done, self.index)
        pe.wait_ge(self.blocks_ready.sem, self.blocks_ready.at(1))
        for j in range(BLOCKS["cmp1"]):
            slot, count = self.arrival(j)
            pe.wait_ge(self.chip.loaded[slot], count)
            w = self.chip.ring[:, slot]
            for i in range(TPB):
                l, f = divmod(j * TPB + i, 2)
                for kv in range(2):
                    rows_ = slice(kv * DH, (kv + 1) * DH)
                    last = nc.tensor.matmul(ps[:, 2 * kv + f, 0:2 * NCMP], w[rows_, i, :],
                                            self.r[rows_, l].rearrange("p g n -> p (g n)"),
                                            start=l == 0, stop=l == CMP_LEN - 1)
            last.then_inc(self.chip.block_done, 1)
        pe.wait_ge(self.hidden.sem, self.hidden.at(1))
        slot, count = self.arrival(BLOCKS["cmp1"])
        pe.wait_ge(self.chip.loaded[slot], count)
        w = self.chip.ring[:, slot]
        for f in range(2):
            nc.tensor.matmul(ps[:, 4, 0:2 * NCMP], w[:, f, :], self.hid[:, f, :], start=f == 0, stop=f == 1)
        for g in range(2):
            for f in range(2):
                last = nc.tensor.matmul(ps[0:NCMP, 5, g * DH:(g + 1) * DH], self.hid[:, 2 + f, g * NCMP:(g + 1) * NCMP],
                                        w[:, 2 + f, 0:DH], start=f == 0, stop=f == 1)
        last.then_inc(self.chip.block_done, 1)
        pe.wait_ge(self.cmp_kept.sem, self.cmp_kept.at(1))

        def scores(u):
            t, g, b = self.units[u]
            if u >= 2:
                pe.wait_ge(self.shifted.sem, self.shifted.at(u - 1))
            half = slice(g * DH, (g + 1) * DH)
            keys = {self.CMP: self.kcm[half, 0:NCMP], self.SEL: p[half, T_KS], self.WIN: p[half, T_KW],
                    self.SWA: p[half, T_SK]}[b]
            w = self.width(t, b)
            for i in range(4):
                q = p[half, (T_SQ if b == self.SWA else T_NQ) + i, t * P:(t + 1) * P]
                last = nc.tensor.matmul(ps[:, 2 * (u % 2) + i // 2, (i % 2) * N:(i % 2) * N + w], q, keys[:, 0:w],
                                        start=True, stop=True)
            last.then_inc(self.scored.sem, 1)

        def turn(u):
            t, g, b = self.units[u]
            pe.wait_ge(self.weighted.sem, self.weighted.at(u + 1))
            if u >= 1:
                pe.wait_ge(self.turned_kept.sem, self.turned_kept.at(u))
            w = min(self.width(t, b), P)
            for j in range(self.key_tiles(t, b)):
                for i in range(4):
                    last = nc.tensor.transpose(ps[0:w, 4 + j, i * P:(i + 1) * P], self.sc[:, u % 2, i, j * P:j * P + w],
                                               self.chip.ident)
            last.then_inc(self.turned.sem, 1)

        def values(u):
            t, g, b = self.units[u]
            if b not in self.o:
                return
            n = 2 * (u // 4) + (b == self.SWA)
            pe.wait_ge(self.turned_kept.sem, self.turned_kept.at(u + 1))
            if n >= 2:
                pe.wait_ge(self.sum_kept.sem, self.sum_kept.at(n - 1))
            for i in range(4):
                if b == self.SWA:
                    parts = [(p[:, T_SV, j * P:(j + 1) * P], self.pts[:, j, i, :]) for j in range(t + 1)]
                else:
                    parts = [(self.vcm[0:NCMP, :], self.pt[0:NCMP, 0, i, :])]
                    parts += [(p[:, T_VS, j * P:(j + 1) * P], self.pt[:, 1 + j, i, :]) for j in range(t + 1)]
                    parts += [(p[:, T_VW, j * P:(j + 1) * P], self.pt[:, 3 + j, i, :]) for j in range(t + 1)]
                for k, (v, weights) in enumerate(parts):
                    last = nc.tensor.matmul(ps[:, 6 + n % 2, i * P:(i + 1) * P], v, weights, start=k == 0, stop=k == len(parts) - 1)
            last.then_inc(self.summed.sem, 1)

        scores(0)
        scores(1)
        for u in range(len(self.units)):
            turn(u)
            if u + 2 < len(self.units):
                scores(u + 2)
            values(u)

    def act(self, act, link):
        nc, ps = self.nc, self.chip.ps
        act.wait_ge(self.chip.stage_done, self.index)
        act.wait_ge(self.chip.block_done, self.block_count(BLOCKS["cmp1"] - 1))
        nc.scalar.activation(self.hid, ps[:, 0:4, 0:2 * NCMP], ACT.Gelu).then_inc(self.hidden.sem, 1)

        def exp(u):
            t, g, b = self.units[u]
            act.wait_ge(self.shifted.sem, self.shifted.at(u + 1))
            if b == self.SWA:
                nc.scalar.activation(self.stat[:, u % 2, 2, :], self.stat[:, u % 2, 2, :], ACT.Exp)
            e = self.sc[:, u % 2, :, 0:self.width(t, b)]
            nc.scalar.activation(e, e, ACT.Exp).then_inc(self.exped.sem, 1)

        def keep(u):
            t, g, b = self.units[u]
            w, k = min(self.width(t, b), P), self.key_tiles(t, b)
            to = self.pts[:, 0:k] if b == self.SWA else self.pt[0:w, (0, 1, 3)[b]:(0, 1, 3)[b] + k]
            act.wait_ge(self.turned.sem, self.turned.at(u + 1))
            nc.scalar.activation(to.rearrange("p j i t -> p j (i t)"), ps[0:w, 4:4 + k, :], ACT.Copy)\
                .then_inc(self.turned_kept.sem, 1)
            if b in self.o:
                n = 2 * (u // 4) + (b == self.SWA)
                half = slice(g * DH, (g + 1) * DH)
                act.wait_ge(self.summed.sem, self.summed.at(n + 1))
                nc.scalar.activation(self.o[b][half, :, t * P:(t + 1) * P],
                                     ps[half, 6 + n % 2, :].rearrange("p (i t) -> p i t", i=4), ACT.Copy)\
                    .then_inc(self.sum_kept.sem, 1)

        exp(0)
        for u in range(len(self.units)):
            if u + 1 < len(self.units):
                exp(u + 1)
            keep(u)
        act.wait_ge(self.sum_kept.sem, self.sum_kept.at(len(self.units) // 2))
        act.sem_inc(self.chip.stage_done, 1)

    def dve(self, dve, link):
        nc, ps, p = self.nc, self.chip.ps, self.p
        v = nc.vector
        dve.wait_ge(self.chip.stage_done, self.index)
        pe_cols = columns(self.chip.vec, "pe", self.layer, CMP_LEN)
        for g in range(2):
            x = p[:, T_KV + g, :]
            blocks = bass.AP(x.tensor, x.offset, [x.ap[0], (1, CMP_LEN), (CMP_STRIDE, NCMP)])
            last = v.tensor_tensor(self.r[:, :, g, :], blocks, pe_cols.unsqueeze(2).broadcast_to([P, CMP_LEN, NCMP]), ALU.add)
        last.then_inc(self.blocks_ready.sem, 1)
        dve.wait_ge(self.chip.block_done, self.block_count(BLOCKS["cmp1"]))
        for g in range(2):
            half = slice(g * DH, (g + 1) * DH)
            v.tensor_copy(self.kcm[half, 0:NCMP], ps[half, 4, g * NCMP:(g + 1) * NCMP])
        v.tensor_copy(self.vcm[0:NCMP, :], ps[0:NCMP, 5, 0:P]).then_inc(self.cmp_kept.sem, 1)

        def shift(u):
            t, g, b = self.units[u]
            w = self.width(t, b)
            sc, st = self.sc[:, u % 2, :, 0:w], self.stat[:, u % 2]
            scores = ps[:, 2 * (u % 2):2 * (u % 2) + 2, :].rearrange("p b (h n) -> p (b h) n", n=N)[:, :, 0:w]
            if b == self.CMP:
                bias = self.cmask[:, t, 0:NCMP].unsqueeze(1).broadcast_to([P, 4, NCMP])
            else:
                h = (8 if b == self.SWA else 0) + 4 * g
                bias = self.bias[:, h:h + 4, N - w:N]
            dve.wait_ge(self.scored.sem, self.scored.at(u + 1))
            if u >= 2:
                dve.wait_ge(self.turned.sem, self.turned.at(u - 1))
            link(v.scalar_tensor_tensor(sc, scores, DH ** -0.5, bias, ALU.mult, ALU.add))
            link(v.tensor_reduce(st[:, 0, :], sc, AX.X, ALU.max))
            if b == self.CMP:
                link(v.tensor_scalar(st[:, 0, :], st[:, 0, :], NEG / 10, None, ALU.max))
            if b == self.SWA:
                sink = columns(self.chip.vec, "sinks", self.layer, 8)[:, 4 * g:4 * g + 4]
                link(v.tensor_tensor(st[:, 0, :], st[:, 0, :], sink, ALU.max))
                link(v.tensor_tensor(st[:, 2, :], sink, st[:, 0, :], ALU.subtract))
            v.tensor_tensor(sc, sc, st[:, 0, :].unsqueeze(2).broadcast_to([P, 4, w]), ALU.subtract)\
                .then_inc(self.shifted.sem, 1)

        def weigh(u):
            t, g, b = self.units[u]
            w = self.width(t, b)
            sc, st = self.sc[:, u % 2, :, 0:w], self.stat[:, u % 2]
            dve.wait_ge(self.exped.sem, self.exped.at(u + 1))
            link(v.tensor_reduce(st[:, 1, :], sc, AX.X, ALU.add))
            if b == self.SWA:
                link(v.tensor_tensor(st[:, 1, :], st[:, 1, :], st[:, 2, :], ALU.add))
            else:
                link(v.tensor_scalar(st[:, 1, :], st[:, 1, :], 1e-30, None, ALU.max))
            link(v.reciprocal(st[:, 1, :], st[:, 1, :]))
            if b != self.SWA:
                a = t * P + 12 * g
                gate = p[:, T_GATE, a:a + 12].rearrange("p (h c) -> p h c", c=3)[:, :, b]
                link(v.tensor_tensor(st[:, 1, :], st[:, 1, :], gate, ALU.mult))
            v.tensor_tensor(sc, sc, st[:, 1, :].unsqueeze(2).broadcast_to([P, 4, w]), ALU.mult)\
                .then_inc(self.weighted.sem, 1)

        shift(0)
        for u in range(len(self.units)):
            if u + 1 < len(self.units):
                shift(u + 1)
            weigh(u)


W_AR, W_B, W_K, W_ST = 14 * N, 14 * N + 8 * N, 14 * N + 12 * N, 14 * N + 16 * N
W_BH, W_KH, W_GATE, W_Y = B_U, B_U + 4 * N, B_U + 8 * N, B_U + 12 * N
W_W1, W_PEND = B_U + 16 * N, B_U + 18 * N
W_TOK = B_BIAS
W_LB = W_TOK + 8 * N
W_LK = W_LB + 8 * N
W_MIX = W_LK + 8 * N
W_W2 = W_MIX + 16 * N
W_SA = W_W2 + 2 * N
W_C0 = W_SA + 2 * N
W_C1 = W_C0 + 4 * N
W_KK = W_C1 + 4 * N
W_A = W_KK + 4 * N


class Rwkv(Stage):

    blocks = BLOCKS["rwkv"]
    LEVELS = 5

    def __init__(self, chip, layer):
        super().__init__(chip)
        at, sig = chip.at, chip.signals
        self.layer = layer
        self.z = at(B_P, 56, N)
        self.ar = at(W_AR, 4, NT, 2, P)
        self.b, self.k, self.bh, self.kh = (at(w, 4, N) for w in (W_B, W_K, W_BH, W_KH))
        self.gate, self.y, self.kk, self.a = (at(w, 4, N) for w in (W_GATE, W_Y, W_KK, W_A))
        self.state = at(W_ST, 4, P)
        self.w1, self.pend = at(W_W1, 4, P), at(W_PEND, 4, NCH)
        self.tok = at(W_TOK, 4, 4, P)
        self.lb, self.lk = at(W_LB, HEADS, 2, P), at(W_LK, HEADS, 2, P)
        self.mix = at(W_MIX, 14, N)
        self.mat = [at(W_MIX + i * 4 * N, HEADS, P) for i in range(4)]
        self.tmp = [at(W_MIX + i * 4 * N, 4, N) for i in range(4)]
        self.e = [at(W_LB, 4, N), at(W_LB + 4 * N, 4, N), at(W_LK, 4, N)]
        self.w2, self.sa = at(W_W2, 4, P), at(W_SA, 4, P)
        self.c = [at(W_C0, 4, N), at(W_C1, 4, N)]
        self.oa = at(B_OA, 4, N)
        self.mask = at(B_CST2, 2 * P)
        self.level = [at(B_CST2 + (2 + i) * P, P) for i in range(self.LEVELS)]
        self.s = {}
        for name, n in [("mixed", 1), ("ranks_ready", 1), ("sig_w", 1), ("sig_a", 1), ("kk_raw", 1), ("kk_sq", 1),
                        ("kk_sum", 1), ("kk_in", 1), ("kk_root", 1), ("c_ready", 1), ("exps", 1), ("end_in", 1),
                        ("end_exp", 1), ("rk", 1), ("rk_sum", 1), ("scaled", 1), ("tok_turned", 8), ("tok_kept", 8),
                        ("l_done", 16), ("l_kept", 16), ("c_masked", 2 * 2 * self.LEVELS), ("x_done", 4 * self.LEVELS),
                        ("x_kept", 4 * self.LEVELS), ("e_done", 4 * self.LEVELS), ("d_done", 4 * self.LEVELS),
                        ("w1_done", 2), ("w1_kept", 2), ("x2_done", 2), ("x2_kept", 2), ("w2_done", 2), ("w2_kept", 2),
                        ("sa_done", NCH), ("sa_kept", NCH), ("s_done", NCH), ("s_kept", NCH + 1), ("y_done", 2), ("y_first", 2),
                        ("y_kept", 2), ("gn_sum", 1), ("gn_centred", 1), ("gn_sq", 1), ("gn_var", 1), ("gn_in", 1), ("gn_root", 1)]:
            self.s[name] = sig("rwkv_" + name, n)

    def pe(self, pe):
        nc, ps, z, s = self.nc, self.chip.ps, self.z, self.s
        mm = nc.tensor.matmul
        pe.wait_ge(self.chip.stage_done, self.index)
        pe.wait_ge(s["ranks_ready"].sem, s["ranks_ready"].at(1))
        slot, count = self.arrival(0)
        pe.wait_ge(self.chip.loaded[slot], count)
        w = self.chip.ring[:, slot]
        for m in range(4):
            at = slice((m % 2) * N, (m % 2 + 1) * N)
            mm(ps[:, m // 2, at], w[0:64, m, :], z[0:64, T_WA], start=True, stop=True)
            mm(ps[:, 2 + m // 2, at], w[64:128, m, :], z[64:128, T_WA], start=True, stop=True)
            last = mm(ps[:, 4 + m // 2, at], w[:, 4 + m, :], z[:, T_G], start=True, stop=True)
        last.then_inc(self.chip.block_done, 1)

        def head_sums(bank, x):
            for i in range(4):
                last = mm(ps[:, bank + i // 2, (i % 2) * N:(i % 2 + 1) * N], self.chip.headones, x[:, i, :], start=True, stop=True)
            return last

        pe.wait_ge(s["kk_sq"].sem, s["kk_sq"].at(1))
        head_sums(6, self.tmp[0]).then_inc(s["kk_sum"].sem, 1)
        pe.wait_ge(s["rk"].sem, s["rk"].at(1))
        head_sums(6, self.kk).then_inc(s["rk_sum"].sem, 1)
        pe.wait_ge(s["scaled"].sem, s["scaled"].at(1))
        for t in range(NT):
            ts = slice(t * P, (t + 1) * P)
            if t:
                pe.wait_ge(s["y_kept"].sem, s["y_kept"].at(t))
            for j, x in enumerate([self.ar[:, :, t, 0, :], self.bh[:, :, ts], self.kh[:, :, ts], z[:, T_V:T_V + 4, ts]]):
                for i in range(4):
                    last = nc.tensor.transpose(ps[:, j, i * P:(i + 1) * P], x[:, i, :], self.chip.ident)
                last.then_inc(s["tok_turned"].sem, 1)
            for x, bank in ((self.b, 4), (self.k, 0)):
                if bank == 0:
                    pe.wait_ge(s["tok_kept"].sem, s["tok_kept"].at(4 * t + 4))
                for b in range(4):
                    two_, e = divmod(b, 2)
                    half = slice(e * DH, (e + 1) * DH)
                    for i in range(2):
                        last = mm(ps[:, bank + b, i * 2 * P:(i + 1) * 2 * P], x[half, 2 * two_ + i, ts],
                                  self.ar[half, 2 * two_ + i, t].rearrange("p a n -> p (a n)"), start=True, stop=True)
                    last.then_inc(s["l_done"].sem, 1)
            pe.wait_ge(s["l_kept"].sem, s["l_kept"].at(8 * t + 8))
            d, dt, x, ct = self.mat
            for lv in range(self.LEVELS):
                for g in range(2):
                    n = (t * self.LEVELS + lv) * 2 + g
                    pe.wait_ge(s["c_masked"].sem, s["c_masked"].at(n + 1))
                    if lv:
                        pe.wait_ge(s["d_done"].sem, s["d_done"].at(n - 1))
                    for h in range(4 * g, 4 * g + 4):
                        last = mm(ps[:, g, (h % 4) * P:(h % 4 + 1) * P], ct[:, h, :], d[:, h, :], start=True, stop=True)
                    last.then_inc(s["x_done"].sem, 1)
                for g in range(2):
                    n = (t * self.LEVELS + lv) * 2 + g
                    pe.wait_ge(s["x_kept"].sem, s["x_kept"].at(n + 1))
                    for h in range(4 * g, 4 * g + 4):
                        at = slice((h % 4) * P, (h % 4 + 1) * P)
                        if lv < self.LEVELS - 1:
                            mm(ps[:, 2 + g, at], dt[:, h, :], x[:, h, :], start=True, stop=True)
                        last = mm(ps[:, 4 + g, at], x[:, h, :], dt[:, h, :], start=True, stop=True)
                    last.then_inc(s["e_done"].sem, 1)
            pe.wait_ge(s["d_done"].sem, s["d_done"].at(2 * self.LEVELS * (t + 1)))
            for h in range(HEADS):
                last = mm(ps[:, h % 2, (h // 2) * P:(h // 2 + 1) * P], self.tok[:, 0, h // 2, :], dt[:, h, :], start=True, stop=True)
            last.then_inc(s["w1_done"].sem, 1)
            for h in range(HEADS):
                last = mm(ps[:, 2, h * DH:(h + 1) * DH], self.lk[:, h, 0, :], self.tok[:, 3, h // 2, (h % 2) * DH:(h % 2 + 1) * DH],
                          start=True, stop=True)
            last.then_inc(s["x2_done"].sem, 1)
            pe.wait_ge(s["x2_kept"].sem, s["x2_kept"].at(t + 1))
            x2 = x[:, 0:4, :]
            for h in range(HEADS):
                last = mm(ps[:, 3, h * DH:(h + 1) * DH], dt[:, h, :], x2[:, h // 2, (h % 2) * DH:(h % 2 + 1) * DH], start=True, stop=True)
            last.then_inc(s["w2_done"].sem, 1)
            pe.wait_ge(s["w1_kept"].sem, s["w1_kept"].at(t + 1))
            pe.wait_ge(s["w2_kept"].sem, s["w2_kept"].at(t + 1))
            for c in range(4):
                n = 4 * t + c
                rows_ = slice(c * CH, (c + 1) * CH)
                pe.wait_ge(s["s_kept"].sem, s["s_kept"].at(n + 1))
                for i in range(4):
                    last = mm(ps[:, 4, i * P:(i + 1) * P], self.w1[:, i, :], self.state[:, i, :], start=True, stop=True)
                last.then_inc(s["sa_done"].sem, 1)
                for i in range(4):
                    mm(ps[:, 5, i * P + c * CH:i * P + (c + 1) * CH], self.state[:, i, :], self.ar[:, i, t, 1, rows_], start=True, stop=True)
                pe.wait_ge(s["sa_kept"].sem, s["sa_kept"].at(n + 1))
                for i in range(4):
                    at = slice(i * P, (i + 1) * P)
                    mm(ps[:, 6, at], self.tok[rows_, 2, i, :], self.tok[rows_, 3, i, :], start=True, stop=False)
                    last = mm(ps[:, 6, at], self.tok[rows_, 1, i, :], self.sa[rows_, i, :], start=False, stop=True)
                last.then_inc(s["s_done"].sem, 1)
            for e in range(2):
                for i in range(4):
                    at, h = slice(i * P, (i + 1) * P), 2 * i + e
                    mm(ps[:, e, at], self.tok[:, 3, i, :], self.lk[:, h, 1, :], start=True, stop=False)
                    last = mm(ps[:, e, at], self.sa[:, i, :], self.lb[:, h, 1, :], start=False, stop=True)
            last.then_inc(s["y_done"].sem, 1)
        pe.wait_ge(s["y_kept"].sem, s["y_kept"].at(2))
        head_sums(2, self.y).then_inc(s["gn_sum"].sem, 1)
        pe.wait_ge(s["gn_sq"].sem, s["gn_sq"].at(1))
        head_sums(4, self.tmp[0]).then_inc(s["gn_var"].sem, 1)

    def act(self, act, link):
        nc, ps, z, s = self.nc, self.chip.ps, self.z, self.s
        copy = nc.scalar.activation
        col = lambda name, i: columns(self.chip.vec, name, self.layer, 4)[:, i:i + 1]
        act.wait_ge(self.chip.stage_done, self.index)
        act.wait_ge(s["mixed"].sem, s["mixed"].at(1))
        copy(z[0:64, T_WA], z[0:64, T_WA], ACT.Tanh)
        copy(z[:, T_G], z[:, T_G], ACT.Sigmoid).then_inc(s["ranks_ready"].sem, 1)
        act.wait_ge(self.chip.block_done, self.block_count(0))
        for i in range(4):
            last = copy(self.c[0][:, i, :], ps[:, i // 2, (i % 2) * N:(i % 2 + 1) * N], ACT.Sigmoid, bias=col("w0", i))
        last.then_inc(s["sig_w"].sem, 1)
        for i in range(4):
            copy(self.a[:, i, :], ps[:, 2 + i // 2, (i % 2) * N:(i % 2 + 1) * N], ACT.Sigmoid, bias=col("a0", i))
        copy(self.gate.rearrange("p (b i) n -> p b (i n)", b=2), ps[:, 4:6, :], ACT.Copy).then_inc(s["sig_a"].sem, 1)
        act.wait_ge(s["kk_raw"].sem, s["kk_raw"].at(1))
        copy(self.tmp[0], self.kk, ACT.Square).then_inc(s["kk_sq"].sem, 1)
        act.wait_ge(s["kk_in"].sem, s["kk_in"].at(1))
        copy(self.tmp[2], self.tmp[1], ACT.Sqrt).then_inc(s["kk_root"].sem, 1)
        act.wait_ge(s["c_ready"].sem, s["c_ready"].at(1))
        copy(self.e[0], self.c[1], ACT.Exp)
        copy(self.e[1], self.c[1], ACT.Exp, scale=-1.0).then_inc(s["exps"].sem, 1)
        act.wait_ge(s["end_in"].sem, s["end_in"].at(1))
        copy(self.e[2], self.e[2], ACT.Exp).then_inc(s["end_exp"].sem, 1)
        for t in range(NT):
            for j in range(4):
                act.wait_ge(s["tok_turned"].sem, s["tok_turned"].at(4 * t + j + 1))
                copy(self.tok[:, j].rearrange("p i n -> p (i n)"), ps[:, j, :], ACT.Copy).then_inc(s["tok_kept"].sem, 1)
            x = self.mat[2]
            for lv in range(self.LEVELS):
                for g in range(2):
                    n = (t * self.LEVELS + lv) * 2 + g
                    act.wait_ge(s["x_done"].sem, s["x_done"].at(n + 1))
                    copy(x[:, 4 * g:4 * g + 4, :].rearrange("p h n -> p (h n)"), ps[:, g, :], ACT.Copy).then_inc(s["x_kept"].sem, 1)
            act.wait_ge(s["w1_done"].sem, s["w1_done"].at(t + 1))
            for e in range(2):
                half = slice(e * DH, (e + 1) * DH)
                last = copy(self.w1[half].rearrange("p i n -> p (i n)"), ps[half, e, :], ACT.Copy, scale=-1.0)
            last.then_inc(s["w1_kept"].sem, 1)
            act.wait_ge(s["x2_done"].sem, s["x2_done"].at(t + 1))
            copy(x[:, 0:4, :].rearrange("p i n -> p (i n)"), ps[:, 2, :], ACT.Copy).then_inc(s["x2_kept"].sem, 1)
            act.wait_ge(s["w2_done"].sem, s["w2_done"].at(t + 1))
            copy(self.w2.rearrange("p i n -> p (i n)"), ps[:, 3, :], ACT.Copy, scale=-1.0).then_inc(s["w2_kept"].sem, 1)
            act.wait_ge(s["y_done"].sem, s["y_done"].at(t + 1))
            copy(self.y[:, :, t * P:(t + 1) * P], ps[:, 5, :].rearrange("p (i n) -> p i n", i=4), ACT.Copy)\
                .then_inc(s["y_first"].sem, 1)
        act.wait_ge(s["gn_centred"].sem, s["gn_centred"].at(1))
        copy(self.tmp[0], self.y, ACT.Square).then_inc(s["gn_sq"].sem, 1)
        act.wait_ge(s["gn_in"].sem, s["gn_in"].at(1))
        copy(self.tmp[2], self.tmp[1], ACT.Sqrt).then_inc(s["gn_root"].sem, 1)

    def dve(self, dve, link):
        nc, ps, z, s = self.nc, self.chip.ps, self.z, self.s
        v = nc.vector
        col = lambda name, i: columns(self.chip.vec, name, self.layer, 4)[:, i:i + 1]
        two = lambda bank: ps[:, bank:bank + 2, :].rearrange("p b (i n) -> p (b i) n", n=N)
        dve.wait_ge(self.chip.stage_done, self.index)
        link(v.tensor_scalar(self.mix[:, :, 0:1], z[:, 0:14, 0:1], -1.0, None, ALU.mult))
        link(v.tensor_tensor(self.mix[:, :, 1:N], z[:, 0:14, 0:N - 1], z[:, 0:14, 1:N], ALU.subtract))
        for i in range(14):
            mu = columns(self.chip.vec, "mu", self.layer, 14)[:, i:i + 1]
            last = v.scalar_tensor_tensor(z[:, i, :], self.mix[:, i, :], mu, z[:, i, :], ALU.mult, ALU.add)
        last.then_inc(s["mixed"].sem, 1)
        dve.wait_ge(s["mixed"].sem, s["mixed"].at(1))
        for i in range(4):
            last = v.tensor_scalar(self.kk[:, i, :], z[:, T_K + i, :], col("k_k", i), None, ALU.mult)
        last.then_inc(s["kk_raw"].sem, 1)
        dve.wait_ge(s["sig_w"].sem, s["sig_w"].at(1))
        c = [x.rearrange("p i (c n) -> p (i c) n", n=CH) for x in self.c]
        link(v.tensor_scalar(self.c[0], self.c[0], -math.exp(-0.5), None, ALU.mult))
        for n in range(5):
            of, to, d = c[n % 2], c[1 - n % 2], 1 << n
            v.tensor_copy(to[:, :, 0:d], of[:, :, 0:d])
            last = v.tensor_tensor(to[:, :, d:CH], of[:, :, d:CH], of[:, :, 0:CH - d], ALU.add)
            if n < 4:
                link(last)
        last.then_inc(s["c_ready"].sem, 1)
        dve.wait_ge(s["c_ready"].sem, s["c_ready"].at(1))
        e2 = self.e[2].rearrange("p i (c n) -> p (i c) n", n=CH)
        v.tensor_tensor(e2, c[1][:, :, CH - 1:CH].broadcast_to([P, 4 * NCH, CH]), c[1], ALU.subtract).then_inc(s["end_in"].sem, 1)
        dve.wait_ge(s["kk_sum"].sem, s["kk_sum"].at(1))
        v.tensor_scalar(self.tmp[1], two(6), 1e-12, None, ALU.max).then_inc(s["kk_in"].sem, 1)
        dve.wait_ge(s["sig_a"].sem, s["sig_a"].at(1))
        t3 = self.tmp[3]
        for i in range(4):
            last = v.tensor_scalar(t3[:, i, :], self.a[:, i, :], 1.0, col("k_a", i), ALU.subtract, ALU.mult)
        link(last)
        k = z[:, T_K:T_K + 4, :]
        dve.wait_ge(s["kk_root"].sem, s["kk_root"].at(1))
        link(v.reciprocal(self.tmp[2], self.tmp[2]))
        link(v.tensor_tensor(self.kk, self.kk, self.tmp[2], ALU.mult))
        link(v.scalar_tensor_tensor(k, t3, 1.0, k, ALU.add, ALU.mult))
        link(v.tensor_tensor(self.a, self.a, self.kk, ALU.mult))
        dve.wait_ge(s["exps"].sem, s["exps"].at(1))
        dve.wait_ge(s["end_exp"].sem, s["end_exp"].at(1))
        e_in, e_inv, e_end = self.e
        split = lambda x: x.rearrange("p i (t c n) -> p (i t) c n", t=NT, n=CH)
        ar = self.ar.rearrange("p i t a (c n) -> p (i t) a c n", n=CH)
        v.tensor_tensor(ar[:, :, 0, :, 1:CH], split(self.kk)[:, :, :, 1:CH], split(e_in)[:, :, :, 0:CH - 1], ALU.mult)
        v.tensor_copy(ar[:, :, 0, :, 0:1], split(self.kk)[:, :, :, 0:1])
        v.tensor_tensor(ar[:, :, 1], split(z[:, T_R:T_R + 4, :]), split(e_in), ALU.mult)
        v.tensor_tensor(self.b, self.a, e_inv, ALU.mult)
        v.tensor_tensor(self.k, k, e_inv, ALU.mult)
        v.tensor_tensor(self.bh, self.a, e_end, ALU.mult)
        v.tensor_tensor(self.kh, k, e_end, ALU.mult)
        link(v.tensor_copy(self.pend, e_in.rearrange("p i (c n) -> p i c n", n=CH)[:, :, :, CH - 1]))
        link(v.tensor_tensor(self.kk, z[:, T_R:T_R + 4, :], k, ALU.mult))
        for i in range(4):
            last = v.tensor_scalar(self.kk[:, i, :], self.kk[:, i, :], col("r_k", i), None, ALU.mult)
        last.then_inc(s["rk"].sem, 1)
        dve.wait_ge(s["rk_sum"].sem, s["rk_sum"].at(1))
        bonus = self.c[1]
        link(v.tensor_tensor(bonus, two(6), z[:, T_V:T_V + 4, :], ALU.mult))
        v.memset(self.state, 0.0).then_inc(s["s_kept"].sem, 1)
        dve.sem_inc(s["scaled"].sem, 1)
        d, dt, x, ct = self.mat
        for t in range(NT):
            ident = self.chip.ident.unsqueeze(1).broadcast_to([P, HEADS, P])
            v.tensor_copy(d, ident)
            link(v.tensor_copy(dt, ident))
            for n, (to, bank) in enumerate([(self.lb, 4), (self.lk, 0)]):
                for b in range(4):
                    two_, e = divmod(b, 2)
                    dve.wait_ge(s["l_done"].sem, s["l_done"].at(8 * t + 4 * n + b + 1))
                    v.tensor_tensor(to[:, 4 * two_ + e:4 * two_ + e + 3:2].rearrange("p h a n -> p h (a n)"),
                                    ps[:, bank + b, :].rearrange("p (h m) -> p h m", h=2),
                                    self.mask.unsqueeze(1).broadcast_to([P, 2, 2 * P]), ALU.mult).then_inc(s["l_kept"].sem, 1)
            dve.wait_ge(s["l_kept"].sem, s["l_kept"].at(8 * t + 8))

            def mask_level(lv, g):
                n = (t * self.LEVELS + lv) * 2 + g
                if lv:
                    dve.wait_ge(s["x_done"].sem, s["x_done"].at(n - 1))
                hs = slice(4 * g, 4 * g + 4)
                v.tensor_tensor(ct[:, hs, :], self.lb[:, hs, 0, :], self.level[lv].unsqueeze(1).broadcast_to([P, 4, P]), ALU.mult)\
                    .then_inc(s["c_masked"].sem, 1)

            mask_level(0, 0)
            mask_level(0, 1)
            for lv in range(self.LEVELS):
                for g in range(2):
                    n = (t * self.LEVELS + lv) * 2 + g
                    hs = slice(4 * g, 4 * g + 4)
                    dve.wait_ge(s["e_done"].sem, s["e_done"].at(n + 1))
                    if lv < self.LEVELS - 1:
                        mask_level(lv + 1, g)
                        v.tensor_tensor(d[:, hs, :], d[:, hs, :], ps[:, 2 + g, :].rearrange("p (h n) -> p h n", h=4), ALU.subtract)
                    v.tensor_tensor(dt[:, hs, :], dt[:, hs, :], ps[:, 4 + g, :].rearrange("p (h n) -> p h n", h=4), ALU.subtract)\
                        .then_inc(s["d_done"].sem, 1)
                    dve.wait_ge(s["d_done"].sem, s["d_done"].at(n + 1))
            dve.wait_ge(s["w2_kept"].sem, s["w2_kept"].at(t + 1))
            for c_ in range(4):
                n = 4 * t + c_
                rows_ = slice(c_ * CH, (c_ + 1) * CH)
                dve.wait_ge(s["sa_done"].sem, s["sa_done"].at(n + 1))
                v.tensor_tensor(self.sa[rows_].rearrange("p i n -> p (i n)"), ps[rows_, 4, :],
                                self.w2[rows_].rearrange("p i n -> p (i n)"), ALU.add).then_inc(s["sa_kept"].sem, 1)
                dve.wait_ge(s["s_done"].sem, s["s_done"].at(n + 1))
                for i in range(4):
                    for e in range(2):
                        half = slice(e * DH, (e + 1) * DH)
                        last = v.scalar_tensor_tensor(self.state[half, i, half], self.state[half, i, half],
                                                      self.pend[half, i, n:n + 1], ps[half, 6, i * P + e * DH:i * P + (e + 1) * DH],
                                                      ALU.mult, ALU.add)
                last.then_inc(s["s_kept"].sem, 1)
                dve.wait_ge(s["s_kept"].sem, s["s_kept"].at(n + 2))
            dve.wait_ge(s["y_first"].sem, s["y_first"].at(t + 1))
            for e in range(2):
                half = slice(e * DH, (e + 1) * DH)
                y = self.y[half, :, t * P:(t + 1) * P]
                last = v.tensor_tensor(y, y, ps[half, e, :].rearrange("p (i n) -> p i n", i=4), ALU.add)
            last.then_inc(s["y_kept"].sem, 1)
        dve.wait_ge(s["gn_sum"].sem, s["gn_sum"].at(1))
        link(v.scalar_tensor_tensor(self.y, two(2), -1.0 / DH, self.y, ALU.mult, ALU.add))
        dve.sem_inc(s["gn_centred"].sem, 1)
        dve.wait_ge(s["gn_var"].sem, s["gn_var"].at(1))
        v.tensor_scalar(self.tmp[1], two(4), 1.0 / DH, GN_EPS, ALU.mult, ALU.add).then_inc(s["gn_in"].sem, 1)
        dve.wait_ge(s["gn_root"].sem, s["gn_root"].at(1))
        link(v.reciprocal(self.tmp[2], self.tmp[2]))
        link(v.tensor_tensor(self.y, self.y, self.tmp[2], ALU.mult))
        for i in range(4):
            last = v.tensor_scalar(self.y[:, i, :], self.y[:, i, :], col("ln_w", i), col("ln_b", i), ALU.mult, ALU.add)
        link(last)
        link(v.tensor_tensor(self.y, self.y, bonus, ALU.add))
        v.tensor_tensor(self.oa, self.y, self.gate, ALU.mult).then_inc(self.chip.stage_done, 1)


class Merge(Stage):

    blocks = BLOCKS["branch"]

    def __init__(self, chip):
        super().__init__(chip)
        self.o = [chip.at(a, 4, N) for a in (B_OA, B_OB, B_OC)]
        self.gates = chip.at(B_P, 56, N)[:, T_GATES:, :]
        self.merged, self.part = chip.at(B_BIAS, KD, N), chip.at(B_BIAS + KD * N, KD, N)
        self.used = chip.signals("branch_used", 3)

    def pe(self, pe):
        pe.wait_ge(self.chip.stage_done, self.index)
        for b in range(3):
            if b == 2:
                pe.wait_ge(self.used.sem, self.used.at(1))
            for j in range(2):
                slot, count = self.arrival(2 * b + j)
                pe.wait_ge(self.chip.loaded[slot], count)
                w = self.chip.ring[:, slot]
                for m in range(4):
                    mm = 4 * j + m
                    for k in range(4):
                        last = self.nc.tensor.matmul(self.chip.ps[:, 4 * (b % 2) + mm // 2, (mm % 2) * N:(mm % 2 + 1) * N],
                                                     w[:, 4 * m + k, :], self.o[b][:, k, :], start=k == 0, stop=k == 3)
                last.then_inc(self.chip.block_done, 1)

    def dve(self, dve, link):
        v = self.nc.vector
        dve.wait_ge(self.chip.stage_done, self.index)
        for b in range(3):
            dve.wait_ge(self.chip.block_done, self.block_count(2 * b + 1))
            product = self.chip.ps[:, 4 * (b % 2):4 * (b % 2) + 4, :].rearrange("p b (m n) -> p (b m) n", n=N)
            v.tensor_tensor(self.part if b else self.merged, product, self.gates[:, KD * b:KD * (b + 1), :], ALU.mult)\
                .then_inc(self.used.sem, 1)
            dve.wait_ge(self.used.sem, self.used.at(b + 1))
            if b:
                last = v.tensor_tensor(self.merged, self.merged, self.part, ALU.add)
                if b == 1:
                    link(last)
        last.then_inc(self.chip.stage_done, 1)


G_GATES = 0
G_Z = NKEYS * N
G_SLOT = G_Z + KD * N
G_HOT = G_SLOT + 3 * N
G_ACT = G_HOT + 2 * 2 * 4 * P
G_Q = 0
G_S = G_Q + 16 * N
G_TOP = G_S + NT * 16 * P
G_IDX = G_TOP + NT * 16 * TOPK
G_REST = G_IDX + NT * 16 * TOPK
G_CAND = G_REST + N
G_HOTK = G_CAND + HEADS * TOPK * TOPK
G_SEL = G_HOTK + HEADS * TOPK * TOPK
G_SQ = 0
G_SMALL = KD * N


class PeerRoute(Stage):

    blocks = BLOCKS["wq"] + BLOCKS["keys"]

    def __init__(self, chip):
        super().__init__(chip)
        at, sig = chip.at, chip.signals
        self.z = at(G_Z, KD, N)
        self.q = at(G_Q, 16, N)
        self.s = at(G_S, NT, 16, P)
        self.top, self.idx = at(G_TOP, NT, 16, TOPK), at(G_IDX, NT, 16, TOPK)
        self.rest = at(G_REST, N)
        self.cand, self.hot = at(G_CAND, HEADS, TOPK, TOPK), at(G_HOTK, HEADS, TOPK, TOPK)
        self.sel = at(G_SEL, NT, 8, HEADS, TOPK)
        self.slot = at(G_SLOT, 3, N)
        self.q_kept = sig("peer_q_kept", 8)
        self.scored = sig("peer_scored", 8)
        self.s_kept = sig("peer_s_kept", 8)
        self.shifted = sig("peer_shifted", NT)
        self.exped = sig("peer_exped", NT)
        self.chosen = sig("peer_chosen", 1)
        self.turned = sig("peer_turned", 3)
        self.slot_kept = sig("peer_slot_kept", 3)

    def pe(self, pe):
        nc, ps = self.nc, self.chip.ps
        pe.wait_ge(self.chip.stage_done, self.index)
        for j in range(8):
            slot, count = self.arrival(j)
            pe.wait_ge(self.chip.loaded[slot], count)
            w = self.chip.ring[:, slot]
            if j >= 4:
                pe.wait_ge(self.q_kept.sem, self.q_kept.at(j - 3))
            for e in range(2):
                for k in range(KD):
                    last = nc.tensor.matmul(ps[:, j % 4, e * N:(e + 1) * N], w[:, e * KD + k, :], self.z[:, k, :],
                                            start=k == 0, stop=k == KD - 1)
            last.then_inc(self.chip.block_done, 1)
        pe.wait_ge(self.q_kept.sem, self.q_kept.at(8))
        slot, count = self.arrival(8)
        pe.wait_ge(self.chip.loaded[slot], count)
        w = self.chip.ring[:, slot]
        for n in range(8):
            t, four = divmod(n, 4)
            if n >= 4:
                pe.wait_ge(self.s_kept.sem, self.s_kept.at(n - 3))
            for i in range(4):
                hp = 4 * four + i
                last = nc.tensor.matmul(ps[:, 4 + n % 4, i * P:(i + 1) * P], self.q[:, hp, t * P:(t + 1) * P], w[:, hp, :],
                                        start=True, stop=True)
            last.then_inc(self.scored.sem, 1)
        pe.wait_ge(self.s_kept.sem, self.s_kept.at(8))
        pe.sem_inc(self.chip.block_done, 1)
        pe.wait_ge(self.chosen.sem, self.chosen.at(1))
        for j in range(3):
            for t in range(NT):
                last = nc.tensor.transpose(ps[:, j, t * P:(t + 1) * P], self.sel[:, t, 5 + j].rearrange("p h k -> p (h k)"),
                                           self.chip.ident)
            last.then_inc(self.turned.sem, 1)

    def act(self, act, link):
        nc, ps = self.nc, self.chip.ps
        act.wait_ge(self.chip.stage_done, self.index)
        for j in range(8):
            act.wait_ge(self.chip.block_done, self.block_count(j))
            nc.scalar.activation(self.q[:, 2 * j:2 * j + 2, :].rearrange("p a n -> p (a n)"), ps[:, j % 4, :], ACT.Copy)\
                .then_inc(self.q_kept.sem, 1)
        for n in range(8):
            t, four = divmod(n, 4)
            act.wait_ge(self.scored.sem, self.scored.at(n + 1))
            nc.scalar.activation(self.s[:, t, 4 * four:4 * four + 4, :].rearrange("p a n -> p (a n)"), ps[:, 4 + n % 4, :], ACT.Copy)\
                .then_inc(self.s_kept.sem, 1)
        for t in range(NT):
            act.wait_ge(self.shifted.sem, self.shifted.at(t + 1))
            nc.scalar.activation(self.sel[:, t, 7], self.sel[:, t, 7], ACT.Exp).then_inc(self.exped.sem, 1)
        for j in range(3):
            act.wait_ge(self.turned.sem, self.turned.at(j + 1))
            nc.scalar.activation(self.slot[:, j, :], ps[:, j, 0:N], ACT.Copy).then_inc(self.slot_kept.sem, 1)
        act.wait_ge(self.slot_kept.sem, self.slot_kept.at(3))
        act.sem_inc(self.chip.stage_done, 1)

    def dve(self, dve, link):
        v = self.nc.vector
        dve.wait_ge(self.chip.stage_done, self.index)

        def best(values, scratch, top, places):
            link(v.max(top[:, 0:8], values))
            v.max_index(places[:, 0:8], top[:, 0:8], values)
            link(v.match_replace(scratch, top[:, 0:8], values, -3e38))
            link(v.max(top[:, 8:16], scratch))
            link(v.max_index(places[:, 8:16], top[:, 8:16], scratch))

        for t in range(NT):
            dve.wait_ge(self.s_kept.sem, self.s_kept.at(4 * t + 4))
            for hp in range(16):
                best(self.s[:, t, hp, :], self.rest[:, 0:P], self.top[:, t, hp, :], self.idx[:, t, hp, :].bitcast(U32))
            link(v.tensor_copy(self.idx[:, t], self.idx[:, t].bitcast(U32)))
            top = self.top[:, t].rearrange("p (h a) k -> p h a k", a=2)
            idx = self.idx[:, t].rearrange("p (h a) k -> p h a k", a=2)
            wide = [P, HEADS, TOPK, TOPK]
            link(v.tensor_tensor(self.cand, top[:, :, 0, :].unsqueeze(3).broadcast_to(wide),
                                 top[:, :, 1, :].unsqueeze(2).broadcast_to(wide), ALU.add))
            sel = self.sel[:, t]
            score, place, rank = sel[:, 0], sel[:, 1], sel[:, 2:4]
            for h in range(HEADS):
                best(self.cand[:, h].rearrange("p a b -> p (a b)"), self.rest, score[:, h, :], place[:, h, :].bitcast(U32))
            link(v.tensor_scalar(rank[:, 0].bitcast(U32), place.bitcast(U32), 4, None, ALU.logical_shift_right))
            link(v.tensor_scalar(rank[:, 1].bitcast(U32), place.bitcast(U32), TOPK - 1, None, ALU.bitwise_and))
            link(v.tensor_copy(rank, rank.bitcast(U32)))
            for a in range(2):
                hot = self.hot.rearrange("p h k j -> p (h k) j")
                choice = rank[:, a].rearrange("p h k -> p (h k)").unsqueeze(2).broadcast_to([P, P, TOPK])
                iota = self.chip.iota[:, 0:TOPK].unsqueeze(1).broadcast_to([P, P, TOPK])
                link(v.tensor_tensor(hot, choice, iota, ALU.is_equal))
                link(v.tensor_tensor(self.hot, self.hot, idx[:, :, a, :].unsqueeze(2).broadcast_to(wide), ALU.mult))
                link(v.tensor_reduce(sel[:, 5 + a].rearrange("p h k -> p (h k)"), hot, AX.X, ALU.add))
            gate = sel[:, 7]
            v.tensor_tensor(gate, score, score[:, :, 0:1].broadcast_to([P, HEADS, TOPK]), ALU.subtract).then_inc(self.shifted.sem, 1)
            dve.wait_ge(self.exped.sem, self.exped.at(t + 1))
            total = sel[:, 4, :, 0]
            link(v.tensor_reduce(total, gate, AX.X, ALU.add))
            link(v.reciprocal(total, total))
            last = v.tensor_tensor(gate, gate, total.unsqueeze(2).broadcast_to([P, HEADS, TOPK]), ALU.mult)
            if t == 0:
                link(last)
        last.then_inc(self.chosen.sem, 1)


class PeerGates(Stage):

    SETS = N // 4

    def __init__(self, chip):
        super().__init__(chip)
        self.slot = chip.at(G_SLOT, 3, N)
        self.hot = chip.at(G_HOT, 2, 2, 4 * P)
        self.gates = chip.at(G_GATES, N * NKEYS)
        self.ready = chip.signals("hot_ready", self.SETS)
        self.done = chip.signals("gates_done", self.SETS)
        self.kept = chip.signals("gates_kept", self.SETS)

    def dve(self, dve, link):
        v = self.nc.vector
        dve.wait_ge(self.chip.stage_done, self.index)

        def body(it, first=False):
            for r in range(2):
                n = it * 2 + r
                if not first:
                    dve.wait_ge(self.done.sem, self.done.at(n - 1))
                for i in range(4):
                    t = n * 4 + i
                    key1, key2, gate = (self.slot[:, j, bass.ds(t, 1)] for j in range(3))
                    v.tensor_scalar(self.hot[:, r, 0, i * P:(i + 1) * P], self.chip.iota, key1, gate, ALU.is_equal, ALU.mult)
                    last = v.tensor_scalar(self.hot[:, r, 1, i * P:(i + 1) * P], self.chip.iota, key2, None, ALU.is_equal)
                last.then_inc(self.ready.sem, 1)

        body(0, first=True)
        with dve.Fori(1, self.SETS // 2) as it:
            body(it)

    def pe(self, pe):
        pe.wait_ge(self.chip.stage_done, self.index)

        def body(it, first=False):
            for r in range(2):
                n = it * 2 + r
                pe.wait_ge(self.ready.sem, self.ready.at(n + 1))
                if not first:
                    pe.wait_ge(self.kept.sem, self.kept.at(n - 1))
                for i in range(4):
                    at = slice(i * P, (i + 1) * P)
                    last = self.nc.tensor.matmul(self.chip.ps[:, r, at], self.hot[:, r, 0, at], self.hot[:, r, 1, at],
                                                 start=True, stop=True)
                last.then_inc(self.done.sem, 1)

        body(0, first=True)
        with pe.Fori(1, self.SETS // 2) as it:
            body(it)

    def act(self, act, link):
        act.wait_ge(self.chip.stage_done, self.index)

        def body(it):
            for r in range(2):
                n = it * 2 + r
                act.wait_ge(self.done.sem, self.done.at(n + 1))
                self.nc.scalar.activation(self.gates[:, bass.ds(n * 4 * NKEYS, 4 * NKEYS)], self.chip.ps[:, r, :], ACT.Copy)\
                    .then_inc(self.kept.sem, 1)

        with act.Fori(0, self.SETS // 2) as it:
            body(it)
        act.wait_ge(self.kept.sem, self.kept.at(self.SETS))
        act.sem_inc(self.chip.stage_done, 1)


class PeerExperts(Stage):

    blocks = BLOCKS["experts"]

    def __init__(self, chip):
        super().__init__(chip)
        self.z = chip.at(G_Z, KD, N)
        self.gates = chip.at(G_GATES, N, NKEYS)
        self.gelu, self.act_ = chip.at(G_ACT, 2, N), chip.at(G_ACT + 2 * N, 2, N)
        self.zero = chip.at(G_HOT, P)
        n = self.blocks
        self.zeroed = chip.signals("expert_zeroed", 1)
        self.closed = chip.signals("expert_closed", 1)
        self.up_done = chip.signals("expert_up_done", n)
        self.gelu_ready = chip.signals("expert_gelu_ready", n)
        self.act_ready = chip.signals("expert_act_ready", n)

    def out(self, m):
        return self.chip.ps[:, 4 + m // 2, (m % 2) * N:(m % 2 + 1) * N]

    def pe(self, pe):
        nc, c, f = self.nc, self.chip, self.b0 % RING
        pe.wait_ge(self.chip.stage_done, self.index)
        pe.wait_ge(self.zeroed.sem, self.zeroed.at(1))

        def add_zero(start):
            for bank in range(4, 8):
                last = nc.tensor.matmul(c.ps[:, bank, :], self.zero, self.z[:, 0:2, :].rearrange("p k n -> p (k n)"),
                                        start=start, stop=not start)
            return last

        def up(it, r, wait):
            b = it * RING + r
            pe.wait_ge(c.loaded[(f + r) % RING], (it + self.b0 // RING + (f + r) // RING + 1) * 16)
            if wait:
                pe.wait_ge(self.gelu_ready.sem, self.gelu_ready.at(b - 1))
            for k in range(KD):
                last = nc.tensor.matmul(c.ps[:, r % 2, 0:N], c.ring[:, (f + r) % RING, k, :], self.z[:, k, :],
                                        start=k == 0, stop=k == KD - 1)
            last.then_inc(self.up_done.sem, 1)

        def down(it, r):
            pe.wait_ge(self.act_ready.sem, self.act_ready.at(it * RING + r + 1))
            for m in range(KD):
                last = nc.tensor.matmul(self.out(m), c.ring[:, (f + r) % RING, KD + m, :], self.act_[:, r % 2, :],
                                        start=False, stop=False)
            last.then_inc(self.chip.block_done, 1)

        add_zero(True)
        for r in range(RING):
            up(0, r, wait=r >= 2)
            if r:
                down(0, r - 1)
        with pe.Fori(1, self.blocks // RING) as it:
            for r in range(RING):
                up(it, r, wait=True)
                down(it - 1 if r == 0 else it, (r - 1) % RING)
        down(self.blocks // RING - 1, RING - 1)
        add_zero(False).then_inc(self.closed.sem, 1)

    def act(self, act, link):
        act.wait_ge(self.chip.stage_done, self.index)

        def body(it, first=False):
            for r in range(RING):
                b = it * RING + r
                act.wait_ge(self.up_done.sem, self.up_done.at(b + 1))
                if not (first and r < 2):
                    act.wait_ge(self.act_ready.sem, self.act_ready.at(b - 1))
                self.nc.scalar.activation(self.gelu[:, r % 2, :], self.chip.ps[:, r % 2, 0:N], ACT.Gelu)\
                    .then_inc(self.gelu_ready.sem, 1)

        body(0, first=True)
        with act.Fori(1, self.blocks // RING) as it:
            body(it)

    def dve(self, dve, link):
        v, c = self.nc.vector, self.chip
        dve.wait_ge(self.chip.stage_done, self.index)
        v.memset(self.zero, 0.0).then_inc(self.zeroed.sem, 1)

        def body(it, first=False):
            for r in range(RING):
                b = it * RING + r
                dve.wait_ge(self.gelu_ready.sem, self.gelu_ready.at(b + 1))
                if not (first and r < 2):
                    dve.wait_ge(c.block_done, b - 1 + self.b0)
                v.tensor_tensor(self.act_[:, r % 2, :], self.gelu[:, r % 2, :],
                                self.gates[:, :, bass.ds(b, 1)].rearrange("p t a -> p (t a)"), ALU.mult)\
                    .then_inc(self.act_ready.sem, 1)

        body(0, first=True)
        with dve.Fori(1, self.blocks // RING) as it:
            body(it)
        dve.wait_ge(self.closed.sem, self.closed.at(1))
        x = c.x[:, :, 0:N]
        v.tensor_tensor(x, x, c.ps[:, 4:8, :].rearrange("p b (m n) -> p (b m) n", n=N), ALU.add).then_inc(self.chip.stage_done, 1)


def second_norm(chip, out, gain, sq, small):
    small = [chip.at(small + i * N, N) for i in range(3)]
    return Norm(chip, chip.at(out, KD, N), chip.at(sq, KD, N), small, N, gain=gain)


def second_network(chip):
    vec = chip.vec[:]
    stages = [second_norm(chip, B_U, columns(vec, "final_g"), B_SQ, B_SMALL), Replace(chip)]
    for layer in range(DEPTH):
        stages += [LoadTables(chip), second_norm(chip, B_U, columns(vec, "ln1", layer, KD), B_SQ, B_SMALL), ProjectIn(chip),
                   Attention(chip, layer), Rwkv(chip, layer)]
        merge = Merge(chip)
        stages += [merge, Project(chip, merge.merged, KD, N),
                   second_norm(chip, G_Z, columns(vec, "ln2", layer, KD), G_SQ, G_SMALL),
                   PeerRoute(chip), PeerGates(chip), PeerExperts(chip)]
    final = second_norm(chip, B_U, columns(vec, "lnf"), B_SQ, B_SMALL)
    return stages + [final, Finish(chip, final.u)]


class Replace(Stage):

    def dve(self, dve, link):
        dve.wait_ge(self.chip.stage_done, self.index)
        self.nc.vector.tensor_copy(self.chip.x[:, :, 0:N], self.chip.at(B_U, KD, N)).then_inc(self.chip.stage_done, 1)


def second_weights(i):
    for layer in range(DEPTH):
        w = i["w_in_2"][layer]
        cut = lambda a, n: w[:, a:a + n]
        pad = lambda a: np.concatenate([a, np.zeros((D, P - a.shape[1]), np.float32)], axis=1)
        heads = lambda a: a.reshape(D, 2, 4, DH).transpose(0, 2, 1, 3).reshape(D, 8 * DH)
        n0 = 14 * P
        nq, (kc, vc, ks, vs, kw, vw) = cut(n0, 512), [cut(n0 + 512 + P * j, P) for j in range(6)]
        gate = cut(n0 + 1280, 24)
        s0 = n0 + 1304
        sq, sk, sv = cut(s0, 512), cut(s0 + 512, P), cut(s0 + 640, P)
        both = [np.concatenate([kc[:, g * DH:(g + 1) * DH], vc[:, g * DH:(g + 1) * DH]], axis=1) for g in range(2)]
        yield pairs(np.concatenate([cut(0, n0), heads(nq), *both, ks, kw, heads(sq), sk, np.zeros((D, P), np.float32),
                                    vs, vw, pad(gate), sv, cut(s0 + 768, 3 * D)], axis=1))
        kv = np.concatenate([i[n][layer].reshape(CMP_LEN, DH, 2, P) for n in ("nsa_ck_w1_2", "nsa_cv_w1_2")], axis=1)
        yield kv.transpose(0, 2, 1, 3).reshape(4, TPB, P, P).transpose(0, 2, 1, 3)
        ck, cv = (i[n][layer].reshape(2, P, DH).transpose(1, 0, 2) for n in ("nsa_ck_w2_2", "nsa_cv_w2_2"))
        small = np.zeros((1, P, TPB, P), np.float32)
        small[0, :, 0:2, :DH], small[0, :, 0:2, DH:], small[0, :, 2:4, :DH] = ck, ck, cv
        yield small
        ranks = np.zeros((1, P, TPB, P), np.float32)
        ranks[0, :64, 0:4], ranks[0, 64:, 0:4] = (i[n][layer].reshape(64, 4, P) for n in ("rwkv_w2_2", "rwkv_a2_2"))
        ranks[0, :, 4:8] = i["rwkv_g2_2"][layer].reshape(P, 4, P)
        yield ranks
        rows_ = lambda a: a.reshape(2, 4, DH, D).transpose(1, 0, 2, 3).reshape(8 * DH, D)
        for a in (i["w_br_a_2"][layer], rows_(i["w_br_b_2"][layer]), rows_(i["w_br_c_2"][layer])):
            yield a.reshape(4, P, 2, 4, P).transpose(2, 1, 3, 0, 4).reshape(2, P, TPB, P)
        yield rows(i["w_out_2"][layer])
        yield pairs(i["peer_wq_2"][layer])
        yield i["peer_subkeys_2"][layer].reshape(TPB, P, P).transpose(2, 0, 1)[None]
        u = i["peer_u_2"][layer].reshape(P, NKEYS, KD, P).transpose(1, 3, 2, 0)
        v = i["peer_v_2"][layer].reshape(P, NKEYS, KD, P).transpose(1, 0, 2, 3)
        yield np.concatenate([u, v], axis=2)


def second_constants():
    p = np.arange(P)
    s, t = p[:, None], p[None, :]
    same = s // CH == t // CH
    parts = [same & (s < t), same & (s <= t)]
    for n in (1, 2, 4, 8, 16):
        parts.append((s // (2 * n) == t // (2 * n)) & (s % (2 * n) < n) & (t % (2 * n) >= n))
    end = np.arange(16) * CMP_STRIDE + CMP_LEN - 1
    seen = [np.where(end[None, :] <= (p + k * P)[:, None], 0.0, NEG) for k in range(NT)]
    return np.concatenate([x.astype(np.float32) for x in parts] + seen, axis=1)


N_INPUT_DMAS = 5


class Finish(Stage):

    def __init__(self, chip, out):
        super().__init__(chip)
        self.out = out
        self.stored = chip.signals("out_stored", 16)

    def act(self, act, link):
        act.wait_ge(self.chip.stage_done, self.index)
        act.dma_start(self.chip.io["out"], self.out).then_inc(self.stored.sem, 16)
        act.wait_ge(self.stored.sem, self.stored.at(16))


def first_network(chip):
    stages = [Start(chip)]
    for layer in range(DEPTH):
        last = layer == DEPTH - 1
        stages.append(Modulation(chip, layer))
        stages += feed_forward(chip, 2 * N, 0)
        stages.append(first_norm(chip, 2 * N, 1))
        if layer == 0:
            fourier = Fourier(chip)
            stages += [fourier, Project(chip, fourier.f, KD, 2 * N, gate=5)]
        else:
            retention = Retention(chip)
            stages += [retention, Project(chip, retention.o, RH * RDV // P, N, gate=5)]
        stages += feed_forward(chip, N if last else 2 * N, 2)
    return stages


def program(nc, io):
    ctx = ExitStack()
    with ctx:
        chip = Chip(nc, ctx, io)
        stages = first_network(chip) + second_network(chip)
        setup_tables = [(chip.x[:], io["x"]), (chip.vec[:], io["vec"]), (chip.cst[:], io["cst"]),
                        (chip.at(A_CST1, NCST1), io["cst1"]), (chip.at(A_WORK + 16 * BIASW, 16 * P + BIASW), io["bias_in"])]
        block = ctx.enter_context(nc.Block())

        @block.sync
        def _(sp):
            assert len(setup_tables) == N_INPUT_DMAS
            for to, of in setup_tables:
                sp.dma_start(to, of).then_inc(chip.inputs_loaded, 16)
            for b in range(RING):
                sp.dma_start(chip.ring[:, b], io["weights"][b]).then_inc(chip.loaded[b], 16)
            rounds = chip.n_blocks // RING
            with sp.Fori(1, rounds) as i:
                for r in range(RING):
                    sp.wait_ge(chip.block_done, (i - 1) * RING + r + 1)
                    sp.dma_start(chip.ring[:, r], io["weights"][bass.ds(i * RING + r, 1)].rearrange("a p t c -> p (a t) c"))\
                        .then_inc(chip.loaded[r], 16)
            for b in range(rounds * RING, chip.n_blocks):
                sp.wait_ge(chip.block_done, b - RING + 1)
                sp.dma_start(chip.ring[:, b % RING], io["weights"][b]).then_inc(chip.loaded[b % RING], 16)

        @block.tensor
        def _(pe):
            for s in stages:
                s.pe(pe)

        @block.scalar
        def _(act):
            link = Link(act, chip.links["act"])
            for s in stages:
                s.act(act, link)

        @block.vector
        def _(dve):
            link = Link(dve, chip.links["dve"])
            for s in stages:
                s.dve(dve, link)

        @block.gpsimd
        def _(pool):
            link = Link(pool, chip.links["pool"])
            for s in stages:
                s.pool(pool, link)
    return chip


def pairs(w):
    k, m = w.shape[0] // P, w.shape[1] // (2 * P)
    return w.reshape(k, P, m, 2, P).transpose(2, 1, 3, 0, 4).reshape(m, P, 2 * k, P)


def rows(w):
    return w.reshape(w.shape[0] // (2 * P), 2, P, KD, P).transpose(0, 2, 1, 3, 4).reshape(-1, P, TPB, P)


def halves(w):
    return w.reshape(KD, P, 2, KF, P).transpose(3, 1, 2, 0, 4).reshape(KF, P, TPB, P)


def retention_in(w):
    qk, v, g = w[:, :2 * D], w[:, 2 * D:2 * D + RH * RDV], w[:, 2 * D + RH * RDV:]
    v = v.reshape(2, 4, P, RH, 4, P).transpose(3, 0, 2, 1, 4, 5).reshape(2 * RH, P, TPB, P)
    return np.concatenate([pairs(qk), v, pairs(g)])


def first_weights(i):
    for layer in range(DEPTH):
        yield pairs(i["w_mod"][layer])
        yield halves(i["ffn_w_in"][layer, 0])
        yield rows(i["ffn_w_out"][layer, 0])
        if layer == 0:
            yield rows(i["fnet_w_out"][0])
        else:
            yield retention_in(i["ret_w_in"][0])
            yield rows(i["ret_w_out"][0])
        yield halves(i["ffn_w_in"][layer, 1])
        yield rows(i["ffn_w_out"][layer, 1])


def features(v):
    return np.asarray(v).reshape(-1, P).T


def vector_table(i):
    cond = np.stack([features(i["c"]), features(i["c_ctx"])], axis=2).reshape(P, -1)
    pe = np.concatenate([np.concatenate([i["nsa_pe_k_2"][l].T, i["nsa_pe_v_2"][l].T]) for l in range(DEPTH)], axis=1)
    wide = lambda a: np.broadcast_to(np.asarray(a).reshape(1, -1), (P, np.asarray(a).size))
    sinks = i["swa_sinks_2"]
    parts = {"cond": cond, "b_mod": features(i["b_mod"]), "norm_g": features(i["norm_g"]),
             "final_g": features(i["final_norm_g"]), "ln1": features(i["ln1_w_2"]), "ln2": features(i["ln2_w_2"]),
             "lnf": features(i["lnf_w_2"]), "mu": features(i["rwkv_mu_2"]), "w0": features(i["rwkv_w0_2"]),
             "a0": features(i["rwkv_a0_2"]), "k_k": features(i["rwkv_k_k_2"]), "k_a": features(i["rwkv_k_a_2"]),
             "r_k": features(i["rwkv_r_k_2"]), "ln_w": features(i["rwkv_ln_w_2"]), "ln_b": features(i["rwkv_ln_b_2"]),
             "pe": pe, "decay": wide(i["ret_decay_logit"]), "sinks": wide(sinks)}
    out = np.concatenate([parts[n] for n in VEC], axis=1)
    assert out.shape == (P, NVEC), out.shape
    return np.ascontiguousarray(out, dtype=np.float32)


def constants():
    f = np.float32
    p = np.arange(P)
    cst = np.stack([np.eye(P), np.ones((P, P)), p[:, None] // DH == p[None, :] // DH,
                    np.broadcast_to(p[None, :], (P, P))], axis=1).astype(f)
    a = 2 * np.pi * np.outer(p, p) / P
    dft = np.concatenate([np.cos(a), np.sin(a)], axis=1)
    n = np.arange(N)
    b = 2 * np.pi * np.outer(n, n) / N
    norm = 1 / math.sqrt(N * P)
    cosn, sinn = ((t * norm).reshape(NT, P, N).transpose(1, 0, 2).reshape(P, -1) for t in (np.cos(b), -np.sin(b)))
    perm = np.zeros((P, P))
    perm[p[:64] + 64, p[:64]] = -1
    perm[p[:64], p[:64] + 64] = 1
    freq = np.exp(-f(math.log(10000.0)) * np.arange(64, dtype=f) / f(64)).astype(f)
    ang = [(t.astype(f)[None, :] * np.tile(freq, 2)[:, None]).astype(f) for t in (n // 64, n % 64)]
    cos, sin = (np.concatenate([t(x) for x in ang], axis=1) for t in (np.cos, np.sin))
    m = np.arange(N)[:, None]
    expo = [np.maximum(n - m, 0), np.maximum(m - n, 0), n - m + N, N - n + m]
    expo = np.concatenate([e.reshape(NT, P, N).transpose(1, 0, 2).reshape(P, -1) for e in expo], axis=1)
    cst1 = np.concatenate([dft, cosn, sinn, perm, cos, sin, expo], axis=1).astype(f)
    assert cst1.shape == (P, NCST1)
    return {"cst": cst, "cst1": cst1, "cst2": second_constants()}


def bias_inputs(table):
    f = np.float32
    d = N - 1 - np.arange(BIASW)
    exact = BUCKETS // 2
    nf = np.maximum(d, exact).astype(f)
    large = exact + (np.log(nf / exact) / f(math.log(MAX_DIST / exact)) * (BUCKETS - exact)).astype(np.int32)
    bucket = np.where(d < exact, np.maximum(d, 0), np.minimum(large, BUCKETS - 1))
    hot = (bucket[None, :] == np.arange(BUCKETS)[:, None]) & (d >= 0)[None, :]
    hot = np.concatenate([hot, (d < 0)[None, :], (d >= SWA_WINDOW)[None, :]]).astype(f)
    masks = np.zeros((2, 16), f)
    masks[0], masks[1, 8:] = NEG, NEG
    left = np.concatenate([table, masks])
    out = np.zeros((P, 16 * P + BIASW), f)
    out[:BUCKETS + 2, :16 * P] = np.broadcast_to(left[:, :, None], (BUCKETS + 2, 16, P)).reshape(BUCKETS + 2, -1)
    out[:BUCKETS + 2, 16 * P:] = hot
    return out


def tokens_last(x):
    return np.asarray(x).reshape(-1, KD, P).transpose(2, 1, 0)


def stream(i):
    total = sum(w.shape[0] for w in _parts(i))
    out = np.zeros((total, P, TPB, P), np.float32)
    b = 0
    for w in _parts(i):
        out[b:b + len(w), :, :w.shape[2], :w.shape[3]] = w
        b += len(w)
    return out


def _parts(i):
    yield from first_weights(i)
    yield from second_weights(i)


def kernel(**inputs):
    import concourse.bacc as bacc
    from concourse.bass_utils import run_bass_kernel_spmd

    i = {k: np.asarray(v) for k, v in inputs.items()}
    arrays = {"x": np.ascontiguousarray(np.concatenate([tokens_last(i["x"]), tokens_last(i["ctx"])], axis=2)),
              "vec": vector_table(i), "bias_in": bias_inputs(i["rel_bias_2"]), "weights": stream(i)}
    arrays.update({k: np.ascontiguousarray(v, dtype=np.float32) for k, v in constants().items()})
    nc = bacc.Bacc("TRN2", target_bir_lowering=False, num_devices=1)
    io = {k: nc.dram_tensor(f"in_{k}", v.shape, F32, kind="ExternalInput").ap() for k, v in arrays.items()}
    io["out"] = nc.dram_tensor("out", (P, KD, N), F32, kind="ExternalOutput").ap()
    io["bias_scratch"] = nc.dram_tensor("bias_scratch", (P, 16, BIASW), F32, kind="Internal").ap()
    program(nc, io)
    r = run_bass_kernel_spmd(nc, [{f"in_{k}": v for k, v in arrays.items()}], core_ids=[0])
    return np.ascontiguousarray(r.results[0]["out"].transpose(2, 1, 0).reshape(1, N, D))
```

```python
import math
from contextlib import ExitStack

import numpy as np
import concourse.bass as bass
from concourse import mybir

F32 = mybir.dt.float32
F32R = mybir.dt.float32r
U32 = mybir.dt.uint32
ACT = mybir.ActivationFunctionType
ALU = mybir.AluOpType
AX = mybir.AxisListType

P = 128
D = 1024
N = 256
KD = D // P
NT = N // P
DEPTH = 2
N_MOD = 9
EPS = 1e-6
FF = 2816
KF = FF // P
TPB = 16
RING = 4
HALF = TPB // 2
ROUNDED = 2
ARENA = 35728

RH, RDK, RDV = 4, 256, 512
DH = 64
GN_EPS = 64e-5
HEADS = 8
CH = 32
NCH = N // CH
CMP_LEN, CMP_STRIDE = 32, 16
NCMP = N // CMP_STRIDE - CMP_LEN // CMP_STRIDE + 1
NEG = -1e30
BUCKETS, MAX_DIST = 32, 128
SWA_WINDOW = 128
NKEYS = 128
TOPK = 16
BIASW = 384

VEC = {}
_n = 0
for _name, _w in [("cond", 2 * KD), ("b_mod", DEPTH * 72), ("norm_g", DEPTH * 3 * KD), ("final_g", KD),
                  ("ln1", DEPTH * KD), ("ln2", DEPTH * KD), ("lnf", KD), ("mu", DEPTH * 14),
                  ("w0", DEPTH * 4), ("a0", DEPTH * 4), ("k_k", DEPTH * 4), ("k_a", DEPTH * 4),
                  ("r_k", DEPTH * 4), ("ln_w", DEPTH * 4), ("ln_b", DEPTH * 4), ("pe", DEPTH * 32),
                  ("decay", 8), ("sinks", DEPTH * 8)]:
    VEC[_name] = (_n, _n + _w)
    _n += _w
NVEC = _n

BLOCKS = {"mod": 36, "ffn_in": KF, "ffn_out": KF // 2, "fnet": KD // 2, "ret_in": 24, "ret_out": 8,
          "in2": 28, "cmp1": 4, "cmp2": 1, "rwkv": 1, "branch": 6, "out2": 4, "wq": 8, "keys": 1,
          "experts": NKEYS}


def columns(table, name, layer=0, width=None):
    a, b = VEC[name]
    if width is None:
        return table[:, a:b]
    return table[:, a + layer * width:a + (layer + 1) * width]


class Signals:

    def __init__(self, nc, ctx):
        self.nc, self.ctx, self.sems, self.total = nc, ctx, {}, {}

    def __call__(self, name, n):
        if name not in self.sems:
            self.sems[name] = self.ctx.enter_context(self.nc.semaphore(name))
            self.total[name] = 0
        base = self.total[name]
        self.total[name] += n
        return Share(self.sems[name], base)


class Share:
    def __init__(self, sem, base):
        self.sem, self.base = sem, base

    def at(self, k):
        return self.base + k


class Link:

    def __init__(self, eng, sem):
        self.eng, self.sem, self.n = eng, sem, 0

    def __call__(self, ins):
        self.n += 1
        ins.then_inc(self.sem, 1)
        self.eng.wait_ge(self.sem, self.n)


class Chip:

    def __init__(self, nc, ctx, io):
        self.nc, self.io = nc, io
        self.signals = Signals(nc, ctx)
        self.next_byte = -(-nc.sbuf_base // 32) * 32
        self.ring, self.ring_rest = self.place("ring", [P, RING, TPB, P], "ring_rest")
        self.x, self.x_parts = self.place("x", [P, KD, 2 * N], "x_parts")
        self.arena_byte = self.next_byte
        self.arena, = self.place("arena", [P, ARENA])
        self.named = {}
        self.rounded, = self.place("rounded", [P, ROUNDED, TPB, P], kind=F32R)
        self.vec, = self.place("vec", [P, NVEC])
        self.cst, = self.place("cst", [P, 4, P])
        self.ident, self.ones = self.cst[:, 0, :], self.cst[:, 1, :]
        self.headones, self.iota = self.cst[:, 2, :], self.cst[:, 3, :]
        self.mods, = self.place("mods", [P, N_MOD, KD, 2])
        self.ps = ctx.enter_context(nc.psum_tensor("ps", [P, 8, 512], F32))
        self.loaded = [ctx.enter_context(nc.semaphore(f"block_loaded{i}")) for i in range(RING)]
        self.rounded_done = [ctx.enter_context(nc.semaphore(f"{n}_half_rounded")) for n in ("first", "second")]
        self.rest_done = [ctx.enter_context(nc.semaphore(f"{n}_half_rest")) for n in ("first", "second")]
        self.block_done = ctx.enter_context(nc.semaphore("block_done"))
        self.stage_done = ctx.enter_context(nc.semaphore("stage_done"))
        self.inputs_loaded = ctx.enter_context(nc.semaphore("inputs_loaded"))
        self.links = {e: ctx.enter_context(nc.semaphore(f"{e}_link")) for e in ("act", "dve", "pool")}
        self.n_blocks = 0
        self.split_blocks = []
        self.n_stages = 0

    def place(self, name, shape, parts=None, kind=F32):
        at = self.next_byte
        self.next_byte += -(-int(np.prod(shape[1:])) // 8) * 32
        out = [self.nc.alloc_sbuf_tensor_at(name, shape, kind, offset=at)]
        if parts:
            out.append(self.nc.alloc_sbuf_tensor_at(parts, shape, F32R, offset=at))
        return out

    def parts_at(self, start, *shape, kind=F32R):
        key = start, shape, kind
        if key not in self.named:
            assert start + int(np.prod(shape)) <= ARENA, (start, shape)
            self.named[key] = self.nc.alloc_sbuf_tensor_at(f"part{len(self.named)}", [P, *shape], kind,
                                                           offset=self.arena_byte + 4 * start)
        return self.named[key][:]

    def at(self, start, *shape):
        size = int(np.prod(shape))
        assert start + size <= ARENA, (start, shape)
        v = self.arena[:, start:start + size]
        names = "abcd"[:len(shape)]
        if len(shape) > 1:
            v = v.rearrange(f"p ({' '.join(names)}) -> p {' '.join(names)}", **dict(zip(names, shape)))
        return v


class Stage:

    blocks = 0
    whole = 0
    next = None

    def __init__(self, chip):
        self.chip, self.nc = chip, chip.nc
        self.index = chip.n_stages
        chip.n_stages += 1
        self.b0 = chip.n_blocks
        chip.n_blocks += self.blocks
        self.split = self.blocks - self.whole
        self.s0 = len(chip.split_blocks)
        chip.split_blocks += [self.b0 + j for j in range(self.split)]
        self.led = False

    def arrival(self, j):
        b = self.b0 + j
        return b % RING, 16 * (b // RING + 1)

    def block_count(self, j):
        return self.b0 + j + 1

    def split_count(self, j):
        return self.s0 + j + 1

    def weights(self, j):
        return self.chip.rounded[:, (self.s0 + j) % ROUNDED], self.chip.ring_rest[:, (self.b0 + j) % RING]

    def round(self, act, j):
        c, s = self.chip, self.s0 + j
        if j >= self.split:
            return
        slot, count = self.arrival(j)
        act.wait_ge(c.loaded[slot], count)
        if s >= ROUNDED:
            act.wait_ge(c.block_done, c.split_blocks[s - ROUNDED] + 1)
        for h in range(2):
            half = slice(h * HALF, (h + 1) * HALF)
            self.nc.scalar.activation(c.rounded[:, s % ROUNDED, half], c.ring[:, slot, half], ACT.Copy)\
                .then_inc(c.rounded_done[h], 1)

    def lead(self, act):
        if not self.led:
            self.led = True
            for j in range(ROUNDED):
                self.round(act, j)

    def product(self, out, w, a, start, stop):
        mm = self.nc.tensor.matmul
        mm(out, w[0], a[0], start=start, stop=False)
        mm(out, w[0], a[1], start=False, stop=False)
        return mm(out, w[1], a[0], start=False, stop=stop)

    def leave_rest(self, r, h, count):
        c, half = self.chip, slice(h * HALF, (h + 1) * HALF)
        slot = (self.b0 + r) % RING
        self.nc.gpsimd.wait_ge(c.rounded_done[h], count)
        self.nc.gpsimd.tensor_tensor(c.ring_rest[:, slot, half], c.ring[:, slot, half],
                                     c.rounded[:, (self.s0 + r) % ROUNDED, half].bitcast(F32), ALU.subtract).then_inc(c.rest_done[h], 1)

    def pe(self, pe):
        pass

    def act(self, act, link):
        pass

    def dve(self, dve, link):
        pass

    def pool(self, pool, link):
        rounds = self.split // RING
        if rounds > 1:
            with pool.Fori(0, rounds) as it:
                for r in range(RING):
                    for h in range(2):
                        self.leave_rest(r, h, self.split_count(it * RING + r))
        else:
            rounds = 0
        for j in range(rounds * RING, self.split):
            for h in range(2):
                self.leave_rest(j, h, self.split_count(j))


A_CST1 = 0
CST1 = {"dft": (0, 256), "cosn": (256, 512), "sinn": (768, 512), "perm": (1280, 128),
        "rope_cos": (1408, 512), "rope_sin": (1920, 512)}
NCST1 = 2432
NEXPO = 4 * 2 * N
A_U = NCST1
A_SQ = A_U + KD * 2 * N
A_WORK = A_SQ + KD * 2 * N
A_SMALL = A_WORK
A_H = A_WORK
A_HR = A_H + KF * 2 * N
A_SILU = A_HR + KF * 2 * N


class Start(Stage):

    def __init__(self, chip):
        super().__init__(chip)
        self.row = chip.signals("bias_rows", 16)
        self.copied = chip.signals("bias_copied", 16)
        self.stored = chip.signals("bias_stored", 16)
        self.rows = chip.at(A_WORK, 16, BIASW)
        self.lhs = chip.at(A_WORK + 16 * BIASW, 16, P)
        self.hot = chip.at(A_WORK + 16 * BIASW + 16 * P, BIASW)

    def pe(self, pe):
        pe.wait_ge(self.chip.inputs_loaded, 16 * N_INPUT_DMAS)
        for h in range(16):
            if h >= 8:
                pe.wait_ge(self.copied.sem, self.copied.at(h - 7))
            self.nc.tensor.matmul(self.chip.ps[:, h % 8, 0:BIASW], self.lhs[0:34, h, :], self.hot[0:34, :],
                                  start=True, stop=True).then_inc(self.row.sem, 1)

    def act(self, act, link):
        act.wait_ge(self.chip.inputs_loaded, 16 * N_INPUT_DMAS)
        for h in range(16):
            act.wait_ge(self.row.sem, self.row.at(h + 1))
            self.nc.scalar.activation(self.rows[:, h, :], self.chip.ps[:, h % 8, 0:BIASW], ACT.Copy)\
                .then_inc(self.copied.sem, 1)
        act.wait_ge(self.copied.sem, self.copied.at(16))
        act.dma_start(self.chip.io["bias_scratch"], self.rows).then_inc(self.stored.sem, 16)
        act.wait_ge(self.stored.sem, self.stored.at(16))
        act.sem_inc(self.chip.stage_done, 1)

    def dve(self, dve, link):
        dve.wait_ge(self.chip.inputs_loaded, 16 * N_INPUT_DMAS)


class Modulation(Stage):

    blocks = BLOCKS["mod"]
    whole = blocks
    GROUPS = blocks // 2

    def __init__(self, chip, layer):
        super().__init__(chip)
        self.layer = layer
        self.silu = chip.signals("cond_ready", 1)
        self.cond = chip.at(A_WORK, KD, 2)
        self.rows = chip.at(A_WORK + KD * 2, self.GROUPS, 512)
        self.rows_kept = chip.signals("mod_rows_kept", self.GROUPS)
        self.turned = chip.signals("mod_turned", 1)

    def act(self, act, link):
        act.wait_ge(self.chip.stage_done, self.index)
        v = columns(self.chip.vec, "cond").rearrange("p (k s) -> p k s", s=2)
        self.nc.scalar.activation(self.cond, v, ACT.Silu).then_inc(self.silu.sem, 1)
        for g in range(self.GROUPS):
            act.wait_ge(self.chip.block_done, self.block_count(2 * g + 1))
            self.nc.scalar.activation(self.rows[0:2, g, :], self.chip.ps[0:2, g % 4, :], ACT.Copy)\
                .then_inc(self.rows_kept.sem, 1)

    def pe(self, pe):
        c, mm = self.chip, self.nc.tensor.matmul
        pe.wait_ge(self.chip.stage_done, self.index)
        pe.wait_ge(self.silu.sem, self.silu.at(1))

        def turn(g):
            pe.wait_ge(self.rows_kept.sem, self.rows_kept.at(g + 1))
            for m in range(4):
                at = 2 * (4 * g + m)
                last = mm(c.ps[:, 7, at:at + 2], self.rows[0:2, g, m * P:(m + 1) * P], c.ident[0:2, 0:2], start=True, stop=True)
            return last

        for g in range(self.GROUPS):
            if g >= 4:
                pe.wait_ge(self.rows_kept.sem, self.rows_kept.at(g - 3))
            for j in (2 * g, 2 * g + 1):
                slot, count = self.arrival(j)
                pe.wait_ge(c.loaded[slot], count)
                for k in range(4):
                    last = mm(c.ps[0:2, g % 4, :], self.cond[:, 4 * (j % 2) + k, :], c.ring[:, slot, 4 * k:4 * k + 4, :],
                              start=j % 2 == 0 and k == 0, stop=j % 2 == 1 and k == 3)
                last.then_inc(c.block_done, 1)
            if g:
                turn(g - 1)
        turn(self.GROUPS - 1).then_inc(self.turned.sem, 1)

    def dve(self, dve, link):
        c, nc = self.chip, self.nc
        dve.wait_ge(self.chip.stage_done, self.index)
        dve.wait_ge(self.turned.sem, self.turned.at(1))
        m = c.mods[:].rearrange("p j d s -> p (j d) s")
        b = columns(c.vec, "b_mod", self.layer, 72).unsqueeze(2).broadcast_to([P, 72, 2])
        link(nc.vector.tensor_tensor(m, c.ps[:, 7, 0:144].rearrange("p (m s) -> p m s", s=2), b, ALU.add))
        for n in range(3):
            g = columns(c.vec, "norm_g", 3 * self.layer + n, KD).unsqueeze(2).broadcast_to([P, KD, 2])
            scale, gate = c.mods[:, 3 * n + 1, :, :], c.mods[:, 3 * n + 2, :, :]
            link(nc.vector.tensor_scalar(scale, scale, 1.0, None, ALU.add))
            link(nc.vector.tensor_tensor(scale, scale, g, ALU.mult))
            if n != 1:
                link(nc.vector.tensor_scalar(gate, gate, 0.5, None, ALU.mult))
        dve.sem_inc(c.stage_done, 1)


class Norm(Stage):

    def __init__(self, chip, out, sq, small, tokens, mod=None, gain=None, parts=None, keep=False):
        super().__init__(chip)
        self.t, self.mod, self.gain, self.keep = tokens, mod, gain, keep
        self.u, self.sq, self.parts = out, sq, parts
        self.ms, self.rt, self.rstd = small
        self.squared = chip.signals("squared", 4)
        self.summed = chip.signals("squares_summed", 1)
        self.mean = chip.signals("mean_square_ready", 1)
        self.root = chip.signals("root_ready", 1)
        self.tiles = [(d, s) for d in range(KD) for s in range(tokens // N)]
        self.scaled = chip.signals("scaled", len(self.tiles))
        self.rounded = chip.signals("input_rounded", len(self.tiles) if parts else 0)
        self.x_kept = chip.signals("x_in_psum", 1 if keep else 0)

    def act(self, act, link):
        c, nc = self.chip, self.nc
        act.wait_ge(self.chip.stage_done, self.index)
        for d in range(0, KD, 2):
            nc.scalar.activation(self.sq[:, d:d + 2, :], c.x[:, d:d + 2, 0:self.t], ACT.Square)\
                .then_inc(self.squared.sem, 1)
        if self.next is not None:
            self.next.lead(act)
        act.wait_ge(self.mean.sem, self.mean.at(1))
        nc.scalar.activation(self.rt, self.ms, ACT.Sqrt).then_inc(self.root.sem, 1)
        if self.keep:
            act.wait_ge(self.x_kept.sem, self.x_kept.at(1))
        if self.parts or self.mod is not None:
            for i, (d, s) in enumerate(self.tiles):
                cols = slice(s * N, (s + 1) * N)
                bias = c.mods[:, 3 * self.mod, d, s:s + 1] if self.mod is not None else 0.0
                act.wait_ge(self.scaled.sem, self.scaled.at(i + 1))
                to = self.parts[0][:, d, cols] if self.parts else self.u[:, d, cols]
                last = nc.scalar.activation(to, self.u[:, d, cols], ACT.Identity, bias=bias)
                if self.parts:
                    last.then_inc(self.rounded.sem, 1)
            if not self.parts:
                last.then_inc(self.chip.stage_done, 1)

    def pe(self, pe):
        c, mm = self.chip, self.nc.tensor.matmul
        pe.wait_ge(self.chip.stage_done, self.index)
        for d in range(KD):
            if d % 2 == 0:
                pe.wait_ge(self.squared.sem, self.squared.at(d // 2 + 1))
            last = mm(c.ps[:, 0, 0:self.t], c.ones, self.sq[:, d, :], start=d == 0, stop=d == KD - 1)
        last.then_inc(self.summed.sem, 1)
        if self.keep:
            for b in range(4):
                last = mm(c.ps[:, 4 + b, :].rearrange("p (m n) -> p m n", m=2), c.ident, c.x[:, 2 * b:2 * b + 2, 0:N],
                          start=True, stop=False)
            last.then_inc(self.x_kept.sem, 1)

    def dve(self, dve, link):
        c, nc = self.chip, self.nc
        dve.wait_ge(self.chip.stage_done, self.index)
        dve.wait_ge(self.summed.sem, self.summed.at(1))
        nc.vector.tensor_scalar(self.ms, c.ps[:, 0, 0:self.t], 1.0 / D, EPS, ALU.mult, ALU.add)\
            .then_inc(self.mean.sem, 1)
        dve.wait_ge(self.root.sem, self.root.at(1))
        link(nc.vector.reciprocal(self.rstd, self.rt))
        for d, s in self.tiles:
            cols = slice(s * N, (s + 1) * N)
            gain = self.gain[:, d:d + 1] if self.mod is None else c.mods[:, 3 * self.mod + 1, d, s:s + 1]
            last = nc.vector.scalar_tensor_tensor(self.u[:, d, cols], c.x[:, d, cols], gain, self.rstd[:, cols],
                                                  ALU.mult, ALU.mult)
            last.then_inc(self.scaled.sem, 1)
        if self.parts:
            for i, (d, s) in enumerate(self.tiles):
                cols = slice(s * N, (s + 1) * N)
                shift = c.mods[:, 3 * self.mod, d, s:s + 1] if self.mod is not None else 0.0
                dve.wait_ge(self.rounded.sem, self.rounded.at(i + 1))
                last = nc.vector.scalar_tensor_tensor(self.parts[1][:, d, cols], self.u[:, d, cols], shift,
                                                      self.parts[0].bitcast(F32)[:, d, cols], ALU.add, ALU.subtract)
            last.then_inc(self.chip.stage_done, 1)
        elif self.mod is None:
            dve.wait_ge(self.scaled.sem, self.scaled.at(len(self.tiles)))
            dve.sem_inc(self.chip.stage_done, 1)


def first_input(chip, tokens):
    return tuple(chip.parts_at(a, KD, 2 * N)[:, :, 0:tokens] for a in (A_SQ, A_U))


def first_norm(chip, tokens, mod, split=True):
    small = [chip.at(A_SMALL + i * 2 * N, 2 * N)[:, 0:tokens] for i in range(3)]
    return Norm(chip, chip.at(A_U, KD, 2 * N)[:, :, 0:tokens], chip.at(A_SQ, KD, 2 * N)[:, :, 0:tokens], small,
                tokens, mod=mod, parts=first_input(chip, tokens) if split else None)


class FeedForwardIn(Stage):

    blocks = BLOCKS["ffn_in"]

    def __init__(self, chip, tokens):
        super().__init__(chip)
        self.t = tokens
        self.u = first_input(chip, tokens)
        cut = lambda v: v[:, :, 0:tokens]
        self.silu = cut(chip.at(A_SILU, 2, 2 * N))
        self.h = cut(chip.parts_at(A_H, KF, 2 * N, kind=F32))
        self.parts = cut(chip.parts_at(A_HR, KF, 2 * N)), cut(chip.parts_at(A_H, KF, 2 * N))
        self.silu_ready = chip.signals("silu_ready", KF)
        self.h_ready = chip.signals("hidden_ready", KF)
        self.h_rounded = chip.signals("hidden_rounded", KF)

    def pe(self, pe):
        c = self.chip
        pe.wait_ge(self.chip.stage_done, self.index)
        for j in range(KF):
            whi, wlo = self.weights(j)
            if j >= 2:
                pe.wait_ge(self.h_ready.sem, self.h_ready.at(j - 1))
            for half in range(2):
                pe.wait_ge(c.rest_done[half], self.split_count(j))
                for k in range(KD):
                    i = half * KD + k
                    last = self.product(c.ps[:, 2 * (j % 2) + half, 0:self.t], (whi[:, i, :], wlo[:, i, :]),
                                        (self.u[0][:, k, :], self.u[1][:, k, :]), k == 0, k == KD - 1)
            last.then_inc(c.block_done, 1)

    def act(self, act, link):
        c, nc = self.chip, self.nc
        self.lead(act)
        act.wait_ge(c.stage_done, self.index)
        for j in range(KF):
            act.wait_ge(c.block_done, self.block_count(j))
            if j >= 2:
                act.wait_ge(self.h_ready.sem, self.h_ready.at(j - 1))
            nc.scalar.activation(self.silu[:, j % 2, :], c.ps[:, 2 * (j % 2), 0:self.t], ACT.Silu)\
                .then_inc(self.silu_ready.sem, 1)
            self.round(act, j + ROUNDED)
            act.wait_ge(self.h_ready.sem, self.h_ready.at(j + 1))
            nc.scalar.activation(self.parts[0][:, j, :], self.h[:, j, :], ACT.Copy).then_inc(self.h_rounded.sem, 1)

    def dve(self, dve, link):
        v = self.nc.vector
        dve.wait_ge(self.chip.stage_done, self.index)
        for j in range(KF):
            dve.wait_ge(self.silu_ready.sem, self.silu_ready.at(j + 1))
            v.tensor_tensor(self.h[:, j, :], self.chip.ps[:, 2 * (j % 2) + 1, 0:self.t], self.silu[:, j % 2, :], ALU.mult)\
                .then_inc(self.h_ready.sem, 1)
            dve.wait_ge(self.h_rounded.sem, self.h_rounded.at(j + 1))
            last = v.tensor_tensor(self.parts[1][:, j, :], self.h[:, j, :], self.parts[0].bitcast(F32)[:, j, :], ALU.subtract)
        last.then_inc(self.chip.stage_done, 1)


class Project(Stage):

    def __init__(self, chip, inp, tiles, tokens, gate=None):
        self.blocks = tiles // 2
        super().__init__(chip)
        self.inp, self.t, self.gate = inp, tokens, gate

    def pe(self, pe):
        c = self.chip
        pe.wait_ge(self.chip.stage_done, self.index)
        for j in range(self.blocks):
            whi, wlo = self.weights(j)
            for k in range(2):
                pe.wait_ge(c.rest_done[k], self.split_count(j))
                for m in range(KD):
                    i = k * KD + m
                    last = self.product(c.ps[:, m, 0:self.t], (whi[:, i, :], wlo[:, i, :]),
                                        (self.inp[0][:, 2 * j + k, :], self.inp[1][:, 2 * j + k, :]),
                                        j == 0 and k == 0, j == self.blocks - 1 and k == 1)
            last.then_inc(c.block_done, 1)

    def act(self, act, link):
        self.lead(act)
        for j in range(ROUNDED, self.blocks):
            self.round(act, j)

    def dve(self, dve, link):
        c = self.chip
        dve.wait_ge(self.chip.stage_done, self.index)
        dve.wait_ge(self.chip.block_done, self.block_count(self.blocks - 1))
        for m in range(KD):
            for s in range(self.t // N):
                cols = slice(s * N, (s + 1) * N)
                gate = 1.0 if self.gate is None else c.mods[:, self.gate, m, s:s + 1]
                last = self.nc.vector.scalar_tensor_tensor(c.x[:, m, cols], c.ps[:, m, cols], gate, c.x[:, m, cols],
                                                           ALU.mult, ALU.add)
        last.then_inc(self.chip.stage_done, 1)


def feed_forward(chip, tokens, mod):
    norm, hidden = first_norm(chip, tokens, mod), FeedForwardIn(chip, tokens)
    return [norm, hidden, Project(chip, hidden.parts, KF, tokens, gate=3 * mod + 2)]


class Fourier(Stage):

    def __init__(self, chip):
        super().__init__(chip)
        cst = chip.at(A_CST1, NCST1)
        self.dft = cst[:, 0:256]
        self.cosn = cst[:, 256:768].rearrange("p (t n) -> p t n", t=NT)
        self.sinn = cst[:, 768:1280].rearrange("p (t n) -> p t n", t=NT)
        self.u = chip.at(A_U, KD, 2 * N)
        self.half = chip.at(A_WORK, 4, NT, 2 * P)
        a_f = A_WORK + 4 * NT * 2 * P
        self.parts = tuple(chip.parts_at(a_f + i * KD * 2 * N, KD, 2 * N) for i in range(2))
        n = 2 * KD
        self.by_feature = chip.signals("dft_by_feature", n)
        self.half_ready = chip.signals("dft_half_ready", n)
        self.by_token = chip.signals("dft_by_token", n)
        self.rounded = chip.signals("dft_rounded", n)
        self.kept = chip.signals("dft_kept", n)

    def pe(self, pe):
        pe.wait_ge(self.chip.stage_done, self.index)
        ps, n = self.chip.ps, 2 * KD

        def along_features(i):
            s, g = divmod(i, KD)
            if i >= 4:
                pe.wait_ge(self.half_ready.sem, self.half_ready.at(i - 3))
            for t in range(NT):
                last = self.nc.tensor.matmul(ps[:, i % 4, t * 256:(t + 1) * 256],
                                             self.u[:, g, s * N + t * P:s * N + (t + 1) * P], self.dft,
                                             start=True, stop=True)
            last.then_inc(self.by_feature.sem, 1)

        def along_tokens(i):
            pe.wait_ge(self.half_ready.sem, self.half_ready.at(i + 1))
            if i >= 4:
                pe.wait_ge(self.kept.sem, self.kept.at(i - 3))
            for t in range(NT):
                self.nc.tensor.matmul(ps[:, 4 + i % 4, 0:N], self.half[:, i % 4, t, 0:P], self.cosn[:, t, :],
                                      start=t == 0, stop=False)
                last = self.nc.tensor.matmul(ps[:, 4 + i % 4, 0:N], self.half[:, i % 4, t, P:2 * P], self.sinn[:, t, :],
                                             start=False, stop=t == NT - 1)
            last.then_inc(self.by_token.sem, 1)

        along_features(0)
        for i in range(n):
            if i + 1 < n:
                along_features(i + 1)
            along_tokens(i)

    def act(self, act, link):
        ps, copy = self.chip.ps, self.nc.scalar.activation
        act.wait_ge(self.chip.stage_done, self.index)

        def half(i):
            act.wait_ge(self.by_feature.sem, self.by_feature.at(i + 1))
            if i >= 4:
                act.wait_ge(self.by_token.sem, self.by_token.at(i - 3))
            copy(self.half[:, i % 4].rearrange("p t c -> p (t c)"), ps[:, i % 4, :], ACT.Copy).then_inc(self.half_ready.sem, 1)

        half(0)
        self.next.lead(act)
        for i in range(2 * KD):
            if i + 1 < 2 * KD:
                half(i + 1)
            s, g = divmod(i, KD)
            act.wait_ge(self.by_token.sem, self.by_token.at(i + 1))
            copy(self.parts[0][:, g, s * N:(s + 1) * N], ps[:, 4 + i % 4, 0:N], ACT.Copy).then_inc(self.rounded.sem, 1)

    def dve(self, dve, link):
        dve.wait_ge(self.chip.stage_done, self.index)
        for i in range(2 * KD):
            s, g = divmod(i, KD)
            cols = slice(s * N, (s + 1) * N)
            dve.wait_ge(self.rounded.sem, self.rounded.at(i + 1))
            last = self.nc.vector.tensor_tensor(self.parts[1][:, g, cols], self.chip.ps[:, 4 + i % 4, 0:N],
                                                self.parts[0].bitcast(F32)[:, g, cols], ALU.subtract)
            last.then_inc(self.kept.sem, 1)
        dve.wait_ge(self.kept.sem, self.kept.at(2 * KD))
        dve.sem_inc(self.chip.stage_done, 1)


R_P = A_U
R_O = R_P + 2 * 4 * N
R_K = A_WORK
R_V = R_K + KD * 2 * N
R_G = R_V + 4 * RH * RDV
R_D = R_G + 16 * N
R_TMP = R_D + RH * 4 * N
R_LG = R_TMP + 2 * 512
R_EXPO = R_LG + 32
assert R_O + 16 * N <= R_K


class Retention(Stage):

    blocks = BLOCKS["ret_in"]

    def __init__(self, chip):
        super().__init__(chip)
        at, sig = chip.at, chip.signals
        cst = at(A_CST1, NCST1)
        self.expo_loaded = sig("expo_loaded", 16)
        self.perm = cst[:, 1280:1408]
        self.cos = cst[:, 1408:1920].rearrange("p (a n) -> p a n", a=2)
        self.sin = cst[:, 1920:2432].rearrange("p (a n) -> p a n", a=2)
        self.expo = at(R_EXPO, 4, 2 * N)
        self.u = first_input(chip, 2 * N)
        self.q, self.k = chip.x[:, :, N:], at(R_K, KD, 2 * N)
        self.v = at(R_V, 4, RH * RDV)
        self.g, self.o = at(R_G, 16, N), at(R_O, 16, N)
        self.d = at(R_D, RH, 4 * N)
        self.tmp = at(R_TMP, 2, 512)
        self.lg = at(R_LG, 4, 8)
        self.p = at(R_P, 2, 4 * N)
        self.sq = at(R_V, 16, N)
        self.parts = chip.parts_at(R_V + 16 * N, 16, N), chip.parts_at(R_O, 16, N)
        self.st = at(R_K, 3, RH * N)
        self.q_kept = sig("ret_q_kept", 4)
        self.k_kept = sig("ret_k_kept", 4)
        self.turned = sig("ret_turned", 16)
        self.rope_done = sig("ret_rope_done", 16)
        self.v_kept = sig("ret_v_kept", 16)
        self.g_kept = sig("ret_g_kept", 8)
        self.lg_exp = sig("ret_lg_exp", 1)
        self.lg_in = sig("ret_lg_in", 1)
        self.lg_out = sig("ret_lg_out", 1)
        self.d_in = sig("ret_d_in", RH)
        self.d_exp = sig("ret_d_exp", RH)
        self.scores = sig("ret_scores", RH)
        self.weighted = sig("ret_weighted", RH)
        self.o_sum = sig("ret_o_sum", RH)
        self.o_kept = sig("ret_o_kept", RH)
        self.mean = sig("ret_mean", 1)
        self.centred = sig("ret_centred", 1)
        self.squares = sig("ret_squares", 1)
        self.var = sig("ret_var", 1)
        self.var_in = sig("ret_var_in", 1)
        self.root = sig("ret_root", 1)
        self.gated = sig("ret_gated", RH)
        self.rounded = sig("ret_rounded", RH)

    def pe(self, pe):
        nc, ps = self.nc, self.chip.ps
        pe.wait_ge(self.chip.stage_done, self.index)

        def columns_of(j, out, tokens):
            whi, wlo = self.weights(j)
            for e in range(2):
                pe.wait_ge(self.chip.rest_done[e], self.split_count(j))
                for k in range(KD):
                    i = e * KD + k
                    last = self.product(out(e), (whi[:, i, :], wlo[:, i, :]),
                                        (self.u[0][:, k, 0:tokens], self.u[1][:, k, 0:tokens]), k == 0, k == KD - 1)
            last.then_inc(self.chip.block_done, 1)

        for j in range(4):
            columns_of(j, lambda e: ps[:, j, e * N:(e + 1) * N], N)
        for j in range(4):
            if j >= 2:
                pe.wait_ge(self.k_kept.sem, self.k_kept.at(j - 1))
            columns_of(4 + j, lambda e: ps[:, 4 + 2 * (j % 2) + e, :], 2 * N)
        pe.wait_ge(self.q_kept.sem, self.q_kept.at(4))
        pe.wait_ge(self.k_kept.sem, self.k_kept.at(4))
        for i in range(16):
            if i >= 4:
                pe.wait_ge(self.rope_done.sem, self.rope_done.at(i - 3))
            t = self.q[:, i, :] if i < KD else self.k[:, i - KD, 0:N]
            nc.tensor.matmul(ps[:, i % 4, 0:N], self.perm, t, start=True, stop=True).then_inc(self.turned.sem, 1)
        pe.wait_ge(self.rope_done.sem, self.rope_done.at(16))
        for h in range(RH):
            if h >= 2:
                pe.wait_ge(self.v_kept.sem, self.v_kept.at(4 * (h - 1)))
            for j in range(2):
                w = self.weights(8 + 2 * h + j)
                for t in range(4):
                    for k in range(4):
                        if t == 0 and k % 2 == 0:
                            pe.wait_ge(self.chip.rest_done[k // 2], self.split_count(8 + 2 * h + j))
                        u = [x[:, 4 * j + k, t * P:(t + 1) * P] for x in self.u]
                        last = self.product(ps[:, 4 * (h % 2) + t, :], u, [x[:, 4 * k:4 * k + 4, :] for x in w],
                                            j == 0 and k == 0, j == 1 and k == 3)
                last.then_inc(self.chip.block_done, 1)
        pe.wait_ge(self.v_kept.sem, self.v_kept.at(16))
        for j in range(8):
            if j >= 4:
                pe.wait_ge(self.g_kept.sem, self.g_kept.at(j - 3))
            columns_of(16 + j, lambda e: ps[:, j % 4, e * N:(e + 1) * N], N)
        pe.wait_ge(self.g_kept.sem, self.g_kept.at(8))
        for h in range(RH):
            if h >= 1:
                pe.wait_ge(self.weighted.sem, self.weighted.at(h))
            for m in range(4):
                for e in range(2):
                    last = nc.tensor.matmul(ps[:, m // 2, (m % 2) * N:(m % 2 + 1) * N],
                                            self.k[:, 2 * h + e, m * P:(m + 1) * P], self.q[:, 2 * h + e, :],
                                            start=e == 0, stop=e == 1)
            last.then_inc(self.scores.sem, 1)
            pe.wait_ge(self.weighted.sem, self.weighted.at(h + 1))
            if h >= 1:
                pe.wait_ge(self.o_kept.sem, self.o_kept.at(h))
            for e in range(4):
                for m in range(4):
                    last = nc.tensor.matmul(ps[:, 2 + e // 2, (e % 2) * N:(e % 2 + 1) * N],
                                            self.v[:, m, h * RDV + e * P:h * RDV + (e + 1) * P],
                                            self.p[:, h % 2, m * N:(m + 1) * N], start=m == 0, stop=m == 3)
            last.then_inc(self.o_sum.sem, 1)
        pe.wait_ge(self.o_kept.sem, self.o_kept.at(RH))
        for h in range(RH):
            for e in range(4):
                last = nc.tensor.matmul(ps[:, 4 + h // 2, (h % 2) * N:(h % 2 + 1) * N], self.chip.ones, self.o[:, 4 * h + e, :],
                                        start=e == 0, stop=e == 3)
        last.then_inc(self.mean.sem, 1)
        pe.wait_ge(self.squares.sem, self.squares.at(1))
        for h in range(RH):
            for e in range(4):
                last = nc.tensor.matmul(ps[:, 6 + h // 2, (h % 2) * N:(h % 2 + 1) * N], self.chip.ones, self.sq[:, 4 * h + e, :],
                                        start=e == 0, stop=e == 3)
        last.then_inc(self.var.sem, 1)

    def act(self, act, link):
        nc, ps = self.nc, self.chip.ps
        self.lead(act)
        act.wait_ge(self.chip.stage_done, self.index)
        act.dma_start(self.expo.rearrange("p e n -> p (e n)"), self.chip.io["expo"]).then_inc(self.expo_loaded.sem, 16)
        for j in range(4):
            self.round(act, j + ROUNDED)
            act.wait_ge(self.chip.block_done, self.block_count(j))
            nc.scalar.activation(self.q[:, 2 * j:2 * j + 2, :], ps[:, j, :].rearrange("p (a n) -> p a n", a=2), ACT.Copy)\
                .then_inc(self.q_kept.sem, 1)
        for j in range(4):
            self.round(act, 4 + j + ROUNDED)
            act.wait_ge(self.chip.block_done, self.block_count(4 + j))
            b = 4 + 2 * (j % 2)
            nc.scalar.activation(self.k[:, 2 * j:2 * j + 2, :], ps[:, b:b + 2, :], ACT.Copy, scale=RDK ** -0.5)\
                .then_inc(self.k_kept.sem, 1)
        act.wait_ge(self.lg_in.sem, self.lg_in.at(1))
        nc.scalar.activation(self.lg[:, 1, :], self.lg[:, 0, :], ACT.Exp, scale=-1.0).then_inc(self.lg_exp.sem, 1)
        act.wait_ge(self.lg_out.sem, self.lg_out.at(1))
        act.wait_ge(self.expo_loaded.sem, self.expo_loaded.at(16))
        for h in range(RH):
            act.wait_ge(self.d_in.sem, self.d_in.at(h + 1))
            nc.scalar.activation(self.d[:, h, 0:512], self.d[:, h, 0:512], ACT.Exp)
            nc.scalar.activation(self.d[:, h, 512:1024], self.expo[:, 2, :], ACT.Exp, scale=self.lg[:, 3, h:h + 1])
            nc.scalar.activation(self.tmp[:, h % 2, :], self.expo[:, 3, :], ACT.Exp, scale=self.lg[:, 3, 4 + h:5 + h])\
                .then_inc(self.d_exp.sem, 1)
        for h in range(RH):
            self.round(act, 8 + 2 * h + ROUNDED)
            self.round(act, 8 + 2 * h + 1 + ROUNDED)
            act.wait_ge(self.chip.block_done, self.block_count(8 + 2 * h + 1))
            for t in range(4):
                nc.scalar.activation(self.v[:, t, h * RDV:(h + 1) * RDV], ps[:, 4 * (h % 2) + t, :], ACT.Copy)\
                    .then_inc(self.v_kept.sem, 1)
        for j in range(8):
            self.round(act, 16 + j + ROUNDED)
            act.wait_ge(self.chip.block_done, self.block_count(16 + j))
            nc.scalar.activation(self.g[:, 2 * j:2 * j + 2, :].rearrange("p a n -> p (a n)"), ps[:, j % 4, :], ACT.Silu)\
                .then_inc(self.g_kept.sem, 1)
        for h in range(RH):
            act.wait_ge(self.o_sum.sem, self.o_sum.at(h + 1))
            nc.scalar.activation(self.o[:, 4 * h:4 * h + 4, :].rearrange("p (b e) n -> p b (e n)", b=2), ps[:, 2:4, :], ACT.Copy)\
                .then_inc(self.o_kept.sem, 1)
        act.wait_ge(self.centred.sem, self.centred.at(1))
        nc.scalar.activation(self.sq, self.o, ACT.Square).then_inc(self.squares.sem, 1)
        act.wait_ge(self.var_in.sem, self.var_in.at(1))
        nc.scalar.activation(self.st[:, 1, :], self.st[:, 0, :], ACT.Sqrt).then_inc(self.root.sem, 1)
        self.next.lead(act)
        for h in range(RH):
            act.wait_ge(self.gated.sem, self.gated.at(h + 1))
            nc.scalar.activation(self.parts[0][:, 4 * h:4 * h + 4, :], self.o[:, 4 * h:4 * h + 4, :], ACT.Copy)\
                .then_inc(self.rounded.sem, 1)

    def dve(self, dve, link):
        nc, ps = self.nc, self.chip.ps
        dve.wait_ge(self.chip.stage_done, self.index)
        lg, v = self.lg, nc.vector
        dec = columns(self.chip.vec, "decay")
        link(v.tensor_scalar(lg[:, 0, :], dec, -1.0, None, ALU.mult))
        v.tensor_tensor(lg[:, 0, :], lg[:, 0, :], dec, ALU.max).then_inc(self.lg_in.sem, 1)
        dve.wait_ge(self.lg_exp.sem, self.lg_exp.at(1))
        link(v.tensor_scalar(lg[:, 0, :], lg[:, 1, :], 2.0, None, ALU.add))
        link(v.reciprocal(lg[:, 0, :], lg[:, 0, :]))
        link(v.tensor_tensor(lg[:, 0, :], lg[:, 0, :], lg[:, 1, :], ALU.mult))
        link(v.tensor_tensor(lg[:, 1, :], lg[:, 0, :], lg[:, 0, :], ALU.mult))
        link(v.tensor_scalar(lg[:, 2, :], lg[:, 1, :], 1.0 / 17, None, ALU.mult))
        for n in range(15, 1, -2):
            link(v.scalar_tensor_tensor(lg[:, 2, :], lg[:, 2, :], 1.0 / n, lg[:, 1, :], ALU.add, ALU.mult))
        link(v.scalar_tensor_tensor(lg[:, 2, :], lg[:, 2, :], 1.0, lg[:, 0, :], ALU.add, ALU.mult))
        link(v.tensor_scalar(lg[:, 3, :], dec, 0.0, None, ALU.min))
        v.scalar_tensor_tensor(lg[:, 3, :], lg[:, 2, :], -2.0, lg[:, 3, :], ALU.mult, ALU.add).then_inc(self.lg_out.sem, 1)
        dve.wait_ge(self.lg_out.sem, self.lg_out.at(1))
        dve.wait_ge(self.expo_loaded.sem, self.expo_loaded.at(16))
        for h in range(RH):
            link(v.tensor_scalar(self.d[:, h, 0:512], self.expo[:, 0, :], lg[:, 3, h:h + 1], None, ALU.mult))
            if h >= 2:
                link(v.tensor_tensor(self.d[:, h - 2, 512:1024], self.d[:, h - 2, 512:1024], self.tmp[:, h % 2, :], ALU.add))
            v.scalar_tensor_tensor(self.d[:, h, 0:512], self.expo[:, 1, :], lg[:, 3, 4 + h:5 + h], self.d[:, h, 0:512],
                                   ALU.mult, ALU.add).then_inc(self.d_in.sem, 1)
            if h >= 1:
                dve.wait_ge(self.d_exp.sem, self.d_exp.at(h))
        dve.wait_ge(self.d_exp.sem, self.d_exp.at(RH))
        for h in range(2, RH):
            link(v.tensor_tensor(self.d[:, h, 512:1024], self.d[:, h, 512:1024], self.tmp[:, h % 2, :], ALU.add))
        dve.wait_ge(self.q_kept.sem, self.q_kept.at(4))
        dve.wait_ge(self.k_kept.sem, self.k_kept.at(4))
        turned_part = self.chip.at(R_TMP, 2, N)
        for i in range(16):
            t = self.q[:, i, :] if i < KD else self.k[:, i - KD, 0:N]
            dve.wait_ge(self.turned.sem, self.turned.at(i + 1))
            link(v.tensor_tensor(turned_part[:, i % 2, :], ps[:, i % 4, 0:N], self.sin[:, i % 2, :], ALU.mult))
            link(v.tensor_tensor(t, t, self.cos[:, i % 2, :], ALU.mult))
            v.tensor_tensor(t, t, turned_part[:, i % 2, :], ALU.add).then_inc(self.rope_done.sem, 1)
        dve.wait_ge(self.g_kept.sem, self.g_kept.at(8))
        for h in range(RH):
            dve.wait_ge(self.scores.sem, self.scores.at(h + 1))
            if h >= 2:
                dve.wait_ge(self.o_sum.sem, self.o_sum.at(h - 1))
            v.tensor_tensor(self.p[:, h % 2, :], ps[:, 0:2, :].rearrange("p b n -> p (b n)"), self.d[:, h, :], ALU.mult)\
                .then_inc(self.weighted.sem, 1)
        dve.wait_ge(self.mean.sem, self.mean.at(1))
        mean, ms, rstd = self.st[:, 2, :], self.st[:, 0, :], self.st[:, 2, :]
        link(v.tensor_scalar(mean, ps[:, 4:6, :].rearrange("p b n -> p (b n)"), 1.0 / RDV, None, ALU.mult))
        for h in range(RH):
            o = self.o[:, 4 * h:4 * h + 4, :]
            last = v.tensor_tensor(o, o, mean[:, h * N:(h + 1) * N].unsqueeze(1).broadcast_to([P, 4, N]), ALU.subtract)
        last.then_inc(self.centred.sem, 1)
        dve.wait_ge(self.var.sem, self.var.at(1))
        v.tensor_scalar(ms, ps[:, 6:8, :].rearrange("p b n -> p (b n)"), 1.0 / RDV, EPS, ALU.mult, ALU.add)\
            .then_inc(self.var_in.sem, 1)
        dve.wait_ge(self.root.sem, self.root.at(1))
        link(v.reciprocal(rstd, self.st[:, 1, :]))
        for h in range(RH):
            tiles = slice(4 * h, 4 * h + 4)
            o = self.o[:, tiles, :]
            link(v.tensor_tensor(o, o, rstd[:, h * N:(h + 1) * N].unsqueeze(1).broadcast_to([P, 4, N]), ALU.mult))
            v.tensor_tensor(o, o, self.g[:, tiles, :], ALU.mult).then_inc(self.gated.sem, 1)
        for h in range(RH):
            tiles = slice(4 * h, 4 * h + 4)
            dve.wait_ge(self.rounded.sem, self.rounded.at(h + 1))
            last = v.tensor_tensor(self.parts[1][:, tiles, :], self.o[:, tiles, :],
                                   self.parts[0].bitcast(F32)[:, tiles, :], ALU.subtract)
        last.then_inc(self.chip.stage_done, 1)


B_P = 0
B_U = 56 * N
B_SQ = B_U + KD * N
B_SMALL = B_SQ + KD * N
B_OB = 19200
B_OC = B_OB + 4 * N
B_OA = B_OC + 4 * N
B_CST2 = B_OA + 4 * N
NCST2 = 2 * P + 5 * P + 2 * 16
B_BIAS = 23328
assert B_CST2 + NCST2 <= B_BIAS
B_WORK = B_BIAS + 16 * N

T_R, T_K, T_V, T_WA, T_G = 0, 4, 8, 12, 13
T_NQ, T_KV, T_KS, T_KW = 14, 18, 20, 21
T_SQ, T_SK = 22, 26
T_VS, T_VW, T_GATE, T_SV = 28, 29, 30, 31
T_GATES = 32
TOKEN_BLOCKS = (14, 15)


class LoadTables(Stage):

    def __init__(self, chip):
        super().__init__(chip)
        self.n = chip.signals("tables_loaded", 32)

    def act(self, act, link):
        c = self.chip
        act.wait_ge(self.chip.stage_done, self.index)
        act.dma_start(c.at(B_CST2, NCST2), c.io["cst2"]).then_inc(self.n.sem, 16)
        s = c.io["bias_scratch"]
        skewed = bass.AP(s.tensor, s.offset + P - 1, [[16 * BIASW - 1, P], [BIASW, 16], [1, N]])
        act.dma_start(c.at(B_BIAS, 16, N), skewed).then_inc(self.n.sem, 16)
        act.wait_ge(self.n.sem, self.n.at(32))
        act.sem_inc(self.chip.stage_done, 1)


def second_input(chip):
    return chip.parts_at(B_SQ, KD, N), chip.parts_at(B_U, KD, N)


class ProjectIn(Stage):

    blocks = BLOCKS["in2"]

    def __init__(self, chip):
        super().__init__(chip)
        self.u = second_input(chip)
        self.p = chip.at(B_P, 56, N)
        self.kept = chip.signals("projection_kept", self.blocks)

    def pe(self, pe):
        c, ps = self.chip, self.chip.ps
        pe.wait_ge(c.stage_done, self.index)
        for j in range(self.blocks):
            whi, wlo = self.weights(j)
            if j >= 8:
                pe.wait_ge(self.kept.sem, self.kept.at(j - 7))
            pe.wait_ge(c.rest_done[0], self.split_count(j))
            if j in TOKEN_BLOCKS:
                pe.wait_ge(c.rest_done[1], self.split_count(j))
                for t in range(NT):
                    out = ps[:, j % 8, :].rearrange("p (e t c) -> p e t c", e=2, t=NT)[:, :, t, :]
                    for k in range(KD):
                        last = self.product(out, [u[:, k, t * P:(t + 1) * P] for u in self.u],
                                            [w[:, k:TPB:KD, :] for w in (whi, wlo)], k == 0, k == KD - 1)
            else:
                for e in range(2):
                    if e:
                        pe.wait_ge(c.rest_done[1], self.split_count(j))
                    for k in range(KD):
                        i = e * KD + k
                        last = self.product(ps[:, j % 8, e * N:(e + 1) * N], (whi[:, i, :], wlo[:, i, :]),
                                            [u[:, k, :] for u in self.u], k == 0, k == KD - 1)
            last.then_inc(c.block_done, 1)

    def act(self, act, link):
        nc, ps = self.nc, self.chip.ps
        self.lead(act)
        act.wait_ge(self.chip.stage_done, self.index)
        for j in range(self.blocks):
            self.round(act, j + ROUNDED)
            act.wait_ge(self.chip.block_done, self.block_count(j))
            to = self.p[:, 2 * j:2 * j + 2, :].rearrange("p a n -> p (a n)")
            if 2 * j == T_GATE:
                nc.scalar.activation(to[:, N:], ps[:, j % 8, N:], ACT.Copy)
                last = nc.scalar.activation(to[:, :N], ps[:, j % 8, :N], ACT.Sigmoid)
            else:
                last = nc.scalar.activation(to, ps[:, j % 8, :], ACT.Sigmoid if 2 * j >= T_GATES else ACT.Copy)
            last.then_inc(self.kept.sem, 1)
        act.wait_ge(self.kept.sem, self.kept.at(self.blocks))
        act.sem_inc(self.chip.stage_done, 1)


class Attention(Stage):

    blocks = BLOCKS["cmp1"] + BLOCKS["cmp2"]
    whole = blocks
    CMP, SEL, WIN, SWA = range(4)
    units = [(t, g, b) for t in range(NT) for g in range(2) for b in range(4)]

    def __init__(self, chip, layer):
        super().__init__(chip)
        at, sig = chip.at, chip.signals
        self.layer = layer
        self.p = at(B_P, 56, N)
        self.o = {self.WIN: at(B_OB, 4, N), self.SWA: at(B_OC, 4, N)}
        self.bias = at(B_BIAS, 16, N)
        self.cmask = at(B_CST2 + 7 * P, 2, 16)
        n = B_U
        self.r = at(n, CMP_LEN, 2, NCMP)
        n += CMP_LEN * 2 * NCMP
        self.hid = at(n, 4, 2 * NCMP)
        n += 4 * 2 * NCMP
        self.kcm, self.vcm = at(n, 16), at(n + 16, P)
        n += 16 + P
        self.stat = at(n, 2, 8, 4)
        self.sc = at(B_WORK, 2, 4, N)
        self.pt = at(B_WORK + 8 * N, 5, 4, P)
        self.pts = at(B_WORK + 8 * N + 20 * P, 2, 4, P)
        u = len(self.units)
        self.blocks_ready = sig("cmp_blocks_ready", 1)
        self.hidden = sig("cmp_hidden", 1)
        self.compressed = sig("cmp_done", 1)
        self.cmp_kept = sig("cmp_kept", 1)
        self.scored = sig("attn_scored", u)
        self.shifted = sig("attn_shifted", u)
        self.exped = sig("attn_exped", u)
        self.weighted = sig("attn_weighted", u)
        self.turned = sig("attn_turned", u)
        self.turned_kept = sig("attn_turned_kept", u)
        self.summed = sig("attn_summed", u // 2)
        self.sum_kept = sig("attn_sum_kept", u // 2)

    def width(self, t, b):
        return NCMP if b == self.CMP else (t + 1) * P

    def key_tiles(self, t, b):
        return 1 if b == self.CMP else t + 1

    def pe(self, pe):
        nc, ps, p = self.nc, self.chip.ps, self.p
        pe.wait_ge(self.chip.stage_done, self.index)
        pe.wait_ge(self.blocks_ready.sem, self.blocks_ready.at(1))
        for j in range(BLOCKS["cmp1"]):
            slot, count = self.arrival(j)
            pe.wait_ge(self.chip.loaded[slot], count)
            w = self.chip.ring[:, slot]
            for i in range(TPB):
                l, f = divmod(j * TPB + i, 2)
                for kv in range(2):
                    rows_ = slice(kv * DH, (kv + 1) * DH)
                    last = nc.tensor.matmul(ps[:, 2 * kv + f, 0:2 * NCMP], w[rows_, i, :],
                                            self.r[rows_, l].rearrange("p g n -> p (g n)"),
                                            start=l == 0, stop=l == CMP_LEN - 1)
            last.then_inc(self.chip.block_done, 1)
        pe.wait_ge(self.hidden.sem, self.hidden.at(1))
        slot, count = self.arrival(BLOCKS["cmp1"])
        pe.wait_ge(self.chip.loaded[slot], count)
        w = self.chip.ring[:, slot]
        for f in range(2):
            nc.tensor.matmul(ps[:, 4, 0:2 * NCMP], w[:, f, :], self.hid[:, f, :], start=f == 0, stop=f == 1)
        for g in range(2):
            for f in range(2):
                last = nc.tensor.matmul(ps[0:NCMP, 5, g * DH:(g + 1) * DH], self.hid[:, 2 + f, g * NCMP:(g + 1) * NCMP],
                                        w[:, 2 + f, 0:DH], start=f == 0, stop=f == 1)
        last.then_inc(self.chip.block_done, 1)
        pe.wait_ge(self.cmp_kept.sem, self.cmp_kept.at(1))

        def scores(u):
            t, g, b = self.units[u]
            if u >= 2:
                pe.wait_ge(self.shifted.sem, self.shifted.at(u - 1))
            half = slice(g * DH, (g + 1) * DH)
            keys = {self.CMP: self.kcm[half, 0:NCMP], self.SEL: p[half, T_KS], self.WIN: p[half, T_KW],
                    self.SWA: p[half, T_SK]}[b]
            w = self.width(t, b)
            for i in range(4):
                q = p[half, (T_SQ if b == self.SWA else T_NQ) + i, t * P:(t + 1) * P]
                last = nc.tensor.matmul(ps[:, 2 * (u % 2) + i // 2, (i % 2) * N:(i % 2) * N + w], q, keys[:, 0:w],
                                        start=True, stop=True)
            last.then_inc(self.scored.sem, 1)

        def turn(u):
            t, g, b = self.units[u]
            pe.wait_ge(self.weighted.sem, self.weighted.at(u + 1))
            if u >= 1:
                pe.wait_ge(self.turned_kept.sem, self.turned_kept.at(u))
            w = min(self.width(t, b), P)
            for j in range(self.key_tiles(t, b)):
                for i in range(4):
                    last = nc.tensor.transpose(ps[0:w, 4 + j, i * P:(i + 1) * P], self.sc[:, u % 2, i, j * P:j * P + w],
                                               self.chip.ident)
            last.then_inc(self.turned.sem, 1)

        def values(u):
            t, g, b = self.units[u]
            if b not in self.o:
                return
            n = 2 * (u // 4) + (b == self.SWA)
            pe.wait_ge(self.turned_kept.sem, self.turned_kept.at(u + 1))
            if n >= 2:
                pe.wait_ge(self.sum_kept.sem, self.sum_kept.at(n - 1))
            for i in range(4):
                if b == self.SWA:
                    parts = [(p[:, T_SV, j * P:(j + 1) * P], self.pts[:, j, i, :]) for j in range(t + 1)]
                else:
                    parts = [(self.vcm[0:NCMP, :], self.pt[0:NCMP, 0, i, :])]
                    parts += [(p[:, T_VS, j * P:(j + 1) * P], self.pt[:, 1 + j, i, :]) for j in range(t + 1)]
                    parts += [(p[:, T_VW, j * P:(j + 1) * P], self.pt[:, 3 + j, i, :]) for j in range(t + 1)]
                for k, (v, weights) in enumerate(parts):
                    last = nc.tensor.matmul(ps[:, 6 + n % 2, i * P:(i + 1) * P], v, weights, start=k == 0, stop=k == len(parts) - 1)
            last.then_inc(self.summed.sem, 1)

        scores(0)
        scores(1)
        for u in range(len(self.units)):
            turn(u)
            if u + 2 < len(self.units):
                scores(u + 2)
            values(u)

    def act(self, act, link):
        nc, ps = self.nc, self.chip.ps
        act.wait_ge(self.chip.stage_done, self.index)
        act.wait_ge(self.chip.block_done, self.block_count(BLOCKS["cmp1"] - 1))
        nc.scalar.activation(self.hid, ps[:, 0:4, 0:2 * NCMP], ACT.Gelu).then_inc(self.hidden.sem, 1)

        def exp(u):
            t, g, b = self.units[u]
            act.wait_ge(self.shifted.sem, self.shifted.at(u + 1))
            if b == self.SWA:
                nc.scalar.activation(self.stat[:, u % 2, 2, :], self.stat[:, u % 2, 2, :], ACT.Exp)
            e = self.sc[:, u % 2, :, 0:self.width(t, b)]
            nc.scalar.activation(e, e, ACT.Exp).then_inc(self.exped.sem, 1)

        def keep(u):
            t, g, b = self.units[u]
            w, k = min(self.width(t, b), P), self.key_tiles(t, b)
            to = self.pts[:, 0:k] if b == self.SWA else self.pt[0:w, (0, 1, 3)[b]:(0, 1, 3)[b] + k]
            act.wait_ge(self.turned.sem, self.turned.at(u + 1))
            nc.scalar.activation(to.rearrange("p j i t -> p j (i t)"), ps[0:w, 4:4 + k, :], ACT.Copy)\
                .then_inc(self.turned_kept.sem, 1)
            if b in self.o:
                n = 2 * (u // 4) + (b == self.SWA)
                half = slice(g * DH, (g + 1) * DH)
                act.wait_ge(self.summed.sem, self.summed.at(n + 1))
                nc.scalar.activation(self.o[b][half, :, t * P:(t + 1) * P],
                                     ps[half, 6 + n % 2, :].rearrange("p (i t) -> p i t", i=4), ACT.Copy)\
                    .then_inc(self.sum_kept.sem, 1)

        exp(0)
        for u in range(len(self.units)):
            if u + 1 < len(self.units):
                exp(u + 1)
            keep(u)
        act.wait_ge(self.sum_kept.sem, self.sum_kept.at(len(self.units) // 2))
        act.sem_inc(self.chip.stage_done, 1)

    def dve(self, dve, link):
        nc, ps, p = self.nc, self.chip.ps, self.p
        v = nc.vector
        dve.wait_ge(self.chip.stage_done, self.index)
        pe_cols = columns(self.chip.vec, "pe", self.layer, CMP_LEN)
        for g in range(2):
            x = p[:, T_KV + g, :]
            blocks = bass.AP(x.tensor, x.offset, [x.ap[0], (1, CMP_LEN), (CMP_STRIDE, NCMP)])
            last = v.tensor_tensor(self.r[:, :, g, :], blocks, pe_cols.unsqueeze(2).broadcast_to([P, CMP_LEN, NCMP]), ALU.add)
        last.then_inc(self.blocks_ready.sem, 1)
        dve.wait_ge(self.chip.block_done, self.block_count(BLOCKS["cmp1"]))
        for g in range(2):
            half = slice(g * DH, (g + 1) * DH)
            v.tensor_copy(self.kcm[half, 0:NCMP], ps[half, 4, g * NCMP:(g + 1) * NCMP])
        v.tensor_copy(self.vcm[0:NCMP, :], ps[0:NCMP, 5, 0:P]).then_inc(self.cmp_kept.sem, 1)

        def shift(u):
            t, g, b = self.units[u]
            w = self.width(t, b)
            sc, st = self.sc[:, u % 2, :, 0:w], self.stat[:, u % 2]
            scores = ps[:, 2 * (u % 2):2 * (u % 2) + 2, :].rearrange("p b (h n) -> p (b h) n", n=N)[:, :, 0:w]
            if b == self.CMP:
                bias = self.cmask[:, t, 0:NCMP].unsqueeze(1).broadcast_to([P, 4, NCMP])
            else:
                h = (8 if b == self.SWA else 0) + 4 * g
                bias = self.bias[:, h:h + 4, N - w:N]
            dve.wait_ge(self.scored.sem, self.scored.at(u + 1))
            if u >= 2:
                dve.wait_ge(self.turned.sem, self.turned.at(u - 1))
            link(v.scalar_tensor_tensor(sc, scores, DH ** -0.5, bias, ALU.mult, ALU.add))
            link(v.tensor_reduce(st[:, 0, :], sc, AX.X, ALU.max))
            if b == self.CMP:
                link(v.tensor_scalar(st[:, 0, :], st[:, 0, :], NEG / 10, None, ALU.max))
            if b == self.SWA:
                sink = columns(self.chip.vec, "sinks", self.layer, 8)[:, 4 * g:4 * g + 4]
                link(v.tensor_tensor(st[:, 0, :], st[:, 0, :], sink, ALU.max))
                link(v.tensor_tensor(st[:, 2, :], sink, st[:, 0, :], ALU.subtract))
            v.tensor_tensor(sc, sc, st[:, 0, :].unsqueeze(2).broadcast_to([P, 4, w]), ALU.subtract)\
                .then_inc(self.shifted.sem, 1)

        def weigh(u):
            t, g, b = self.units[u]
            w = self.width(t, b)
            sc, st = self.sc[:, u % 2, :, 0:w], self.stat[:, u % 2]
            dve.wait_ge(self.exped.sem, self.exped.at(u + 1))
            link(v.tensor_reduce(st[:, 1, :], sc, AX.X, ALU.add))
            if b == self.SWA:
                link(v.tensor_tensor(st[:, 1, :], st[:, 1, :], st[:, 2, :], ALU.add))
            else:
                link(v.tensor_scalar(st[:, 1, :], st[:, 1, :], 1e-30, None, ALU.max))
            link(v.reciprocal(st[:, 1, :], st[:, 1, :]))
            if b != self.SWA:
                a = t * P + 12 * g
                gate = p[:, T_GATE, a:a + 12].rearrange("p (h c) -> p h c", c=3)[:, :, b]
                link(v.tensor_tensor(st[:, 1, :], st[:, 1, :], gate, ALU.mult))
            v.tensor_tensor(sc, sc, st[:, 1, :].unsqueeze(2).broadcast_to([P, 4, w]), ALU.mult)\
                .then_inc(self.weighted.sem, 1)

        shift(0)
        for u in range(len(self.units)):
            if u + 1 < len(self.units):
                shift(u + 1)
            weigh(u)


W_AR, W_B, W_K, W_ST = 14 * N, 14 * N + 8 * N, 14 * N + 12 * N, 14 * N + 16 * N
W_BH, W_KH, W_GATE, W_KK = B_U, B_U + 4 * N, B_U + 8 * N, B_U + 12 * N
W_W1, W_PEND = B_U + 16 * N, B_U + 18 * N
W_TOK = B_BIAS
W_LB = W_TOK + 8 * N
W_LK = W_LB + 8 * N
W_MIX = W_LK + 8 * N
W_W2 = W_MIX + 16 * N
W_SA = W_W2 + 2 * N
W_C0 = W_W2
W_C1 = W_SA + 2 * N


class Rwkv(Stage):

    blocks = BLOCKS["rwkv"]
    whole = blocks
    LEVELS = 5

    def __init__(self, chip, layer):
        super().__init__(chip)
        at, sig = chip.at, chip.signals
        self.layer = layer
        self.z = at(B_P, 56, N)
        self.ar = at(W_AR, 4, NT, 2, P)
        self.b, self.k, self.bh, self.kh = (at(w, 4, N) for w in (W_B, W_K, W_BH, W_KH))
        self.gate, self.kk = at(W_GATE, 4, N), at(W_KK, 4, N)
        self.y, self.a = chip.x[:, 0:4, N:], chip.x[:, 4:8, N:]
        self.state = at(W_ST, 4, P)
        self.w1, self.pend = at(W_W1, 4, P), at(W_PEND, 4, NCH)
        self.tok = at(W_TOK, 4, 4, P)
        self.lb, self.lk = at(W_LB, HEADS, 2, P), at(W_LK, HEADS, 2, P)
        self.mix = at(W_MIX, 14, N)
        self.mat = [at(W_MIX + i * 4 * N, HEADS, P) for i in range(4)]
        self.tmp = [at(W_MIX + i * 4 * N, 4, N) for i in range(4)]
        self.e = [at(W_LB, 4, N), at(W_LB + 4 * N, 4, N), at(W_LK, 4, N)]
        self.w2, self.sa = at(W_W2, 4, P), at(W_SA, 4, P)
        self.c = [at(W_C0, 4, N), at(W_C1, 4, N)]
        self.oa = at(B_OA, 4, N)
        self.mask = at(B_CST2, 2 * P)
        self.level = [at(B_CST2 + (2 + i) * P, P) for i in range(self.LEVELS)]
        self.s = {}
        for name, n in [("mixed", 1), ("ranks_ready", 1), ("sig_w", 1), ("sig_a", 1), ("kk_raw", 1), ("kk_sq", 1),
                        ("kk_sum", 1), ("kk_in", 1), ("kk_root", 1), ("c_ready", 1), ("exps", 1), ("end_in", 1),
                        ("end_exp", 1), ("rk", 1), ("rk_sum", 1), ("scaled", 1), ("tok_turned", 8), ("tok_kept", 8),
                        ("l_done", 16), ("l_kept", 16), ("c_masked", 2 * 2 * self.LEVELS), ("x_done", 4 * self.LEVELS),
                        ("x_kept", 4 * self.LEVELS), ("e_done", 4 * self.LEVELS), ("d_done", 4 * self.LEVELS),
                        ("w1_done", 2), ("w1_kept", 2), ("x2_done", 2), ("x2_kept", 2), ("w2_done", 2), ("w2_kept", 2),
                        ("sa_done", NCH), ("sa_kept", NCH), ("s_done", NCH), ("s_kept", NCH + 1), ("y_done", 2), ("y_first", 2),
                        ("y_kept", 2), ("gn_sum", 1), ("gn_centred", 1), ("gn_sq", 1), ("gn_var", 1), ("gn_in", 1), ("gn_root", 1)]:
            self.s[name] = sig("rwkv_" + name, n)

    def pe(self, pe):
        nc, ps, z, s = self.nc, self.chip.ps, self.z, self.s
        mm = nc.tensor.matmul
        pe.wait_ge(self.chip.stage_done, self.index)
        pe.wait_ge(s["ranks_ready"].sem, s["ranks_ready"].at(1))
        slot, count = self.arrival(0)
        pe.wait_ge(self.chip.loaded[slot], count)
        w = self.chip.ring[:, slot]
        for m in range(4):
            at = slice((m % 2) * N, (m % 2 + 1) * N)
            mm(ps[:, m // 2, at], w[0:64, m, :], z[0:64, T_WA], start=True, stop=True)
            mm(ps[:, 2 + m // 2, at], w[64:128, m, :], z[64:128, T_WA], start=True, stop=True)
            last = mm(ps[:, 4 + m // 2, at], w[:, 4 + m, :], z[:, T_G], start=True, stop=True)
        last.then_inc(self.chip.block_done, 1)

        def head_sums(bank, x):
            for i in range(4):
                last = mm(ps[:, bank + i // 2, (i % 2) * N:(i % 2 + 1) * N], self.chip.headones, x[:, i, :], start=True, stop=True)
            return last

        pe.wait_ge(s["kk_sq"].sem, s["kk_sq"].at(1))
        head_sums(6, self.tmp[0]).then_inc(s["kk_sum"].sem, 1)
        pe.wait_ge(s["rk"].sem, s["rk"].at(1))
        head_sums(6, self.kk).then_inc(s["rk_sum"].sem, 1)
        pe.wait_ge(s["scaled"].sem, s["scaled"].at(1))
        for t in range(NT):
            ts = slice(t * P, (t + 1) * P)
            if t:
                pe.wait_ge(s["y_kept"].sem, s["y_kept"].at(t))
            for j, x in enumerate([self.ar[:, :, t, 0, :], self.bh[:, :, ts], self.kh[:, :, ts], z[:, T_V:T_V + 4, ts]]):
                for i in range(4):
                    last = nc.tensor.transpose(ps[:, j, i * P:(i + 1) * P], x[:, i, :], self.chip.ident)
                last.then_inc(s["tok_turned"].sem, 1)
            for x, bank in ((self.b, 4), (self.k, 0)):
                if bank == 0:
                    pe.wait_ge(s["tok_kept"].sem, s["tok_kept"].at(4 * t + 4))
                for b in range(4):
                    two_, e = divmod(b, 2)
                    half = slice(e * DH, (e + 1) * DH)
                    for i in range(2):
                        last = mm(ps[:, bank + b, i * 2 * P:(i + 1) * 2 * P], x[half, 2 * two_ + i, ts],
                                  self.ar[half, 2 * two_ + i, t].rearrange("p a n -> p (a n)"), start=True, stop=True)
                    last.then_inc(s["l_done"].sem, 1)
            pe.wait_ge(s["l_kept"].sem, s["l_kept"].at(8 * t + 8))
            d, dt, x, ct = self.mat
            for lv in range(self.LEVELS):
                for g in range(2):
                    n = (t * self.LEVELS + lv) * 2 + g
                    pe.wait_ge(s["c_masked"].sem, s["c_masked"].at(n + 1))
                    if lv:
                        pe.wait_ge(s["d_done"].sem, s["d_done"].at(n - 1))
                    for h in range(4 * g, 4 * g + 4):
                        last = mm(ps[:, g, (h % 4) * P:(h % 4 + 1) * P], ct[:, h, :], d[:, h, :], start=True, stop=True)
                    last.then_inc(s["x_done"].sem, 1)
                for g in range(2):
                    n = (t * self.LEVELS + lv) * 2 + g
                    pe.wait_ge(s["x_kept"].sem, s["x_kept"].at(n + 1))
                    for h in range(4 * g, 4 * g + 4):
                        at = slice((h % 4) * P, (h % 4 + 1) * P)
                        if lv < self.LEVELS - 1:
                            mm(ps[:, 2 + g, at], dt[:, h, :], x[:, h, :], start=True, stop=True)
                        last = mm(ps[:, 4 + g, at], x[:, h, :], dt[:, h, :], start=True, stop=True)
                    last.then_inc(s["e_done"].sem, 1)
            pe.wait_ge(s["d_done"].sem, s["d_done"].at(2 * self.LEVELS * (t + 1)))
            for h in range(HEADS):
                last = mm(ps[:, h % 2, (h // 2) * P:(h // 2 + 1) * P], self.tok[:, 0, h // 2, :], dt[:, h, :], start=True, stop=True)
            last.then_inc(s["w1_done"].sem, 1)
            for h in range(HEADS):
                last = mm(ps[:, 2, h * DH:(h + 1) * DH], self.lk[:, h, 0, :], self.tok[:, 3, h // 2, (h % 2) * DH:(h % 2 + 1) * DH],
                          start=True, stop=True)
            last.then_inc(s["x2_done"].sem, 1)
            pe.wait_ge(s["x2_kept"].sem, s["x2_kept"].at(t + 1))
            x2 = x[:, 0:4, :]
            for h in range(HEADS):
                last = mm(ps[:, 3, h * DH:(h + 1) * DH], dt[:, h, :], x2[:, h // 2, (h % 2) * DH:(h % 2 + 1) * DH], start=True, stop=True)
            last.then_inc(s["w2_done"].sem, 1)
            pe.wait_ge(s["w1_kept"].sem, s["w1_kept"].at(t + 1))
            pe.wait_ge(s["w2_kept"].sem, s["w2_kept"].at(t + 1))
            for c in range(4):
                n = 4 * t + c
                rows_ = slice(c * CH, (c + 1) * CH)
                pe.wait_ge(s["s_kept"].sem, s["s_kept"].at(n + 1))
                for i in range(4):
                    last = mm(ps[:, 4, i * P:(i + 1) * P], self.w1[:, i, :], self.state[:, i, :], start=True, stop=True)
                last.then_inc(s["sa_done"].sem, 1)
                for i in range(4):
                    mm(ps[:, 5, i * P + c * CH:i * P + (c + 1) * CH], self.state[:, i, :], self.ar[:, i, t, 1, rows_], start=True, stop=True)
                pe.wait_ge(s["sa_kept"].sem, s["sa_kept"].at(n + 1))
                for i in range(4):
                    at = slice(i * P, (i + 1) * P)
                    mm(ps[:, 6, at], self.tok[rows_, 2, i, :], self.tok[rows_, 3, i, :], start=True, stop=False)
                    last = mm(ps[:, 6, at], self.tok[rows_, 1, i, :], self.sa[rows_, i, :], start=False, stop=True)
                last.then_inc(s["s_done"].sem, 1)
            for e in range(2):
                for i in range(4):
                    at, h = slice(i * P, (i + 1) * P), 2 * i + e
                    mm(ps[:, e, at], self.tok[:, 3, i, :], self.lk[:, h, 1, :], start=True, stop=False)
                    last = mm(ps[:, e, at], self.sa[:, i, :], self.lb[:, h, 1, :], start=False, stop=True)
            last.then_inc(s["y_done"].sem, 1)
        pe.wait_ge(s["y_kept"].sem, s["y_kept"].at(2))
        head_sums(2, self.y).then_inc(s["gn_sum"].sem, 1)
        pe.wait_ge(s["gn_sq"].sem, s["gn_sq"].at(1))
        head_sums(4, self.tmp[0]).then_inc(s["gn_var"].sem, 1)

    def act(self, act, link):
        nc, ps, z, s = self.nc, self.chip.ps, self.z, self.s
        copy = nc.scalar.activation
        col = lambda name, i: columns(self.chip.vec, name, self.layer, 4)[:, i:i + 1]
        act.wait_ge(self.chip.stage_done, self.index)
        act.wait_ge(s["mixed"].sem, s["mixed"].at(1))
        copy(z[0:64, T_WA], z[0:64, T_WA], ACT.Tanh)
        copy(z[:, T_G], z[:, T_G], ACT.Sigmoid).then_inc(s["ranks_ready"].sem, 1)
        act.wait_ge(self.chip.block_done, self.block_count(0))
        for i in range(4):
            last = copy(self.c[0][:, i, :], ps[:, i // 2, (i % 2) * N:(i % 2 + 1) * N], ACT.Sigmoid, bias=col("w0", i))
        last.then_inc(s["sig_w"].sem, 1)
        for i in range(4):
            copy(self.a[:, i, :], ps[:, 2 + i // 2, (i % 2) * N:(i % 2 + 1) * N], ACT.Sigmoid, bias=col("a0", i))
        copy(self.gate.rearrange("p (b i) n -> p b (i n)", b=2), ps[:, 4:6, :], ACT.Copy).then_inc(s["sig_a"].sem, 1)
        act.wait_ge(s["kk_raw"].sem, s["kk_raw"].at(1))
        copy(self.tmp[0], self.kk, ACT.Square).then_inc(s["kk_sq"].sem, 1)
        act.wait_ge(s["kk_in"].sem, s["kk_in"].at(1))
        copy(self.tmp[2], self.tmp[1], ACT.Sqrt).then_inc(s["kk_root"].sem, 1)
        act.wait_ge(s["c_ready"].sem, s["c_ready"].at(1))
        copy(self.e[0], self.c[1], ACT.Exp)
        copy(self.e[1], self.c[1], ACT.Exp, scale=-1.0).then_inc(s["exps"].sem, 1)
        act.wait_ge(s["end_in"].sem, s["end_in"].at(1))
        copy(self.e[2], self.e[2], ACT.Exp).then_inc(s["end_exp"].sem, 1)
        for t in range(NT):
            for j in range(4):
                act.wait_ge(s["tok_turned"].sem, s["tok_turned"].at(4 * t + j + 1))
                copy(self.tok[:, j].rearrange("p i n -> p (i n)"), ps[:, j, :], ACT.Copy).then_inc(s["tok_kept"].sem, 1)
            x = self.mat[2]
            for lv in range(self.LEVELS):
                for g in range(2):
                    n = (t * self.LEVELS + lv) * 2 + g
                    act.wait_ge(s["x_done"].sem, s["x_done"].at(n + 1))
                    copy(x[:, 4 * g:4 * g + 4, :].rearrange("p h n -> p (h n)"), ps[:, g, :], ACT.Copy).then_inc(s["x_kept"].sem, 1)
            act.wait_ge(s["w1_done"].sem, s["w1_done"].at(t + 1))
            for e in range(2):
                half = slice(e * DH, (e + 1) * DH)
                last = copy(self.w1[half].rearrange("p i n -> p (i n)"), ps[half, e, :], ACT.Copy, scale=-1.0)
            last.then_inc(s["w1_kept"].sem, 1)
            act.wait_ge(s["x2_done"].sem, s["x2_done"].at(t + 1))
            copy(x[:, 0:4, :].rearrange("p i n -> p (i n)"), ps[:, 2, :], ACT.Copy).then_inc(s["x2_kept"].sem, 1)
            act.wait_ge(s["w2_done"].sem, s["w2_done"].at(t + 1))
            copy(self.w2.rearrange("p i n -> p (i n)"), ps[:, 3, :], ACT.Copy, scale=-1.0).then_inc(s["w2_kept"].sem, 1)
            act.wait_ge(s["y_done"].sem, s["y_done"].at(t + 1))
            copy(self.y[:, :, t * P:(t + 1) * P], ps[:, 5, :].rearrange("p (i n) -> p i n", i=4), ACT.Copy)\
                .then_inc(s["y_first"].sem, 1)
        act.wait_ge(s["gn_centred"].sem, s["gn_centred"].at(1))
        copy(self.tmp[0], self.y, ACT.Square).then_inc(s["gn_sq"].sem, 1)
        act.wait_ge(s["gn_in"].sem, s["gn_in"].at(1))
        copy(self.tmp[2], self.tmp[1], ACT.Sqrt).then_inc(s["gn_root"].sem, 1)

    def dve(self, dve, link):
        nc, ps, z, s = self.nc, self.chip.ps, self.z, self.s
        v = nc.vector
        col = lambda name, i: columns(self.chip.vec, name, self.layer, 4)[:, i:i + 1]
        two = lambda bank: ps[:, bank:bank + 2, :].rearrange("p b (i n) -> p (b i) n", n=N)
        dve.wait_ge(self.chip.stage_done, self.index)
        link(v.tensor_scalar(self.mix[:, :, 0:1], z[:, 0:14, 0:1], -1.0, None, ALU.mult))
        link(v.tensor_tensor(self.mix[:, :, 1:N], z[:, 0:14, 0:N - 1], z[:, 0:14, 1:N], ALU.subtract))
        for i in range(14):
            mu = columns(self.chip.vec, "mu", self.layer, 14)[:, i:i + 1]
            last = v.scalar_tensor_tensor(z[:, i, :], self.mix[:, i, :], mu, z[:, i, :], ALU.mult, ALU.add)
        last.then_inc(s["mixed"].sem, 1)
        dve.wait_ge(s["mixed"].sem, s["mixed"].at(1))
        for i in range(4):
            last = v.tensor_scalar(self.kk[:, i, :], z[:, T_K + i, :], col("k_k", i), None, ALU.mult)
        last.then_inc(s["kk_raw"].sem, 1)
        dve.wait_ge(s["sig_w"].sem, s["sig_w"].at(1))
        c = [x.rearrange("p i (c n) -> p (i c) n", n=CH) for x in self.c]
        link(v.tensor_scalar(self.c[0], self.c[0], -math.exp(-0.5), None, ALU.mult))
        for n in range(5):
            of, to, d = c[n % 2], c[1 - n % 2], 1 << n
            v.tensor_copy(to[:, :, 0:d], of[:, :, 0:d])
            last = v.tensor_tensor(to[:, :, d:CH], of[:, :, d:CH], of[:, :, 0:CH - d], ALU.add)
            if n < 4:
                link(last)
        last.then_inc(s["c_ready"].sem, 1)
        dve.wait_ge(s["c_ready"].sem, s["c_ready"].at(1))
        e2 = self.e[2].rearrange("p i (c n) -> p (i c) n", n=CH)
        v.tensor_tensor(e2, c[1][:, :, CH - 1:CH].broadcast_to([P, 4 * NCH, CH]), c[1], ALU.subtract).then_inc(s["end_in"].sem, 1)
        dve.wait_ge(s["kk_sum"].sem, s["kk_sum"].at(1))
        v.tensor_scalar(self.tmp[1], two(6), 1e-12, None, ALU.max).then_inc(s["kk_in"].sem, 1)
        dve.wait_ge(s["sig_a"].sem, s["sig_a"].at(1))
        t3 = self.tmp[3]
        for i in range(4):
            last = v.tensor_scalar(t3[:, i, :], self.a[:, i, :], 1.0, col("k_a", i), ALU.subtract, ALU.mult)
        link(last)
        k = z[:, T_K:T_K + 4, :]
        dve.wait_ge(s["kk_root"].sem, s["kk_root"].at(1))
        link(v.reciprocal(self.tmp[2], self.tmp[2]))
        link(v.tensor_tensor(self.kk, self.kk, self.tmp[2], ALU.mult))
        link(v.scalar_tensor_tensor(k, t3, 1.0, k, ALU.add, ALU.mult))
        link(v.tensor_tensor(self.a, self.a, self.kk, ALU.mult))
        dve.wait_ge(s["exps"].sem, s["exps"].at(1))
        dve.wait_ge(s["end_exp"].sem, s["end_exp"].at(1))
        e_in, e_inv, e_end = self.e
        split = lambda x: x.rearrange("p i (t c n) -> p (i t) c n", t=NT, n=CH)
        ar = self.ar.rearrange("p i t a (c n) -> p (i t) a c n", n=CH)
        v.tensor_tensor(ar[:, :, 0, :, 1:CH], split(self.kk)[:, :, :, 1:CH], split(e_in)[:, :, :, 0:CH - 1], ALU.mult)
        v.tensor_copy(ar[:, :, 0, :, 0:1], split(self.kk)[:, :, :, 0:1])
        v.tensor_tensor(ar[:, :, 1], split(z[:, T_R:T_R + 4, :]), split(e_in), ALU.mult)
        v.tensor_tensor(self.b, self.a, e_inv, ALU.mult)
        v.tensor_tensor(self.k, k, e_inv, ALU.mult)
        v.tensor_tensor(self.bh, self.a, e_end, ALU.mult)
        v.tensor_tensor(self.kh, k, e_end, ALU.mult)
        link(v.tensor_copy(self.pend, e_in.rearrange("p i (c n) -> p i c n", n=CH)[:, :, :, CH - 1]))
        link(v.tensor_tensor(self.kk, z[:, T_R:T_R + 4, :], k, ALU.mult))
        for i in range(4):
            last = v.tensor_scalar(self.kk[:, i, :], self.kk[:, i, :], col("r_k", i), None, ALU.mult)
        last.then_inc(s["rk"].sem, 1)
        dve.wait_ge(s["rk_sum"].sem, s["rk_sum"].at(1))
        bonus = self.c[1]
        link(v.tensor_tensor(bonus, two(6), z[:, T_V:T_V + 4, :], ALU.mult))
        v.memset(self.state, 0.0).then_inc(s["s_kept"].sem, 1)
        dve.sem_inc(s["scaled"].sem, 1)
        d, dt, x, ct = self.mat
        for t in range(NT):
            ident = self.chip.ident.unsqueeze(1).broadcast_to([P, HEADS, P])
            v.tensor_copy(d, ident)
            link(v.tensor_copy(dt, ident))
            for n, (to, bank) in enumerate([(self.lb, 4), (self.lk, 0)]):
                for b in range(4):
                    two_, e = divmod(b, 2)
                    dve.wait_ge(s["l_done"].sem, s["l_done"].at(8 * t + 4 * n + b + 1))
                    v.tensor_tensor(to[:, 4 * two_ + e:4 * two_ + e + 3:2].rearrange("p h a n -> p h (a n)"),
                                    ps[:, bank + b, :].rearrange("p (h m) -> p h m", h=2),
                                    self.mask.unsqueeze(1).broadcast_to([P, 2, 2 * P]), ALU.mult).then_inc(s["l_kept"].sem, 1)
            dve.wait_ge(s["l_kept"].sem, s["l_kept"].at(8 * t + 8))

            def mask_level(lv, g):
                n = (t * self.LEVELS + lv) * 2 + g
                if lv:
                    dve.wait_ge(s["x_done"].sem, s["x_done"].at(n - 1))
                hs = slice(4 * g, 4 * g + 4)
                v.tensor_tensor(ct[:, hs, :], self.lb[:, hs, 0, :], self.level[lv].unsqueeze(1).broadcast_to([P, 4, P]), ALU.mult)\
                    .then_inc(s["c_masked"].sem, 1)

            mask_level(0, 0)
            mask_level(0, 1)
            for lv in range(self.LEVELS):
                for g in range(2):
                    n = (t * self.LEVELS + lv) * 2 + g
                    hs = slice(4 * g, 4 * g + 4)
                    dve.wait_ge(s["e_done"].sem, s["e_done"].at(n + 1))
                    if lv < self.LEVELS - 1:
                        mask_level(lv + 1, g)
                        v.tensor_tensor(d[:, hs, :], d[:, hs, :], ps[:, 2 + g, :].rearrange("p (h n) -> p h n", h=4), ALU.subtract)
                    v.tensor_tensor(dt[:, hs, :], dt[:, hs, :], ps[:, 4 + g, :].rearrange("p (h n) -> p h n", h=4), ALU.subtract)\
                        .then_inc(s["d_done"].sem, 1)
                    dve.wait_ge(s["d_done"].sem, s["d_done"].at(n + 1))
            dve.wait_ge(s["w2_kept"].sem, s["w2_kept"].at(t + 1))
            for c_ in range(4):
                n = 4 * t + c_
                rows_ = slice(c_ * CH, (c_ + 1) * CH)
                dve.wait_ge(s["sa_done"].sem, s["sa_done"].at(n + 1))
                v.tensor_tensor(self.sa[rows_].rearrange("p i n -> p (i n)"), ps[rows_, 4, :],
                                self.w2[rows_].rearrange("p i n -> p (i n)"), ALU.add).then_inc(s["sa_kept"].sem, 1)
                dve.wait_ge(s["s_done"].sem, s["s_done"].at(n + 1))
                for i in range(4):
                    for e in range(2):
                        half = slice(e * DH, (e + 1) * DH)
                        last = v.scalar_tensor_tensor(self.state[half, i, half], self.state[half, i, half],
                                                      self.pend[half, i, n:n + 1], ps[half, 6, i * P + e * DH:i * P + (e + 1) * DH],
                                                      ALU.mult, ALU.add)
                last.then_inc(s["s_kept"].sem, 1)
                dve.wait_ge(s["s_kept"].sem, s["s_kept"].at(n + 2))
            dve.wait_ge(s["y_first"].sem, s["y_first"].at(t + 1))
            for e in range(2):
                half = slice(e * DH, (e + 1) * DH)
                y = self.y[half, :, t * P:(t + 1) * P]
                last = v.tensor_tensor(y, y, ps[half, e, :].rearrange("p (i n) -> p i n", i=4), ALU.add)
            last.then_inc(s["y_kept"].sem, 1)
        dve.wait_ge(s["gn_sum"].sem, s["gn_sum"].at(1))
        link(v.scalar_tensor_tensor(self.y, two(2), -1.0 / DH, self.y, ALU.mult, ALU.add))
        dve.sem_inc(s["gn_centred"].sem, 1)
        dve.wait_ge(s["gn_var"].sem, s["gn_var"].at(1))
        v.tensor_scalar(self.tmp[1], two(4), 1.0 / DH, GN_EPS, ALU.mult, ALU.add).then_inc(s["gn_in"].sem, 1)
        dve.wait_ge(s["gn_root"].sem, s["gn_root"].at(1))
        link(v.reciprocal(self.tmp[2], self.tmp[2]))
        link(v.tensor_tensor(self.y, self.y, self.tmp[2], ALU.mult))
        for i in range(4):
            last = v.tensor_scalar(self.y[:, i, :], self.y[:, i, :], col("ln_w", i), col("ln_b", i), ALU.mult, ALU.add)
        link(last)
        link(v.tensor_tensor(self.y, self.y, bonus, ALU.add))
        v.tensor_tensor(self.oa, self.y, self.gate, ALU.mult).then_inc(self.chip.stage_done, 1)


class Merge(Stage):

    blocks = BLOCKS["branch"]

    def __init__(self, chip):
        super().__init__(chip)
        places = (B_OA, B_OB, B_OC)
        self.o = [chip.at(a, 4, N) for a in places]
        self.o_parts = [(chip.parts_at(B_U + b * 4 * N, 4, N), chip.parts_at(a, 4, N)) for b, a in enumerate(places)]
        self.gates = chip.at(B_P, 56, N)[:, T_GATES:, :]
        self.merged, self.part = chip.at(B_BIAS, KD, N), chip.at(B_BIAS + KD * N, KD, N)
        self.parts = chip.parts_at(B_BIAS + 2 * KD * N, KD, N), chip.parts_at(B_BIAS, KD, N)
        self.rounded = chip.signals("branch_rounded", 3)
        self.ready = chip.signals("branch_split", 3)
        self.used = chip.signals("branch_used", 3)
        self.merged_ready = chip.signals("merged_ready", 2)
        self.merged_rounded = chip.signals("merged_rounded", 2)

    def pe(self, pe):
        c = self.chip
        pe.wait_ge(c.stage_done, self.index)
        for b in range(3):
            pe.wait_ge(self.ready.sem, self.ready.at(b + 1))
            if b == 2:
                pe.wait_ge(self.used.sem, self.used.at(1))
            for j in range(2):
                whi, wlo = self.weights(2 * b + j)
                for m in range(4):
                    if m % 2 == 0:
                        pe.wait_ge(c.rest_done[m // 2], self.split_count(2 * b + j))
                    mm = 4 * j + m
                    for k in range(4):
                        i = 4 * m + k
                        last = self.product(c.ps[:, 4 * (b % 2) + mm // 2, (mm % 2) * N:(mm % 2 + 1) * N],
                                            (whi[:, i, :], wlo[:, i, :]), [o[:, k, :] for o in self.o_parts[b]], k == 0, k == 3)
                last.then_inc(c.block_done, 1)

    def act(self, act, link):
        copy = self.nc.scalar.activation
        self.lead(act)
        act.wait_ge(self.chip.stage_done, self.index)
        for b in range(3):
            copy(self.o_parts[b][0], self.o[b], ACT.Copy).then_inc(self.rounded.sem, 1)
        for j in range(ROUNDED, self.blocks):
            self.round(act, j)
        self.next.lead(act)
        for i in range(2):
            tiles = slice(4 * i, 4 * i + 4)
            act.wait_ge(self.merged_ready.sem, self.merged_ready.at(i + 1))
            copy(self.parts[0][:, tiles, :], self.merged[:, tiles, :], ACT.Copy).then_inc(self.merged_rounded.sem, 1)

    def dve(self, dve, link):
        v = self.nc.vector
        dve.wait_ge(self.chip.stage_done, self.index)
        for b in range(3):
            dve.wait_ge(self.rounded.sem, self.rounded.at(b + 1))
            v.tensor_tensor(self.o_parts[b][1], self.o[b], self.o_parts[b][0].bitcast(F32), ALU.subtract)\
                .then_inc(self.ready.sem, 1)
        for b in range(3):
            dve.wait_ge(self.chip.block_done, self.block_count(2 * b + 1))
            product = self.chip.ps[:, 4 * (b % 2):4 * (b % 2) + 4, :].rearrange("p b (m n) -> p (b m) n", n=N)
            v.tensor_tensor(self.part if b else self.merged, product, self.gates[:, KD * b:KD * (b + 1), :], ALU.mult)\
                .then_inc(self.used.sem, 1)
            dve.wait_ge(self.used.sem, self.used.at(b + 1))
            if b == 1:
                link(v.tensor_tensor(self.merged, self.merged, self.part, ALU.add))
        for i in range(2):
            tiles = slice(4 * i, 4 * i + 4)
            v.tensor_tensor(self.merged[:, tiles, :], self.merged[:, tiles, :], self.part[:, tiles, :], ALU.add)\
                .then_inc(self.merged_ready.sem, 1)
        for i in range(2):
            tiles = slice(4 * i, 4 * i + 4)
            dve.wait_ge(self.merged_rounded.sem, self.merged_rounded.at(i + 1))
            last = v.tensor_tensor(self.parts[1][:, tiles, :], self.merged[:, tiles, :],
                                   self.parts[0].bitcast(F32)[:, tiles, :], ALU.subtract)
        last.then_inc(self.chip.stage_done, 1)


G_GATES = 0
G_SLOT = NKEYS * N
G_HOT = G_SLOT + 3 * N
G_GELU = G_SLOT
G_ACT = G_GELU + 2 * N
G_Q = 0
G_S = G_Q + 16 * N
G_TOP = G_S + NT * 16 * P
G_IDX = G_TOP + NT * 16 * TOPK
G_REST = G_IDX + NT * 16 * TOPK
G_CAND = G_REST + N
G_HOTK = G_CAND + HEADS * TOPK * TOPK
G_SEL = G_HOTK + HEADS * TOPK * TOPK
G_SQ = 0
G_SMALL = KD * N


def expert_input(chip):
    return chip.x_parts[:, :, 0:N], chip.x_parts[:, :, N:]


class PeerRoute(Stage):

    blocks = BLOCKS["wq"] + BLOCKS["keys"]
    whole = BLOCKS["keys"]

    def __init__(self, chip):
        super().__init__(chip)
        at, sig = chip.at, chip.signals
        self.z = expert_input(chip)
        self.q = at(G_Q, 16, N)
        self.s = at(G_S, NT, 16, P)
        self.top, self.idx = at(G_TOP, NT, 16, TOPK), at(G_IDX, NT, 16, TOPK)
        self.rest = at(G_REST, N)
        self.cand, self.hot = at(G_CAND, HEADS, TOPK, TOPK), at(G_HOTK, HEADS, TOPK, TOPK)
        self.sel = at(G_SEL, NT, 8, HEADS, TOPK)
        self.slot = at(G_SLOT, 3, N)
        self.q_kept = sig("peer_q_kept", 8)
        self.scored = sig("peer_scored", 8)
        self.s_kept = sig("peer_s_kept", 8)
        self.shifted = sig("peer_shifted", NT)
        self.exped = sig("peer_exped", NT)
        self.chosen = sig("peer_chosen", 1)
        self.turned = sig("peer_turned", 3)
        self.slot_kept = sig("peer_slot_kept", 3)

    def pe(self, pe):
        nc, ps = self.nc, self.chip.ps
        pe.wait_ge(self.chip.stage_done, self.index)
        for j in range(8):
            whi, wlo = self.weights(j)
            if j >= 4:
                pe.wait_ge(self.q_kept.sem, self.q_kept.at(j - 3))
            for e in range(2):
                pe.wait_ge(self.chip.rest_done[e], self.split_count(j))
                for k in range(KD):
                    i = e * KD + k
                    last = self.product(ps[:, j % 4, e * N:(e + 1) * N], (whi[:, i, :], wlo[:, i, :]),
                                        [z[:, k, :] for z in self.z], k == 0, k == KD - 1)
            last.then_inc(self.chip.block_done, 1)
        pe.wait_ge(self.q_kept.sem, self.q_kept.at(8))
        slot, count = self.arrival(8)
        pe.wait_ge(self.chip.loaded[slot], count)
        w = self.chip.ring[:, slot]
        for n in range(8):
            t, four = divmod(n, 4)
            if n >= 4:
                pe.wait_ge(self.s_kept.sem, self.s_kept.at(n - 3))
            for i in range(4):
                hp = 4 * four + i
                last = nc.tensor.matmul(ps[:, n % 4, i * P:(i + 1) * P], self.q[:, hp, t * P:(t + 1) * P], w[:, hp, :],
                                        start=True, stop=True)
            last.then_inc(self.scored.sem, 1)
        pe.wait_ge(self.s_kept.sem, self.s_kept.at(8))
        pe.sem_inc(self.chip.block_done, 1)
        pe.wait_ge(self.chosen.sem, self.chosen.at(1))
        for j in range(3):
            for t in range(NT):
                last = nc.tensor.transpose(ps[:, j, t * P:(t + 1) * P], self.sel[:, t, 5 + j].rearrange("p h k -> p (h k)"),
                                           self.chip.ident)
            last.then_inc(self.turned.sem, 1)

    def act(self, act, link):
        nc, ps = self.nc, self.chip.ps
        self.lead(act)
        act.wait_ge(self.chip.stage_done, self.index)
        for j in range(8):
            self.round(act, j + ROUNDED)
            act.wait_ge(self.chip.block_done, self.block_count(j))
            nc.scalar.activation(self.q[:, 2 * j:2 * j + 2, :].rearrange("p a n -> p (a n)"), ps[:, j % 4, :], ACT.Copy)\
                .then_inc(self.q_kept.sem, 1)
        for n in range(8):
            t, four = divmod(n, 4)
            act.wait_ge(self.scored.sem, self.scored.at(n + 1))
            nc.scalar.activation(self.s[:, t, 4 * four:4 * four + 4, :].rearrange("p a n -> p (a n)"), ps[:, n % 4, :], ACT.Copy)\
                .then_inc(self.s_kept.sem, 1)
        for t in range(NT):
            act.wait_ge(self.shifted.sem, self.shifted.at(t + 1))
            nc.scalar.activation(self.sel[:, t, 7], self.sel[:, t, 7], ACT.Exp).then_inc(self.exped.sem, 1)
        for j in range(3):
            act.wait_ge(self.turned.sem, self.turned.at(j + 1))
            nc.scalar.activation(self.slot[:, j, :], ps[:, j, 0:N], ACT.Copy).then_inc(self.slot_kept.sem, 1)
        act.wait_ge(self.slot_kept.sem, self.slot_kept.at(3))
        act.sem_inc(self.chip.stage_done, 1)

    def dve(self, dve, link):
        v = self.nc.vector
        dve.wait_ge(self.chip.stage_done, self.index)

        def best(values, scratch, top, places):
            link(v.max(top[:, 0:8], values))
            v.max_index(places[:, 0:8], top[:, 0:8], values)
            link(v.match_replace(scratch, top[:, 0:8], values, -3e38))
            link(v.max(top[:, 8:16], scratch))
            link(v.max_index(places[:, 8:16], top[:, 8:16], scratch))

        for t in range(NT):
            dve.wait_ge(self.s_kept.sem, self.s_kept.at(4 * t + 4))
            for hp in range(16):
                best(self.s[:, t, hp, :], self.rest[:, 0:P], self.top[:, t, hp, :], self.idx[:, t, hp, :].bitcast(U32))
            link(v.tensor_copy(self.idx[:, t], self.idx[:, t].bitcast(U32)))
            top = self.top[:, t].rearrange("p (h a) k -> p h a k", a=2)
            idx = self.idx[:, t].rearrange("p (h a) k -> p h a k", a=2)
            wide = [P, HEADS, TOPK, TOPK]
            link(v.tensor_tensor(self.cand, top[:, :, 0, :].unsqueeze(3).broadcast_to(wide),
                                 top[:, :, 1, :].unsqueeze(2).broadcast_to(wide), ALU.add))
            sel = self.sel[:, t]
            score, place, rank = sel[:, 0], sel[:, 1], sel[:, 2:4]
            for h in range(HEADS):
                best(self.cand[:, h].rearrange("p a b -> p (a b)"), self.rest, score[:, h, :], place[:, h, :].bitcast(U32))
            link(v.tensor_scalar(rank[:, 0].bitcast(U32), place.bitcast(U32), 4, None, ALU.logical_shift_right))
            link(v.tensor_scalar(rank[:, 1].bitcast(U32), place.bitcast(U32), TOPK - 1, None, ALU.bitwise_and))
            link(v.tensor_copy(rank, rank.bitcast(U32)))
            for a in range(2):
                hot = self.hot.rearrange("p h k j -> p (h k) j")
                choice = rank[:, a].rearrange("p h k -> p (h k)").unsqueeze(2).broadcast_to([P, P, TOPK])
                iota = self.chip.iota[:, 0:TOPK].unsqueeze(1).broadcast_to([P, P, TOPK])
                link(v.tensor_tensor(hot, choice, iota, ALU.is_equal))
                link(v.tensor_tensor(self.hot, self.hot, idx[:, :, a, :].unsqueeze(2).broadcast_to(wide), ALU.mult))
                link(v.tensor_reduce(sel[:, 5 + a].rearrange("p h k -> p (h k)"), hot, AX.X, ALU.add))
            gate = sel[:, 7]
            v.tensor_tensor(gate, score, score[:, :, 0:1].broadcast_to([P, HEADS, TOPK]), ALU.subtract).then_inc(self.shifted.sem, 1)
            dve.wait_ge(self.exped.sem, self.exped.at(t + 1))
            total = sel[:, 4, :, 0]
            link(v.tensor_reduce(total, gate, AX.X, ALU.add))
            link(v.reciprocal(total, total))
            last = v.tensor_tensor(gate, gate, total.unsqueeze(2).broadcast_to([P, HEADS, TOPK]), ALU.mult)
            if t == 0:
                link(last)
        last.then_inc(self.chosen.sem, 1)


class PeerGates(Stage):

    SETS = N // 4

    def __init__(self, chip):
        super().__init__(chip)
        self.slot = chip.at(G_SLOT, 3, N)
        self.hot = chip.at(G_HOT, 2, 2, 4 * P)
        self.gates = chip.at(G_GATES, N * NKEYS)
        self.ready = chip.signals("hot_ready", self.SETS)
        self.done = chip.signals("gates_done", self.SETS)
        self.kept = chip.signals("gates_kept", self.SETS)

    def dve(self, dve, link):
        v = self.nc.vector
        dve.wait_ge(self.chip.stage_done, self.index)

        def body(it, first=False):
            for r in range(2):
                n = it * 2 + r
                if not first:
                    dve.wait_ge(self.done.sem, self.done.at(n - 1))
                for i in range(4):
                    t = n * 4 + i
                    key1, key2, gate = (self.slot[:, j, bass.ds(t, 1)] for j in range(3))
                    v.tensor_scalar(self.hot[:, r, 0, i * P:(i + 1) * P], self.chip.iota, key1, gate, ALU.is_equal, ALU.mult)
                    last = v.tensor_scalar(self.hot[:, r, 1, i * P:(i + 1) * P], self.chip.iota, key2, None, ALU.is_equal)
                last.then_inc(self.ready.sem, 1)

        body(0, first=True)
        with dve.Fori(1, self.SETS // 2) as it:
            body(it)

    def pe(self, pe):
        pe.wait_ge(self.chip.stage_done, self.index)

        def body(it, first=False):
            for r in range(2):
                n = it * 2 + r
                pe.wait_ge(self.ready.sem, self.ready.at(n + 1))
                if not first:
                    pe.wait_ge(self.kept.sem, self.kept.at(n - 1))
                for i in range(4):
                    at = slice(i * P, (i + 1) * P)
                    last = self.nc.tensor.matmul(self.chip.ps[:, r, at], self.hot[:, r, 0, at], self.hot[:, r, 1, at],
                                                 start=True, stop=True)
                last.then_inc(self.done.sem, 1)

        body(0, first=True)
        with pe.Fori(1, self.SETS // 2) as it:
            body(it)

    def act(self, act, link):
        act.wait_ge(self.chip.stage_done, self.index)

        def body(it):
            for r in range(2):
                n = it * 2 + r
                act.wait_ge(self.done.sem, self.done.at(n + 1))
                self.nc.scalar.activation(self.gates[:, bass.ds(n * 4 * NKEYS, 4 * NKEYS)], self.chip.ps[:, r, :], ACT.Copy)\
                    .then_inc(self.kept.sem, 1)

        with act.Fori(0, self.SETS // 2) as it:
            body(it)
        act.wait_ge(self.kept.sem, self.kept.at(self.SETS))
        act.sem_inc(self.chip.stage_done, 1)


class PeerExperts(Stage):

    blocks = BLOCKS["experts"]

    def __init__(self, chip):
        super().__init__(chip)
        self.z = expert_input(chip)
        self.gates = chip.at(G_GATES, N, NKEYS)
        self.gelu = chip.at(G_GELU, 2, N)
        self.parts = chip.parts_at(G_ACT, 2, N), chip.parts_at(G_ACT + 2 * N, 2, N)
        self.zero = chip.at(G_ACT + 4 * N, P)
        n = self.blocks
        self.zeroed = chip.signals("expert_zeroed", 1)
        self.closed = chip.signals("expert_closed", 1)
        self.up_done = chip.signals("expert_up_done", n)
        self.gelu_ready = chip.signals("expert_gelu_ready", n)
        self.gated = chip.signals("expert_gated", n)
        self.act_rounded = chip.signals("expert_act_rounded", n)
        self.act_ready = chip.signals("expert_act_ready", n)

    def out(self, m):
        return self.chip.ps[:, 4 + m // 2, (m % 2) * N:(m % 2 + 1) * N]

    def pe(self, pe):
        nc, c = self.nc, self.chip
        pe.wait_ge(self.chip.stage_done, self.index)

        def up(it, r, wait):
            b = it * RING + r
            whi, wlo = self.weights(r)
            pe.wait_ge(c.rest_done[0], self.split_count(b))
            if wait:
                pe.wait_ge(self.gelu_ready.sem, self.gelu_ready.at(b - 1))
            for k in range(KD):
                last = self.product(c.ps[:, r % 2, 0:N], (whi[:, k, :], wlo[:, k, :]), [z[:, k, :] for z in self.z],
                                    k == 0, k == KD - 1)
            last.then_inc(self.up_done.sem, 1)

        def down(it, r):
            b = it * RING + r
            whi, wlo = self.weights(r)
            pe.wait_ge(c.rest_done[1], self.split_count(b))
            pe.wait_ge(self.act_ready.sem, self.act_ready.at(b + 1))
            for m in range(KD):
                last = self.product(self.out(m), (whi[:, KD + m, :], wlo[:, KD + m, :]), [a[:, r % 2, :] for a in self.parts],
                                    False, False)
            last.then_inc(c.block_done, 1)

        for r in range(RING):
            up(0, r, wait=r >= 2)
            if r:
                down(0, r - 1)
        with pe.Fori(1, self.blocks // RING) as it:
            for r in range(RING):
                up(it, r, wait=True)
                down(it - 1 if r == 0 else it, (r - 1) % RING)
        down(self.blocks // RING - 1, RING - 1)
        pe.wait_ge(self.zeroed.sem, self.zeroed.at(1))
        for bank in range(4, 8):
            last = nc.tensor.matmul(c.ps[:, bank, :], self.zero, c.cst[:], start=False, stop=True)
        last.then_inc(self.closed.sem, 1)

    def act(self, act, link):
        c, copy = self.chip, self.nc.scalar.activation
        n = self.blocks
        self.lead(act)
        act.wait_ge(c.stage_done, self.index)

        def body(it, first=False, last=False):
            for r in range(RING):
                b = it * RING + r
                act.wait_ge(self.up_done.sem, self.up_done.at(b + 1))
                if not (first and r < 2):
                    act.wait_ge(self.gated.sem, self.gated.at(b - 1))
                    act.wait_ge(self.act_ready.sem, self.act_ready.at(b - 1))
                copy(self.gelu[:, r % 2, :], c.ps[:, r % 2, 0:N], ACT.Gelu).then_inc(self.gelu_ready.sem, 1)
                if not (last and r + ROUNDED >= RING):
                    self.round_next(act, it, r + ROUNDED, 0)
                act.wait_ge(self.gated.sem, self.gated.at(b + 1))
                if not (first and r < 2):
                    act.wait_ge(c.block_done, self.block_count(b - 2))
                copy(self.parts[0][:, r % 2, :], self.gelu[:, r % 2, :], ACT.Copy).then_inc(self.act_rounded.sem, 1)
                if not (first and r == 0) and not (last and r + 1 >= RING):
                    act.wait_ge(c.block_done, self.block_count(b - 1))
                    self.round_next(act, it, r + 1, 1)

        body(0, first=True)
        with act.Fori(1, n // RING - 1) as it:
            body(it)
        body(n // RING - 1, last=True)

    def round_next(self, act, it, r, h):
        c, half = self.chip, slice(h * HALF, (h + 1) * HALF)
        f = self.b0 % RING + r
        act.wait_ge(c.loaded[f % RING], (it + self.b0 // RING + f // RING + 1) * 16)
        self.nc.scalar.activation(c.rounded[:, (self.s0 + r) % ROUNDED, half], c.ring[:, f % RING, half], ACT.Copy)\
            .then_inc(c.rounded_done[h], 1)

    def pool(self, pool, link):
        n = self.blocks
        self.leave_rest(0, 0, self.split_count(0))
        self.leave_rest(0, 1, self.split_count(0))
        self.leave_rest(1, 0, self.split_count(1))
        self.leave_rest(1, 1, self.split_count(1))
        self.leave_rest(2, 0, self.split_count(2))
        self.leave_rest(3, 0, self.split_count(3))
        self.leave_rest(2, 1, self.split_count(2))
        with pool.Fori(1, n // RING) as it:
            for r in range(RING):
                b = it * RING + r
                self.leave_rest(r, 0, self.split_count(b))
                self.leave_rest((r - 1) % RING, 1, self.split_count(b - 1))
        self.leave_rest(RING - 1, 1, self.split_count(n - 1))

    def dve(self, dve, link):
        v, c = self.nc.vector, self.chip
        dve.wait_ge(self.chip.stage_done, self.index)
        v.memset(self.zero, 0.0).then_inc(self.zeroed.sem, 1)

        def body(it, first=False):
            for r in range(RING):
                b = it * RING + r
                gelu = self.gelu[:, r % 2, :]
                dve.wait_ge(self.gelu_ready.sem, self.gelu_ready.at(b + 1))
                v.tensor_tensor(gelu, gelu, self.gates[:, :, bass.ds(b, 1)].rearrange("p t a -> p (t a)"), ALU.mult)\
                    .then_inc(self.gated.sem, 1)
                dve.wait_ge(self.act_rounded.sem, self.act_rounded.at(b + 1))
                v.tensor_tensor(self.parts[1][:, r % 2, :], gelu, self.parts[0].bitcast(F32)[:, r % 2, :], ALU.subtract)\
                    .then_inc(self.act_ready.sem, 1)

        body(0, first=True)
        with dve.Fori(1, self.blocks // RING) as it:
            body(it)
        dve.wait_ge(self.closed.sem, self.closed.at(1))
        v.tensor_copy(c.x[:, :, 0:N], c.ps[:, 4:8, :].rearrange("p b (m n) -> p (b m) n", n=N)).then_inc(c.stage_done, 1)


def second_norm(chip, gain, split=False):
    small = [chip.at(B_SMALL + i * N, N) for i in range(3)]
    return Norm(chip, chip.at(B_U, KD, N), chip.at(B_SQ, KD, N), small, N, gain=gain, parts=second_input(chip) if split else None)


def expert_norm(chip, gain):
    small = [chip.at(G_SMALL + i * N, N) for i in range(3)]
    return Norm(chip, chip.x[:, :, N:], chip.at(G_SQ, KD, N), small, N, gain=gain, parts=expert_input(chip), keep=True)


def second_network(chip):
    vec = chip.vec[:]
    stages = [second_norm(chip, columns(vec, "final_g")), Replace(chip)]
    for layer in range(DEPTH):
        stages += [LoadTables(chip), second_norm(chip, columns(vec, "ln1", layer, KD), split=True), ProjectIn(chip),
                   Attention(chip, layer), Rwkv(chip, layer)]
        merge = Merge(chip)
        stages += [merge, Project(chip, merge.parts, KD, N),
                   expert_norm(chip, columns(vec, "ln2", layer, KD)),
                   PeerRoute(chip), PeerGates(chip), PeerExperts(chip)]
    final = second_norm(chip, columns(vec, "lnf"))
    return stages + [final, Finish(chip, final.u)]


class Replace(Stage):

    def dve(self, dve, link):
        dve.wait_ge(self.chip.stage_done, self.index)
        self.nc.vector.tensor_copy(self.chip.x[:, :, 0:N], self.chip.at(B_U, KD, N)).then_inc(self.chip.stage_done, 1)


def second_weights(i):
    for layer in range(DEPTH):
        w = i["w_in_2"][layer]
        cut = lambda a, n: w[:, a:a + n]
        pad = lambda a: np.concatenate([a, np.zeros((D, P - a.shape[1]), np.float32)], axis=1)
        heads = lambda a: a.reshape(D, 2, 4, DH).transpose(0, 2, 1, 3).reshape(D, 8 * DH)
        n0 = 14 * P
        nq, (kc, vc, ks, vs, kw, vw) = cut(n0, 512), [cut(n0 + 512 + P * j, P) for j in range(6)]
        gate = cut(n0 + 1280, 24)
        s0 = n0 + 1304
        sq, sk, sv = cut(s0, 512), cut(s0 + 512, P), cut(s0 + 640, P)
        both = [np.concatenate([kc[:, g * DH:(g + 1) * DH], vc[:, g * DH:(g + 1) * DH]], axis=1) for g in range(2)]
        yield pairs(np.concatenate([cut(0, n0), heads(nq), *both, ks, kw, heads(sq), sk, np.zeros((D, P), np.float32),
                                    vs, vw, pad(gate), sv, cut(s0 + 768, 3 * D)], axis=1))
        kv = np.concatenate([i[n][layer].reshape(CMP_LEN, DH, 2, P) for n in ("nsa_ck_w1_2", "nsa_cv_w1_2")], axis=1)
        yield kv.transpose(0, 2, 1, 3).reshape(4, TPB, P, P).transpose(0, 2, 1, 3)
        ck, cv = (i[n][layer].reshape(2, P, DH).transpose(1, 0, 2) for n in ("nsa_ck_w2_2", "nsa_cv_w2_2"))
        small = np.zeros((1, P, TPB, P), np.float32)
        small[0, :, 0:2, :DH], small[0, :, 0:2, DH:], small[0, :, 2:4, :DH] = ck, ck, cv
        yield small
        ranks = np.zeros((1, P, TPB, P), np.float32)
        ranks[0, :64, 0:4], ranks[0, 64:, 0:4] = (i[n][layer].reshape(64, 4, P) for n in ("rwkv_w2_2", "rwkv_a2_2"))
        ranks[0, :, 4:8] = i["rwkv_g2_2"][layer].reshape(P, 4, P)
        yield ranks
        rows_ = lambda a: a.reshape(2, 4, DH, D).transpose(1, 0, 2, 3).reshape(8 * DH, D)
        for a in (i["w_br_a_2"][layer], rows_(i["w_br_b_2"][layer]), rows_(i["w_br_c_2"][layer])):
            yield a.reshape(4, P, 2, 4, P).transpose(2, 1, 3, 0, 4).reshape(2, P, TPB, P)
        yield rows(i["w_out_2"][layer])
        yield pairs(i["peer_wq_2"][layer])
        yield i["peer_subkeys_2"][layer].reshape(TPB, P, P).transpose(2, 0, 1)[None]
        u = i["peer_u_2"][layer].reshape(P, NKEYS, KD, P).transpose(1, 3, 2, 0)
        v = i["peer_v_2"][layer].reshape(P, NKEYS, KD, P).transpose(1, 0, 2, 3)
        yield np.concatenate([u, v], axis=2)


def second_constants():
    p = np.arange(P)
    s, t = p[:, None], p[None, :]
    same = s // CH == t // CH
    parts = [same & (s < t), same & (s <= t)]
    for n in (1, 2, 4, 8, 16):
        parts.append((s // (2 * n) == t // (2 * n)) & (s % (2 * n) < n) & (t % (2 * n) >= n))
    end = np.arange(16) * CMP_STRIDE + CMP_LEN - 1
    seen = [np.where(end[None, :] <= (p + k * P)[:, None], 0.0, NEG) for k in range(NT)]
    return np.concatenate([x.astype(np.float32) for x in parts] + seen, axis=1)


N_INPUT_DMAS = 5


class Finish(Stage):

    def __init__(self, chip, out):
        super().__init__(chip)
        self.out = out
        self.stored = chip.signals("out_stored", 16)

    def act(self, act, link):
        act.wait_ge(self.chip.stage_done, self.index)
        act.dma_start(self.chip.io["out"], self.out).then_inc(self.stored.sem, 16)
        act.wait_ge(self.stored.sem, self.stored.at(16))


def first_network(chip):
    stages = [Start(chip)]
    for layer in range(DEPTH):
        last = layer == DEPTH - 1
        stages.append(Modulation(chip, layer))
        stages += feed_forward(chip, 2 * N, 0)
        stages.append(first_norm(chip, 2 * N, 1, split=layer > 0))
        if layer == 0:
            fourier = Fourier(chip)
            stages += [fourier, Project(chip, fourier.parts, KD, 2 * N, gate=5)]
        else:
            retention = Retention(chip)
            stages += [retention, Project(chip, retention.parts, RH * RDV // P, N, gate=5)]
        stages += feed_forward(chip, N if last else 2 * N, 2)
    return stages


def program(nc, io):
    ctx = ExitStack()
    with ctx:
        chip = Chip(nc, ctx, io)
        stages = first_network(chip) + second_network(chip)
        for stage, after in zip(stages, stages[1:]):
            stage.next = after
        setup_tables = [(chip.x[:], io["x"]), (chip.vec[:], io["vec"]), (chip.cst[:], io["cst"]),
                        (chip.at(A_CST1, NCST1), io["cst1"]), (chip.at(A_WORK + 16 * BIASW, 16 * P + BIASW), io["bias_in"])]
        block = ctx.enter_context(nc.Block())

        @block.sync
        def _(sp):
            assert len(setup_tables) == N_INPUT_DMAS
            for to, of in setup_tables:
                sp.dma_start(to, of).then_inc(chip.inputs_loaded, 16)
            for b in range(RING):
                sp.dma_start(chip.ring[:, b], io["weights"][b]).then_inc(chip.loaded[b], 16)
            rounds = chip.n_blocks // RING
            with sp.Fori(1, rounds) as i:
                for r in range(RING):
                    sp.wait_ge(chip.block_done, (i - 1) * RING + r + 1)
                    sp.dma_start(chip.ring[:, r], io["weights"][bass.ds(i * RING + r, 1)].rearrange("a p t c -> p (a t) c"))\
                        .then_inc(chip.loaded[r], 16)
            for b in range(rounds * RING, chip.n_blocks):
                sp.wait_ge(chip.block_done, b - RING + 1)
                sp.dma_start(chip.ring[:, b % RING], io["weights"][b]).then_inc(chip.loaded[b % RING], 16)

        @block.tensor
        def _(pe):
            for s in stages:
                s.pe(pe)

        @block.scalar
        def _(act):
            link = Link(act, chip.links["act"])
            for s in stages:
                s.act(act, link)

        @block.vector
        def _(dve):
            link = Link(dve, chip.links["dve"])
            for s in stages:
                s.dve(dve, link)

        @block.gpsimd
        def _(pool):
            link = Link(pool, chip.links["pool"])
            for s in stages:
                s.pool(pool, link)
    return chip


def pairs(w):
    k, m = w.shape[0] // P, w.shape[1] // (2 * P)
    return w.reshape(k, P, m, 2, P).transpose(2, 1, 3, 0, 4).reshape(m, P, 2 * k, P)


def rows(w):
    return w.reshape(w.shape[0] // (2 * P), 2, P, KD, P).transpose(0, 2, 1, 3, 4).reshape(-1, P, TPB, P)


def halves(w):
    return w.reshape(KD, P, 2, KF, P).transpose(3, 1, 2, 0, 4).reshape(KF, P, TPB, P)


def wide_blocks(w):
    return w.reshape(2, 4, P, -1, 4, P).transpose(3, 0, 2, 1, 4, 5).reshape(-1, P, TPB, P)


def retention_in(w):
    qk, v, g = w[:, :2 * D], w[:, 2 * D:2 * D + RH * RDV], w[:, 2 * D + RH * RDV:]
    return np.concatenate([pairs(qk), wide_blocks(v), pairs(g)])


def first_weights(i):
    for layer in range(DEPTH):
        yield wide_blocks(i["w_mod"][layer])
        yield halves(i["ffn_w_in"][layer, 0])
        yield rows(i["ffn_w_out"][layer, 0])
        if layer == 0:
            yield rows(i["fnet_w_out"][0])
        else:
            yield retention_in(i["ret_w_in"][0])
            yield rows(i["ret_w_out"][0])
        yield halves(i["ffn_w_in"][layer, 1])
        yield rows(i["ffn_w_out"][layer, 1])


def features(v):
    return np.asarray(v).reshape(-1, P).T


def vector_table(i):
    cond = np.stack([features(i["c"]), features(i["c_ctx"])], axis=2).reshape(P, -1)
    pe = np.concatenate([np.concatenate([i["nsa_pe_k_2"][l].T, i["nsa_pe_v_2"][l].T]) for l in range(DEPTH)], axis=1)
    wide = lambda a: np.broadcast_to(np.asarray(a).reshape(1, -1), (P, np.asarray(a).size))
    sinks = i["swa_sinks_2"]
    parts = {"cond": cond, "b_mod": features(i["b_mod"]), "norm_g": features(i["norm_g"]),
             "final_g": features(i["final_norm_g"]), "ln1": features(i["ln1_w_2"]), "ln2": features(i["ln2_w_2"]),
             "lnf": features(i["lnf_w_2"]), "mu": features(i["rwkv_mu_2"]), "w0": features(i["rwkv_w0_2"]),
             "a0": features(i["rwkv_a0_2"]), "k_k": features(i["rwkv_k_k_2"]), "k_a": features(i["rwkv_k_a_2"]),
             "r_k": features(i["rwkv_r_k_2"]), "ln_w": features(i["rwkv_ln_w_2"]), "ln_b": features(i["rwkv_ln_b_2"]),
             "pe": pe, "decay": wide(i["ret_decay_logit"]), "sinks": wide(sinks)}
    out = np.concatenate([parts[n] for n in VEC], axis=1)
    assert out.shape == (P, NVEC), out.shape
    return np.ascontiguousarray(out, dtype=np.float32)


def constants():
    f = np.float32
    p = np.arange(P)
    cst = np.stack([np.eye(P), np.ones((P, P)), p[:, None] // DH == p[None, :] // DH,
                    np.broadcast_to(p[None, :], (P, P))], axis=1).astype(f)
    a = 2 * np.pi * np.outer(p, p) / P
    dft = np.concatenate([np.cos(a), np.sin(a)], axis=1)
    n = np.arange(N)
    b = 2 * np.pi * np.outer(n, n) / N
    norm = 1 / math.sqrt(N * P)
    cosn, sinn = ((t * norm).reshape(NT, P, N).transpose(1, 0, 2).reshape(P, -1) for t in (np.cos(b), -np.sin(b)))
    perm = np.zeros((P, P))
    perm[p[:64] + 64, p[:64]] = -1
    perm[p[:64], p[:64] + 64] = 1
    freq = np.exp(-f(math.log(10000.0)) * np.arange(64, dtype=f) / f(64)).astype(f)
    ang = [(t.astype(f)[None, :] * np.tile(freq, 2)[:, None]).astype(f) for t in (n // 64, n % 64)]
    cos, sin = (np.concatenate([t(x) for x in ang], axis=1) for t in (np.cos, np.sin))
    m = np.arange(N)[:, None]
    expo = [np.maximum(n - m, 0), np.maximum(m - n, 0), n - m + N, N - n + m]
    expo = np.concatenate([e.reshape(NT, P, N).transpose(1, 0, 2).reshape(P, -1) for e in expo], axis=1)
    cst1 = np.concatenate([dft, cosn, sinn, perm, cos, sin], axis=1).astype(f)
    assert cst1.shape == (P, NCST1)
    return {"cst": cst, "cst1": cst1, "expo": expo, "cst2": second_constants()}


def bias_inputs(table):
    f = np.float32
    d = N - 1 - np.arange(BIASW)
    exact = BUCKETS // 2
    nf = np.maximum(d, exact).astype(f)
    large = exact + (np.log(nf / exact) / f(math.log(MAX_DIST / exact)) * (BUCKETS - exact)).astype(np.int32)
    bucket = np.where(d < exact, np.maximum(d, 0), np.minimum(large, BUCKETS - 1))
    hot = (bucket[None, :] == np.arange(BUCKETS)[:, None]) & (d >= 0)[None, :]
    hot = np.concatenate([hot, (d < 0)[None, :], (d >= SWA_WINDOW)[None, :]]).astype(f)
    masks = np.zeros((2, 16), f)
    masks[0], masks[1, 8:] = NEG, NEG
    left = np.concatenate([table, masks])
    out = np.zeros((P, 16 * P + BIASW), f)
    out[:BUCKETS + 2, :16 * P] = np.broadcast_to(left[:, :, None], (BUCKETS + 2, 16, P)).reshape(BUCKETS + 2, -1)
    out[:BUCKETS + 2, 16 * P:] = hot
    return out


def tokens_last(x):
    return np.asarray(x).reshape(-1, KD, P).transpose(2, 1, 0)


def stream(i):
    total = sum(w.shape[0] for w in _parts(i))
    out = np.zeros((total, P, TPB, P), np.float32)
    b = 0
    for w in _parts(i):
        out[b:b + len(w), :, :w.shape[2], :w.shape[3]] = w
        b += len(w)
    return out


def _parts(i):
    yield from first_weights(i)
    yield from second_weights(i)


def kernel(**inputs):
    import concourse.bacc as bacc
    from concourse.bass_utils import run_bass_kernel_spmd

    i = {k: np.asarray(v) for k, v in inputs.items()}
    arrays = {"x": np.ascontiguousarray(np.concatenate([tokens_last(i["x"]), tokens_last(i["ctx"])], axis=2)),
              "vec": vector_table(i), "bias_in": bias_inputs(i["rel_bias_2"]), "weights": stream(i)}
    arrays.update({k: np.ascontiguousarray(v, dtype=np.float32) for k, v in constants().items()})
    nc = bacc.Bacc("TRN2", target_bir_lowering=False, num_devices=1)
    io = {k: nc.dram_tensor(f"in_{k}", v.shape, F32, kind="ExternalInput").ap() for k, v in arrays.items()}
    io["out"] = nc.dram_tensor("out", (P, KD, N), F32, kind="ExternalOutput").ap()
    io["bias_scratch"] = nc.dram_tensor("bias_scratch", (P, 16, BIASW), F32, kind="Internal").ap()
    program(nc, io)
    r = run_bass_kernel_spmd(nc, [{f"in_{k}": v for k, v in arrays.items()}], core_ids=[0])
    return np.ascontiguousarray(r.results[0]["out"].transpose(2, 1, 0).reshape(1, N, D))
```

```python
import math
from contextlib import ExitStack

import numpy as np
import concourse.bass as bass
from concourse import mybir

F32 = mybir.dt.float32
F32R = mybir.dt.float32r
U32 = mybir.dt.uint32
ACT = mybir.ActivationFunctionType
ALU = mybir.AluOpType
AX = mybir.AxisListType

P = 128
D = 1024
N = 256
KD = D // P
NT = N // P
DEPTH = 2
N_MOD = 9
EPS = 1e-6
FF = 2816
KF = FF // P
TPB = 16
RING = 4
HALF = TPB // 2
ROUNDED = 2
ARENA = 35728

RH, RDK, RDV = 4, 256, 512
DH = 64
GN_EPS = 64e-5
HEADS = 8
CH = 32
NCH = N // CH
CMP_LEN, CMP_STRIDE = 32, 16
NCMP = N // CMP_STRIDE - CMP_LEN // CMP_STRIDE + 1
NEG = -1e30
BUCKETS, MAX_DIST = 32, 128
SWA_WINDOW = 128
NKEYS = 128
TOPK = 16
BIASW = 384

VEC = {}
_n = 0
for _name, _w in [("cond", 2 * KD), ("b_mod", DEPTH * 72), ("norm_g", DEPTH * 3 * KD), ("final_g", KD),
                  ("ln1", DEPTH * KD), ("ln2", DEPTH * KD), ("lnf", KD), ("mu", DEPTH * 14),
                  ("w0", DEPTH * 4), ("a0", DEPTH * 4), ("k_k", DEPTH * 4), ("k_a", DEPTH * 4),
                  ("r_k", DEPTH * 4), ("ln_w", DEPTH * 4), ("ln_b", DEPTH * 4), ("pe", DEPTH * 32),
                  ("decay", 8), ("sinks", DEPTH * 8)]:
    VEC[_name] = (_n, _n + _w)
    _n += _w
NVEC = _n

BLOCKS = {"mod": 36, "ffn_in": KF, "ffn_out": KF // 2, "fnet": KD // 2, "ret_in": 24, "ret_out": 8,
          "in2": 28, "cmp1": 4, "cmp2": 1, "rwkv": 1, "branch": 6, "out2": 4, "wq": 8,
          "experts": NKEYS}


def columns(table, name, layer=0, width=None):
    a, b = VEC[name]
    if width is None:
        return table[:, a:b]
    return table[:, a + layer * width:a + (layer + 1) * width]


class Signals:

    def __init__(self, nc, ctx):
        self.nc, self.ctx, self.sems, self.total = nc, ctx, {}, {}

    def __call__(self, name, n):
        if name not in self.sems:
            self.sems[name] = self.ctx.enter_context(self.nc.semaphore(name))
            self.total[name] = 0
        base = self.total[name]
        self.total[name] += n
        return Share(self.sems[name], base)


class Share:
    def __init__(self, sem, base):
        self.sem, self.base = sem, base

    def at(self, k):
        return self.base + k


class Link:

    def __init__(self, eng, sem):
        self.eng, self.sem, self.n = eng, sem, 0

    def __call__(self, ins):
        self.n += 1
        ins.then_inc(self.sem, 1)
        self.eng.wait_ge(self.sem, self.n)


class Chip:

    def __init__(self, nc, ctx, io):
        self.nc, self.io = nc, io
        self.signals = Signals(nc, ctx)
        self.next_byte = -(-nc.sbuf_base // 32) * 32
        self.ring, self.ring_rest = self.place("ring", [P, RING, TPB, P], "ring_rest")
        self.x, self.x_parts = self.place("x", [P, KD, 2 * N], "x_parts")
        self.arena_byte = self.next_byte
        self.arena, = self.place("arena", [P, ARENA])
        self.named = {}
        self.rounded, = self.place("rounded", [P, ROUNDED, TPB, P], kind=F32R)
        self.vec, = self.place("vec", [P, NVEC])
        self.cst, = self.place("cst", [P, 4, P])
        self.ident, self.ones = self.cst[:, 0, :], self.cst[:, 1, :]
        self.headones, self.iota = self.cst[:, 2, :], self.cst[:, 3, :]
        self.mods, = self.place("mods", [P, N_MOD, KD, 2])
        self.ps = ctx.enter_context(nc.psum_tensor("ps", [P, 8, 512], F32))
        self.loaded = [ctx.enter_context(nc.semaphore(f"block_loaded{i}")) for i in range(RING)]
        self.rounded_done = [ctx.enter_context(nc.semaphore(f"{n}_half_rounded")) for n in ("first", "second")]
        self.rest_done = [ctx.enter_context(nc.semaphore(f"{n}_half_rest")) for n in ("first", "second")]
        self.block_done = ctx.enter_context(nc.semaphore("block_done"))
        self.stage_done = ctx.enter_context(nc.semaphore("stage_done"))
        self.setup_loaded = ctx.enter_context(nc.semaphore("setup_loaded"))
        self.inputs_loaded = ctx.enter_context(nc.semaphore("inputs_loaded"))
        self.links = {e: ctx.enter_context(nc.semaphore(f"{e}_link")) for e in ("act", "dve", "pool")}
        self.n_blocks = 0
        self.split_blocks = []
        self.n_stages = 0

    def place(self, name, shape, parts=None, kind=F32):
        at = self.next_byte
        self.next_byte += -(-int(np.prod(shape[1:])) // 8) * 32
        out = [self.nc.alloc_sbuf_tensor_at(name, shape, kind, offset=at)]
        if parts:
            out.append(self.nc.alloc_sbuf_tensor_at(parts, shape, F32R, offset=at))
        return out

    def parts_at(self, start, *shape, kind=F32R):
        key = start, shape, kind
        if key not in self.named:
            assert start + int(np.prod(shape)) <= ARENA, (start, shape)
            self.named[key] = self.nc.alloc_sbuf_tensor_at(f"part{len(self.named)}", [P, *shape], kind,
                                                           offset=self.arena_byte + 4 * start)
        return self.named[key][:]

    def at(self, start, *shape):
        size = int(np.prod(shape))
        assert start + size <= ARENA, (start, shape)
        v = self.arena[:, start:start + size]
        names = "abcd"[:len(shape)]
        if len(shape) > 1:
            v = v.rearrange(f"p ({' '.join(names)}) -> p {' '.join(names)}", **dict(zip(names, shape)))
        return v


class Stage:

    blocks = 0
    whole = 0
    before = next = None

    def __init__(self, chip):
        self.chip, self.nc = chip, chip.nc
        self.index = chip.n_stages
        chip.n_stages += 1
        self.b0 = chip.n_blocks
        chip.n_blocks += self.blocks
        self.split = self.blocks - self.whole
        self.s0 = len(chip.split_blocks)
        chip.split_blocks += [self.b0 + j for j in range(self.split)]
        self.led = False

    def arrival(self, j):
        b = self.b0 + j
        return b % RING, 16 * (b // RING + 1)

    def block_count(self, j):
        return self.b0 + j + 1

    def split_count(self, j):
        return self.s0 + j + 1

    def weights(self, j):
        return self.chip.rounded[:, (self.s0 + j) % ROUNDED], self.chip.ring_rest[:, (self.b0 + j) % RING]

    def round(self, act, j):
        c, s = self.chip, self.s0 + j
        if j >= self.split:
            return
        slot, count = self.arrival(j)
        act.wait_ge(c.loaded[slot], count)
        if s >= ROUNDED:
            act.wait_ge(c.block_done, c.split_blocks[s - ROUNDED] + 1)
        for h in range(2):
            half = slice(h * HALF, (h + 1) * HALF)
            self.nc.scalar.activation(c.rounded[:, s % ROUNDED, half], c.ring[:, slot, half], ACT.Copy)\
                .then_inc(c.rounded_done[h], 1)

    def lead(self, act):
        if not self.led:
            self.led = True
            for j in range(ROUNDED):
                self.round(act, j)

    def product(self, out, w, a, start, stop):
        mm = self.nc.tensor.matmul
        mm(out, w[0], a[0], start=start, stop=False)
        mm(out, w[0], a[1], start=False, stop=False)
        return mm(out, w[1], a[0], start=False, stop=stop)

    def input_tile(self, pe, k):
        ready = self.before.input_split
        pe.wait_ge(ready.sem, ready.at((k + 1) * self.before.t // N))

    def leave_rest(self, r, h, count, eng=None):
        c, half = self.chip, slice(h * HALF, (h + 1) * HALF)
        slot = (self.b0 + r) % RING
        eng = eng or self.nc.gpsimd
        eng.wait_ge(c.rounded_done[h], count)
        eng.tensor_tensor(c.ring_rest[:, slot, half], c.ring[:, slot, half],
                                     c.rounded[:, (self.s0 + r) % ROUNDED, half].bitcast(F32), ALU.subtract).then_inc(c.rest_done[h], 1)

    def pe(self, pe):
        pass

    def act(self, act, link):
        pass

    def dve(self, dve, link):
        pass

    def pool(self, pool, link):
        rounds = self.split // RING
        if rounds > 1:
            with pool.Fori(0, rounds) as it:
                for r in range(RING):
                    for h in range(2):
                        self.leave_rest(r, h, self.split_count(it * RING + r))
        else:
            rounds = 0
        for j in range(rounds * RING, self.split):
            for h in range(2):
                self.leave_rest(j, h, self.split_count(j))


A_CST1 = 0
CST1 = {"dft": (0, 256), "cosn": (256, 512), "sinn": (768, 512), "perm": (1280, 128),
        "rope_cos": (1408, 512), "rope_sin": (1920, 512)}
NCST1 = 2432
NEXPO = 4 * 2 * N
A_U = NCST1
A_SQ = A_U + KD * 2 * N
A_WORK = A_SQ + KD * 2 * N
A_SMALL = A_WORK
A_H = A_WORK
A_HR = A_H + KF * 2 * N
A_SILU = A_HR + KF * 2 * N
A_BIAS = A_WORK + 10240


class Start(Stage):

    def __init__(self, chip):
        super().__init__(chip)
        self.row = chip.signals("bias_rows", 16)
        self.copied = chip.signals("bias_copied", 16)
        self.stored = chip.signals("bias_stored", 16)
        self.rows = chip.at(A_BIAS, 16, BIASW)
        self.lhs = chip.at(A_BIAS + 16 * BIASW, 16, P)
        self.hot = chip.at(A_BIAS + 16 * BIASW + 16 * P, BIASW)

    def pe(self, pe):
        pe.wait_ge(self.chip.setup_loaded, 16 * N_SETUP)
        for h in range(16):
            if h >= 8:
                pe.wait_ge(self.copied.sem, self.copied.at(h - 7))
            self.nc.tensor.matmul(self.chip.ps[:, h % 8, 0:BIASW], self.lhs[0:34, h, :], self.hot[0:34, :],
                                  start=True, stop=True).then_inc(self.row.sem, 1)

    def act(self, act, link):
        for h in range(16):
            act.wait_ge(self.row.sem, self.row.at(h + 1))
            self.nc.scalar.activation(self.rows[:, h, :], self.chip.ps[:, h % 8, 0:BIASW], ACT.Copy)\
                .then_inc(self.copied.sem, 1)
        act.wait_ge(self.copied.sem, self.copied.at(16))
        act.dma_start(self.chip.io["bias_scratch"], self.rows).then_inc(self.stored.sem, 16)
        act.sem_inc(self.chip.stage_done, 1)


class Modulation(Stage):

    blocks = BLOCKS["mod"]
    GROUPS = blocks // 2

    def __init__(self, chip, layer, start=None):
        super().__init__(chip)
        self.layer, self.start = layer, start
        self.silu = chip.signals("cond_ready", 1)
        self.cond_rounded = chip.signals("cond_rounded", 1)
        self.cond_split = chip.signals("cond_split", 1)
        self.cond = chip.at(A_WORK, KD, 2)
        self.parts = chip.parts_at(A_WORK + KD * 2, KD, 4)
        self.rows = chip.at(A_WORK + KD * 6, self.GROUPS, 512)
        self.rows_kept = chip.signals("mod_rows_kept", self.GROUPS)
        self.turned = chip.signals("turned", 1)

    def act(self, act, link):
        c, copy = self.chip, self.nc.scalar.activation
        self.lead(act)
        act.wait_ge(c.stage_done, self.index)
        v = columns(c.vec, "cond").rearrange("p (k s) -> p k s", s=2)
        copy(self.cond, v, ACT.Silu).then_inc(self.silu.sem, 1)
        act.wait_ge(self.silu.sem, self.silu.at(1))
        copy(self.parts[:, :, 0:2], self.cond, ACT.Copy).then_inc(self.cond_rounded.sem, 1)
        for g in range(self.GROUPS):
            self.round(act, 2 * g + ROUNDED)
            self.round(act, 2 * g + 1 + ROUNDED)
            act.wait_ge(c.block_done, self.block_count(2 * g + 1))
            copy(self.rows[0:4, g, :], c.ps[0:4, g % 4, :], ACT.Copy).then_inc(self.rows_kept.sem, 1)

    def pe(self, pe):
        c, mm = self.chip, self.nc.tensor.matmul
        pe.wait_ge(c.stage_done, self.index)
        pe.wait_ge(self.cond_split.sem, self.cond_split.at(1))

        def turn(g):
            pe.wait_ge(self.rows_kept.sem, self.rows_kept.at(g + 1))
            for m in range(4):
                at = 4 * (4 * g + m)
                last = self.nc.tensor.transpose(c.ps[:, 7, at:at + 4], self.rows[0:4, g, m * P:(m + 1) * P], c.ident[0:4, 0:4])
            return last

        for g in range(self.GROUPS):
            if g >= 4:
                pe.wait_ge(self.rows_kept.sem, self.rows_kept.at(g - 3))
            for j in (2 * g, 2 * g + 1):
                w = self.weights(j)
                for k in range(4):
                    if k % 2 == 0:
                        pe.wait_ge(c.rest_done[k // 2], self.split_count(j))
                    for i, part in enumerate(w):
                        last = mm(c.ps[0:4, g % 4, :], self.parts[:, 4 * (j % 2) + k, :], part[:, 4 * k:4 * k + 4, :],
                                  start=j % 2 == 0 and k == 0 and i == 0, stop=j % 2 == 1 and k == 3 and i == 1)
                last.then_inc(c.block_done, 1)
            if g:
                turn(g - 1)
        turn(self.GROUPS - 1).then_inc(self.turned.sem, 1)

    def pool(self, pool, link):
        with pool.Fori(0, self.blocks // RING) as it:
            for r in range(RING):
                self.leave_rest(r, 0, self.split_count(it * RING + r))

    def dve(self, dve, link):
        c, nc = self.chip, self.nc
        dve.wait_ge(self.chip.stage_done, self.index)
        dve.wait_ge(self.cond_rounded.sem, self.cond_rounded.at(1))
        nc.vector.tensor_tensor(self.parts[:, :, 2:4], self.cond, self.parts[:, :, 0:2].bitcast(F32), ALU.subtract)\
            .then_inc(self.cond_split.sem, 1)
        with dve.Fori(0, self.blocks // RING) as it:
            for r in range(RING):
                self.leave_rest(r, 1, self.split_count(it * RING + r), nc.vector)
        dve.wait_ge(self.turned.sem, self.turned.at(1))
        m = c.mods[:].rearrange("p j d s -> p (j d) s")
        b = columns(c.vec, "b_mod", self.layer, 72).unsqueeze(2).broadcast_to([P, 72, 2])
        turned = c.ps[:, 7, 0:288].rearrange("p (m s) -> p m s", s=4)
        link(nc.vector.tensor_tensor(m, turned[:, :, 0:2], b, ALU.add))
        link(nc.vector.tensor_tensor(m, m, turned[:, :, 2:4], ALU.add))
        for n in range(3):
            g = columns(c.vec, "norm_g", 3 * self.layer + n, KD).unsqueeze(2).broadcast_to([P, KD, 2])
            scale, gate = c.mods[:, 3 * n + 1, :, :], c.mods[:, 3 * n + 2, :, :]
            link(nc.vector.tensor_scalar(scale, scale, 1.0, None, ALU.add))
            link(nc.vector.tensor_tensor(scale, scale, g, ALU.mult))
            if n != 1:
                link(nc.vector.tensor_scalar(gate, gate, 0.5, None, ALU.mult))
        if self.start:
            dve.wait_ge(c.inputs_loaded, 16 * N_INPUTS)
            dve.wait_ge(self.start.stored.sem, self.start.stored.at(16))
        dve.sem_inc(c.stage_done, 1)


class Norm(Stage):

    def __init__(self, chip, out, sq, small, tokens, mod=None, gain=None, parts=None, keep=False):
        super().__init__(chip)
        self.t, self.mod, self.gain, self.keep = tokens, mod, gain, keep
        self.u, self.sq, self.parts = out, sq, parts
        self.ms, self.rt, self.rstd = small
        self.squared = chip.signals("squared", 4)
        self.summed = chip.signals("squares_summed", 1)
        self.mean = chip.signals("mean_square_ready", 1)
        self.root = chip.signals("root_ready", 1)
        self.tiles = [(d, s) for d in range(KD) for s in range(tokens // N)]
        self.scaled = chip.signals("scaled", len(self.tiles))
        self.rounded = chip.signals("input_rounded", len(self.tiles) if parts else 0)
        self.input_split = chip.signals("input_split", len(self.tiles) if parts else 0)
        self.x_kept = chip.signals("x_in_psum", 1 if keep else 0)

    def act(self, act, link):
        c, nc = self.chip, self.nc
        early = isinstance(self.before, Project)
        if not early:
            act.wait_ge(self.chip.stage_done, self.index)
        for d in range(0, KD, 2):
            if early:
                act.wait_ge(self.before.x_ready.sem, self.before.x_ready.at(d + 2))
            nc.scalar.activation(self.sq[:, d:d + 2, :], c.x[:, d:d + 2, 0:self.t], ACT.Square)\
                .then_inc(self.squared.sem, 1)
        if self.next is not None:
            self.next.lead(act)
        act.wait_ge(self.mean.sem, self.mean.at(1))
        nc.scalar.activation(self.rt, self.ms, ACT.Sqrt).then_inc(self.root.sem, 1)
        if self.keep:
            act.wait_ge(self.x_kept.sem, self.x_kept.at(1))
        if self.parts or self.mod is not None:
            for i, (d, s) in enumerate(self.tiles):
                cols = slice(s * N, (s + 1) * N)
                bias = c.mods[:, 3 * self.mod, d, s:s + 1] if self.mod is not None else 0.0
                act.wait_ge(self.scaled.sem, self.scaled.at(i + 1))
                to = self.parts[0][:, d, cols] if self.parts else self.u[:, d, cols]
                last = nc.scalar.activation(to, self.u[:, d, cols], ACT.Identity, bias=bias)
                if self.parts:
                    last.then_inc(self.rounded.sem, 1)
            if not self.parts:
                last.then_inc(self.chip.stage_done, 1)

    def pe(self, pe):
        c, mm = self.chip, self.nc.tensor.matmul
        for d in range(KD):
            if d % 2 == 0:
                pe.wait_ge(self.squared.sem, self.squared.at(d // 2 + 1))
            last = mm(c.ps[:, 0, 0:self.t], c.ones, self.sq[:, d, :], start=d == 0, stop=d == KD - 1)
        last.then_inc(self.summed.sem, 1)
        if self.keep:
            for b in range(4):
                last = mm(c.ps[:, 4 + b, :].rearrange("p (m n) -> p m n", m=2), c.ident, c.x[:, 2 * b:2 * b + 2, 0:N],
                          start=True, stop=False)
            last.then_inc(self.x_kept.sem, 1)

    def dve(self, dve, link):
        c, nc = self.chip, self.nc
        dve.wait_ge(self.chip.stage_done, self.index)
        dve.wait_ge(self.summed.sem, self.summed.at(1))
        nc.vector.tensor_scalar(self.ms, c.ps[:, 0, 0:self.t], 1.0 / D, EPS, ALU.mult, ALU.add)\
            .then_inc(self.mean.sem, 1)
        dve.wait_ge(self.root.sem, self.root.at(1))
        link(nc.vector.reciprocal(self.rstd, self.rt))

        def rest_of(i):
            d, s = self.tiles[i]
            cols = slice(s * N, (s + 1) * N)
            shift = c.mods[:, 3 * self.mod, d, s:s + 1] if self.mod is not None else 0.0
            dve.wait_ge(self.rounded.sem, self.rounded.at(i + 1))
            nc.vector.scalar_tensor_tensor(self.parts[1][:, d, cols], self.u[:, d, cols], shift,
                                           self.parts[0].bitcast(F32)[:, d, cols], ALU.add, ALU.subtract)\
                .then_inc(self.input_split.sem, 1)

        for i, (d, s) in enumerate(self.tiles):
            cols = slice(s * N, (s + 1) * N)
            gain = self.gain[:, d:d + 1] if self.mod is None else c.mods[:, 3 * self.mod + 1, d, s:s + 1]
            last = nc.vector.scalar_tensor_tensor(self.u[:, d, cols], c.x[:, d, cols], gain, self.rstd[:, cols],
                                                  ALU.mult, ALU.mult)
            last.then_inc(self.scaled.sem, 1)
            if self.parts and i >= 2:
                rest_of(i - 2)
        if self.parts:
            rest_of(len(self.tiles) - 2)
            rest_of(len(self.tiles) - 1)
            dve.wait_ge(self.input_split.sem, self.input_split.at(len(self.tiles)))
            dve.sem_inc(c.stage_done, 1)
        elif self.mod is None:
            dve.wait_ge(self.scaled.sem, self.scaled.at(len(self.tiles)))
            dve.sem_inc(self.chip.stage_done, 1)


def first_input(chip, tokens):
    return tuple(chip.parts_at(a, KD, 2 * N)[:, :, 0:tokens] for a in (A_SQ, A_U))


def first_norm(chip, tokens, mod, split=True):
    small = [chip.at(A_SMALL + i * 2 * N, 2 * N)[:, 0:tokens] for i in range(3)]
    return Norm(chip, chip.at(A_U, KD, 2 * N)[:, :, 0:tokens], chip.at(A_SQ, KD, 2 * N)[:, :, 0:tokens], small,
                tokens, mod=mod, parts=first_input(chip, tokens) if split else None)


class FeedForwardIn(Stage):

    blocks = BLOCKS["ffn_in"]

    def __init__(self, chip, tokens):
        super().__init__(chip)
        self.t = tokens
        self.u = first_input(chip, tokens)
        cut = lambda v: v[:, :, 0:tokens]
        self.silu = cut(chip.at(A_SILU, 2, 2 * N))
        self.h = cut(chip.parts_at(A_H, KF, 2 * N, kind=F32))
        self.parts = cut(chip.parts_at(A_HR, KF, 2 * N)), cut(chip.parts_at(A_H, KF, 2 * N))
        self.silu_ready = chip.signals("silu_ready", KF)
        self.h_ready = chip.signals("hidden_ready", KF)
        self.h_rounded = chip.signals("hidden_rounded", KF)
        self.h_split = chip.signals("hidden_split", KF)

    def pe(self, pe):
        c = self.chip
        for j in range(KF):
            whi, wlo = self.weights(j)
            if j >= 2:
                pe.wait_ge(self.h_ready.sem, self.h_ready.at(j - 1))
            for half in range(2):
                pe.wait_ge(c.rest_done[half], self.split_count(j))
                for k in range(KD):
                    i = half * KD + k
                    if j == 0 and half == 0:
                        self.input_tile(pe, k)
                    last = self.product(c.ps[:, 2 * (j % 2) + half, 0:self.t], (whi[:, i, :], wlo[:, i, :]),
                                        (self.u[0][:, k, :], self.u[1][:, k, :]), k == 0, k == KD - 1)
            last.then_inc(c.block_done, 1)

    def act(self, act, link):
        c, nc = self.chip, self.nc
        self.lead(act)
        act.wait_ge(c.stage_done, self.index)
        for j in range(KF):
            act.wait_ge(c.block_done, self.block_count(j))
            if j >= 2:
                act.wait_ge(self.h_ready.sem, self.h_ready.at(j - 1))
            nc.scalar.activation(self.silu[:, j % 2, :], c.ps[:, 2 * (j % 2), 0:self.t], ACT.Silu)\
                .then_inc(self.silu_ready.sem, 1)
            self.round(act, j + ROUNDED)
            act.wait_ge(self.h_ready.sem, self.h_ready.at(j + 1))
            nc.scalar.activation(self.parts[0][:, j, :], self.h[:, j, :], ACT.Copy).then_inc(self.h_rounded.sem, 1)

    def dve(self, dve, link):
        v = self.nc.vector
        dve.wait_ge(self.chip.stage_done, self.index)
        for j in range(KF):
            dve.wait_ge(self.silu_ready.sem, self.silu_ready.at(j + 1))
            v.tensor_tensor(self.h[:, j, :], self.chip.ps[:, 2 * (j % 2) + 1, 0:self.t], self.silu[:, j % 2, :], ALU.mult)\
                .then_inc(self.h_ready.sem, 1)
            dve.wait_ge(self.h_rounded.sem, self.h_rounded.at(j + 1))
            v.tensor_tensor(self.parts[1][:, j, :], self.h[:, j, :], self.parts[0].bitcast(F32)[:, j, :], ALU.subtract)\
                .then_inc(self.h_split.sem, 1)
        dve.wait_ge(self.h_split.sem, self.h_split.at(KF))
        dve.sem_inc(self.chip.stage_done, 1)


class Project(Stage):

    def __init__(self, chip, inp, tiles, tokens, gate=None, hidden=None):
        self.blocks = tiles // 2
        super().__init__(chip)
        self.inp, self.t, self.gate, self.hidden = inp, tokens, gate, hidden
        self.out_done = chip.signals("project_out_done", KD)
        self.x_ready = chip.signals("project_x_ready", KD)

    def pe(self, pe):
        c = self.chip
        if not self.hidden:
            pe.wait_ge(self.chip.stage_done, self.index)
        for j in range(self.blocks):
            whi, wlo = self.weights(j)
            for k in range(2):
                pe.wait_ge(c.rest_done[k], self.split_count(j))
                if self.hidden:
                    pe.wait_ge(self.hidden.h_split.sem, self.hidden.h_split.at(2 * j + k + 1))
                first, last = j == 0 and k == 0, j == self.blocks - 1 and k == 1
                for m in (*range(4, KD), *range(4)) if first else range(KD):
                    if self.hidden and first and m == 0:
                        pe.wait_ge(self.hidden.h_ready.sem, self.hidden.h_ready.at(KF))
                    i = k * KD + m
                    out = self.product(c.ps[:, m, 0:self.t], (whi[:, i, :], wlo[:, i, :]), self.inp(2 * j + k), first, last)
                    if last:
                        out.then_inc(self.out_done.sem, 1)
            if last:
                pe.wait_ge(self.out_done.sem, self.out_done.at(KD))
                pe.sem_inc(c.block_done, 1)
            else:
                out.then_inc(c.block_done, 1)

    def act(self, act, link):
        self.lead(act)
        for j in range(ROUNDED, self.blocks):
            self.round(act, j)
        self.next.lead(act)

    def dve(self, dve, link):
        c = self.chip
        dve.wait_ge(self.chip.stage_done, self.index)
        for m in range(KD):
            dve.wait_ge(self.out_done.sem, self.out_done.at(m + 1))
            for s in range(self.t // N):
                cols = slice(s * N, (s + 1) * N)
                gate = 1.0 if self.gate is None else c.mods[:, self.gate, m, s:s + 1]
                last = self.nc.vector.scalar_tensor_tensor(c.x[:, m, cols], c.ps[:, m, cols], gate, c.x[:, m, cols],
                                                           ALU.mult, ALU.add)
            last.then_inc(self.x_ready.sem, 1)
        dve.wait_ge(self.x_ready.sem, self.x_ready.at(KD))
        dve.sem_inc(self.chip.stage_done, 1)


def tiles_of(parts):
    return lambda i: [x[:, i, :] for x in parts]


def feed_forward(chip, tokens, mod):
    norm, hidden = first_norm(chip, tokens, mod), FeedForwardIn(chip, tokens)
    return [norm, hidden, Project(chip, tiles_of(hidden.parts), KF, tokens, gate=3 * mod + 2, hidden=hidden)]


class Fourier(Stage):

    def __init__(self, chip):
        super().__init__(chip)
        cst = chip.at(A_CST1, NCST1)
        self.dft = cst[:, 0:256]
        self.cosn = cst[:, 256:768].rearrange("p (t n) -> p t n", t=NT)
        self.sinn = cst[:, 768:1280].rearrange("p (t n) -> p t n", t=NT)
        self.u = chip.at(A_U, KD, 2 * N)
        self.half = chip.at(A_WORK, 4, NT, 2 * P)
        a_f = A_WORK + 4 * NT * 2 * P
        self.parts = tuple(chip.parts_at(a_f + i * KD * 2 * N, KD, 2 * N) for i in range(2))
        n = 2 * KD
        self.by_feature = chip.signals("dft_by_feature", n)
        self.half_ready = chip.signals("dft_half_ready", n)
        self.by_token = chip.signals("dft_by_token", n)
        self.rounded = chip.signals("rounded", n)
        self.kept = chip.signals("dft_kept", n)

    def pe(self, pe):
        pe.wait_ge(self.chip.stage_done, self.index)
        ps, n = self.chip.ps, 2 * KD

        def along_features(i):
            s, g = divmod(i, KD)
            if i >= 4:
                pe.wait_ge(self.half_ready.sem, self.half_ready.at(i - 3))
            for t in range(NT):
                last = self.nc.tensor.matmul(ps[:, i % 4, t * 256:(t + 1) * 256],
                                             self.u[:, g, s * N + t * P:s * N + (t + 1) * P], self.dft,
                                             start=True, stop=True)
            last.then_inc(self.by_feature.sem, 1)

        def along_tokens(i):
            pe.wait_ge(self.half_ready.sem, self.half_ready.at(i + 1))
            if i >= 4:
                pe.wait_ge(self.kept.sem, self.kept.at(i - 3))
            for t in range(NT):
                self.nc.tensor.matmul(ps[:, 4 + i % 4, 0:N], self.half[:, i % 4, t, 0:P], self.cosn[:, t, :],
                                      start=t == 0, stop=False)
                last = self.nc.tensor.matmul(ps[:, 4 + i % 4, 0:N], self.half[:, i % 4, t, P:2 * P], self.sinn[:, t, :],
                                             start=False, stop=t == NT - 1)
            last.then_inc(self.by_token.sem, 1)

        along_features(0)
        for i in range(n):
            if i + 1 < n:
                along_features(i + 1)
            along_tokens(i)

    def act(self, act, link):
        ps, copy = self.chip.ps, self.nc.scalar.activation
        act.wait_ge(self.chip.stage_done, self.index)

        def half(i):
            act.wait_ge(self.by_feature.sem, self.by_feature.at(i + 1))
            if i >= 4:
                act.wait_ge(self.by_token.sem, self.by_token.at(i - 3))
            copy(self.half[:, i % 4].rearrange("p t c -> p (t c)"), ps[:, i % 4, :], ACT.Copy).then_inc(self.half_ready.sem, 1)

        half(0)
        self.next.lead(act)
        for i in range(2 * KD):
            if i + 1 < 2 * KD:
                half(i + 1)
            s, g = divmod(i, KD)
            act.wait_ge(self.by_token.sem, self.by_token.at(i + 1))
            copy(self.parts[0][:, g, s * N:(s + 1) * N], ps[:, 4 + i % 4, 0:N], ACT.Copy).then_inc(self.rounded.sem, 1)

    def dve(self, dve, link):
        dve.wait_ge(self.chip.stage_done, self.index)
        for i in range(2 * KD):
            s, g = divmod(i, KD)
            cols = slice(s * N, (s + 1) * N)
            dve.wait_ge(self.rounded.sem, self.rounded.at(i + 1))
            last = self.nc.vector.tensor_tensor(self.parts[1][:, g, cols], self.chip.ps[:, 4 + i % 4, 0:N],
                                                self.parts[0].bitcast(F32)[:, g, cols], ALU.subtract)
            last.then_inc(self.kept.sem, 1)
        dve.wait_ge(self.kept.sem, self.kept.at(2 * KD))
        dve.sem_inc(self.chip.stage_done, 1)


R_P = A_U
R_O = R_P + 2 * 4 * N
R_K = A_WORK
R_V = R_K + KD * 2 * N
R_G = R_V + 4 * RH * RDV
R_D = R_G + 16 * N
R_TMP = R_D + RH * 4 * N
R_LG = R_TMP + 2 * 512
R_EXPO = R_LG + 32
assert R_O + 16 * N + 6 * N <= R_K


class Retention(Stage):

    blocks = BLOCKS["ret_in"]

    def __init__(self, chip):
        super().__init__(chip)
        at, sig = chip.at, chip.signals
        cst = at(A_CST1, NCST1)
        self.expo_loaded = sig("expo_loaded", 16)
        self.perm = cst[:, 1280:1408]
        self.cos = cst[:, 1408:1920].rearrange("p (a n) -> p a n", a=2)
        self.sin = cst[:, 1920:2432].rearrange("p (a n) -> p a n", a=2)
        self.expo = at(R_EXPO, 4, 2 * N)
        self.u = first_input(chip, 2 * N)
        self.q, self.k = chip.x[:, :, N:], at(R_K, KD, 2 * N)
        self.v = at(R_V, 4, RH * RDV)
        self.g, self.o = at(R_G, 16, N), at(R_O, 16, N)
        self.d = at(R_D, RH, 4 * N)
        self.tmp = at(R_TMP, 2, 512)
        self.lg = at(R_LG, 4, 8)
        self.p = at(R_P, 2, 4 * N)
        self.sq = at(R_EXPO, 2, 4, N)
        self.st = at(R_O + 16 * N, 2, 3, N)
        self.rounded_o = chip.parts_at(R_V, 4, RH, RDV)
        self.rest_o = chip.parts_at(R_O, 16, N)
        self.q_kept = sig("q_kept", 4)
        self.k_kept = sig("ret_k_kept", 4)
        self.turned = sig("turned", 16)
        self.rope_done = sig("ret_rope_done", 16)
        self.v_kept = sig("ret_v_kept", 16)
        self.g_kept = sig("ret_g_kept", 8)
        self.lg_exp = sig("ret_lg_exp", 1)
        self.lg_in = sig("ret_lg_in", 1)
        self.lg_out = sig("ret_lg_out", 1)
        self.d_in = sig("ret_d_in", RH)
        self.d_exp = sig("ret_d_exp", RH)
        self.scores = sig("scored", RH)
        self.weighted = sig("weighted", RH)
        self.o_sum = sig("summed", RH)
        self.o_kept = sig("sum_kept", RH)
        self.mean = sig("ret_mean", RH)
        self.centred = sig("ret_centred", RH)
        self.squares = sig("ret_squares", RH)
        self.var = sig("ret_var", RH)
        self.var_in = sig("ret_var_in", RH)
        self.root = sig("ret_root", RH)
        self.gated = sig("ret_gated", RH)
        self.rounded = sig("rounded", RH)

    def output_tile(self, i):
        return self.rounded_o[:, i % 4, i // 4, 0:N], self.rest_o[:, i, :]

    def pe(self, pe):
        nc, ps = self.nc, self.chip.ps

        def columns_of(j, out, tokens):
            whi, wlo = self.weights(j)
            for e in range(2):
                pe.wait_ge(self.chip.rest_done[e], self.split_count(j))
                for k in range(KD):
                    i = e * KD + k
                    if j == 0 and e == 0:
                        self.input_tile(pe, k)
                    last = self.product(out(e), (whi[:, i, :], wlo[:, i, :]),
                                        (self.u[0][:, k, 0:tokens], self.u[1][:, k, 0:tokens]), k == 0, k == KD - 1)
            last.then_inc(self.chip.block_done, 1)

        for j in range(4):
            columns_of(j, lambda e: ps[:, j, e * N:(e + 1) * N], N)
        for j in range(4):
            if j >= 2:
                pe.wait_ge(self.k_kept.sem, self.k_kept.at(j - 1))
            columns_of(4 + j, lambda e: ps[:, 4 + 2 * (j % 2) + e, :], 2 * N)
        pe.wait_ge(self.q_kept.sem, self.q_kept.at(4))
        pe.wait_ge(self.k_kept.sem, self.k_kept.at(4))
        for h in range(RH):
            if h >= 2:
                pe.wait_ge(self.v_kept.sem, self.v_kept.at(4 * (h - 1)))
            for j in range(2):
                w = self.weights(8 + 2 * h + j)
                for t in range(4):
                    for k in range(4):
                        if t == 0 and k % 2 == 0:
                            pe.wait_ge(self.chip.rest_done[k // 2], self.split_count(8 + 2 * h + j))
                        u = [x[:, 4 * j + k, t * P:(t + 1) * P] for x in self.u]
                        last = self.product(ps[:, 4 * (h % 2) + t, :], u, [x[:, 4 * k:4 * k + 4, :] for x in w],
                                            j == 0 and k == 0, j == 1 and k == 3)
                last.then_inc(self.chip.block_done, 1)
        for j in range(8):
            if j == 0:
                pe.wait_ge(self.v_kept.sem, self.v_kept.at(12))
            if j >= 4:
                pe.wait_ge(self.g_kept.sem, self.g_kept.at(j - 3))
            columns_of(16 + j, lambda e: ps[:, j % 4, e * N:(e + 1) * N], N)
            if j == 0:
                pe.wait_ge(self.v_kept.sem, self.v_kept.at(16))
            for i in (2 * j, 2 * j + 1):
                if i >= 4:
                    pe.wait_ge(self.rope_done.sem, self.rope_done.at(i - 3))
                t = self.q[:, i, :] if i < KD else self.k[:, i - KD, 0:N]
                nc.tensor.matmul(ps[:, 4 + i % 4, 0:N], self.perm, t, start=True, stop=True).then_inc(self.turned.sem, 1)
        pe.wait_ge(self.g_kept.sem, self.g_kept.at(8))
        pe.wait_ge(self.rope_done.sem, self.rope_done.at(16))

        def scores(h):
            if h >= 1:
                pe.wait_ge(self.weighted.sem, self.weighted.at(h))
            for m in range(4):
                for e in range(2):
                    last = nc.tensor.matmul(ps[:, m // 2, (m % 2) * N:(m % 2 + 1) * N],
                                            self.k[:, 2 * h + e, m * P:(m + 1) * P], self.q[:, 2 * h + e, :],
                                            start=e == 0, stop=e == 1)
            last.then_inc(self.scores.sem, 1)

        def outputs(h):
            pe.wait_ge(self.weighted.sem, self.weighted.at(h + 1))
            if h >= 1:
                pe.wait_ge(self.o_kept.sem, self.o_kept.at(h))
            for e in range(4):
                for m in range(4):
                    last = nc.tensor.matmul(ps[:, 2 + e // 2, (e % 2) * N:(e % 2 + 1) * N],
                                            self.v[:, m, h * RDV + e * P:h * RDV + (e + 1) * P],
                                            self.p[:, h % 2, m * N:(m + 1) * N], start=m == 0, stop=m == 3)
            last.then_inc(self.o_sum.sem, 1)

        def mean(h):
            pe.wait_ge(self.o_kept.sem, self.o_kept.at(h + 1))
            if h >= 2:
                pe.wait_ge(self.centred.sem, self.centred.at(h - 1))
            for e in range(4):
                last = nc.tensor.matmul(ps[:, 4 + h % 2, 0:N], self.chip.ones, self.o[:, 4 * h + e, :], start=e == 0, stop=e == 3)
            last.then_inc(self.mean.sem, 1)

        def variance(h):
            pe.wait_ge(self.squares.sem, self.squares.at(h + 1))
            if h >= 2:
                pe.wait_ge(self.var_in.sem, self.var_in.at(h - 1))
            for e in range(4):
                last = nc.tensor.matmul(ps[:, 6 + h % 2, 0:N], self.chip.ones, self.sq[:, h % 2, e, :], start=e == 0, stop=e == 3)
            last.then_inc(self.var.sem, 1)

        scores(0)
        for h in range(RH):
            outputs(h)
            if h + 1 < RH:
                scores(h + 1)
            if h >= 1:
                variance(h - 1)
            mean(h)
        variance(RH - 1)

    def act(self, act, link):
        nc, ps = self.nc, self.chip.ps
        self.lead(act)
        act.wait_ge(self.chip.stage_done, self.index)
        act.dma_start(self.expo.rearrange("p e n -> p (e n)"), self.chip.io["expo"]).then_inc(self.expo_loaded.sem, 16)
        for j in range(4):
            self.round(act, j + ROUNDED)
            act.wait_ge(self.chip.block_done, self.block_count(j))
            nc.scalar.activation(self.q[:, 2 * j:2 * j + 2, :], ps[:, j, :].rearrange("p (a n) -> p a n", a=2), ACT.Copy)\
                .then_inc(self.q_kept.sem, 1)
        for j in range(4):
            self.round(act, 4 + j + ROUNDED)
            act.wait_ge(self.chip.block_done, self.block_count(4 + j))
            b = 4 + 2 * (j % 2)
            nc.scalar.activation(self.k[:, 2 * j:2 * j + 2, :], ps[:, b:b + 2, :], ACT.Copy, scale=RDK ** -0.5)\
                .then_inc(self.k_kept.sem, 1)
        act.wait_ge(self.lg_in.sem, self.lg_in.at(1))
        nc.scalar.activation(self.lg[:, 1, :], self.lg[:, 0, :], ACT.Exp, scale=-1.0).then_inc(self.lg_exp.sem, 1)
        act.wait_ge(self.lg_out.sem, self.lg_out.at(1))
        act.wait_ge(self.expo_loaded.sem, self.expo_loaded.at(16))
        for h in range(RH):
            act.wait_ge(self.d_in.sem, self.d_in.at(h + 1))
            nc.scalar.activation(self.d[:, h, 0:512], self.d[:, h, 0:512], ACT.Exp)
            nc.scalar.activation(self.d[:, h, 512:1024], self.expo[:, 2, :], ACT.Exp, scale=self.lg[:, 3, h:h + 1])
            nc.scalar.activation(self.tmp[:, h % 2, :], self.expo[:, 3, :], ACT.Exp, scale=self.lg[:, 3, 4 + h:5 + h])\
                .then_inc(self.d_exp.sem, 1)
        for h in range(RH):
            self.round(act, 8 + 2 * h + ROUNDED)
            self.round(act, 8 + 2 * h + 1 + ROUNDED)
            act.wait_ge(self.chip.block_done, self.block_count(8 + 2 * h + 1))
            for t in range(4):
                nc.scalar.activation(self.v[:, t, h * RDV:(h + 1) * RDV], ps[:, 4 * (h % 2) + t, :], ACT.Copy)\
                    .then_inc(self.v_kept.sem, 1)
        for j in range(8):
            self.round(act, 16 + j + ROUNDED)
            act.wait_ge(self.chip.block_done, self.block_count(16 + j))
            nc.scalar.activation(self.g[:, 2 * j:2 * j + 2, :].rearrange("p a n -> p (a n)"), ps[:, j % 4, :], ACT.Silu)\
                .then_inc(self.g_kept.sem, 1)
        self.next.lead(act)

        def keep(h):
            act.wait_ge(self.o_sum.sem, self.o_sum.at(h + 1))
            nc.scalar.activation(self.o[:, 4 * h:4 * h + 4, :].rearrange("p (b e) n -> p b (e n)", b=2), ps[:, 2:4, :], ACT.Copy)\
                .then_inc(self.o_kept.sem, 1)

        def square(h):
            act.wait_ge(self.centred.sem, self.centred.at(h + 1))
            if h >= 2:
                act.wait_ge(self.var.sem, self.var.at(h - 1))
            nc.scalar.activation(self.sq[:, h % 2], self.o[:, 4 * h:4 * h + 4, :], ACT.Square).then_inc(self.squares.sem, 1)

        def root(h):
            act.wait_ge(self.var_in.sem, self.var_in.at(h + 1))
            nc.scalar.activation(self.st[:, h % 2, 1, :], self.st[:, h % 2, 0, :], ACT.Sqrt).then_inc(self.root.sem, 1)

        def round_output(h):
            act.wait_ge(self.gated.sem, self.gated.at(h + 1))
            nc.scalar.activation(self.rounded_o[:, :, h, 0:N], self.o[:, 4 * h:4 * h + 4, :], ACT.Copy).then_inc(self.rounded.sem, 1)

        for h in range(RH + 2):
            if h < RH:
                keep(h)
            if h >= 2:
                root(h - 2)
            if 1 <= h <= RH:
                square(h - 1)
            if h >= 2:
                round_output(h - 2)

    def dve(self, dve, link):
        nc, ps = self.nc, self.chip.ps
        dve.wait_ge(self.chip.stage_done, self.index)
        lg, v = self.lg, nc.vector
        dec = columns(self.chip.vec, "decay")
        link(v.tensor_scalar(lg[:, 0, :], dec, -1.0, None, ALU.mult))
        v.tensor_tensor(lg[:, 0, :], lg[:, 0, :], dec, ALU.max).then_inc(self.lg_in.sem, 1)
        dve.wait_ge(self.lg_exp.sem, self.lg_exp.at(1))
        link(v.tensor_scalar(lg[:, 0, :], lg[:, 1, :], 2.0, None, ALU.add))
        link(v.reciprocal(lg[:, 0, :], lg[:, 0, :]))
        link(v.tensor_tensor(lg[:, 0, :], lg[:, 0, :], lg[:, 1, :], ALU.mult))
        link(v.tensor_tensor(lg[:, 1, :], lg[:, 0, :], lg[:, 0, :], ALU.mult))
        link(v.tensor_scalar(lg[:, 2, :], lg[:, 1, :], 1.0 / 17, None, ALU.mult))
        for n in range(15, 1, -2):
            link(v.scalar_tensor_tensor(lg[:, 2, :], lg[:, 2, :], 1.0 / n, lg[:, 1, :], ALU.add, ALU.mult))
        link(v.scalar_tensor_tensor(lg[:, 2, :], lg[:, 2, :], 1.0, lg[:, 0, :], ALU.add, ALU.mult))
        link(v.tensor_scalar(lg[:, 3, :], dec, 0.0, None, ALU.min))
        v.scalar_tensor_tensor(lg[:, 3, :], lg[:, 2, :], -2.0, lg[:, 3, :], ALU.mult, ALU.add).then_inc(self.lg_out.sem, 1)
        dve.wait_ge(self.lg_out.sem, self.lg_out.at(1))
        dve.wait_ge(self.expo_loaded.sem, self.expo_loaded.at(16))
        for h in range(RH):
            link(v.tensor_scalar(self.d[:, h, 0:512], self.expo[:, 0, :], lg[:, 3, h:h + 1], None, ALU.mult))
            if h >= 2:
                link(v.tensor_tensor(self.d[:, h - 2, 512:1024], self.d[:, h - 2, 512:1024], self.tmp[:, h % 2, :], ALU.add))
            v.scalar_tensor_tensor(self.d[:, h, 0:512], self.expo[:, 1, :], lg[:, 3, 4 + h:5 + h], self.d[:, h, 0:512],
                                   ALU.mult, ALU.add).then_inc(self.d_in.sem, 1)
            if h >= 1:
                dve.wait_ge(self.d_exp.sem, self.d_exp.at(h))
        dve.wait_ge(self.d_exp.sem, self.d_exp.at(RH))
        for h in range(2, RH):
            link(v.tensor_tensor(self.d[:, h, 512:1024], self.d[:, h, 512:1024], self.tmp[:, h % 2, :], ALU.add))
        dve.wait_ge(self.q_kept.sem, self.q_kept.at(4))
        dve.wait_ge(self.k_kept.sem, self.k_kept.at(4))
        turned_part = self.chip.at(R_TMP, 2, N)
        for i in range(16):
            t = self.q[:, i, :] if i < KD else self.k[:, i - KD, 0:N]
            dve.wait_ge(self.turned.sem, self.turned.at(i + 1))
            link(v.tensor_tensor(turned_part[:, i % 2, :], ps[:, 4 + i % 4, 0:N], self.sin[:, i % 2, :], ALU.mult))
            link(v.tensor_tensor(t, t, self.cos[:, i % 2, :], ALU.mult))
            v.tensor_tensor(t, t, turned_part[:, i % 2, :], ALU.add).then_inc(self.rope_done.sem, 1)
        dve.wait_ge(self.g_kept.sem, self.g_kept.at(8))

        def weigh(h):
            dve.wait_ge(self.scores.sem, self.scores.at(h + 1))
            if h >= 2:
                dve.wait_ge(self.o_sum.sem, self.o_sum.at(h - 1))
            v.tensor_tensor(self.p[:, h % 2, :], ps[:, 0:2, :].rearrange("p b n -> p (b n)"), self.d[:, h, :], ALU.mult)\
                .then_inc(self.weighted.sem, 1)

        every = [P, 4, N]
        ms, root, rstd, mean = ([self.st[:, b, i, :] for b in range(2)] for i in (0, 1, 1, 2))
        output = lambda h: self.o[:, 4 * h:4 * h + 4, :]

        def centre(h):
            dve.wait_ge(self.mean.sem, self.mean.at(h + 1))
            link(v.tensor_scalar(mean[h % 2], ps[:, 4 + h % 2, 0:N], 1.0 / RDV, None, ALU.mult))
            v.tensor_tensor(output(h), output(h), mean[h % 2].unsqueeze(1).broadcast_to(every), ALU.subtract)\
                .then_inc(self.centred.sem, 1)

        def spread(h):
            dve.wait_ge(self.var.sem, self.var.at(h + 1))
            v.tensor_scalar(ms[h % 2], ps[:, 6 + h % 2, 0:N], 1.0 / RDV, EPS, ALU.mult, ALU.add).then_inc(self.var_in.sem, 1)

        def scale(h):
            dve.wait_ge(self.root.sem, self.root.at(h + 1))
            link(v.reciprocal(rstd[h % 2], root[h % 2]))
            link(v.tensor_tensor(output(h), output(h), rstd[h % 2].unsqueeze(1).broadcast_to(every), ALU.mult))
            v.tensor_tensor(output(h), output(h), self.g[:, 4 * h:4 * h + 4, :], ALU.mult).then_inc(self.gated.sem, 1)

        def rest_of(h):
            dve.wait_ge(self.rounded.sem, self.rounded.at(h + 1))
            return v.tensor_tensor(self.rest_o[:, 4 * h:4 * h + 4, :], output(h), self.rounded_o.bitcast(F32)[:, :, h, 0:N], ALU.subtract)

        weigh(0)
        for h in range(1, RH + 2):
            if h < RH:
                weigh(h)
            if h >= 2:
                spread(h - 2)
            if h <= RH:
                centre(h - 1)
            if h >= 2:
                scale(h - 2)
            if h >= 3:
                rest_of(h - 3)
        rest_of(RH - 1).then_inc(self.chip.stage_done, 1)


B_P = 0
B_U = 56 * N
B_SQ = B_U + KD * N
B_SMALL = B_SQ + KD * N
B_OB = 19200
B_OC = B_OB + 4 * N
B_OA = B_OC + 4 * N
B_CST2 = B_OA + 4 * N
NCST2 = 2 * P + 5 * P + 2 * 16
B_BIAS = 23328
assert B_CST2 + NCST2 <= B_BIAS
B_WORK = B_BIAS + 16 * N

T_R, T_K, T_V, T_WA, T_G = 0, 4, 8, 12, 13
T_NQ, T_KV, T_KS, T_KW = 14, 18, 20, 21
T_SQ, T_SK = 22, 26
T_VS, T_VW, T_GATE, T_SV = 28, 29, 30, 31
T_GATES = 32
TOKEN_BLOCKS = (14, 15)


class LoadTables(Stage):

    def __init__(self, chip):
        super().__init__(chip)
        self.n = chip.signals("tables_loaded", 32)

    def act(self, act, link):
        c = self.chip
        act.wait_ge(self.chip.stage_done, self.index)
        act.dma_start(c.at(B_CST2, NCST2), c.io["cst2"]).then_inc(self.n.sem, 16)
        s = c.io["bias_scratch"]
        skewed = bass.AP(s.tensor, s.offset + P - 1, [[16 * BIASW - 1, P], [BIASW, 16], [1, N]])
        act.dma_start(c.at(B_BIAS, 16, N), skewed).then_inc(self.n.sem, 16)
        act.sem_inc(self.chip.stage_done, 1)


def second_input(chip):
    return chip.parts_at(B_SQ, KD, N), chip.parts_at(B_U, KD, N)


class ProjectIn(Stage):

    blocks = BLOCKS["in2"]
    BANKS = 6
    SQUARES, NORMS, ROOTS = 10, 12, 14

    def __init__(self, chip):
        super().__init__(chip)
        self.u = second_input(chip)
        self.p = chip.at(B_P, 56, N)
        self.kept = chip.signals("projection_kept", self.blocks)

    def pe(self, pe):
        c, ps = self.chip, self.chip.ps
        for j in range(self.blocks):
            whi, wlo = self.weights(j)
            if j == self.NORMS:
                self.next.next.norms_pe(pe)
            if j >= self.BANKS:
                pe.wait_ge(self.kept.sem, self.kept.at(j - self.BANKS + 1))
            pe.wait_ge(c.rest_done[0], self.split_count(j))
            if j in TOKEN_BLOCKS:
                pe.wait_ge(c.rest_done[1], self.split_count(j))
                for t in range(NT):
                    out = ps[:, j % self.BANKS, :].rearrange("p (e t c) -> p e t c", e=2, t=NT)[:, :, t, :]
                    for k in range(KD):
                        last = self.product(out, [u[:, k, t * P:(t + 1) * P] for u in self.u],
                                            [w[:, k:TPB:KD, :] for w in (whi, wlo)], k == 0, k == KD - 1)
            else:
                for e in range(2):
                    if e:
                        pe.wait_ge(c.rest_done[1], self.split_count(j))
                    for k in range(KD):
                        i = e * KD + k
                        if j == 0 and e == 0:
                            self.input_tile(pe, k)
                        last = self.product(ps[:, j % self.BANKS, e * N:(e + 1) * N], (whi[:, i, :], wlo[:, i, :]),
                                            [u[:, k, :] for u in self.u], k == 0, k == KD - 1)
            last.then_inc(c.block_done, 1)

    def act(self, act, link):
        nc, ps = self.nc, self.chip.ps
        self.lead(act)
        act.wait_ge(self.chip.stage_done, self.index)
        for j in range(self.blocks):
            self.round(act, j + ROUNDED)
            act.wait_ge(self.chip.block_done, self.block_count(j))
            to = self.p[:, 2 * j:2 * j + 2, :].rearrange("p a n -> p (a n)")
            if 2 * j == T_GATE:
                nc.scalar.activation(to[:, N:], ps[:, j % self.BANKS, N:], ACT.Copy)
                last = nc.scalar.activation(to[:, :N], ps[:, j % self.BANKS, :N], ACT.Sigmoid)
            else:
                last = nc.scalar.activation(to, ps[:, j % self.BANKS, :], ACT.Sigmoid if 2 * j >= T_GATES else ACT.Copy)
            last.then_inc(self.kept.sem, 1)
            if j == self.SQUARES:
                self.next.next.square_act(act)
            if j == self.ROOTS:
                self.next.next.root_act(act)
        act.wait_ge(self.kept.sem, self.kept.at(self.blocks))
        act.sem_inc(self.chip.stage_done, 1)

    def dve(self, dve, link):
        dve.wait_ge(self.kept.sem, self.kept.at(T_NQ // 2))
        self.next.next.token_shift(dve, link)
        self.next.next.norms_dve(dve, link)
        dve.wait_ge(self.kept.sem, self.kept.at(T_KV // 2 + 1))
        self.next.gather_blocks(dve)


class Attention(Stage):

    blocks = BLOCKS["rwkv"] + BLOCKS["cmp1"] + BLOCKS["cmp2"]
    whole = blocks
    FIRST = BLOCKS["rwkv"]
    CMP, SEL, WIN, SWA = range(4)
    BUFS = 4
    LEAD = 3
    units = [(t, g, b) for t in range(NT) for g in range(2) for b in range(4)]

    def __init__(self, chip, layer, tables):
        super().__init__(chip)
        at, sig = chip.at, chip.signals
        self.layer, self.tables = layer, tables
        self.p = at(B_P, 56, N)
        self.o = {self.WIN: at(B_OB, 4, N), self.SWA: at(B_OC, 4, N)}
        self.bias = at(B_BIAS, 16, N)
        self.cmask = at(B_CST2 + 7 * P, 2, 16)
        self.r = at(W_R, CMP_LEN, 2, 2, NCMP)
        n = B_U
        self.hid_rows = at(n, 2 * P)
        n += 2 * P
        self.hid = at(n, 4, 2 * NCMP)
        n += 4 * 2 * NCMP
        self.kcm, self.vcm = at(n, 16), at(n + 16, P)
        n += 16 + P
        assert n + self.BUFS * 8 * 4 <= W_PEND
        self.stat = at(n, self.BUFS, 8, 4)
        self.sc = at(B_WORK, self.BUFS, 4, N)
        n = B_WORK + self.BUFS * 4 * N
        self.pt = at(n, 5, 4, P)
        self.pts = at(n + 20 * P, 2, 4, P)
        u = len(self.units)
        self.blocks_ready = sig("cmp_blocks_ready", 1)
        self.hidden = sig("cmp_hidden", 1)
        self.hidden_turned = sig("cmp_hidden_turned", 1)
        self.hidden_kept = sig("cmp_hidden_kept", 1)
        self.compressed = sig("cmp_done", 1)
        self.cmp_kept = sig("cmp_kept", 1)
        self.scored = sig("scored", u)
        self.biased = sig("attn_biased", u)
        self.shifted = sig("shifted", u)
        self.exped = sig("exped", u)
        self.scale_ready = sig("attn_scale_ready", u)
        self.weighted = sig("weighted", u)
        self.turned = sig("turned", u)
        self.turned_kept = sig("attn_turned_kept", u)
        self.summed = sig("summed", u // 2)
        self.sum_kept = sig("sum_kept", u // 2)

    def width(self, t, b):
        return NCMP if b == self.CMP else (t + 1) * P

    def key_tiles(self, t, b):
        return 1 if b == self.CMP else t + 1

    def pe(self, pe):
        nc, ps, p = self.nc, self.chip.ps, self.p
        pe.wait_ge(self.chip.stage_done, self.index)
        rwkv = self.next
        slot, count = self.arrival(0)
        pe.wait_ge(self.chip.loaded[slot], count)
        rwkv.prepare_pe(pe, self.chip.ring[:, slot])
        pe.wait_ge(rwkv.s["sig_w"].sem, rwkv.s["sig_w"].at(1))
        pe.wait_ge(self.blocks_ready.sem, self.blocks_ready.at(1))
        for j in range(BLOCKS["cmp1"]):
            slot, count = self.arrival(self.FIRST + j)
            pe.wait_ge(self.chip.loaded[slot], count)
            w = self.chip.ring[:, slot]
            for i in range(HALF):
                l = j * HALF + i
                last = nc.tensor.matmul(ps[0:4 * NCMP, 0, 0:2 * P], self.r[:, l].rearrange("p a g n -> p (a g n)"),
                                        w[:, 2 * i:2 * i + 2, :], start=l == 0, stop=l == CMP_LEN - 1)
            last.then_inc(self.chip.block_done, 1)
        pe.wait_ge(self.hidden.sem, self.hidden.at(1))
        for f in range(2):
            last = nc.tensor.transpose(ps[:, 1, f * 4 * NCMP:(f + 1) * 4 * NCMP], self.hid_rows[0:4 * NCMP, f * P:(f + 1) * P],
                                       self.chip.ident[0:4 * NCMP, 0:4 * NCMP])
        last.then_inc(self.hidden_turned.sem, 1)
        pe.wait_ge(self.hidden_kept.sem, self.hidden_kept.at(1))
        pe.wait_ge(rwkv.s["sig_a"].sem, rwkv.s["sig_a"].at(1))
        slot, count = self.arrival(self.blocks - 1)
        pe.wait_ge(self.chip.loaded[slot], count)
        w = self.chip.ring[:, slot]
        for f in range(2):
            nc.tensor.matmul(ps[:, 4, 0:2 * NCMP], w[:, f, :], self.hid[:, 2 * f, :], start=f == 0, stop=f == 1)
        for g in range(2):
            for f in range(2):
                last = nc.tensor.matmul(ps[0:NCMP, 5, g * DH:(g + 1) * DH], self.hid[:, 2 * f + 1, g * NCMP:(g + 1) * NCMP],
                                        w[:, 2 + f, 0:DH], start=f == 0, stop=f == 1)
        last.then_inc(self.chip.block_done, 1)
        pe.wait_ge(self.cmp_kept.sem, self.cmp_kept.at(1))

        def scores(u):
            t, g, b = self.units[u]
            if u >= 2:
                pe.wait_ge(self.biased.sem, self.biased.at(u - 1))
            half = slice(g * DH, (g + 1) * DH)
            keys = {self.CMP: self.kcm[half, 0:NCMP], self.SEL: p[half, T_KS], self.WIN: p[half, T_KW],
                    self.SWA: p[half, T_SK]}[b]
            w = self.width(t, b)
            for i in range(4):
                q = p[half, (T_SQ if b == self.SWA else T_NQ) + i, t * P:(t + 1) * P]
                last = nc.tensor.matmul(ps[:, 2 * (u % 2) + i // 2, (i % 2) * N:(i % 2) * N + w], q, keys[:, 0:w],
                                        start=True, stop=True)
            last.then_inc(self.scored.sem, 1)

        def turn(u):
            t, g, b = self.units[u]
            pe.wait_ge(self.weighted.sem, self.weighted.at(u + 1))
            if u >= 1:
                pe.wait_ge(self.turned_kept.sem, self.turned_kept.at(u))
            w = min(self.width(t, b), P)
            for j in range(self.key_tiles(t, b)):
                for i in range(4):
                    last = nc.tensor.transpose(ps[0:w, 4 + j, i * P:(i + 1) * P], self.sc[:, u % self.BUFS, i, j * P:j * P + w],
                                               self.chip.ident)
            last.then_inc(self.turned.sem, 1)

        def values(u):
            t, g, b = self.units[u]
            if b not in self.o:
                return
            n = 2 * (u // 4) + (b == self.SWA)
            pe.wait_ge(self.turned_kept.sem, self.turned_kept.at(u + 1))
            if n >= 2:
                pe.wait_ge(self.sum_kept.sem, self.sum_kept.at(n - 1))
            for i in range(4):
                if b == self.SWA:
                    parts = [(p[:, T_SV, j * P:(j + 1) * P], self.pts[:, j, i, :]) for j in range(t + 1)]
                else:
                    parts = [(self.vcm[0:NCMP, :], self.pt[0:NCMP, 0, i, :])]
                    parts += [(p[:, T_VS, j * P:(j + 1) * P], self.pt[:, 1 + j, i, :]) for j in range(t + 1)]
                    parts += [(p[:, T_VW, j * P:(j + 1) * P], self.pt[:, 3 + j, i, :]) for j in range(t + 1)]
                for k, (v, weights) in enumerate(parts):
                    last = nc.tensor.matmul(ps[:, 6 + n % 2, i * P:(i + 1) * P], v, weights, start=k == 0, stop=k == len(parts) - 1)
            last.then_inc(self.summed.sem, 1)

        for u in range(self.LEAD):
            scores(u)
        for u in range(len(self.units)):
            if u + self.LEAD < len(self.units):
                scores(u + self.LEAD)
            turn(u)
            if u:
                values(u - 1)
        values(len(self.units) - 1)

    def act(self, act, link):
        nc, ps = self.nc, self.chip.ps
        act.wait_ge(self.chip.stage_done, self.index)
        self.next.prepare_act(act, self.block_count(0))
        act.wait_ge(self.chip.block_done, self.block_count(self.blocks - 2))
        nc.scalar.activation(self.hid_rows[0:4 * NCMP, :], ps[0:4 * NCMP, 0, 0:2 * P], ACT.Gelu).then_inc(self.hidden.sem, 1)
        act.wait_ge(self.hidden_turned.sem, self.hidden_turned.at(1))
        nc.scalar.activation(self.hid.rearrange("p a n -> p (a n)"), ps[:, 1, 0:8 * NCMP], ACT.Copy).then_inc(self.hidden_kept.sem, 1)

        def exp(u):
            t, g, b = self.units[u]
            act.wait_ge(self.shifted.sem, self.shifted.at(u + 1))
            if b == self.SWA:
                nc.scalar.activation(self.stat[:, u % self.BUFS, 2, :], self.stat[:, u % self.BUFS, 2, :], ACT.Exp)
            e = self.sc[:, u % self.BUFS, :, 0:self.width(t, b)]
            nc.scalar.activation(e, e, ACT.Exp).then_inc(self.exped.sem, 1)

        def keep(u):
            t, g, b = self.units[u]
            w, k = min(self.width(t, b), P), self.key_tiles(t, b)
            to = self.pts[:, 0:k] if b == self.SWA else self.pt[0:w, (0, 1, 3)[b]:(0, 1, 3)[b] + k]
            act.wait_ge(self.turned.sem, self.turned.at(u + 1))
            nc.scalar.activation(to.rearrange("p j i t -> p j (i t)"), ps[0:w, 4:4 + k, :], ACT.Copy)\
                .then_inc(self.turned_kept.sem, 1)

        def keep_sum(u):
            t, g, b = self.units[u]
            if b in self.o:
                n = 2 * (u // 4) + (b == self.SWA)
                half = slice(g * DH, (g + 1) * DH)
                act.wait_ge(self.summed.sem, self.summed.at(n + 1))
                nc.scalar.activation(self.o[b][half, :, t * P:(t + 1) * P],
                                     ps[half, 6 + n % 2, :].rearrange("p (i t) -> p i t", i=4), ACT.Copy)\
                    .then_inc(self.sum_kept.sem, 1)

        exp(0)
        exp(1)
        for u in range(len(self.units)):
            if u + 2 < len(self.units):
                exp(u + 2)
            keep(u)
            if u:
                keep_sum(u - 1)
        keep_sum(len(self.units) - 1)
        act.wait_ge(self.sum_kept.sem, self.sum_kept.at(len(self.units) // 2))
        act.sem_inc(self.chip.stage_done, 1)

    def gather_blocks(self, dve):
        v, p = self.nc.vector, self.p
        pe_cols = columns(self.chip.vec, "pe", self.layer, CMP_LEN)
        v.memset(self.r[0:DH, :, 1], 0.0)
        v.memset(self.r[DH:P, :, 0], 0.0)
        for g in range(2):
            for a in range(2):
                half = slice(a * DH, (a + 1) * DH)
                x = p[half, T_KV + g, :]
                blocks = bass.AP(x.tensor, x.offset, [x.ap[0], (1, CMP_LEN), (CMP_STRIDE, NCMP)])
                last = v.tensor_tensor(self.r[half, :, a, g, :], blocks,
                                       pe_cols[half].unsqueeze(2).broadcast_to([DH, CMP_LEN, NCMP]), ALU.add)
        last.then_inc(self.blocks_ready.sem, 1)

    def dve(self, dve, link):
        nc, ps, p = self.nc, self.chip.ps, self.p
        v = nc.vector
        dve.wait_ge(self.chip.stage_done, self.index)
        self.next.prepare_dve(dve, link)
        dve.wait_ge(self.chip.block_done, self.block_count(self.blocks - 1))
        for g in range(2):
            half = slice(g * DH, (g + 1) * DH)
            v.tensor_copy(self.kcm[half, 0:NCMP], ps[half, 4, g * NCMP:(g + 1) * NCMP])
        v.tensor_copy(self.vcm[0:NCMP, :], ps[0:NCMP, 5, 0:P]).then_inc(self.cmp_kept.sem, 1)
        dve.wait_ge(self.tables.n.sem, self.tables.n.at(32))

        def shift(u):
            t, g, b = self.units[u]
            w = self.width(t, b)
            sc, st = self.sc[:, u % self.BUFS, :, 0:w], self.stat[:, u % self.BUFS]
            scores = ps[:, 2 * (u % 2):2 * (u % 2) + 2, :].rearrange("p b (h n) -> p (b h) n", n=N)[:, :, 0:w]
            if b == self.CMP:
                bias = self.cmask[:, t, 0:NCMP].unsqueeze(1).broadcast_to([P, 4, NCMP])
            else:
                h = (8 if b == self.SWA else 0) + 4 * g
                bias = self.bias[:, h:h + 4, N - w:N]
            dve.wait_ge(self.scored.sem, self.scored.at(u + 1))
            if u >= self.BUFS:
                dve.wait_ge(self.turned.sem, self.turned.at(u - self.BUFS + 1))
            v.scalar_tensor_tensor(sc, scores, DH ** -0.5, bias, ALU.mult, ALU.add).then_inc(self.biased.sem, 1)
            dve.wait_ge(self.biased.sem, self.biased.at(u + 1))
            link(v.tensor_reduce(st[:, 0, :], sc, AX.X, ALU.max))
            if b == self.CMP:
                link(v.tensor_scalar(st[:, 0, :], st[:, 0, :], NEG / 10, None, ALU.max))
            if b == self.SWA:
                sink = columns(self.chip.vec, "sinks", self.layer, 8)[:, 4 * g:4 * g + 4]
                link(v.tensor_tensor(st[:, 0, :], st[:, 0, :], sink, ALU.max))
                link(v.tensor_tensor(st[:, 2, :], sink, st[:, 0, :], ALU.subtract))
            v.tensor_tensor(sc, sc, st[:, 0, :].unsqueeze(2).broadcast_to([P, 4, w]), ALU.subtract)\
                .then_inc(self.shifted.sem, 1)

        def weigh(u):
            t, g, b = self.units[u]
            w = self.width(t, b)
            sc, st = self.sc[:, u % self.BUFS, :, 0:w], self.stat[:, u % self.BUFS]
            dve.wait_ge(self.exped.sem, self.exped.at(u + 1))
            link(v.tensor_reduce(st[:, 1, :], sc, AX.X, ALU.add))
            if b == self.SWA:
                link(v.tensor_tensor(st[:, 1, :], st[:, 1, :], st[:, 2, :], ALU.add))
            else:
                link(v.tensor_scalar(st[:, 1, :], st[:, 1, :], 1e-30, None, ALU.max))
            last = v.reciprocal(st[:, 1, :], st[:, 1, :])
            if b != self.SWA:
                link(last)
                a = t * P + 12 * g
                gate = p[:, T_GATE, a:a + 12].rearrange("p (h c) -> p h c", c=3)[:, :, b]
                last = v.tensor_tensor(st[:, 1, :], st[:, 1, :], gate, ALU.mult)
            last.then_inc(self.scale_ready.sem, 1)

        shift(0)
        shift(1)
        for u in range(len(self.units)):
            weigh(u)
            if u + 2 < len(self.units):
                shift(u + 2)

    def pool(self, pool, link):
        pool.wait_ge(self.chip.stage_done, self.index)
        self.next.prepare_pool(pool, link)
        for u, (t, g, b) in enumerate(self.units):
            sc = self.sc[:, u % self.BUFS, :, 0:self.width(t, b)]
            pool.wait_ge(self.scale_ready.sem, self.scale_ready.at(u + 1))
            self.nc.gpsimd.tensor_tensor(sc, sc, self.stat[:, u % self.BUFS, 1, :].unsqueeze(2).broadcast_to([P, 4, self.width(t, b)]),
                                         ALU.mult).then_inc(self.weighted.sem, 1)


W_PEND = B_U + 648
W_A = B_U + 3 * N
W_KH, W_GATE, W_B = W_A + 4 * N, W_A + 8 * N, W_A + 12 * N
assert W_B + 4 * N <= B_OB
W_C = B_WORK
W_E = W_C + 8 * N
W_TMP = W_E + 8 * N
W_R = W_TMP + 8 * N
W_Y, W_ST, W_GN = 14 * N, 18 * N, 20 * N
W_TOK = B_BIAS
W_LB = W_TOK + 8 * N
W_LK = W_LB + 8 * N
W_MIX = W_LK + 8 * N
W_W2 = W_MIX + 16 * N
W_SA, W_W1 = W_W2 + 2 * N, W_W2 + 4 * N


class Rwkv(Stage):

    LEVELS = 5

    def __init__(self, chip, layer):
        super().__init__(chip)
        at, sig = chip.at, chip.signals
        self.layer = layer
        self.z = at(B_P, 56, N)
        self.A, self.b, self.kh = at(W_A, 4, N), at(W_B, 4, N), at(W_KH, 4, N)
        self.R, self.k = self.z[:, T_R:T_R + 4, :], self.z[:, T_K:T_K + 4, :]
        self.gate, self.pend = at(W_GATE, 4, N), at(W_PEND, 4, NCH)
        self.kk, self.a = chip.x[:, 0:4, N:], chip.x[:, 4:8, N:]
        self.bh = self.a
        self.c = [at(W_C, 4, N), at(W_C + 4 * N, 4, N)]
        self.e = [at(W_E, 4, N), at(W_E + 4 * N, 4, N), self.c[0]]
        self.norm, self.t3 = at(W_TMP, 4, N), at(W_TMP + 4 * N, 4, N)
        self.y, self.state = at(W_Y, 4, N), at(W_ST, 4, P)
        self.w1 = at(W_W1, 4, P)
        self.tok = at(W_TOK, 4, 4, P)
        self.lb, self.lk = at(W_LB, HEADS, 2, P), at(W_LK, HEADS, 2, P)
        self.mat = [at(W_MIX + i * 4 * N, HEADS, P) for i in range(4)]
        self.w2, self.sa = at(W_W2, 4, P), at(W_SA, 4, P)
        self.gn = at(W_GN, 4, P), at(W_GN + 4 * P, 4, P)
        self.oa = at(B_OA, 4, N)
        self.mask = at(B_CST2, 2 * P)
        self.level = [at(B_CST2 + (2 + i) * P, P) for i in range(self.LEVELS)]
        self.s = {}
        for name, n in [("mixed", 1), ("decay_done", 1), ("rate_done", 1), ("ak_ready", 1), ("hats_ready", 1), ("ab_ready", 1), ("rk_raw", 1),
                        ("ranks_ready", 1), ("sig_w", 1), ("sig_a", 1), ("kk_raw", 1), ("kk_sq", 1),
                        ("kk_sum", 1), ("kk_in", 1), ("kk_root", 1), ("c_ready", 1), ("exps", 1), ("end_in", 1),
                        ("end_exp", 1), ("rk", 1), ("rk_sum", 2), ("tok_turned", 8), ("tok_kept", 8),
                        ("l_done", 16), ("l_kept", 16), ("c_masked", 2 * 2 * self.LEVELS), ("x_done", 4 * self.LEVELS),
                        ("x_kept", 4 * (self.LEVELS - 1)), ("e_done", 4 * (self.LEVELS - 1)), ("d_done", 4 * self.LEVELS),
                        ("w1_done", 2), ("w1_kept", 2), ("x2_done", 2), ("x2_kept", 2), ("w2_done", 2), ("w2_kept", 2),
                        ("sa_done", NCH), ("sa_kept", NCH), ("s_done", NCH), ("s_kept", NCH + 1), ("y_done", 2), ("y_first", 2),
                        ("y_kept", 2), ("gn_sum", 2), ("gn_centred", 2), ("gn_sq", 2), ("gn_var", 2), ("gn_in", 2), ("gn_root", 2)]:
            self.s[name] = sig("rwkv_" + name, n)

    def prepare_pe(self, pe, w):
        ps, z, s, mm = self.chip.ps, self.z, self.s, self.nc.tensor.matmul
        at = lambda bank, m: ps[:, bank + m // 2, (m % 2) * N:(m % 2 + 1) * N]
        pe.wait_ge(s["ranks_ready"].sem, s["ranks_ready"].at(1))
        for m in range(4):
            last = mm(at(0, m), w[0:64, m, :], z[0:64, T_WA], start=True, stop=True)
        last.then_inc(s["decay_done"].sem, 1)
        for m in range(4):
            last = mm(at(2, m), w[64:128, m, :], z[64:128, T_WA], start=True, stop=True)
        last.then_inc(s["rate_done"].sem, 1)
        for m in range(4):
            last = mm(at(4, m), w[:, 4 + m, :], z[:, T_G], start=True, stop=True)
        last.then_inc(self.chip.block_done, 1)

    def norms_pe(self, pe):
        s = self.s
        pe.wait_ge(s["kk_sq"].sem, s["kk_sq"].at(1))
        for i in range(4):
            last = self.nc.tensor.matmul(self.chip.ps[:, 6 + i // 2, (i % 2) * N:(i % 2 + 1) * N], self.chip.headones,
                                         self.norm[:, i, :], start=True, stop=True)
        last.then_inc(s["kk_sum"].sem, 1)

    def square_act(self, act):
        s = self.s
        act.wait_ge(s["kk_raw"].sem, s["kk_raw"].at(1))
        self.nc.scalar.activation(self.norm, self.kk, ACT.Square).then_inc(s["kk_sq"].sem, 1)

    def root_act(self, act):
        s = self.s
        act.wait_ge(s["kk_in"].sem, s["kk_in"].at(1))
        self.nc.scalar.activation(self.norm, self.norm, ACT.Sqrt).then_inc(s["kk_root"].sem, 1)

    def norms_dve(self, dve, link):
        z, s, v = self.z, self.s, self.nc.vector
        for i in range(4):
            last = v.tensor_scalar(self.kk[:, i, :], z[:, T_K + i, :], columns(self.chip.vec, "k_k", self.layer, 4)[:, i:i + 1],
                                   None, ALU.mult)
        last.then_inc(s["kk_raw"].sem, 1)
        dve.wait_ge(s["kk_sum"].sem, s["kk_sum"].at(1))
        sums = self.chip.ps[:, 6:8, :].rearrange("p b (i n) -> p (b i) n", n=N)
        v.tensor_scalar(self.norm, sums, 1e-12, None, ALU.max).then_inc(s["kk_in"].sem, 1)
        dve.wait_ge(s["kk_root"].sem, s["kk_root"].at(1))
        link(v.reciprocal(self.norm, self.norm))
        link(v.tensor_tensor(self.kk, self.kk, self.norm, ALU.mult))

    def pe(self, pe):
        nc, ps, z, s = self.nc, self.chip.ps, self.z, self.s
        mm = nc.tensor.matmul
        pe.wait_ge(self.chip.stage_done, self.index)

        def half_sums(bank, x):
            for i in range(4):
                last = mm(ps[:, bank, i * P:(i + 1) * P], self.chip.headones, x[:, i, :], start=True, stop=True)
            return last

        def sums(t):
            half_sums(7, self.y[:, :, t * P:(t + 1) * P]).then_inc(s["gn_sum"].sem, 1)

        def squares(t):
            pe.wait_ge(s["gn_sq"].sem, s["gn_sq"].at(t + 1))
            half_sums(6, self.gn[0]).then_inc(s["gn_var"].sem, 1)

        def bonus(t):
            pe.wait_ge(s["rk"].sem, s["rk"].at(1))
            pe.wait_ge(s["gn_centred"].sem, s["gn_centred"].at(t + 1))
            half_sums(7, self.kk[:, :, t * P:(t + 1) * P]).then_inc(s["rk_sum"].sem, 1)

        for t in range(NT):
            ts = slice(t * P, (t + 1) * P)
            if t:
                pe.wait_ge(s["y_kept"].sem, s["y_kept"].at(t))
            for j, x in enumerate([self.A[:, :, ts], self.bh[:, :, ts], self.kh[:, :, ts], z[:, T_V:T_V + 4, ts]]):
                for i in range(4):
                    last = nc.tensor.transpose(ps[:, j, i * P:(i + 1) * P], x[:, i, :], self.chip.ident)
                last.then_inc(s["tok_turned"].sem, 1)
            for x, bank in ((self.b, 4), (self.k, 0)):
                if bank == 0:
                    pe.wait_ge(s["tok_kept"].sem, s["tok_kept"].at(4 * t + 4))
                for b in range(4):
                    two_, e = divmod(b, 2)
                    half = slice(e * DH, (e + 1) * DH)
                    for i in range(2):
                        r = self.R[half, 2 * two_ + i, ts]
                        ra = bass.AP(r.tensor, r.offset, [r.ap[0], (W_A - B_P - T_R * N, 2), (1, P)])
                        last = mm(ps[:, bank + b, i * 2 * P:(i + 1) * 2 * P], x[half, 2 * two_ + i, ts], ra, start=True, stop=True)
                    last.then_inc(s["l_done"].sem, 1)
            pe.wait_ge(s["l_kept"].sem, s["l_kept"].at(8 * t + 8))
            d, dt, x, ct = self.mat
            for lv in range(self.LEVELS):
                for g in range(2):
                    n = (t * self.LEVELS + lv) * 2 + g
                    pe.wait_ge(s["c_masked"].sem, s["c_masked"].at(n + 1))
                    if lv:
                        pe.wait_ge(s["d_done"].sem, s["d_done"].at(n - 1))
                    for h in range(4 * g, 4 * g + 4):
                        last = mm(ps[:, g, (h % 4) * P:(h % 4 + 1) * P], ct[:, h, :], d[:, h, :], start=True, stop=True)
                    last.then_inc(s["x_done"].sem, 1)
                if t:
                    if lv == 0:
                        sums(0)
                    if lv == 2:
                        squares(0)
                    if lv == 3:
                        bonus(0)
                if lv == 0:
                    continue
                for g in range(2):
                    n = (t * (self.LEVELS - 1) + lv - 1) * 2 + g
                    pe.wait_ge(s["x_kept"].sem, s["x_kept"].at(n + 1))
                    for h in range(4 * g, 4 * g + 4):
                        at = slice((h % 4) * P, (h % 4 + 1) * P)
                        if lv < self.LEVELS - 1:
                            mm(ps[:, 2 + g, at], dt[:, h, :], x[:, h, :], start=True, stop=True)
                        last = mm(ps[:, 4 + g, at], x[:, h, :], dt[:, h, :], start=True, stop=True)
                    last.then_inc(s["e_done"].sem, 1)
            pe.wait_ge(s["d_done"].sem, s["d_done"].at(2 * self.LEVELS * (t + 1)))
            for h in range(HEADS):
                last = mm(ps[:, h % 2, (h // 2) * P:(h // 2 + 1) * P], self.tok[:, 0, h // 2, :], dt[:, h, :], start=True, stop=True)
            last.then_inc(s["w1_done"].sem, 1)
            for h in range(HEADS):
                last = mm(ps[:, 2, h * DH:(h + 1) * DH], self.lk[:, h, 1, :], self.tok[:, 3, h // 2, (h % 2) * DH:(h % 2 + 1) * DH],
                          start=True, stop=True)
            last.then_inc(s["x2_done"].sem, 1)
            pe.wait_ge(s["x2_kept"].sem, s["x2_kept"].at(t + 1))
            x2 = x[:, 0:4, :]
            for h in range(HEADS):
                last = mm(ps[:, 3, h * DH:(h + 1) * DH], dt[:, h, :], x2[:, h // 2, (h % 2) * DH:(h % 2 + 1) * DH], start=True, stop=True)
            last.then_inc(s["w2_done"].sem, 1)
            pe.wait_ge(s["w1_kept"].sem, s["w1_kept"].at(t + 1))
            pe.wait_ge(s["w2_kept"].sem, s["w2_kept"].at(t + 1))
            def keys_values(c):
                rows_ = slice(c * CH, (c + 1) * CH)
                for i in range(4):
                    mm(ps[:, c % 2, i * P:(i + 1) * P], self.tok[rows_, 2, i, :], self.tok[rows_, 3, i, :], start=True, stop=True)

            keys_values(0)
            for c in range(4):
                n = 4 * t + c
                rows_ = slice(c * CH, (c + 1) * CH)
                pe.wait_ge(s["s_kept"].sem, s["s_kept"].at(n + 1))
                for i in range(4):
                    last = mm(ps[:, 4, i * P:(i + 1) * P], self.w1[:, i, :], self.state[:, i, :], start=True, stop=True)
                last.then_inc(s["sa_done"].sem, 1)
                for i in range(4):
                    mm(ps[:, 5, i * P + c * CH:i * P + (c + 1) * CH], self.state[:, i, :], self.R[:, i, n * CH:(n + 1) * CH], start=True, stop=True)
                pe.wait_ge(s["sa_kept"].sem, s["sa_kept"].at(n + 1))
                for i in range(4):
                    last = mm(ps[:, 2 + c % 2, i * P:(i + 1) * P], self.tok[rows_, 1, i, :], self.sa[rows_, i, :],
                              start=True, stop=True)
                last.then_inc(s["s_done"].sem, 1)
                if c < 3:
                    keys_values(c + 1)
            for e in range(2):
                for i in range(4):
                    at, h = slice(i * P, (i + 1) * P), 2 * i + e
                    mm(ps[:, 6 + e, at], self.tok[:, 3, i, :], self.lk[:, h, 0, :], start=True, stop=False)
                    last = mm(ps[:, 6 + e, at], self.sa[:, i, :], self.lb[:, h, 0, :], start=False, stop=True)
            last.then_inc(s["y_done"].sem, 1)
        pe.wait_ge(s["y_kept"].sem, s["y_kept"].at(2))
        sums(1)
        self.next.branch(pe, 0, 0)
        squares(1)
        bonus(1)
        self.next.branch(pe, 0, 1)
        self.next.branch(pe, 1, 0)

    def prepare_act(self, act, ranks):
        ps, z, s, copy = self.chip.ps, self.z, self.s, self.nc.scalar.activation
        col = lambda name, i: columns(self.chip.vec, name, self.layer, 4)[:, i:i + 1]
        act.wait_ge(s["mixed"].sem, s["mixed"].at(1))
        copy(z[0:64, T_WA], z[0:64, T_WA], ACT.Tanh)
        copy(z[:, T_G], z[:, T_G], ACT.Sigmoid).then_inc(s["ranks_ready"].sem, 1)
        act.wait_ge(s["decay_done"].sem, s["decay_done"].at(1))
        for i in range(4):
            last = copy(self.c[0][:, i, :], ps[:, i // 2, (i % 2) * N:(i % 2 + 1) * N], ACT.Sigmoid, bias=col("w0", i))
        last.then_inc(s["sig_w"].sem, 1)
        act.wait_ge(s["rate_done"].sem, s["rate_done"].at(1))
        for i in range(4):
            copy(self.a[:, i, :], ps[:, 2 + i // 2, (i % 2) * N:(i % 2 + 1) * N], ACT.Sigmoid, bias=col("a0", i))
        act.wait_ge(self.chip.block_done, ranks)
        copy(self.gate.rearrange("p (b i) n -> p b (i n)", b=2), ps[:, 4:6, :], ACT.Copy).then_inc(s["sig_a"].sem, 1)
        act.wait_ge(s["c_ready"].sem, s["c_ready"].at(1))
        copy(self.e[0], self.c[1], ACT.Exp)
        copy(self.e[1], self.c[1], ACT.Exp, scale=-1.0).then_inc(s["exps"].sem, 1)
        act.wait_ge(s["end_in"].sem, s["end_in"].at(1))
        copy(self.e[2], self.e[2], ACT.Exp).then_inc(s["end_exp"].sem, 1)

    def act(self, act, link):
        nc, ps, z, s = self.nc, self.chip.ps, self.z, self.s
        copy = nc.scalar.activation
        col = lambda name, i: columns(self.chip.vec, name, self.layer, 4)[:, i:i + 1]
        act.wait_ge(self.chip.stage_done, self.index)

        def square(t):
            act.wait_ge(s["gn_centred"].sem, s["gn_centred"].at(t + 1))
            copy(self.gn[0], self.y[:, :, t * P:(t + 1) * P], ACT.Square).then_inc(s["gn_sq"].sem, 1)

        def root(t):
            act.wait_ge(s["gn_in"].sem, s["gn_in"].at(t + 1))
            copy(self.gn[1], self.gn[0], ACT.Sqrt).then_inc(s["gn_root"].sem, 1)

        for t in range(NT):
            for j in range(4):
                act.wait_ge(s["tok_turned"].sem, s["tok_turned"].at(4 * t + j + 1))
                copy(self.tok[:, j].rearrange("p i n -> p (i n)"), ps[:, j, :], ACT.Copy).then_inc(s["tok_kept"].sem, 1)
            x = self.mat[2]
            for lv in range(1, self.LEVELS):
                for g in range(2):
                    n = (t * self.LEVELS + lv) * 2 + g
                    act.wait_ge(s["x_done"].sem, s["x_done"].at(n + 1))
                    copy(x[:, 4 * g:4 * g + 4, :].rearrange("p h n -> p (h n)"), ps[:, g, :], ACT.Copy).then_inc(s["x_kept"].sem, 1)
                if t and lv == 2:
                    square(0)
                if t and lv == 4:
                    root(0)
            act.wait_ge(s["w1_done"].sem, s["w1_done"].at(t + 1))
            for e in range(2):
                half = slice(e * DH, (e + 1) * DH)
                last = copy(self.w1[half].rearrange("p i n -> p (i n)"), ps[half, e, :], ACT.Copy, scale=-1.0)
            last.then_inc(s["w1_kept"].sem, 1)
            act.wait_ge(s["x2_done"].sem, s["x2_done"].at(t + 1))
            copy(x[:, 0:4, :].rearrange("p i n -> p (i n)"), ps[:, 2, :], ACT.Copy).then_inc(s["x2_kept"].sem, 1)
            act.wait_ge(s["w2_done"].sem, s["w2_done"].at(t + 1))
            copy(self.w2.rearrange("p i n -> p (i n)"), ps[:, 3, :], ACT.Copy, scale=-1.0).then_inc(s["w2_kept"].sem, 1)
            if t:
                self.next.round_output(act, 0)
                self.next.round_output(act, 1)
                self.next.lead(act)
            act.wait_ge(s["y_done"].sem, s["y_done"].at(t + 1))
            copy(self.y[:, :, t * P:(t + 1) * P], ps[:, 5, :].rearrange("p (i n) -> p i n", i=4), ACT.Copy)\
                .then_inc(s["y_first"].sem, 1)
        square(1)
        self.next.round(act, 2)
        root(1)
        self.next.round(act, 3)

    def prepare_dve(self, dve, link):
        ps, z, s, v = self.chip.ps, self.z, self.s, self.nc.vector
        col = lambda name, i: columns(self.chip.vec, name, self.layer, 4)[:, i:i + 1]
        two = lambda bank: ps[:, bank:bank + 2, :].rearrange("p b (i n) -> p (b i) n", n=N)
        dve.wait_ge(s["sig_w"].sem, s["sig_w"].at(1))
        c = [x.rearrange("p i (c n) -> p (i c) n", n=CH) for x in self.c]
        link(v.tensor_scalar(self.c[0], self.c[0], -math.exp(-0.5), None, ALU.mult))
        for n in range(5):
            of, to, d = c[n % 2], c[1 - n % 2], 1 << n
            v.tensor_copy(to[:, :, 0:d], of[:, :, 0:d])
            last = v.tensor_tensor(to[:, :, d:CH], of[:, :, d:CH], of[:, :, 0:CH - d], ALU.add)
            if n < 4:
                link(last)
        last.then_inc(s["c_ready"].sem, 1)
        dve.wait_ge(s["c_ready"].sem, s["c_ready"].at(1))
        e2 = self.e[2].rearrange("p i (c n) -> p (i c) n", n=CH)
        v.tensor_tensor(e2, c[1][:, :, CH - 1:CH].broadcast_to([P, 4 * NCH, CH]), c[1], ALU.subtract).then_inc(s["end_in"].sem, 1)
        dve.wait_ge(s["sig_a"].sem, s["sig_a"].at(1))
        t3 = self.t3
        for i in range(4):
            last = v.tensor_scalar(t3[:, i, :], self.a[:, i, :], 1.0, col("k_a", i), ALU.subtract, ALU.mult)
        link(last)
        k = z[:, T_K:T_K + 4, :]
        link(v.scalar_tensor_tensor(k, t3, 1.0, k, ALU.add, ALU.mult))
        v.tensor_tensor(self.a, self.a, self.kk, ALU.mult).then_inc(s["ak_ready"].sem, 1)
        dve.wait_ge(s["ak_ready"].sem, s["ak_ready"].at(1))
        dve.wait_ge(s["exps"].sem, s["exps"].at(1))
        dve.wait_ge(s["end_exp"].sem, s["end_exp"].at(1))
        e_in, e_inv, e_end = self.e
        split = lambda x: x.rearrange("p i (c n) -> p i c n", n=CH)
        for i in range(4):
            A, kk, e = (x[:, i, :].rearrange("p (c n) -> p c n", n=CH) for x in (self.A, self.kk, e_in))
            v.tensor_tensor(A[:, :, 1:CH], kk[:, :, 1:CH], e[:, :, 0:CH - 1], ALU.mult)
            v.tensor_copy(A[:, :, 0:1], kk[:, :, 0:1])
        v.tensor_copy(self.pend, split(e_in)[:, :, :, CH - 1])
        v.tensor_tensor(self.b, self.a, e_inv, ALU.mult).then_inc(s["ab_ready"].sem, 1)
        dve.wait_ge(s["rk_raw"].sem, s["rk_raw"].at(1))
        v.tensor_tensor(self.R, self.R, e_in, ALU.mult)
        link(v.tensor_tensor(self.k, self.k, e_inv, ALU.mult))
        dve.wait_ge(s["hats_ready"].sem, s["hats_ready"].at(1))

    def dve(self, dve, link):
        nc, ps, z, s = self.nc, self.chip.ps, self.z, self.s
        v = nc.vector
        col = lambda name, i: columns(self.chip.vec, name, self.layer, 4)[:, i:i + 1]
        two = lambda bank: ps[:, bank:bank + 2, :].rearrange("p b (i n) -> p (b i) n", n=N)
        dve.wait_ge(self.chip.stage_done, self.index)
        v.memset(self.state, 0.0).then_inc(s["s_kept"].sem, 1)
        d, dt, x, ct = self.mat

        def centre(t):
            y = self.y[:, :, t * P:(t + 1) * P]
            dve.wait_ge(s["gn_sum"].sem, s["gn_sum"].at(t + 1))
            v.scalar_tensor_tensor(y, ps[:, 7, :].rearrange("p (i n) -> p i n", i=4), -1.0 / DH, y, ALU.mult, ALU.add)\
                .then_inc(s["gn_centred"].sem, 1)

        def spread(t):
            dve.wait_ge(s["gn_var"].sem, s["gn_var"].at(t + 1))
            v.tensor_scalar(self.gn[0], ps[:, 6, :].rearrange("p (i n) -> p i n", i=4), 1.0 / DH, GN_EPS, ALU.mult, ALU.add)\
                .then_inc(s["gn_in"].sem, 1)

        def finish(t):
            ts = slice(t * P, (t + 1) * P)
            y = self.y[:, :, ts]
            dve.wait_ge(s["gn_root"].sem, s["gn_root"].at(t + 1))
            link(v.reciprocal(self.gn[1], self.gn[1]))
            link(v.tensor_tensor(y, y, self.gn[1], ALU.mult))
            for i in range(4):
                last = v.tensor_scalar(y[:, i, :], y[:, i, :], col("ln_w", i), col("ln_b", i), ALU.mult, ALU.add)
            link(last)
            dve.wait_ge(s["rk_sum"].sem, s["rk_sum"].at(t + 1))
            bonus = self.kk[:, :, ts]
            link(v.tensor_tensor(bonus, ps[:, 7, :].rearrange("p (i n) -> p i n", i=4), z[:, T_V:T_V + 4, ts], ALU.mult))
            link(v.tensor_tensor(y, y, bonus, ALU.add))
            return v.tensor_tensor(self.oa[:, :, ts], y, self.gate[:, :, ts], ALU.mult)

        for t in range(NT):
            ident = self.chip.ident.unsqueeze(1).broadcast_to([P, HEADS, P])
            v.tensor_copy(d, ident)
            link(v.tensor_copy(dt, ident))
            for n, (to, bank) in enumerate([(self.lb, 4), (self.lk, 0)]):
                for b in range(4):
                    two_, e = divmod(b, 2)
                    dve.wait_ge(s["l_done"].sem, s["l_done"].at(8 * t + 4 * n + b + 1))
                    v.tensor_tensor(to[:, 4 * two_ + e:4 * two_ + e + 3:2].rearrange("p h a n -> p h (a n)"),
                                    ps[:, bank + b, :].rearrange("p (h m) -> p h m", h=2),
                                    self.mask.unsqueeze(1).broadcast_to([P, 2, 2 * P]), ALU.mult).then_inc(s["l_kept"].sem, 1)
            dve.wait_ge(s["l_kept"].sem, s["l_kept"].at(8 * t + 8))

            def mask_level(lv, g):
                n = (t * self.LEVELS + lv) * 2 + g
                if lv:
                    dve.wait_ge(s["x_done"].sem, s["x_done"].at(n - 1))
                hs = slice(4 * g, 4 * g + 4)
                v.tensor_tensor(ct[:, hs, :], self.lb[:, hs, 1, :], self.level[lv].unsqueeze(1).broadcast_to([P, 4, P]), ALU.mult)\
                    .then_inc(s["c_masked"].sem, 1)

            mask_level(0, 0)
            mask_level(0, 1)
            for lv in range(self.LEVELS):
                for g in range(2):
                    n = (t * self.LEVELS + lv) * 2 + g
                    hs = slice(4 * g, 4 * g + 4)
                    if lv == 0:
                        dve.wait_ge(s["x_done"].sem, s["x_done"].at(n + 1))
                        dve.wait_ge(s["c_masked"].sem, s["c_masked"].at(n + 1))
                        v.tensor_tensor(d[:, hs, :], d[:, hs, :], ps[:, g, :].rearrange("p (h n) -> p h n", h=4), ALU.subtract)
                        v.tensor_tensor(dt[:, hs, :], dt[:, hs, :], ct[:, hs, :], ALU.subtract).then_inc(s["d_done"].sem, 1)
                        dve.wait_ge(s["d_done"].sem, s["d_done"].at(n + 1))
                        mask_level(1, g)
                        continue
                    if lv < self.LEVELS - 1:
                        mask_level(lv + 1, g)
                    dve.wait_ge(s["e_done"].sem, s["e_done"].at(n - 2 * t - 1))
                    if lv < self.LEVELS - 1:
                        v.tensor_tensor(d[:, hs, :], d[:, hs, :], ps[:, 2 + g, :].rearrange("p (h n) -> p h n", h=4), ALU.subtract)
                    v.tensor_tensor(dt[:, hs, :], dt[:, hs, :], ps[:, 4 + g, :].rearrange("p (h n) -> p h n", h=4), ALU.subtract)\
                        .then_inc(s["d_done"].sem, 1)
                    dve.wait_ge(s["d_done"].sem, s["d_done"].at(n + 1))
                if t:
                    if lv == 1:
                        centre(0)
                    if lv == 3:
                        spread(0)
                    if lv == 4:
                        finish(0)
            dve.wait_ge(s["w2_kept"].sem, s["w2_kept"].at(t + 1))
            for c_ in range(4):
                n = 4 * t + c_
                rows_ = slice(c_ * CH, (c_ + 1) * CH)
                halves = [slice(e * DH, (e + 1) * DH) for e in range(2)]
                decayed = [self.gn[0][half, :, 0:DH] for half in halves]
                ends = [ps[half, :, :].rearrange("p b (i n) -> p b i n", n=P)[:, :, :, half] for half in halves]
                for e, half in enumerate(halves):
                    v.tensor_tensor(decayed[e], self.state[half, :, half], self.pend[half, :, n:n + 1].broadcast_to([DH, 4, DH]), ALU.mult)
                dve.wait_ge(s["sa_done"].sem, s["sa_done"].at(n + 1))
                last = v.tensor_tensor(self.sa[rows_].rearrange("p i n -> p (i n)"), ps[rows_, 4, :],
                                       self.w2[rows_].rearrange("p i n -> p (i n)"), ALU.add)
                last.then_inc(s["sa_kept"].sem, 1)
                dve.wait_ge(s["sa_kept"].sem, s["sa_kept"].at(n + 1))
                for e in range(2):
                    last = v.tensor_tensor(decayed[e], decayed[e], ends[e][:, c_ % 2], ALU.add)
                link(last)
                dve.wait_ge(s["s_done"].sem, s["s_done"].at(n + 1))
                for e, half in enumerate(halves):
                    last = v.tensor_tensor(self.state[half, :, half], decayed[e], ends[e][:, 2 + c_ % 2], ALU.add)
                last.then_inc(s["s_kept"].sem, 1)
                dve.wait_ge(s["s_kept"].sem, s["s_kept"].at(n + 2))
            dve.wait_ge(s["y_first"].sem, s["y_first"].at(t + 1))
            for e in range(2):
                half = slice(e * DH, (e + 1) * DH)
                y = self.y[half, :, t * P:(t + 1) * P]
                last = v.tensor_tensor(y, y, ps[half, 6 + e, :].rearrange("p (i n) -> p i n", i=4), ALU.add)
            last.then_inc(s["y_kept"].sem, 1)
        centre(1)
        spread(1)
        finish(1).then_inc(self.chip.stage_done, 1)

    def token_shift(self, dve, link):
        v, z, s = self.nc.vector, self.z, self.s
        part = self.chip.x[:, 0:7, N:]
        for i in range(2):
            zs = z[:, 7 * i:7 * i + 7, :]
            mu = columns(self.chip.vec, "mu", self.layer, 14)
            link(v.tensor_scalar(part[:, :, 0:1], zs[:, :, 0:1], -1.0, None, ALU.mult))
            link(v.tensor_tensor(part[:, :, 1:N], zs[:, :, 0:N - 1], zs[:, :, 1:N], ALU.subtract))
            for j in range(7):
                n = 7 * i + j
                last = v.scalar_tensor_tensor(z[:, n, :], part[:, j, :], mu[:, n:n + 1], z[:, n, :], ALU.mult, ALU.add)
            if i == 0:
                link(last)
        last.then_inc(s["mixed"].sem, 1)
        dve.wait_ge(s["mixed"].sem, s["mixed"].at(1))

    def prepare_pool(self, pool, link):
        g, z, s = self.nc.gpsimd, self.z, self.s
        pool.wait_ge(s["end_exp"].sem, s["end_exp"].at(1))
        pool.wait_ge(s["ak_ready"].sem, s["ak_ready"].at(1))
        g.tensor_tensor(self.kh, self.k, self.e[2], ALU.mult)
        pool.wait_ge(s["ab_ready"].sem, s["ab_ready"].at(1))
        g.tensor_tensor(self.kk, self.R, self.k, ALU.mult).then_inc(s["rk_raw"].sem, 1)
        g.tensor_tensor(self.bh, self.a, self.e[2], ALU.mult).then_inc(s["hats_ready"].sem, 1)
        pool.wait_ge(s["rk_raw"].sem, s["rk_raw"].at(1))
        r_k = columns(self.chip.vec, "r_k", self.layer, 4).unsqueeze(2).broadcast_to([P, 4, N])
        g.tensor_tensor(self.kk, self.kk, r_k, ALU.mult).then_inc(s["rk"].sem, 1)


class Merge(Stage):

    blocks = BLOCKS["branch"]

    ORDER = 1, 2, 0

    def __init__(self, chip):
        super().__init__(chip)
        places = [(B_OA, B_OB, B_OC)[b] for b in self.ORDER]
        self.o = [chip.at(a, 4, N) for a in places]
        self.o_parts = [(chip.parts_at(to, 4, N), chip.parts_at(a, 4, N)) for to, a in zip((W_A, W_KH, W_B), places)]
        gates = chip.at(B_P, 56, N)[:, T_GATES:, :]
        self.gates = [gates[:, KD * b:KD * (b + 1), :] for b in self.ORDER]
        self.merged, self.part = chip.at(B_BIAS, KD, N), chip.at(B_BIAS + KD * N, KD, N)
        self.parts = chip.parts_at(B_BIAS + 2 * KD * N, KD, N), chip.parts_at(B_BIAS, KD, N)
        self.rounded = chip.signals("branch_rounded", 3)
        self.ready = chip.signals("branch_split", 3)
        self.used = chip.signals("branch_used", 2)
        self.merged_ready = chip.signals("merged_ready", 4)
        self.merged_rounded = chip.signals("rounded", 4)

    def branch(self, pe, b, j):
        c = self.chip
        if j == 0:
            pe.wait_ge(self.ready.sem, self.ready.at(b + 1))
        whi, wlo = self.weights(2 * b + j)
        for m in range(4):
            if m % 2 == 0:
                pe.wait_ge(c.rest_done[m // 2], self.split_count(2 * b + j))
            mm = 4 * j + m
            for k in range(4):
                i = 4 * m + k
                last = self.product(c.ps[:, 4 * (b % 2) + mm // 2, (mm % 2) * N:(mm % 2 + 1) * N],
                                    (whi[:, i, :], wlo[:, i, :]), [o[:, k, :] for o in self.o_parts[b]], k == 0, k == 3)
        last.then_inc(c.block_done, 1)

    def pe(self, pe):
        pe.wait_ge(self.chip.stage_done, self.index)
        self.branch(pe, 1, 1)
        pe.wait_ge(self.used.sem, self.used.at(1))
        for j in range(2):
            self.branch(pe, 2, j)

    def round_output(self, act, b):
        self.nc.scalar.activation(self.o_parts[b][0], self.o[b], ACT.Copy).then_inc(self.rounded.sem, 1)

    def act(self, act, link):
        copy = self.nc.scalar.activation
        act.wait_ge(self.chip.stage_done, self.index)
        self.round_output(act, 2)
        for j in (4, 5):
            self.round(act, j)
        self.next.led = True
        for i in range(4):
            if i % 2 == 0:
                self.next.round(act, i // 2)
            tiles = slice(2 * i, 2 * i + 2)
            act.wait_ge(self.merged_ready.sem, self.merged_ready.at(i + 1))
            copy(self.parts[0][:, tiles, :], self.merged[:, tiles, :], ACT.Copy).then_inc(self.merged_rounded.sem, 1)

    def pool(self, pool, link):
        def output(b):
            pool.wait_ge(self.rounded.sem, self.rounded.at(b + 1))
            self.nc.gpsimd.tensor_tensor(self.o_parts[b][1], self.o[b], self.o_parts[b][0].bitcast(F32), ALU.subtract)\
                .then_inc(self.ready.sem, 1)

        output(0)
        for j in range(self.blocks):
            if j == 1:
                output(1)
            if j == 4:
                output(2)
            for h in range(2):
                self.leave_rest(j, h, self.split_count(j))

    def dve(self, dve, link):
        v = self.nc.vector

        def product(b, tiles):
            ps = self.chip.ps[:, 4 * (b % 2):4 * (b % 2) + 4, :].rearrange("p b (m n) -> p (b m) n", n=N)
            return v.tensor_tensor((self.part if b else self.merged)[:, tiles, :], ps[:, tiles, :], self.gates[b][:, tiles, :], ALU.mult)

        def rest(i):
            tiles = slice(2 * i, 2 * i + 2)
            dve.wait_ge(self.merged_rounded.sem, self.merged_rounded.at(i + 1))
            return v.tensor_tensor(self.parts[1][:, tiles, :], self.merged[:, tiles, :],
                                   self.parts[0].bitcast(F32)[:, tiles, :], ALU.subtract)

        dve.wait_ge(self.chip.stage_done, self.index)
        for b in range(2):
            dve.wait_ge(self.chip.block_done, self.block_count(2 * b + 1))
            product(b, slice(0, KD)).then_inc(self.used.sem, 1)
            dve.wait_ge(self.used.sem, self.used.at(b + 1))
        link(v.tensor_tensor(self.merged, self.merged, self.part, ALU.add))
        for i in range(4):
            tiles = slice(2 * i, 2 * i + 2)
            if i % 2 == 0:
                dve.wait_ge(self.chip.block_done, self.block_count(4 + i // 2))
            link(product(2, tiles))
            v.tensor_tensor(self.merged[:, tiles, :], self.merged[:, tiles, :], self.part[:, tiles, :], ALU.add)\
                .then_inc(self.merged_ready.sem, 1)
            if i:
                rest(i - 1)
        rest(3).then_inc(self.chip.stage_done, 1)


G_GATES = 0
G_SLOT = NKEYS * N
G_HOT = G_SLOT + 3 * N
G_GELU = G_SLOT
G_ACT = G_GELU + 2 * N
G_Q = 0
G_KEYS = G_Q + 16 * N
G_S = G_KEYS + 16 * P
G_TOP = G_S + 16 * NT * P
G_IDX = G_TOP + 16 * NT * TOPK
G_REST = G_IDX + 16 * NT * TOPK
HALF_K = TOPK // 2
PAST = TOPK + (HALF_K - 1) * HALF_K
PAIRS = PAST + HALF_K
G_CAND = G_REST + 4 * P + NT * PAIRS
G_HOTK = G_CAND + NT * PAIRS
G_SEL = G_HOTK + HEADS * 2 * NT * TOPK * TOPK
G_SQ = 0
G_SMALL = KD * N


def expert_input(chip):
    return chip.x_parts[:, :, 0:N], chip.x_parts[:, :, N:]


class PeerRoute(Stage):

    blocks = BLOCKS["wq"]

    def __init__(self, chip, layer):
        super().__init__(chip)
        at, sig = chip.at, chip.signals
        self.layer = layer
        self.z = expert_input(chip)
        self.q, self.keys = at(G_Q, 16, N), at(G_KEYS, 16, P)
        self.s = at(G_S, HEADS, NT, 2, P)
        self.top, self.idx = at(G_TOP, HEADS, NT * 2, TOPK), at(G_IDX, HEADS, NT * 2, TOPK)
        self.others = at(G_REST, 4, P)
        self.other_pairs = at(G_REST + 4 * P, NT, PAIRS)
        self.cand = at(G_CAND, NT, PAIRS)
        self.hot = at(G_HOTK, HEADS, 2, NT, TOPK * TOPK)
        self.sel = at(G_SEL, NT, 8, HEADS, TOPK)
        self.slot = at(G_SLOT, 3, N)
        self.keys_loaded = sig("peer_keys_loaded", 16)
        self.q_kept = sig("q_kept", HEADS)
        self.scored = sig("scored", HEADS)
        self.s_kept = sig("peer_s_kept", HEADS)
        self.ranked = sig("peer_ranked", HEADS)
        self.multiplied = sig("peer_multiplied", HEADS)
        self.added = sig("peer_added", 3 * HEADS)
        self.looked_up = sig("peer_looked_up", HEADS)
        self.shifted = sig("shifted", 1)
        self.exped = sig("exped", 1)
        self.chosen = sig("peer_chosen", 1)
        self.turned = sig("turned", 3)
        self.slot_kept = sig("peer_slot_kept", 3)

    def pe(self, pe):
        nc, ps = self.nc, self.chip.ps

        def queries(j):
            whi, wlo = self.weights(j)
            if j >= 2:
                pe.wait_ge(self.q_kept.sem, self.q_kept.at(j - 1))
            for e in range(2):
                pe.wait_ge(self.chip.rest_done[e], self.split_count(j))
                for k in range(KD):
                    i = e * KD + k
                    if j == 0 and e == 0:
                        self.input_tile(pe, k)
                    last = self.product(ps[:, j % 2, e * N:(e + 1) * N], (whi[:, i, :], wlo[:, i, :]),
                                        [z[:, k, :] for z in self.z], k == 0, k == KD - 1)
            last.then_inc(self.chip.block_done, 1)

        def scores(h):
            pe.wait_ge(self.q_kept.sem, self.q_kept.at(h + 1))
            if h >= 2:
                pe.wait_ge(self.s_kept.sem, self.s_kept.at(h - 1))
            for t in range(NT):
                for a in range(2):
                    at = (2 * t + a) * P
                    last = nc.tensor.matmul(ps[:, 2 + h % 2, at:at + P], self.q[:, 2 * h + a, t * P:(t + 1) * P],
                                            self.keys[:, 2 * h + a, :], start=True, stop=True)
            last.then_inc(self.scored.sem, 1)

        for j in range(HEADS):
            queries(j)
            if j == 1:
                pe.wait_ge(self.keys_loaded.sem, self.keys_loaded.at(16))
            if j:
                scores(j - 1)
        scores(HEADS - 1)
        pe.wait_ge(self.looked_up.sem, self.looked_up.at(HEADS))
        for j in range(3):
            if j == 2:
                pe.wait_ge(self.chosen.sem, self.chosen.at(1))
            for t in range(NT):
                last = nc.tensor.transpose(ps[:, j, t * P:(t + 1) * P], self.sel[:, t, 5 + j].rearrange("p h k -> p (h k)"),
                                           self.chip.ident)
            last.then_inc(self.turned.sem, 1)

    def act(self, act, link):
        copy, ps = self.nc.scalar.activation, self.chip.ps
        self.lead(act)
        act.wait_ge(self.chip.stage_done, self.index)
        act.dma_start(self.keys, self.chip.io["keys"][self.layer]).then_inc(self.keys_loaded.sem, 16)

        def keep_scores(h):
            act.wait_ge(self.scored.sem, self.scored.at(h + 1))
            copy(self.s[:, h].rearrange("p t a n -> p (t a n)"), ps[:, 2 + h % 2, :], ACT.Copy).then_inc(self.s_kept.sem, 1)

        for j in range(HEADS):
            act.wait_ge(self.chip.block_done, self.block_count(j))
            copy(self.q[:, 2 * j:2 * j + 2, :].rearrange("p a n -> p (a n)"), ps[:, j % 2, :], ACT.Copy).then_inc(self.q_kept.sem, 1)
            self.round(act, j + ROUNDED)
            if j:
                keep_scores(j - 1)
        keep_scores(HEADS - 1)
        self.next.next.lead(act)
        act.wait_ge(self.shifted.sem, self.shifted.at(1))
        copy(self.sel[:, :, 7], self.sel[:, :, 7], ACT.Exp).then_inc(self.exped.sem, 1)
        for j in range(3):
            act.wait_ge(self.turned.sem, self.turned.at(j + 1))
            copy(self.slot[:, j, :], ps[:, j, 0:N], ACT.Copy).then_inc(self.slot_kept.sem, 1)
        act.wait_ge(self.slot_kept.sem, self.slot_kept.at(3))
        act.sem_inc(self.chip.stage_done, 1)

    def pool(self, pool, link):
        super().pool(pool, link)
        g = self.nc.gpsimd
        for h in range(HEADS):
            pool.wait_ge(self.ranked.sem, self.ranked.at(h + 1))
            for a in range(2):
                for t in range(NT):
                    hot = self.hot[:, h, a, t].rearrange("p (k j) -> p k j", j=TOPK)
                    last = g.tensor_tensor(hot, hot, self.idx[:, h, 2 * t + a, :].unsqueeze(1).broadcast_to([P, TOPK, TOPK]), ALU.mult)
            last.then_inc(self.multiplied.sem, 1)
            pool.wait_ge(self.multiplied.sem, self.multiplied.at(h + 1))
            hot = self.hot[:, h].rearrange("p a t (k j) -> p (a t k) j", j=TOPK)
            for n, width in enumerate((8, 4, 2)):
                g.tensor_tensor(hot[:, :, 0:width], hot[:, :, 0:width], hot[:, :, width:2 * width], ALU.add).then_inc(self.added.sem, 1)
                pool.wait_ge(self.added.sem, self.added.at(3 * h + n + 1))
            for a in range(2):
                one = self.hot[:, h, a].rearrange("p t (k j) -> p t k j", j=TOPK)
                last = g.tensor_tensor(self.sel[:, :, 5 + a, h, :], one[:, :, :, 0], one[:, :, :, 1], ALU.add)
            last.then_inc(self.looked_up.sem, 1)
            if HEADS - 2 * ROUNDED - 1 <= h < HEADS - 1:
                self.next.next.first_rest(h - (HEADS - 2 * ROUNDED - 1))

    def dve(self, dve, link):
        v = self.nc.vector
        dve.wait_ge(self.chip.stage_done, self.index)

        def best(rows):
            for values, others, top, places in rows:
                last = v.max(top[:, 0:8], values)
            link(last)
            for values, others, top, places in rows:
                v.max_index(places[:, 0:8], top[:, 0:8], values)
                last = v.match_replace(others, top[:, 0:8], values, -3e38)
            link(last)
            for values, others, top, places in rows:
                last = v.max(top[:, 8:16], others)
            link(last)
            for values, others, top, places in rows:
                last = v.max_index(places[:, 8:16], top[:, 8:16], others)
            link(last)

        def sum_pairs(h):
            first, second = [self.top[:, h].rearrange("p (t a) k -> p t a k", a=2)[:, :, a] for a in range(2)]
            square = [P, NT, HALF_K - 1, HALF_K]
            v.tensor_tensor(self.cand[:, :, 0:TOPK], second, first[:, :, 0:1].broadcast_to([P, NT, TOPK]), ALU.add)
            v.tensor_tensor(self.cand[:, :, TOPK:PAST].rearrange("p t (i j) -> p t i j", j=HALF_K),
                            first[:, :, 1:HALF_K].unsqueeze(3).broadcast_to(square),
                            second[:, :, 0:HALF_K].unsqueeze(2).broadcast_to(square), ALU.add)
            last = v.tensor_tensor(self.cand[:, :, PAST:PAIRS], first[:, :, HALF_K:TOPK],
                                   second[:, :, 0:1].broadcast_to([P, NT, HALF_K]), ALU.add)
            v.tensor_copy(self.idx[:, h], self.idx[:, h].bitcast(U32))
            return last

        def find_ranks(h):
            place, eighth, rest, past, other, early = [self.sel[:, :, i, h, :] for i in (1, 2, 3, 4, 6, 7)]
            v.tensor_scalar(eighth.bitcast(U32), place.bitcast(U32), 3, None, ALU.logical_shift_right)
            link(v.tensor_scalar(rest.bitcast(U32), place.bitcast(U32), HALF_K - 1, None, ALU.bitwise_and))
            found = self.sel[:, :, 1:4, h, :]
            link(v.tensor_copy(found, found.bitcast(U32)))
            v.tensor_scalar(past, place, float(PAST - HALF_K), 0.0, ALU.subtract, ALU.max)
            link(v.scalar_tensor_tensor(early, place, float(TOPK), place, ALU.is_lt, ALU.mult))
            v.scalar_tensor_tensor(eighth, eighth, -1.0, past, ALU.add, ALU.max)
            link(v.scalar_tensor_tensor(other, past, float(HALF_K), rest, ALU.is_lt, ALU.mult))
            link(v.tensor_tensor(rest, other, early, ALU.max))
            every = [P, NT, TOPK, TOPK]
            for a, rank in enumerate((eighth, rest)):
                last = v.tensor_tensor(self.hot[:, h, a].rearrange("p t (k j) -> p t k j", j=TOPK),
                                       rank.unsqueeze(3).broadcast_to(every),
                                       self.chip.iota[:, 0:TOPK].unsqueeze(1).unsqueeze(1).broadcast_to(every), ALU.is_equal)
            last.then_inc(self.ranked.sem, 1)

        for h in range(HEADS + 1):
            rows = []
            if h:
                rows += [(self.cand[:, t], self.other_pairs[:, t, :], self.sel[:, t, 0, h - 1, :],
                          self.sel[:, t, 1, h - 1, :].bitcast(U32)) for t in range(NT)]
            if h < HEADS:
                dve.wait_ge(self.s_kept.sem, self.s_kept.at(h + 1))
                rows += [(self.s[:, h, i // 2, i % 2, :], self.others[:, i, :], self.top[:, h, i, :],
                          self.idx[:, h, i, :].bitcast(U32)) for i in range(4)]
            best(rows)
            if h < HEADS:
                last = sum_pairs(h)
            if h:
                find_ranks(h - 1)
            else:
                link(last)
        score, gate = self.sel[:, :, 0], self.sel[:, :, 7]
        wide = [P, NT, HEADS, TOPK]
        v.tensor_tensor(gate, score, score[:, :, :, 0:1].broadcast_to(wide), ALU.subtract).then_inc(self.shifted.sem, 1)
        dve.wait_ge(self.exped.sem, self.exped.at(1))
        total = self.sel[:, :, 4, :, 0]
        link(v.tensor_reduce(total, gate, AX.X, ALU.add))
        link(v.reciprocal(total, total))
        v.tensor_tensor(gate, gate, total.unsqueeze(3).broadcast_to(wide), ALU.mult).then_inc(self.chosen.sem, 1)


class PeerGates(Stage):

    SET = 2
    SETS = N // SET
    BUFS = 4

    def __init__(self, chip):
        super().__init__(chip)
        self.slot = chip.at(G_SLOT, 3, N)
        self.hot = chip.at(G_HOT, self.BUFS, 2, self.SET, P)
        self.gates = chip.at(G_GATES, N * NKEYS)
        self.hot_ready = chip.signals("hot_ready", self.SETS)
        self.weighted = chip.signals("weighted", self.SETS)
        self.done = chip.signals("gates_done", self.SETS)
        self.kept = chip.signals("gates_kept", self.SETS)

    def dve(self, dve, link):
        dve.wait_ge(self.chip.stage_done, self.index)
        wide = [P, 2, self.SET, P]

        def body(it, first=False):
            for r in range(self.BUFS):
                n = it * self.BUFS + r
                if not first:
                    dve.wait_ge(self.done.sem, self.done.at(n - self.BUFS + 1))
                self.nc.vector.tensor_tensor(self.hot[:, r], self.chip.iota.unsqueeze(1).unsqueeze(1).broadcast_to(wide),
                                             self.slot[:, 0:2, bass.ds(n * self.SET, self.SET)].unsqueeze(3).broadcast_to(wide),
                                             ALU.is_equal).then_inc(self.hot_ready.sem, 1)

        body(0, first=True)
        with dve.Fori(1, self.SETS // self.BUFS) as it:
            body(it)

    def pool(self, pool, link):
        pool.wait_ge(self.chip.stage_done, self.index)
        with pool.Fori(0, self.SETS // self.BUFS) as it:
            for r in range(self.BUFS):
                n = it * self.BUFS + r
                hot = self.hot[:, r, 0]
                pool.wait_ge(self.hot_ready.sem, self.hot_ready.at(n + 1))
                self.nc.gpsimd.tensor_tensor(hot, hot, self.slot[:, 2, bass.ds(n * self.SET, self.SET)].unsqueeze(2)
                                             .broadcast_to([P, self.SET, P]), ALU.mult).then_inc(self.weighted.sem, 1)

    def pe(self, pe):
        pe.wait_ge(self.chip.stage_done, self.index)

        def body(it, first=False):
            for r in range(self.BUFS):
                n = it * self.BUFS + r
                pe.wait_ge(self.weighted.sem, self.weighted.at(n + 1))
                if not first:
                    pe.wait_ge(self.kept.sem, self.kept.at(n - self.BUFS + 1))
                for i in range(self.SET):
                    last = self.nc.tensor.matmul(self.chip.ps[:, r, i * P:(i + 1) * P], self.hot[:, r, 0, i], self.hot[:, r, 1, i],
                                                 start=True, stop=True)
                last.then_inc(self.done.sem, 1)

        body(0, first=True)
        with pe.Fori(1, self.SETS // self.BUFS) as it:
            body(it)

    def act(self, act, link):
        act.wait_ge(self.chip.stage_done, self.index)
        self.next.lead(act)
        width = self.SET * NKEYS
        with act.Fori(0, self.SETS // self.BUFS) as it:
            for r in range(self.BUFS):
                n = it * self.BUFS + r
                act.wait_ge(self.done.sem, self.done.at(n + 1))
                self.nc.scalar.activation(self.gates[:, bass.ds(n * width, width)], self.chip.ps[:, r, 0:width], ACT.Copy)\
                    .then_inc(self.kept.sem, 1)
        act.wait_ge(self.kept.sem, self.kept.at(self.SETS))
        act.sem_inc(self.chip.stage_done, 1)


class PeerExperts(Stage):

    blocks = BLOCKS["experts"]

    def __init__(self, chip):
        super().__init__(chip)
        self.z = expert_input(chip)
        self.gates = chip.at(G_GATES, N, NKEYS)
        self.gelu = chip.at(G_GELU, 2, N)
        self.parts = chip.parts_at(G_ACT, 2, N), chip.parts_at(G_ACT + 2 * N, 2, N)
        self.zero = chip.at(G_ACT + 4 * N, P)
        n = self.blocks
        self.zeroed = chip.signals("expert_zeroed", 1)
        self.closed = chip.signals("expert_closed", 1)
        self.up_done = chip.signals("expert_up_done", n)
        self.gelu_ready = chip.signals("expert_gelu_ready", n)
        self.gated = chip.signals("expert_gated", n)
        self.act_rounded = chip.signals("expert_act_rounded", n)
        self.act_ready = chip.signals("expert_act_ready", n)

    def out(self, m):
        return self.chip.ps[:, 4 + m // 2, (m % 2) * N:(m % 2 + 1) * N]

    def pe(self, pe):
        nc, c = self.nc, self.chip
        pe.wait_ge(self.chip.stage_done, self.index)

        def up(it, r, wait):
            b = it * RING + r
            whi, wlo = self.weights(r)
            pe.wait_ge(c.rest_done[0], self.split_count(b))
            if wait:
                pe.wait_ge(self.gelu_ready.sem, self.gelu_ready.at(b - 1))
            for k in range(KD):
                last = self.product(c.ps[:, r % 2, 0:N], (whi[:, k, :], wlo[:, k, :]), [z[:, k, :] for z in self.z],
                                    k == 0, k == KD - 1)
            last.then_inc(self.up_done.sem, 1)

        def down(it, r):
            b = it * RING + r
            whi, wlo = self.weights(r)
            pe.wait_ge(c.rest_done[1], self.split_count(b))
            pe.wait_ge(self.act_ready.sem, self.act_ready.at(b + 1))
            for m in range(KD):
                last = self.product(self.out(m), (whi[:, KD + m, :], wlo[:, KD + m, :]), [a[:, r % 2, :] for a in self.parts],
                                    False, False)
            last.then_inc(c.block_done, 1)

        for r in range(RING):
            up(0, r, wait=r >= 2)
            if r:
                down(0, r - 1)
        with pe.Fori(1, self.blocks // RING) as it:
            for r in range(RING):
                up(it, r, wait=True)
                down(it - 1 if r == 0 else it, (r - 1) % RING)
        down(self.blocks // RING - 1, RING - 1)
        pe.wait_ge(self.zeroed.sem, self.zeroed.at(1))
        for bank in range(4, 8):
            last = nc.tensor.matmul(c.ps[:, bank, :], self.zero, c.cst[:], start=False, stop=True)
        last.then_inc(self.closed.sem, 1)

    def act(self, act, link):
        c, copy = self.chip, self.nc.scalar.activation
        n = self.blocks
        self.lead(act)
        act.wait_ge(c.stage_done, self.index)

        def body(it, first=False, last=False):
            for r in range(RING):
                b = it * RING + r
                act.wait_ge(self.up_done.sem, self.up_done.at(b + 1))
                if not (first and r < 2):
                    act.wait_ge(self.gated.sem, self.gated.at(b - 1))
                    act.wait_ge(self.act_ready.sem, self.act_ready.at(b - 1))
                copy(self.gelu[:, r % 2, :], c.ps[:, r % 2, 0:N], ACT.Gelu).then_inc(self.gelu_ready.sem, 1)
                if not (last and r + ROUNDED >= RING):
                    self.round_next(act, it, r + ROUNDED, 0)
                act.wait_ge(self.gated.sem, self.gated.at(b + 1))
                if not (first and r < 2):
                    act.wait_ge(c.block_done, self.block_count(b - 2))
                copy(self.parts[0][:, r % 2, :], self.gelu[:, r % 2, :], ACT.Copy).then_inc(self.act_rounded.sem, 1)
                if not (first and r == 0) and not (last and r + 1 >= RING):
                    act.wait_ge(c.block_done, self.block_count(b - 1))
                    self.round_next(act, it, r + 1, 1)

        body(0, first=True)
        with act.Fori(1, n // RING - 1) as it:
            body(it)
        body(n // RING - 1, last=True)

    def round_next(self, act, it, r, h):
        c, half = self.chip, slice(h * HALF, (h + 1) * HALF)
        f = self.b0 % RING + r
        act.wait_ge(c.loaded[f % RING], (it + self.b0 // RING + f // RING + 1) * 16)
        self.nc.scalar.activation(c.rounded[:, (self.s0 + r) % ROUNDED, half], c.ring[:, f % RING, half], ACT.Copy)\
            .then_inc(c.rounded_done[h], 1)

    def first_rest(self, i):
        j, h = divmod(i, 2)
        self.leave_rest(j, h, self.split_count(j))

    def pool(self, pool, link):
        n = self.blocks
        self.leave_rest(2, 0, self.split_count(2))
        self.leave_rest(3, 0, self.split_count(3))
        self.leave_rest(2, 1, self.split_count(2))
        with pool.Fori(1, n // RING) as it:
            for r in range(RING):
                b = it * RING + r
                self.leave_rest(r, 0, self.split_count(b))
                self.leave_rest((r - 1) % RING, 1, self.split_count(b - 1))
        self.leave_rest(RING - 1, 1, self.split_count(n - 1))

    def dve(self, dve, link):
        v, c = self.nc.vector, self.chip
        dve.wait_ge(self.chip.stage_done, self.index)
        v.memset(self.zero, 0.0).then_inc(self.zeroed.sem, 1)

        def body(it, first=False):
            for r in range(RING):
                b = it * RING + r
                gelu = self.gelu[:, r % 2, :]
                dve.wait_ge(self.gelu_ready.sem, self.gelu_ready.at(b + 1))
                v.tensor_tensor(gelu, gelu, self.gates[:, :, bass.ds(b, 1)].rearrange("p t a -> p (t a)"), ALU.mult)\
                    .then_inc(self.gated.sem, 1)
                dve.wait_ge(self.act_rounded.sem, self.act_rounded.at(b + 1))
                v.tensor_tensor(self.parts[1][:, r % 2, :], gelu, self.parts[0].bitcast(F32)[:, r % 2, :], ALU.subtract)\
                    .then_inc(self.act_ready.sem, 1)

        body(0, first=True)
        with dve.Fori(1, self.blocks // RING) as it:
            body(it)
        dve.wait_ge(self.closed.sem, self.closed.at(1))
        v.tensor_copy(c.x[:, :, 0:N], c.ps[:, 4:8, :].rearrange("p b (m n) -> p (b m) n", n=N)).then_inc(c.stage_done, 1)


def second_norm(chip, gain, split=False):
    small = [chip.at(B_SMALL + i * N, N) for i in range(3)]
    return Norm(chip, chip.at(B_U, KD, N), chip.at(B_SQ, KD, N), small, N, gain=gain, parts=second_input(chip) if split else None)


def expert_norm(chip, gain):
    small = [chip.at(G_SMALL + i * N, N) for i in range(3)]
    return Norm(chip, chip.x[:, :, N:], chip.at(G_SQ, KD, N), small, N, gain=gain, parts=expert_input(chip), keep=True)


def second_network(chip):
    vec = chip.vec[:]
    stages = [second_norm(chip, columns(vec, "final_g")), Replace(chip)]
    for layer in range(DEPTH):
        tables = LoadTables(chip)
        stages += [tables, second_norm(chip, columns(vec, "ln1", layer, KD), split=True), ProjectIn(chip),
                   Attention(chip, layer, tables), Rwkv(chip, layer)]
        merge = Merge(chip)
        stages += [merge, Project(chip, tiles_of(merge.parts), KD, N),
                   expert_norm(chip, columns(vec, "ln2", layer, KD)),
                   PeerRoute(chip, layer), PeerGates(chip), PeerExperts(chip)]
    final = second_norm(chip, columns(vec, "lnf"))
    return stages + [final, Finish(chip, final.u)]


class Replace(Stage):

    def dve(self, dve, link):
        dve.wait_ge(self.chip.stage_done, self.index)
        self.nc.vector.tensor_copy(self.chip.x[:, :, 0:N], self.chip.at(B_U, KD, N)).then_inc(self.chip.stage_done, 1)


def second_weights(i):
    for layer in range(DEPTH):
        w = i["w_in_2"][layer]
        cut = lambda a, n: w[:, a:a + n]
        pad = lambda a: np.concatenate([a, np.zeros((D, P - a.shape[1]), np.float32)], axis=1)
        heads = lambda a: a.reshape(D, 2, 4, DH).transpose(0, 2, 1, 3).reshape(D, 8 * DH)
        n0 = 14 * P
        nq, (kc, vc, ks, vs, kw, vw) = cut(n0, 512), [cut(n0 + 512 + P * j, P) for j in range(6)]
        gate = cut(n0 + 1280, 24)
        s0 = n0 + 1304
        sq, sk, sv = cut(s0, 512), cut(s0 + 512, P), cut(s0 + 640, P)
        both = [np.concatenate([kc[:, g * DH:(g + 1) * DH], vc[:, g * DH:(g + 1) * DH]], axis=1) for g in range(2)]
        yield pairs(np.concatenate([cut(0, n0), heads(nq), *both, ks, kw, heads(sq), sk, np.zeros((D, P), np.float32),
                                    vs, vw, pad(gate), sv, cut(s0 + 768, 3 * D)], axis=1))
        ranks = np.zeros((1, P, TPB, P), np.float32)
        ranks[0, :64, 0:4], ranks[0, 64:, 0:4] = (i[n][layer].reshape(64, 4, P) for n in ("rwkv_w2_2", "rwkv_a2_2"))
        ranks[0, :, 4:8] = i["rwkv_g2_2"][layer].reshape(P, 4, P)
        yield ranks
        kv = np.concatenate([i[n][layer].reshape(CMP_LEN, DH, 2, P) for n in ("nsa_ck_w1_2", "nsa_cv_w1_2")], axis=1)
        yield kv.transpose(0, 2, 1, 3).reshape(4, TPB, P, P).transpose(0, 2, 1, 3)
        ck, cv = (i[n][layer].reshape(2, P, DH).transpose(1, 0, 2) for n in ("nsa_ck_w2_2", "nsa_cv_w2_2"))
        small = np.zeros((1, P, TPB, P), np.float32)
        small[0, :, 0:2, :DH], small[0, :, 0:2, DH:], small[0, :, 2:4, :DH] = ck, ck, cv
        yield small
        rows_ = lambda a: a.reshape(2, 4, DH, D).transpose(1, 0, 2, 3).reshape(8 * DH, D)
        for a in (rows_(i["w_br_b_2"][layer]), rows_(i["w_br_c_2"][layer]), i["w_br_a_2"][layer]):
            yield a.reshape(4, P, 2, 4, P).transpose(2, 1, 3, 0, 4).reshape(2, P, TPB, P)
        yield rows(i["w_out_2"][layer])
        yield pairs(i["peer_wq_2"][layer])
        u = i["peer_u_2"][layer].reshape(P, NKEYS, KD, P).transpose(1, 3, 2, 0)
        v = i["peer_v_2"][layer].reshape(P, NKEYS, KD, P).transpose(1, 0, 2, 3)
        yield np.concatenate([u, v], axis=2)


def second_constants():
    p = np.arange(P)
    s, t = p[:, None], p[None, :]
    same = s // CH == t // CH
    parts = [same & (s <= t), same & (s < t)]
    for n in (1, 2, 4, 8, 16):
        parts.append((s // (2 * n) == t // (2 * n)) & (s % (2 * n) < n) & (t % (2 * n) >= n))
    end = np.arange(16) * CMP_STRIDE + CMP_LEN - 1
    seen = [np.where(end[None, :] <= (p + k * P)[:, None], 0.0, NEG) for k in range(NT)]
    return np.concatenate([x.astype(np.float32) for x in parts] + seen, axis=1)


N_SETUP = 3
N_INPUTS = 2


class Finish(Stage):

    def __init__(self, chip, out):
        super().__init__(chip)
        self.out = out
        self.stored = chip.signals("out_stored", 16)

    def act(self, act, link):
        act.wait_ge(self.chip.stage_done, self.index)
        act.dma_start(self.chip.io["out"], self.out).then_inc(self.stored.sem, 16)
        act.wait_ge(self.stored.sem, self.stored.at(16))


def first_network(chip):
    start = Start(chip)
    stages = [start]
    for layer in range(DEPTH):
        last = layer == DEPTH - 1
        stages.append(Modulation(chip, layer, start if layer == 0 else None))
        stages += feed_forward(chip, 2 * N, 0)
        stages.append(first_norm(chip, 2 * N, 1, split=layer > 0))
        if layer == 0:
            fourier = Fourier(chip)
            stages += [fourier, Project(chip, tiles_of(fourier.parts), KD, 2 * N, gate=5)]
        else:
            retention = Retention(chip)
            stages += [retention, Project(chip, retention.output_tile, RH * RDV // P, N, gate=5)]
        stages += feed_forward(chip, N if last else 2 * N, 2)
    return stages


def program(nc, io):
    ctx = ExitStack()
    with ctx:
        chip = Chip(nc, ctx, io)
        stages = first_network(chip) + second_network(chip)
        for stage, after in zip(stages, stages[1:]):
            stage.next, after.before = after, stage
        setup = [(chip.vec[:], io["vec"]), (chip.cst[:], io["cst"]), (chip.at(A_BIAS + 16 * BIASW, 16 * P + BIASW), io["bias_in"])]
        inputs = [(chip.x[:], io["x"]), (chip.at(A_CST1, NCST1), io["cst1"])]
        assert (len(setup), len(inputs)) == (N_SETUP, N_INPUTS)
        block = ctx.enter_context(nc.Block())

        @block.sync
        def _(sp):
            for to, of in setup:
                sp.dma_start(to, of).then_inc(chip.setup_loaded, 16)
            for b in range(RING):
                sp.dma_start(chip.ring[:, b], io["weights"][b]).then_inc(chip.loaded[b], 16)
            for to, of in inputs:
                sp.dma_start(to, of).then_inc(chip.inputs_loaded, 16)
            rounds = chip.n_blocks // RING
            with sp.Fori(1, rounds) as i:
                for r in range(RING):
                    sp.wait_ge(chip.block_done, (i - 1) * RING + r + 1)
                    sp.dma_start(chip.ring[:, r], io["weights"][bass.ds(i * RING + r, 1)].rearrange("a p t c -> p (a t) c"))\
                        .then_inc(chip.loaded[r], 16)
            for b in range(rounds * RING, chip.n_blocks):
                sp.wait_ge(chip.block_done, b - RING + 1)
                sp.dma_start(chip.ring[:, b % RING], io["weights"][b]).then_inc(chip.loaded[b % RING], 16)

        @block.tensor
        def _(pe):
            for s in stages:
                s.pe(pe)

        @block.scalar
        def _(act):
            link = Link(act, chip.links["act"])
            for s in stages:
                s.act(act, link)

        @block.vector
        def _(dve):
            link = Link(dve, chip.links["dve"])
            for s in stages:
                s.dve(dve, link)

        @block.gpsimd
        def _(pool):
            link = Link(pool, chip.links["pool"])
            for s in stages:
                s.pool(pool, link)
    return chip


def pairs(w):
    k, m = w.shape[0] // P, w.shape[1] // (2 * P)
    return w.reshape(k, P, m, 2, P).transpose(2, 1, 3, 0, 4).reshape(m, P, 2 * k, P)


def rows(w):
    return w.reshape(w.shape[0] // (2 * P), 2, P, KD, P).transpose(0, 2, 1, 3, 4).reshape(-1, P, TPB, P)


def halves(w):
    return w.reshape(KD, P, 2, KF, P).transpose(3, 1, 2, 0, 4).reshape(KF, P, TPB, P)


def wide_blocks(w):
    return w.reshape(2, 4, P, -1, 4, P).transpose(3, 0, 2, 1, 4, 5).reshape(-1, P, TPB, P)


def retention_in(w):
    qk, v, g = w[:, :2 * D], w[:, 2 * D:2 * D + RH * RDV], w[:, 2 * D + RH * RDV:]
    return np.concatenate([pairs(qk), wide_blocks(v), pairs(g)])


def first_weights(i):
    for layer in range(DEPTH):
        yield wide_blocks(i["w_mod"][layer])
        yield halves(i["ffn_w_in"][layer, 0])
        yield rows(i["ffn_w_out"][layer, 0])
        if layer == 0:
            yield rows(i["fnet_w_out"][0])
        else:
            yield retention_in(i["ret_w_in"][0])
            yield rows(i["ret_w_out"][0])
        yield halves(i["ffn_w_in"][layer, 1])
        yield rows(i["ffn_w_out"][layer, 1])


def features(v):
    return np.asarray(v).reshape(-1, P).T


def vector_table(i):
    cond = np.stack([features(i["c"]), features(i["c_ctx"])], axis=2).reshape(P, -1)
    pe = np.concatenate([np.concatenate([i["nsa_pe_k_2"][l].T, i["nsa_pe_v_2"][l].T]) for l in range(DEPTH)], axis=1)
    wide = lambda a: np.broadcast_to(np.asarray(a).reshape(1, -1), (P, np.asarray(a).size))
    sinks = i["swa_sinks_2"]
    parts = {"cond": cond, "b_mod": features(i["b_mod"]), "norm_g": features(i["norm_g"]),
             "final_g": features(i["final_norm_g"]), "ln1": features(i["ln1_w_2"]), "ln2": features(i["ln2_w_2"]),
             "lnf": features(i["lnf_w_2"]), "mu": features(i["rwkv_mu_2"]), "w0": features(i["rwkv_w0_2"]),
             "a0": features(i["rwkv_a0_2"]), "k_k": features(i["rwkv_k_k_2"]), "k_a": features(i["rwkv_k_a_2"]),
             "r_k": features(i["rwkv_r_k_2"]), "ln_w": features(i["rwkv_ln_w_2"]), "ln_b": features(i["rwkv_ln_b_2"]),
             "pe": pe, "decay": wide(i["ret_decay_logit"]), "sinks": wide(sinks)}
    out = np.concatenate([parts[n] for n in VEC], axis=1)
    assert out.shape == (P, NVEC), out.shape
    return np.ascontiguousarray(out, dtype=np.float32)


def constants():
    f = np.float32
    p = np.arange(P)
    cst = np.stack([np.eye(P), np.ones((P, P)), p[:, None] // DH == p[None, :] // DH,
                    np.broadcast_to(p[None, :], (P, P))], axis=1).astype(f)
    a = 2 * np.pi * np.outer(p, p) / P
    dft = np.concatenate([np.cos(a), np.sin(a)], axis=1)
    n = np.arange(N)
    b = 2 * np.pi * np.outer(n, n) / N
    norm = 1 / math.sqrt(N * P)
    cosn, sinn = ((t * norm).reshape(NT, P, N).transpose(1, 0, 2).reshape(P, -1) for t in (np.cos(b), -np.sin(b)))
    perm = np.zeros((P, P))
    perm[p[:64] + 64, p[:64]] = -1
    perm[p[:64], p[:64] + 64] = 1
    freq = np.exp(-f(math.log(10000.0)) * np.arange(64, dtype=f) / f(64)).astype(f)
    ang = [(t.astype(f)[None, :] * np.tile(freq, 2)[:, None]).astype(f) for t in (n // 64, n % 64)]
    cos, sin = (np.concatenate([t(x) for x in ang], axis=1) for t in (np.cos, np.sin))
    m = np.arange(N)[:, None]
    expo = [np.maximum(n - m, 0), np.maximum(m - n, 0), n - m + N, N - n + m]
    expo = np.concatenate([e.reshape(NT, P, N).transpose(1, 0, 2).reshape(P, -1) for e in expo], axis=1)
    cst1 = np.concatenate([dft, cosn, sinn, perm, cos, sin], axis=1).astype(f)
    assert cst1.shape == (P, NCST1)
    return {"cst": cst, "cst1": cst1, "expo": expo, "cst2": second_constants()}


def bias_inputs(table):
    f = np.float32
    d = N - 1 - np.arange(BIASW)
    exact = BUCKETS // 2
    nf = np.maximum(d, exact).astype(f)
    large = exact + (np.log(nf / exact) / f(math.log(MAX_DIST / exact)) * (BUCKETS - exact)).astype(np.int32)
    bucket = np.where(d < exact, np.maximum(d, 0), np.minimum(large, BUCKETS - 1))
    hot = (bucket[None, :] == np.arange(BUCKETS)[:, None]) & (d >= 0)[None, :]
    hot = np.concatenate([hot, (d < 0)[None, :], (d >= SWA_WINDOW)[None, :]]).astype(f)
    masks = np.zeros((2, 16), f)
    masks[0], masks[1, 8:] = NEG, NEG
    left = np.concatenate([table, masks])
    out = np.zeros((P, 16 * P + BIASW), f)
    out[:BUCKETS + 2, :16 * P] = np.broadcast_to(left[:, :, None], (BUCKETS + 2, 16, P)).reshape(BUCKETS + 2, -1)
    out[:BUCKETS + 2, 16 * P:] = hot
    return out


def tokens_last(x):
    return np.asarray(x).reshape(-1, KD, P).transpose(2, 1, 0)


def stream(i):
    total = sum(w.shape[0] for w in _parts(i))
    out = np.zeros((total, P, TPB, P), np.float32)
    b = 0
    for w in _parts(i):
        out[b:b + len(w), :, :w.shape[2], :w.shape[3]] = w
        b += len(w)
    return out


def _parts(i):
    yield from first_weights(i)
    yield from second_weights(i)


def kernel(**inputs):
    import concourse.bacc as bacc
    from concourse.bass_utils import run_bass_kernel_spmd

    i = {k: np.asarray(v) for k, v in inputs.items()}
    arrays = {"x": np.ascontiguousarray(np.concatenate([tokens_last(i["x"]), tokens_last(i["ctx"])], axis=2)),
              "vec": vector_table(i), "bias_in": bias_inputs(i["rel_bias_2"]), "weights": stream(i),
              "keys": np.ascontiguousarray(i["peer_subkeys_2"].reshape(DEPTH, 16, P, P).transpose(0, 3, 1, 2))}
    arrays.update({k: np.ascontiguousarray(v, dtype=np.float32) for k, v in constants().items()})
    nc = bacc.Bacc("TRN2", target_bir_lowering=False, num_devices=1)
    io = {k: nc.dram_tensor(f"in_{k}", v.shape, F32, kind="ExternalInput").ap() for k, v in arrays.items()}
    io["out"] = nc.dram_tensor("out", (P, KD, N), F32, kind="ExternalOutput").ap()
    io["bias_scratch"] = nc.dram_tensor("bias_scratch", (P, 16, BIASW), F32, kind="Internal").ap()
    program(nc, io)
    r = run_bass_kernel_spmd(nc, [{f"in_{k}": v for k, v in arrays.items()}], core_ids=[0])
    return np.ascontiguousarray(r.results[0]["out"].transpose(2, 1, 0).reshape(1, N, D))
```
